# Optimizing a Trainium2 kernel written in Bass

```python
import jax, jax.numpy as jnp
from jax import lax
import numpy as np

D_MODEL = 1024
BATCH = 1
SEQ = 256
DEPTH = 1

CHUNK = 64
EPS = 1e-6
RWKV_HEAD = 64
RWKV_HEADS = 8
RWKV_WIDTH = RWKV_HEADS * RWKV_HEAD
DECAY_LORA = 64
ICLR_LORA = 64
GATE_LORA = 128
GN_EPS = 64e-5
MLSTM_HEADS = 4
MLSTM_DK = 64
MLSTM_DV = 128
MLSTM_QK = MLSTM_HEADS * MLSTM_DK
MLSTM_WIDTH = MLSTM_HEADS * MLSTM_DV
CONV_WIDTH = 4
GATE_SOFTCAP = 15.0
MIX_WIDTH = RWKV_WIDTH + MLSTM_WIDTH
RWKV_COLS = 3 * RWKV_WIDTH + DECAY_LORA + ICLR_LORA + GATE_LORA
MLSTM_COLS = 2 * MLSTM_QK + 2 * MLSTM_WIDTH + 2 * MLSTM_HEADS
IN_COLS = RWKV_COLS + MLSTM_COLS
N_GROUPS = 4
EXPERTS_PER_GROUP = 8
N_EXPERTS = N_GROUPS * EXPERTS_PER_GROUP
TOP_K = 2
D_EXPERT = 256


def rms_norm(x, w):
    xf = x.astype(jnp.float32)
    y = xf * lax.rsqrt(jnp.mean(xf * xf, axis=-1, keepdims=True) + EPS)
    return (y * w.astype(jnp.float32)).astype(x.dtype)

def modulate(xn, shift, scale):
    return xn * (1.0 + scale[:, None, :]) + shift[:, None, :]

def token_shift(u, mu):
    prev = jnp.pad(u, ((0, 0), (1, 0), (0, 0)))[:, :-1]
    return u + (prev - u) * mu

def causal_dwconv(u, w, b):
    ch = u.shape[-1]
    out = lax.conv_general_dilated(
        u, w[:, None, :].astype(u.dtype), window_strides=(1,),
        padding=[(w.shape[0] - 1, 0)], dimension_numbers=('NWC', 'WIO', 'NWC'),
        feature_group_count=ch)
    return out + b

def softcap(z):
    return GATE_SOFTCAP * jnp.tanh(z / GATE_SOFTCAP)

def rwkv7_group(u, mu, w0, w_up, a0, a_up, g_up, k_k, k_a, r_k, gn_w, gn_b):
    bsz, seq, _ = u.shape
    f32 = jnp.float32
    u = token_shift(u, mu)
    o1 = RWKV_WIDTH
    o2 = 2 * RWKV_WIDTH
    o3 = 3 * RWKV_WIDTH
    o4 = o3 + DECAY_LORA
    o5 = o4 + ICLR_LORA
    r, k, v, wd, ad, gd = jnp.split(u, [o1, o2, o3, o4, o5], axis=-1)
    w_log = -jax.nn.softplus(-(w0 + jnp.tanh(wd) @ w_up)) - 0.5
    decay = jnp.exp(-jnp.exp(w_log.astype(f32)))
    a = jax.nn.sigmoid(a0 + ad @ a_up)
    g = jax.nn.sigmoid(gd) @ g_up
    heads = lambda t: t.reshape(bsz, seq, RWKV_HEADS, RWKV_HEAD).astype(f32)
    kk = heads(k * k_k)
    kk = kk / jnp.maximum(jnp.sqrt(jnp.sum(kk * kk, axis=-1, keepdims=True)), 1e-12)
    k = k * (1.0 + (a - 1.0) * k_a)
    r_h, k_h, v_h, w_h, a_h = heads(r), heads(k), heads(v), heads(decay), heads(a)
    b_h = kk * a_h

    def step(state, inp):
        r_t, w_t, k_t, v_t, kk_t, b_t = inp
        sa = jnp.einsum('bhij,bhj->bhi', state, -kk_t)
        state = (state * w_t[:, :, None, :] + sa[..., None] * b_t[:, :, None, :]
                 + v_t[..., None] * k_t[:, :, None, :])
        return state, jnp.einsum('bhij,bhj->bhi', state, r_t)

    xs = tuple(jnp.swapaxes(t, 0, 1) for t in (r_h, w_h, k_h, v_h, kk, b_h))
    state0 = jnp.zeros((bsz, RWKV_HEADS, RWKV_HEAD, RWKV_HEAD), f32)
    _, y = lax.scan(step, state0, xs)
    y = jnp.swapaxes(y, 0, 1)
    mean = jnp.mean(y, axis=-1, keepdims=True)
    var = jnp.mean(jnp.square(y - mean), axis=-1, keepdims=True)
    y = (y - mean) * lax.rsqrt(var + GN_EPS)
    y = y.reshape(bsz, seq, RWKV_WIDTH) * gn_w + gn_b
    bonus = jnp.sum(r_h * k_h * r_k.astype(f32), axis=-1, keepdims=True) * v_h
    y = (y + bonus.reshape(bsz, seq, RWKV_WIDTH)) * g
    return y.astype(u.dtype)

def to_chunks(t):
    bsz, seq, nh = t.shape[:3]
    t = t.reshape((bsz, seq // CHUNK, CHUNK, nh) + t.shape[3:])
    return t.transpose((1, 0, 3, 2) + tuple(range(4, t.ndim)))

def mlstm_chunkwise(q, k, v, log_i, log_f):
    bsz, seq = q.shape[:2]
    f32 = jnp.float32
    causal = jnp.tril(jnp.ones((CHUNK, CHUNK), dtype=bool))

    def step(carry, inp):
        c_mat, n_vec, m = carry
        qc, kc, vc, li, lf = inp
        b = jnp.cumsum(lf, axis=-1)
        d_mat = jnp.where(causal, b[..., :, None] - b[..., None, :] + li[..., None, :], -jnp.inf)
        inter = b + m[..., None]
        m_t = jnp.maximum(inter, jnp.max(d_mat, axis=-1))
        scores = jnp.einsum('bhtd,bhsd->bhts', qc, kc) * jnp.exp(d_mat - m_t[..., None])
        w_inter = jnp.exp(inter - m_t)
        num = (jnp.einsum('bhts,bhsv->bhtv', scores, vc)
               + w_inter[..., None] * jnp.einsum('bhtd,bhdv->bhtv', qc, c_mat))
        den = jnp.sum(scores, axis=-1) + w_inter * jnp.einsum('bhtd,bhd->bht', qc, n_vec)
        h = num / jnp.maximum(jnp.abs(den), jnp.exp(-m_t))[..., None]
        end_log = b[..., -1:] - b + li
        m_new = jnp.maximum(b[..., -1] + m, jnp.max(end_log, axis=-1))
        carry_w = jnp.exp(b[..., -1] + m - m_new)
        kw = kc * jnp.exp(end_log - m_new[..., None])[..., None]
        c_mat = carry_w[..., None, None] * c_mat + jnp.einsum('bhsd,bhsv->bhdv', kw, vc)
        n_vec = carry_w[..., None] * n_vec + jnp.sum(kw, axis=-2)
        return (c_mat, n_vec, m_new), h

    carry0 = (jnp.zeros((bsz, MLSTM_HEADS, MLSTM_DK, MLSTM_DV), f32),
              jnp.zeros((bsz, MLSTM_HEADS, MLSTM_DK), f32),
              jnp.zeros((bsz, MLSTM_HEADS), f32))
    xs = (to_chunks(q * (MLSTM_DK ** -0.5)), to_chunks(k), to_chunks(v),
          to_chunks(log_i), to_chunks(log_f))
    _, h = lax.scan(step, carry0, xs)
    return h.transpose(1, 0, 3, 2, 4).reshape(bsz, seq, MLSTM_HEADS, MLSTM_DV)

def mlstm_group(u, conv_w, conv_b, i_b, f_b, hn_w):
    bsz, seq, _ = u.shape
    f32 = jnp.float32
    o1 = 2 * MLSTM_QK
    o2 = o1 + MLSTM_WIDTH
    o3 = o2 + MLSTM_WIDTH
    o4 = o3 + MLSTM_HEADS
    qk, v, o, ig, fg = jnp.split(u, [o1, o2, o3, o4], axis=-1)
    qk = jax.nn.silu(causal_dwconv(qk, conv_w, conv_b))
    q, k = jnp.split(qk, 2, axis=-1)
    log_i = softcap((ig + i_b).astype(f32))
    log_f = jax.nn.log_sigmoid(softcap((fg + f_b).astype(f32)))
    heads_k = lambda t: t.reshape(bsz, seq, MLSTM_HEADS, MLSTM_DK).astype(f32)
    h = mlstm_chunkwise(heads_k(q), heads_k(k),
                        v.reshape(bsz, seq, MLSTM_HEADS, MLSTM_DV).astype(f32), log_i, log_f)
    h = h * lax.rsqrt(jnp.mean(h * h, axis=-1, keepdims=True) + EPS)
    h = h.reshape(bsz, seq, MLSTM_WIDTH) * hn_w
    return (h * jax.nn.sigmoid(o.astype(f32))).astype(u.dtype)

def hier_moe(xn, w_group, b_group, w_router, b_router, w_gate, w_up, w_down):
    bsz, seq, _ = xn.shape
    f32 = jnp.float32
    g_logits = (xn @ w_group + b_group).astype(f32)
    g_prob = jax.nn.softmax(g_logits, axis=-1)
    g_idx = jnp.argmax(g_logits, axis=-1)
    g_onehot = jax.nn.one_hot(g_idx, N_GROUPS, dtype=f32)
    g_w = jnp.max(g_prob, axis=-1)
    e_logits = (xn @ w_router + b_router).astype(f32).reshape(bsz, seq, N_GROUPS, EXPERTS_PER_GROUP)
    sel = jnp.sum(e_logits * g_onehot[..., None], axis=2)
    top_v, top_i = lax.top_k(sel, TOP_K)
    top_w = jax.nn.softmax(top_v, axis=-1)
    within = jnp.sum(jax.nn.one_hot(top_i, EXPERTS_PER_GROUP, dtype=f32) * top_w[..., None], axis=-2)
    combine = (g_onehot[..., None] * within[..., None, :] * g_w[..., None, None])
    combine = combine.reshape(bsz, seq, N_EXPERTS).astype(xn.dtype)

    def per_sequence(args):
        xs, cw = args
        hg = jnp.einsum('sd,edf->sef', xs, w_gate)
        hu = jnp.einsum('sd,edf->sef', xs, w_up)
        act = jax.nn.silu(hg) * hu * cw[..., None]
        return jnp.einsum('sef,efd->sd', act, w_down)

    return lax.map(per_sequence, (xn, combine))

def first_inputs(seed: int = 0) -> dict:
    key = jax.random.key(seed)
    ks = jax.random.split(key, 32)
    L, D = DEPTH, D_MODEL

    def nrm(i, shape, scale):
        return scale * jax.random.normal(ks[i], shape, jnp.float32)

    def uni(i, shape, lo, hi):
        return jax.random.uniform(ks[i], shape, jnp.float32, lo, hi)

    return {
        'x': nrm(0, (BATCH, SEQ, D), 1.0),
        'c': nrm(1, (BATCH, D), 1.0),
        'ada_w': nrm(2, (L, D, 6 * D), 0.5 * D ** -0.5),
        'ada_b': nrm(3, (L, 6 * D), 0.01),
        'mix_norm_w': 1.0 + nrm(4, (L, D), 0.02),
        'w_in': nrm(5, (L, D, IN_COLS), D ** -0.5),
        'rwkv_mu': uni(6, (L, RWKV_COLS), 0.0, 1.0),
        'rwkv_w0': uni(7, (L, RWKV_WIDTH), -4.0, 0.0),
        'rwkv_w_up': nrm(8, (L, DECAY_LORA, RWKV_WIDTH), DECAY_LORA ** -0.5),
        'rwkv_a0': nrm(9, (L, RWKV_WIDTH), 0.5),
        'rwkv_a_up': nrm(10, (L, ICLR_LORA, RWKV_WIDTH), ICLR_LORA ** -0.5),
        'rwkv_g_up': nrm(11, (L, GATE_LORA, RWKV_WIDTH), GATE_LORA ** -0.5),
        'rwkv_k_k': 0.85 + nrm(12, (L, RWKV_WIDTH), 0.05),
        'rwkv_k_a': 1.0 + nrm(13, (L, RWKV_WIDTH), 0.05),
        'rwkv_r_k': nrm(14, (L, RWKV_HEADS, RWKV_HEAD), 0.1),
        'rwkv_gn_w': 1.0 + nrm(15, (L, RWKV_WIDTH), 0.02),
        'rwkv_gn_b': nrm(16, (L, RWKV_WIDTH), 0.01),
        'mlstm_conv_w': nrm(17, (L, CONV_WIDTH, 2 * MLSTM_QK), CONV_WIDTH ** -0.5),
        'mlstm_conv_b': nrm(18, (L, 2 * MLSTM_QK), 0.01),
        'mlstm_i_b': -3.0 + nrm(19, (L, MLSTM_HEADS), 0.1),
        'mlstm_f_b': jnp.linspace(3.0, 6.0, MLSTM_HEADS, dtype=jnp.float32)[None, :] + nrm(20, (L, MLSTM_HEADS), 0.1),
        'mlstm_hn_w': 1.0 + nrm(21, (L, MLSTM_WIDTH), 0.02),
        'w_out': nrm(22, (L, MIX_WIDTH, D), MIX_WIDTH ** -0.5),
        'ffn_norm_w': 1.0 + nrm(23, (L, D), 0.02),
        'moe_w_group': nrm(24, (L, D, N_GROUPS), D ** -0.5),
        'moe_b_group': nrm(25, (L, N_GROUPS), 0.01),
        'moe_w_router': nrm(26, (L, D, N_EXPERTS), D ** -0.5),
        'moe_b_router': nrm(27, (L, N_EXPERTS), 0.01),
        'moe_w_gate': nrm(28, (L, N_EXPERTS, D, D_EXPERT), D ** -0.5),
        'moe_w_up': nrm(29, (L, N_EXPERTS, D, D_EXPERT), D ** -0.5),
        'moe_w_down': nrm(30, (L, N_EXPERTS, D_EXPERT, D), D_EXPERT ** -0.5),
        'final_norm_w': 1.0 + nrm(31, (D,), 0.02),
    }

def first_block(x, c, ada_w, ada_b, mix_norm_w, w_in, rwkv_mu, rwkv_w0, rwkv_w_up, rwkv_a0,
              rwkv_a_up, rwkv_g_up, rwkv_k_k, rwkv_k_a, rwkv_r_k, rwkv_gn_w, rwkv_gn_b,
              mlstm_conv_w, mlstm_conv_b, mlstm_i_b, mlstm_f_b, mlstm_hn_w, w_out, ffn_norm_w,
              moe_w_group, moe_b_group, moe_w_router, moe_b_router, moe_w_gate, moe_w_up,
              moe_w_down, final_norm_w):
    for l in range(DEPTH):
        mod = jax.nn.silu(c) @ ada_w[l] + ada_b[l]
        sh_m, sc_m, g_m, sh_f, sc_f, g_f = jnp.split(mod, 6, axis=-1)
        h = modulate(rms_norm(x, mix_norm_w[l]), sh_m, sc_m)
        proj = h @ w_in[l]
        y_r = rwkv7_group(proj[..., :RWKV_COLS], rwkv_mu[l], rwkv_w0[l], rwkv_w_up[l], rwkv_a0[l],
                          rwkv_a_up[l], rwkv_g_up[l], rwkv_k_k[l], rwkv_k_a[l], rwkv_r_k[l],
                          rwkv_gn_w[l], rwkv_gn_b[l])
        y_m = mlstm_group(proj[..., RWKV_COLS:], mlstm_conv_w[l], mlstm_conv_b[l], mlstm_i_b[l],
                          mlstm_f_b[l], mlstm_hn_w[l])
        y = jnp.concatenate([y_r, y_m], axis=-1) @ w_out[l]
        x = x + g_m[:, None, :] * y
        h = modulate(rms_norm(x, ffn_norm_w[l]), sh_f, sc_f)
        y = hier_moe(h, moe_w_group[l], moe_b_group[l], moe_w_router[l], moe_b_router[l],
                     moe_w_gate[l], moe_w_up[l], moe_w_down[l])
        x = x + g_f[:, None, :] * y
    return rms_norm(x, final_norm_w)


DEPTH_2 = 2

N_EVEN = (DEPTH_2 + 1) // 2
N_ODD = DEPTH_2 // 2

GLA_HEADS = 4
GLA_DK = 64
GLA_DV = 128
GLA_RANK = 16
GLA_TAU = 16.0
GLA_CHUNK = 64
GLA_QK = GLA_HEADS * GLA_DK
GLA_V = GLA_HEADS * GLA_DV

SWA_HEADS = 8
SWA_KV_HEADS = 2
SWA_HEAD_DIM = 64
SWA_GROUP = SWA_HEADS // SWA_KV_HEADS
WINDOW = 128
SWA_BLOCK = 128
SWA_Q = SWA_HEADS * SWA_HEAD_DIM
SWA_KV = SWA_KV_HEADS * SWA_HEAD_DIM

N_BUCKETS = 32
MAX_DISTANCE = 128

IN_SPLITS = (GLA_QK, GLA_QK, GLA_V, GLA_V, GLA_RANK, SWA_Q, SWA_KV, SWA_KV)
IN_COLS_2 = GLA_QK + GLA_QK + GLA_V + GLA_V + GLA_RANK + SWA_Q + SWA_KV + SWA_KV
MIX_OUT = GLA_V + SWA_Q

POOL_WINDOWS = (2, 4, 8, 16)
POOL_GROUP = D_MODEL // 4

D_FF = 4 * D_MODEL


def rms_norm_2(x, w):
    xf = x.astype(jnp.float32)
    y = xf * lax.rsqrt(jnp.mean(xf * xf, axis=-1, keepdims=True) + EPS)
    return (y * w.astype(jnp.float32)).astype(x.dtype)

def ada_modulation(c, w, b):
    mod = jax.nn.silu(c) @ w + b
    shift, scale, gate = jnp.split(mod, 3, axis=-1)
    return shift[:, None], scale[:, None], gate[:, None]

def t5_bucket(dist):
    max_exact = N_BUCKETS // 2
    d = np.maximum(dist, 1).astype(np.float64)
    large = max_exact + (np.log(d / max_exact) / np.log(MAX_DISTANCE / max_exact)
                         * (N_BUCKETS - max_exact)).astype(np.int32)
    large = np.minimum(large, N_BUCKETS - 1)
    return np.where(dist < max_exact, dist, large).astype(np.int32)

def gla_chunked(q, k, v, log_a):
    B, S, H, dk = q.shape
    dv = v.shape[-1]
    C = GLA_CHUNK
    nc = S // C
    f32 = jnp.float32
    qf = (q.astype(f32) * dk ** -0.5).reshape(B, nc, C, H, dk)
    kf = k.astype(f32).reshape(B, nc, C, H, dk)
    vf = v.astype(f32).reshape(B, nc, C, H, dv)
    b = jnp.cumsum(log_a.reshape(B, nc, C, H, dk), axis=2)
    b_last = b[:, :, -1]
    q_t = qf * jnp.exp(b)
    k_t = kf * jnp.exp(-b)
    k_end = kf * jnp.exp(b_last[:, :, None] - b)
    causal = jnp.tril(jnp.ones((C, C), dtype=bool))
    a = jnp.einsum('bnihd,bnjhd->bnhij', q_t, k_t)
    a = jnp.where(causal, a, 0.0)
    o_intra = jnp.einsum('bnhij,bnjhe->bnihe', a, vf)
    d_state = jnp.einsum('bnjhd,bnjhe->bnhde', k_end, vf)
    decay = jnp.exp(b_last)

    def step(s_prev, inp):
        ds, dec = inp
        return dec[..., None] * s_prev + ds, s_prev

    _, s_in = lax.scan(step, jnp.zeros((B, H, dk, dv), f32),
                       (jnp.moveaxis(d_state, 1, 0), jnp.moveaxis(decay, 1, 0)))
    s_in = jnp.moveaxis(s_in, 0, 1)
    o_inter = jnp.einsum('bnihd,bnhde->bnihe', q_t, s_in)
    return (o_intra + o_inter).reshape(B, S, H, dv)

def sliding_window_attention(q, k, v, rel_bias, sinks):
    B, S = q.shape[0], q.shape[1]
    nb = S // SWA_BLOCK
    L = SWA_BLOCK
    f32 = jnp.float32
    qb = q.reshape(B, nb, L, SWA_KV_HEADS, SWA_GROUP, SWA_HEAD_DIM)

    def band(t):
        tb = t.reshape(B, nb, L, SWA_KV_HEADS, SWA_HEAD_DIM)
        prev = jnp.pad(tb, ((0, 0), (1, 0), (0, 0), (0, 0), (0, 0)))[:, :-1]
        return jnp.concatenate([prev, tb], axis=2)

    kb, vb = band(k), band(v)
    s = jnp.einsum('bnqhgd,bnkhd->bnhgqk', qb, kb,
                   preferred_element_type=f32) * (SWA_HEAD_DIM ** -0.5)
    qi = np.arange(L)[:, None] + L
    kj = np.arange(2 * L)[None, :]
    dist = qi - kj
    valid = (dist >= 0) & (dist < WINDOW)
    bucket = t5_bucket(np.maximum(dist, 0))
    bias = jnp.transpose(rel_bias[jnp.asarray(bucket)].astype(f32), (2, 0, 1))
    s = s + bias.reshape(SWA_KV_HEADS, SWA_GROUP, L, 2 * L)
    blk_ok = (np.arange(nb)[:, None, None] > 0) | (np.arange(2 * L)[None, None, :] >= L)
    mask = valid[None] & blk_ok
    s = jnp.where(jnp.asarray(mask)[None, :, None, None], s, -1e30)
    sink = sinks.astype(f32).reshape(SWA_KV_HEADS, SWA_GROUP)[None, None, :, :, None, None]
    m = jnp.maximum(jnp.max(s, axis=-1, keepdims=True), sink)
    p = jnp.exp(s - m)
    p = p / (jnp.sum(p, axis=-1, keepdims=True) + jnp.exp(sink - m))
    o = jnp.einsum('bnhgqk,bnkhd->bnqhgd', p, vb.astype(f32))
    return o.reshape(B, S, SWA_Q).astype(q.dtype)

def hybrid_attention_mixer(h, w_in, gla_w_gate, gla_b_gate, gla_norm_w, sinks, rel_bias, w_out):
    B, S, _ = h.shape
    proj = h @ w_in
    offs = np.cumsum(IN_SPLITS)[:-1].tolist()
    gq, gk, gv, gg, glr, sq, sk, sv = jnp.split(proj, offs, axis=-1)
    gate_logits = (glr @ gla_w_gate + gla_b_gate).astype(jnp.float32)
    log_a = (jax.nn.log_sigmoid(gate_logits) / GLA_TAU).reshape(B, S, GLA_HEADS, GLA_DK)
    o_gla = gla_chunked(gq.reshape(B, S, GLA_HEADS, GLA_DK), gk.reshape(B, S, GLA_HEADS, GLA_DK),
                        gv.reshape(B, S, GLA_HEADS, GLA_DV), log_a).astype(h.dtype)
    o_gla = rms_norm_2(o_gla, gla_norm_w) * jax.nn.silu(gg.reshape(B, S, GLA_HEADS, GLA_DV))
    o_gla = o_gla.reshape(B, S, GLA_V)
    o_swa = sliding_window_attention(sq.reshape(B, S, SWA_HEADS, SWA_HEAD_DIM),
                                     sk.reshape(B, S, SWA_KV_HEADS, SWA_HEAD_DIM),
                                     sv.reshape(B, S, SWA_KV_HEADS, SWA_HEAD_DIM), rel_bias, sinks)
    return jnp.concatenate([o_gla, o_swa], axis=-1) @ w_out

def multiscale_pool_mixer(h, pool_w, pool_scale):
    B, S, _ = h.shape
    hf = h.astype(jnp.float32)
    cs = jnp.cumsum(hf, axis=1)
    t = jnp.arange(S)
    outs = []
    for gi, w in enumerate(POOL_WINDOWS):
        lo, hi = gi * POOL_GROUP, (gi + 1) * POOL_GROUP
        csg = cs[..., lo:hi]
        lag = jnp.pad(csg, ((0, 0), (w, 0), (0, 0)))[:, :S]
        cnt = jnp.minimum(t + 1, w).astype(jnp.float32)[None, :, None]
        pooled = (csg - lag) / cnt - hf[..., lo:hi]
        outs.append(pooled.astype(h.dtype) @ pool_w[gi])
    return jnp.concatenate(outs, axis=-1) * pool_scale

def squared_relu_mlp(h, w1, w2):
    return jnp.square(jax.nn.relu(h @ w1)) @ w2

def second_inputs(seed: int = 0) -> dict:
    key = jax.random.key(seed)
    ks = jax.random.split(key, 17)
    f32 = jnp.float32
    nrm = lambda k, s: jax.random.normal(k, s, f32)
    return {
        "x": nrm(ks[0], (BATCH, SEQ, D_MODEL)),
        "c": nrm(ks[1], (BATCH, D_MODEL)),
        "norm_w": 1.0 + 0.05 * nrm(ks[2], (DEPTH_2, 2, D_MODEL)),
        "ada_w": nrm(ks[3], (DEPTH_2, 2, D_MODEL, 3 * D_MODEL)) * (0.5 * D_MODEL ** -0.5),
        "ada_b": 0.01 * nrm(ks[4], (DEPTH_2, 2, 3 * D_MODEL)),
        "attn_w_in": nrm(ks[5], (N_EVEN, D_MODEL, IN_COLS_2)) * D_MODEL ** -0.5,
        "gla_w_gate": nrm(ks[6], (N_EVEN, GLA_RANK, GLA_QK)) * GLA_RANK ** -0.5,
        "gla_b_gate": 0.1 * nrm(ks[7], (N_EVEN, GLA_QK)),
        "gla_norm_w": 1.0 + 0.05 * nrm(ks[8], (N_EVEN, GLA_DV)),
        "attn_sinks": 0.5 * nrm(ks[9], (N_EVEN, SWA_HEADS)),
        "attn_w_out": nrm(ks[10], (N_EVEN, MIX_OUT, D_MODEL)) * MIX_OUT ** -0.5,
        "rel_bias": 0.5 * nrm(ks[11], (N_BUCKETS, SWA_HEADS)),
        "pool_w": nrm(ks[12], (N_ODD, 4, POOL_GROUP, POOL_GROUP)) * POOL_GROUP ** -0.5,
        "pool_scale": 1.0 + 0.1 * nrm(ks[13], (N_ODD, D_MODEL)),
        "mlp_w1": nrm(ks[14], (DEPTH_2, D_MODEL, D_FF)) * D_MODEL ** -0.5,
        "mlp_w2": nrm(ks[15], (DEPTH_2, D_FF, D_MODEL)) * D_FF ** -0.5,
        "final_norm_w": 1.0 + 0.05 * nrm(ks[16], (D_MODEL,)),
    }

def second_block(x, c, norm_w, ada_w, ada_b, attn_w_in, gla_w_gate, gla_b_gate, gla_norm_w,
              attn_sinks, attn_w_out, rel_bias, pool_w, pool_scale, mlp_w1, mlp_w2, final_norm_w):
    for layer in range(DEPTH_2):
        i = layer // 2
        shift, scale, gate = ada_modulation(c, ada_w[layer, 0], ada_b[layer, 0])
        h = rms_norm_2(x, norm_w[layer, 0]) * (1.0 + scale) + shift
        if layer % 2 == 0:
            y = hybrid_attention_mixer(h, attn_w_in[i], gla_w_gate[i], gla_b_gate[i], gla_norm_w[i],
                                       attn_sinks[i], rel_bias, attn_w_out[i])
        else:
            y = multiscale_pool_mixer(h, pool_w[i], pool_scale[i])
        x = x + (gate * y).astype(x.dtype)
        shift, scale, gate = ada_modulation(c, ada_w[layer, 1], ada_b[layer, 1])
        h = rms_norm_2(x, norm_w[layer, 1]) * (1.0 + scale) + shift
        x = x + (gate * squared_relu_mlp(h, mlp_w1[layer], mlp_w2[layer])).astype(x.dtype)
    return rms_norm_2(x, final_norm_w)


def setup_inputs(seed=0):
    out = dict(first_inputs(seed))
    for name, value in second_inputs(seed + 1).items():
        if name != "x":
            out[name + "_2"] = value
    return out


def reference(
    x, c, ada_w, ada_b, mix_norm_w, w_in, rwkv_mu, rwkv_w0, rwkv_w_up, rwkv_a0, rwkv_a_up,
    rwkv_g_up, rwkv_k_k, rwkv_k_a, rwkv_r_k, rwkv_gn_w, rwkv_gn_b, mlstm_conv_w, mlstm_conv_b,
    mlstm_i_b, mlstm_f_b, mlstm_hn_w, w_out, ffn_norm_w, moe_w_group, moe_b_group, moe_w_router,
    moe_b_router, moe_w_gate, moe_w_up, moe_w_down, final_norm_w, c_2, norm_w_2, ada_w_2,
    ada_b_2, attn_w_in_2, gla_w_gate_2, gla_b_gate_2, gla_norm_w_2, attn_sinks_2, attn_w_out_2,
    rel_bias_2, pool_w_2, pool_scale_2, mlp_w1_2, mlp_w2_2, final_norm_w_2,
):
    x = first_block(
        x, c, ada_w, ada_b, mix_norm_w, w_in, rwkv_mu, rwkv_w0, rwkv_w_up, rwkv_a0, rwkv_a_up,
        rwkv_g_up, rwkv_k_k, rwkv_k_a, rwkv_r_k, rwkv_gn_w, rwkv_gn_b, mlstm_conv_w,
        mlstm_conv_b, mlstm_i_b, mlstm_f_b, mlstm_hn_w, w_out, ffn_norm_w, moe_w_group,
        moe_b_group, moe_w_router, moe_b_router, moe_w_gate, moe_w_up, moe_w_down, final_norm_w,
    )
    return second_block(
        x, c_2, norm_w_2, ada_w_2, ada_b_2, attn_w_in_2, gla_w_gate_2, gla_b_gate_2,
        gla_norm_w_2, attn_sinks_2, attn_w_out_2, rel_bias_2, pool_w_2, pool_scale_2, mlp_w1_2,
        mlp_w2_2, final_norm_w_2,
    )


_drawn_inputs = setup_inputs


def setup_inputs(seed=0):
    import zlib

    import numpy as np

    out = dict(_drawn_inputs(seed))
    spreads = {}
    factors = {'ada_b': 4.535,
     'mix_norm_w': 8.0,
     'rwkv_w_up': 25.304,
     'rwkv_k_k': 200.0,
     'rwkv_k_a': 4.478,
     'rwkv_gn_w': 64.0,
     'rwkv_gn_b': 200.0,
     'mlstm_conv_b': 200.0,
     'mlstm_i_b': 64.0,
     'mlstm_hn_w': 64.0,
     'ffn_norm_w': 34.528,
     'moe_b_group': 64.0,
     'moe_b_router': 64.0,
     'final_norm_w': 2.718,
     'gla_b_gate_2': 8.0,
     'gla_norm_w_2': 23.933,
     'attn_sinks_2': 200.0,
     'rwkv_w0': 8.0,
     'mlstm_conv_w': 8.0,
     'mlstm_f_b': 8.0,
     'ada_b_2': 2.956,
     'rel_bias_2': 20.594,
     'pool_scale_2': 5.947}
    for name, (base, spread) in spreads.items():
        noise = np.random.default_rng([zlib.crc32(name.encode()), seed]).standard_normal(out[name].shape)
        drawn = base * np.exp(spread * noise) if base else spread * noise
        out[name] = __import__('jax').numpy.asarray(drawn.astype(out[name].dtype))
    for name, factor in factors.items():
        out[name] = (out[name] * factor).astype(out[name].dtype)
    return out
```

```python
from contextlib import ExitStack

import concourse.bass as bass
from concourse import mybir

F32 = mybir.dt.float32
BF16 = mybir.dt.bfloat16
ALU = mybir.AluOpType
ACT = mybir.ActivationFunctionType
AX_X = mybir.AxisListType.X

P = 128
D = 1024
SEQ = 256
TT = SEQ // P
KT = D // P
CH = 64
NC = SEQ // CH
EPS = 1e-6
GN_EPS = 64e-5
DECAY = 0.6065306597126334
RW_TILES = 14
IN_SLOTS = 13
NE = 32
FE = 256
SLOT = 2048
RING = 8
CAP = 15.0
NG, EG = 4, 8
E_BODY = 8
FF_SLOTS = 4
GLA_H, GLA_DV = 4, 128
SWA_H = 8
N_BUCKETS, MAX_DIST, WINDOW = 32, 128, 128
BIG = -1e30

STEP = {
    "c.ident": 7, "c.zeros": 16, "c.masks": 39, "n.rstd": 1, "m.rs": 1, "r.zero": 5, "y.rs": 1, "y.free": 4,
    "q.rstd": 1, "f.rstd": 1, "bn.rstd": 1, "bp.zero": 3, "bg.rs": 1, "l0.rstd": 1, "pn.rstd": 1, "pp.zero":
    9, "l1.rstd": 1, "z.rstd": 1, "c.sig": 1, "n.sq": 2, "n.a": 6, "w.a": 13, "w.tanh": 15, "m.sig": 1,
    "m.lf": 3, "m.exp": 5, "r.u": 2, "r.sig": 10, "r.gtok": 11, "r.exp": 13, "r.sqrt": 14, "r.pad": 18,
    "r.tok": 21, "i.a": 40, "o.hT": 4, "q.sq": 2, "q.a": 6, "e.expg": 1, "e.expd": 2, "e.bias": 10, "f.sq": 2,
    "bn.sq": 2, "bn.a": 6, "bp.a": 13, "bg.glr": 1, "bg.zb": 3, "bg.ln": 6, "bg.exp": 8, "bg.pad": 10,
    "bg.ket": 11, "bs.exp": 2, "bs.pt": 8, "bo.hT": 4, "l0.sq": 2, "l0.a": 6, "pn.sq": 2, "pn.a": 6, "l1.sq":
    2, "l1.a": 6, "z.sq": 2, "n.ss": 1, "n.xn": 3, "n.mod": 6, "n.v": 10, "w.prmc": 1, "w.gb": 2, "w.pre": 2,
    "w.shift": 23, "w.gate2": 24, "w.gate5": 25, "w.mod": 28, "m.conv": 16, "m.qk": 17, "m.rows": 23, "m.z":
    32, "m.pt": 38, "m.ss": 48, "m.y": 52, "r.sq": 2, "r.scan": 7, "r.rkp": 11, "r.bh": 20, "r.bend": 23,
    "r.bon": 24, "i.done": 56, "y.var": 10, "y.done": 17, "o.x": 8, "q.ss": 1, "q.xn": 3, "q.mod": 3, "q.v":
    7, "e.g": 3, "e.d": 21, "e.cw": 30, "e.relx0": 31, "f.moe": 8, "f.ss": 9, "f.x": 11, "f.mod": 19, "bn.ss":
    1, "bn.xn": 3, "bn.mod": 3, "bn.v": 7, "bg.scan": 4, "bg.kt": 6, "bg.kend": 8, "bg.at": 10, "bg.state":
    22, "bg.ss": 26, "bg.y": 31, "bs.sub": 14, "bs.den": 18, "bs.y": 20, "bo.x": 8, "l0.ss": 1, "l0.xn": 3,
    "l0.mod": 3, "l0.v": 7, "l0.x": 15, "pn.ss": 1, "pn.xn": 3, "pn.mod": 3, "pn.v": 7, "pp.h": 14, "pp.x":
    23, "l1.ss": 1, "l1.xn": 3, "l1.mod": 3, "l1.v": 7, "l1.x": 15, "z.ss": 1, "z.out0": 2, "n.t": 4, "w.prm":
    1, "w.if": 2, "m.bc": 1, "m.sc": 2, "m.num": 3, "r.wa": 1, "r.n2": 2, "r.bonus": 3, "r.tr": 6, "q.t": 4,
    "e.rt": 1, "e.bias0": 2, "bn.t": 4, "bg.lr": 1, "bg.z": 2, "bg.at0": 3, "bg.tr": 5, "bg.ds": 6, "bg.o": 7,
    "bs.s0": 1, "bs.pt0": 7, "bs.o": 13, "l0.t": 4, "pn.t": 4, "pp.mm": 1, "l1.t": 4,
}


class Counter:

    def __init__(self, eng, sem, n=0):
        self.eng, self.sem, self.n = eng, sem, n

    def link(self, ins):
        self.n += 1
        ins.then_inc(self.sem, 1)
        self.eng.wait_ge(self.sem, self.n)

    def mark(self, ins):
        self.n += 1
        ins.then_inc(self.sem, 1)

    def at(self, name):
        assert STEP[name] == self.n, (name, self.n)


def program(nc, A, out):
    ctx = ExitStack()
    with ctx:
        def sb(name, shape, dt=F32):
            return ctx.enter_context(nc.sbuf_tensor(name, shape, dt))

        def sem(name):
            return ctx.enter_context(nc.semaphore(name))

        ps = ctx.enter_context(nc.psum_tensor("ps", [P, 8, 512], F32))

        x_sb = sb("x_sb", [P, TT, D])
        hT = sb("hT", [P, KT, SEQ])
        ring = sb("ring", [P, RING, SLOT])
        macc = sb("macc", [P, 3, D])
        gate1 = sb("gate1", [P, 2, D])
        KB = 256
        arena = sb("arena", [P, 91 * KB])

        def area(kb, words):
            return arena[:, int(kb * KB):int(kb * KB) + words]

        u = area(0, 14 * 256).rearrange("p (i t) -> p i t", t=SEQ)
        grb = area(0, 16 * 128).rearrange("p (g h s) -> p g h s", g=4, h=4)
        lakv = area(8, 1024).rearrange("p (a n) -> p a n", a=TT)
        ar = area(14, 2048).rearrange("p (i k t) -> p i k t", i=4, k=2)
        bhz = area(22, 2048).rearrange("p (h t) -> p h t", h=8)
        khz = area(30, 2048).rearrange("p (h t) -> p h t", h=8)
        vtok = area(38, 1024).rearrange("p (a n) -> p a n", a=TT)
        bend_t = area(42, 1024).rearrange("p (a n) -> p a n", a=TT)
        kend_t = area(46, 1024).rearrange("p (a n) -> p a n", a=TT)
        convraw = area(42, 4 * 259).rearrange("p (i t) -> p i t", i=4)
        rbuf = area(50, 1024).rearrange("p (a n) -> p a n", a=TT)
        ubuf = area(54, 1024).rearrange("p (a n) -> p a n", a=TT)
        xn = area(50, 2048).rearrange("p (a n) -> p a n", a=TT)
        state = area(58, 2048).rearrange("p (c i v) -> p c i v", c=4, i=4)
        raw = area(58, 4 * 257).rearrange("p (b i t) -> p b i t", b=2, i=2)
        gtok = area(66, 1024).rearrange("p (a n) -> p a n", a=TT)
        ytok = area(70, 2048).rearrange("p (a n) -> p a n", a=TT)
        qk = area(78, 1024).rearrange("p (i t) -> p i t", i=4)
        vm = area(82, 1024).rearrange("p (a n) -> p a n", a=TT)
        om = area(87, 1024).rearrange("p (a n) -> p a n", a=TT)
        grk = hT[:, :, :].rearrange("p k t -> p (k t)").rearrange("p (g h s) -> p g h s", g=4, h=4)
        dtmp = sb("dtmp", [P, 512])

        ident = sb("ident", [P, P])
        ones = sb("ones", [P, P])
        headblk = sb("headblk", [P, P])
        headsel = sb("headsel", [P, 2])
        masks = sb("masks", [P, 7, P])
        same16, same32, same64 = masks[:, 0, :], masks[:, 1, :], masks[:, 2, :]
        m_n16t, m_n16 = masks[:, 3, :], masks[:, 0, :]
        m_32, m_64 = masks[:, 1, :], masks[:, 4, :]
        m_ak, m_rb, m_causal = masks[:, 5, :], masks[:, 2, :], masks[:, 6, :]
        reset = sb("reset", [P, SEQ])
        prm = sb("prm", [P, P])
        prm_c = sb("prm_c", [P, 80])
        mu_c, w0_c, a0_c, kk_c = prm_c[:, 0:14], prm_c[:, 14:18], prm_c[:, 18:22], prm_c[:, 22:26]
        ka_c, rk_c, cb_c, cw_c = prm_c[:, 26:30], prm_c[:, 30:34], prm_c[:, 34:38], prm_c[:, 38:54]
        ccol = sb("ccol", [P, 16])
        csig = sb("csig", [P, 16])
        adab_c = sb("adab_c", [P, 6, 8])
        norm_c = sb("norm_c", [P, 2, 8])
        mod_c = sb("mod_c", [P, 4, 8])
        small = sb("small", [P, 64])
        nhalf = sb("nhalf", [P, 16])
        wup = sb("wup", [P, 2, 512])
        gup = area(47, 512)
        w_if = sb("w_if", [P, 8, 36])
        rowp = macc[:, 0:2, :].rearrange("p v n -> p (v n)")[:, 0:1536].rearrange("p (i n) -> p i n", i=3)
        gate_b = sb("gate_b", [36, 2])
        bon = sb("bon", [P, TT, 8])
        mrow = arena[0:64, 14 * KB:20 * KB].rearrange("p (i t) -> p i t", i=6)
        sel4 = arena[0:4, 20 * KB:22 * KB].rearrange("p (h n) -> p h n", h=4)

        v = {s: sem("v_" + s) for s in "c n w m r i s y o q e f bn bp bg bs bo l0 pn pp l1 z".split()}
        a = {s: sem("a_" + s) for s in "c n w m r i s o q e f bn bp bg bs bo l0 pn l1 z".split()}
        g = {s: sem("g_" + s) for s in "c n m r y q f bn bp bg l0 pn pp l1 z".split()}
        t = {s: sem("t_" + s) for s in "n w m r i o q e bn bg bs bo l0 pn pp l1".split()}
        ring_in = [sem(f"ring_in{i}") for i in range(RING)]
        x_in, c_in, prm_in, par_in, gate_in, row_in = (
            sem(n) for n in ("x_in", "c_in", "prm_in", "par_in", "gate_in", "row_in"))
        v_ada = sem("v_ada")
        t_win = sem("t_win")
        s_out = sem("s_out")

        wout_in = sem("wout_in")
        t_ada, t_as, t_u, t_ds, t_y, t_out = (sem(n) for n in ("t_ada", "t_as", "t_u", "t_ds", "t_y", "t_out"))

        def tmp(i):
            return ring[:, i // 2, 1024 * (i % 2):1024 * (i % 2) + 1024].rearrange("p (i t) -> p i t", i=4)

        lw, cum, av, pcum, pinv, kn, kx, sq, kmod, bh, kh, bend, kend, rkp = (tmp(i) for i in range(14))
        ysq = ring[:, 6, 0:1024].rearrange("p (a n) -> p a n", a=TT)
        mz = ring[:, 0, 0:4 * 384].rearrange("p (h n) -> p h n", h=4)
        msq = ring[:, 1, 0:1024].rearrange("p (a n) -> p a n", a=TT)
        mcol = ring[:, 2, 0:128].rearrange("p (a n) -> p a n", a=TT)
        mem = ring[:, 2, 128:136].rearrange("p (a n) -> p a n", a=TT)
        qsig = area(50, 1024).rearrange("p (i t) -> p i t", i=4)
        pend = sb("pend", [P, 4, NC])

        w_rt = area(0, KT * 36).rearrange("p (t n) -> p t n", t=KT)
        b_rt = area(2, 36)
        lg = area(3, 2 * 36).rearrange("p (a n) -> p a n", a=TT)
        rt = area(4, 16 * 64).rearrange("p (i a n) -> p i a n", i=16, a=TT)
        cw = area(8, TT * NE).rearrange("p (a e) -> p a e", a=TT)
        rev = area(9, 8)
        revi = area(9.5, 8).bitcast(mybir.dt.int32)
        sg = area(10, TT * FE).rearrange("p (a n) -> p a n", a=TT)
        gact = area(12, TT * FE).rearrange("p (a n) -> p a n", a=TT)
        eact = area(14, TT * FE).rearrange("p (a n) -> p a n", a=TT)
        eact_t = area(16, TT * FE).rearrange("p (a f n) -> p a f n", a=TT, f=2)
        gate2 = area(20, 4 * D).rearrange("p (m n) -> p m n", m=4)
        mod2 = area(36, 4 * 32).rearrange("p (m n) -> p m n", m=4)
        adab2_c = area(37, 64).rearrange("p (m n) -> p m n", m=8)
        norm2_c = area(37.5, 32).rearrange("p (m n) -> p m n", m=4)
        sink_b = area(38, 8)
        w_glr = area(38.5, KT * 16).rearrange("p (t n) -> p t n", t=KT)
        w_gg = arena[0:16, 39 * KB:40 * KB]
        vg = area(0, 1024).rearrange("p (a n) -> p a n", a=TT)
        ggs = area(4, 1024).rearrange("p (a n) -> p a n", a=TT)
        sq_t = area(8, 1024).rearrange("p (i t) -> p i t", i=4)
        kz = area(12, 1024).rearrange("p (k h t) -> p k h t", k=2, h=2)
        svt = area(16, 256).rearrange("p (a n) -> p a n", a=TT)
        glr_t = arena[0:16, 17 * KB:18 * KB]
        swm = area(18, 64)
        f2 = lambda kb: area(kb, 512).rearrange("p (i t) -> p i t", i=2)
        zb, az, nb2, eb, enb, kend2 = (f2(kb) for kb in (40, 42, 44, 46, 48, 50))
        ket = area(52, 512).rearrange("p (a n) -> p a n", a=TT)
        at = area(54, 1024).rearrange("p (a h t) -> p a h t", a=TT, h=4)
        ktz = area(58, 1024).rearrange("p (h t) -> p h t", h=4)
        sg_state = area(64, 2048).rearrange("p (c i v) -> p c i v", c=4, i=2)
        qg, kg = f2(72), f2(74)
        gdec = area(76, 8).rearrange("p (i c) -> p i c", i=2)
        ggn = area(76.5, GLA_DV)
        gsq = area(78, 1024).rearrange("p (a n) -> p a n", a=TT)
        sc = area(40, 8 * 384).rearrange("p (h k) -> p h k", h=8)
        p_t = area(52, 24 * P).rearrange("p (j q) -> p j q", j=24)
        bias8 = area(83, 8 * 256).rearrange("p (h k) -> p h k", h=8)
        ebc = area(78, 384)
        hots = arena[0:64, int(79.5 * KB):int(79.5 * KB) + 384]
        rel_sb = arena[0:64, 81 * KB:81 * KB + 8]
        relx = arena[0:64, int(81.25 * KB):int(81.25 * KB) + P]
        y2 = macc[:, 0:2, :]
        PAD = 16
        hp = area(0, 8 * 272).rearrange("p (k t) -> p k t", k=KT)
        pa = area(9, 8 * 272).rearrange("p (k t) -> p k t", k=KT)
        pb_ = area(40, 6 * 272).rearrange("p (k t) -> p k t", k=6)
        pinvc = area(58, 4 * 256).rearrange("p (g t) -> p g t", g=4)
        pcnt = area(62, 256)
        pcnti = area(63, 256).bitcast(mybir.dt.int32)
        poolw = area(64, 2048).rearrange("p (g r n) -> p g r n", g=4, r=2)
        psc_b = area(72, 1024)
        frl = area(40, 1024).rearrange("p (a n) -> p a n", a=TT)
        fact = area(44, 1024).rearrange("p (a n) -> p a n", a=TT)
        fact_t = area(48, 1024).rearrange("p (a f n) -> p a f n", a=TT, f=4)
        nrm_b = area(0, D)
        zeros_b = sb("zeros_b", [P, P], BF16)[:, :]
        ring_zero = sb("ring_zero", [P, 512], BF16)[:, :]

        moe_in = [sem(f"moe_in{i}") for i in range(6)]
        ada2_in = [sem(f"ada2_in{i}") for i in range(2)]
        rt_in, par2_in, bias_out, bias_in, nrm_in, pool_in = (
            sem(n) for n in ("rt_in", "par2_in", "bias_out", "bias_in", "nrm_in", "pool_in"))
        t_gu, t_tr, t_dn, a_moe, v_moe, v_ada2, v_mod, t_mod = (
            sem(n) for n in ("t_gu", "t_tr", "t_dn", "a_moe", "v_moe", "v_ada2", "v_mod", "t_mod"))
        ring2 = [sem(f"ring2_{i}") for i in range(RING)]
        t_bin, t_bout, nrm2_in, hot_in = (sem(n) for n in ("t_bin", "t_bout", "nrm2_in", "hot_in"))
        mlp_in = [sem(f"mlp_in{i}") for i in range(RING)]
        t_up, t_ft, t_fd, a_mlp, v_mlp = (sem(n) for n in ("t_up", "t_ft", "t_fd", "a_mlp", "v_mlp"))
        scratch_d = nc.dram_tensor("bias_rows", (SWA_H, P * 384), F32, kind="Internal").ap()
        CREDIT = 4
        in2_cols = [0, 256, 512, 768, 1024, 1280, 1552, 1808, 2064]
        stream2 = [("in", c0) for c0 in in2_cols] + [("out", q) for q in range(4)]
        ones2 = arena[0:4, 86 * KB:87 * KB]

        def scratch(i):
            return ring[:, i, :].rearrange("p (g h s) -> p g h s", g=4, h=4)

        iF, iA, iB, iC, iD, iQ = (scratch(i) for i in range(6))

        def chunk2(x):
            return x.rearrange("p i (c s) -> p i c s", s=CH)

        def bank_of(step, gi):
            return (4 * step + gi) % 8

        def bank4(step, gi):
            return ps[:, bank_of(step, gi), :].rearrange("p (h s) -> p h s", h=4)

        INV_T = [
            ("F", None, None, None, None, None),
            ("G", bhz, 0, None, None, None),
            ("G", khz, 0, None, None, ("a", 0)),
            ("G", bhz, 1, None, None, ("v", 0)),
            ("G", khz, 1, None, None, ("v", 1)),
            ("V", iD, None, None, 1, ("v", 4)),
            ("M", iB, iA, None, 2, ("v", 5)),
            ("M", iA, iB, None, 2, ("v", 6)),
            ("M", iC, iQ, 1, 3, ("a", 1)),
            ("M", iD, iC, 2, None, ("a", 2)),
            ("M", iC, iD, None, None, ("v", 7)),
            ("M", iA, iQ, 3, 7, ("a", 3)),
            ("M", iB, iA, 4, None, ("a", 4)),
            ("M", iC, iQ, 5, 8, ("v", 8)),
            ("T", iQ, None, None, 9, ("a", 5)),
            ("M", iA, iQ, None, 10, ("v", 9)),
            ("M", iD, iB, 7, None, ("a", 6)),
            ("T", iQ, None, None, 11, ("a", 7)),
            ("M", iA, iQ, None, 12, ("v", 11)),
            ("M", iD, iB, 9, None, ("a", 8)),
        ]
        INV_A = [(i, s_, d_) for i, (s_, d_) in enumerate(
            [(0, iF), (6, iC), (7, iD), (9, iA), (10, iB), (12, iC), (14, iD), (15, iB), (17, iD), (18, iB)])]
        INV_V = [
            ("mask", 1, m_n16t, iB),
            ("mask", 2, m_ak, iD),
            ("maskF", None, m_n16, iA),
            ("ident", None, None, iQ),
            ("mask", 3, m_rb, grb),
            ("mask", 4, m_rb, grk),
            ("lakv", 5, None, None),
            ("add", 8, None, iQ),
            ("add", 11, None, iQ),
            ("add", 13, None, iQ),
            ("maskF", None, m_32, iA),
            ("add", 16, None, iQ),
            ("maskF", None, m_64, iA),
            ("add", 19, None, iQ),
        ]
        V_A16 = 2

        block = ctx.enter_context(nc.Block())

        stream = [("ada", n) for n in range(8)]
        for n in range(IN_SLOTS):
            stream += [("win", n), ("ada", 8 + n)]
        stream += [("ada", n) for n in range(21, 24)]
        place = {key: i for i, key in enumerate(stream)}

        def loaded(eng, key):
            eng.wait_ge(ring_in[place[key] % RING], 16 * (place[key] // RING + 1))

        def slot(key):
            return ring[:, place[key] % RING, :]

        def g_norm(pool, st):
            c = Counter(pool, g[st])
            pool.wait_ge(v[st], STEP[st + ".ss"])
            c.link(nc.gpsimd.tensor_tensor(small[:, 0:2], small[:, 0:2], nhalf[:, 0:2], ALU.pow))
            c.at(st + ".rstd")

        def a_norm(act, st, shift, scale):
            c = Counter(act, a[st])
            for tt in range(TT):
                c.link(nc.scalar.activation(xn[:, tt, :], x_sb[:, tt, :], ACT.Square, accum_out=small[:, tt:tt + 1]))
            c.at(st + ".sq")
            act.wait_ge(v[st], STEP[st + ".mod"])
            for k in (2, 3, 6, 7):
                act.wait_ge(t[st], k // 2 + 1)
                c.link(nc.scalar.activation(hT[:, k, :], ps[:, k // 2, 256 * (k % 2):256 * (k % 2) + 256], ACT.Identity,
                                            bias=shift[:, k:k + 1], scale=scale[:, k:k + 1]))
            c.at(st + ".a")

        def v_rstd(dve, c, st):
            dve.wait_ge(a[st], STEP[st + ".sq"])
            c.link(nc.vector.tensor_scalar(small[:, 0:2], small[:, 0:2], 1.0 / D, EPS, ALU.mult, ALU.add))
            c.at(st + ".ss")
            dve.wait_ge(g[st], STEP[st + ".rstd"])

        def v_norm(dve, st, shift, scale, mod=None):
            c = Counter(dve, v[st])
            v_rstd(dve, c, st)
            for tt in range(TT):
                c.link(nc.vector.tensor_scalar(xn[:, tt, :], x_sb[:, tt, :], small[:, tt:tt + 1], None, ALU.mult))
            c.at(st + ".xn")
            if mod:
                mod(c)
            c.at(st + ".mod")
            for k in (0, 1, 4, 5):
                dve.wait_ge(t[st], k // 2 + 1)
                c.link(nc.vector.tensor_scalar(hT[:, k, :], ps[:, k // 2, 256 * (k % 2):256 * (k % 2) + 256],
                                               scale[:, k:k + 1], shift[:, k:k + 1], ALU.mult, ALU.add))
            c.at(st + ".v")

        def t_norm(pe, st, tiles=False):
            c = Counter(pe, t[st])
            pe.wait_ge(v[st], STEP[st + ".xn"])
            for k in range(KT):
                for tt in range(TT):
                    o = (k % 2) * 256 + tt * P
                    src = xn[:, tt, P * k:P * k + P] if tiles else xn[:, tt, k::8]
                    ins = nc.tensor.transpose(ps[:, k // 2, o:o + P], src, ident[:, :])
                if k % 2:
                    c.mark(ins)
            c.at(st + ".t")

        def t_columns(acc, dst):
            for k in range(KT):
                ins = nc.tensor.matmul(dst[:, k:k + 1], acc[:, k::8], ones[:, 0:1], start=True, stop=True)
            return ins

        def sp_tail(sp):
            sp.wait_ge(v["i"], STEP["i.done"])
            for q in range(4):
                sp.dma_start(ring[:, q, :].rearrange("p (t n) -> p t n", t=2),
                             A["w_out"][0].rearrange("(p t) n -> p t n", t=8)[:, 2 * q:2 * q + 2, :]
                             ).then_inc(wout_in, 16)
            sp.wait_ge(v["y"], STEP["y.done"])
            sp.wait_ge(g["y"], STEP["y.free"])
            sp.dma_start(w_rt[:, :, 0:32], A["moe_w_router"][0].rearrange("(p t) n -> p t n", t=8)).then_inc(rt_in, 16)
            sp.dma_start(w_rt[:, :, 32:36], A["moe_w_group"][0].rearrange("(p t) n -> p t n", t=8)).then_inc(rt_in, 16)
            sp.dma_start(b_rt[:, 0:32], A["moe_b_router"].to_broadcast([P, NE])).then_inc(rt_in, 16)
            sp.dma_start(b_rt[:, 32:36], A["moe_b_group"].to_broadcast([P, NG])).then_inc(rt_in, 16)
            for m in range(4):
                sp.dma_start(gate2[:, m, :], A["ada_b_2"][m // 2, m % 2:m % 2 + 1, 2 * D:3 * D].to_broadcast([P, D])
                             ).then_inc(par2_in, 16)
                sp.dma_start(adab2_c[:, 2 * m:2 * m + 2, :],
                             A["ada_b_2"][m // 2, m % 2, 0:2 * D].rearrange("(v p t) -> p v t", p=P, t=8)
                             ).then_inc(par2_in, 16)
                sp.dma_start(norm2_c[:, m, :], A["norm_w_2"][m // 2, m % 2].rearrange("(p t) -> p t", t=8)
                             ).then_inc(par2_in, 16)
            sp.dma_start(sink_b, A["attn_sinks_2"].to_broadcast([P, SWA_H])).then_inc(par2_in, 16)
            sp.dma_start(w_glr[:, :, :], A["attn_w_in_2"][0].rearrange("(p t) n -> p t n", t=8)[:, :, 1536:1552]
                         ).then_inc(par2_in, 16)
            sp.dma_start(w_gg, A["gla_w_gate_2"][0]).then_inc(par2_in, 16)
            sp.wait_ge(t["o"], KT // 2)
            sp.dma_start(ggn, A["gla_norm_w_2"].to_broadcast([P, GLA_DV])).then_inc(par2_in, 16)
            sp.dma_start(rel_sb[0:32, :], A["rel_bias_2"]).then_inc(hot_in, 16)
            sp.dma_start(hots[0:33, :], A["hots"]).then_inc(hot_in, 16)

            w_ada2 = A["ada_w_2"].rearrange("l j (p t) n -> (l j) p t n", t=8)
            with sp.Fori(0, NE // E_BODY) as m:
                for e8 in range(E_BODY):
                    s0 = 3 * (e8 % 2)
                    sp.wait_ge(t_gu, 2 * E_BODY * m + 2 * e8 + 2)
                    for j, name in enumerate(("moe_w_gate", "moe_w_up")):
                        sp.dma_start(ring[:, s0 + j, :], A[name][0, bass.ds(m * E_BODY + e8, 1)]
                                     .rearrange("o (p t) n -> (o p) (t n)", t=8)).then_inc(moe_in[s0 + j], 16)
                    sp.wait_ge(t_dn, 2 * E_BODY * m + 2 * e8 + 2)
                    sp.dma_start(ring[:, s0 + 2, :], A["moe_w_down"][0, bass.ds(m * E_BODY + e8, 1)]
                                 .rearrange("o (p t) n -> (o p) (t n)", t=2)).then_inc(moe_in[s0 + 2], 16)
                    if e8 < 6:
                        for k in (2 * e8, 2 * e8 + 1):
                            vec, q = k // 4, k % 4
                            sp.wait_ge(v_ada2, 24 * m + 2 * k + 2)
                            sp.dma_start(ring[:, 6 + k % 2, :].rearrange("p (t n) -> p t n", t=2),
                                         w_ada2[bass.ds(m, 1), :, 2 * q:2 * q + 2, vec * D:(vec + 1) * D]
                                         .rearrange("o p t n -> (o p) t n")).then_inc(ada2_in[k % 2], 16)
            sp.wait_ge(t_dn, CREDIT + 2 * NE)
            sp.dma_start(nrm_b, A["final_norm_w"].rearrange("(o n) -> o n", o=1).to_broadcast([P, D])).then_inc(nrm_in, 16)
            sp_block2(sp)

        def sp_block2(sp):
            for i, (kind, c0) in enumerate(stream2):
                if i < RING:
                    if i == 6:
                        sp.wait_ge(v_ada2, CREDIT + 24 * 4)
                else:
                    sp.wait_ge(t_bin, i - RING + 1)
                if kind == "in":
                    sp.dma_start(ring[:, i % RING, :].rearrange("p (t n) -> p t n", t=8),
                                 A["attn_w_in_2"][0].rearrange("(p t) n -> p t n", t=8)[:, :, c0:c0 + 256]
                                 ).then_inc(ring2[i % RING], 16)
                else:
                    sp.dma_start(ring[:, i % RING, :].rearrange("p (t n) -> p t n", t=2),
                                 A["attn_w_out_2"][0].rearrange("(p t) n -> p t n", t=8)[:, 2 * c0:2 * c0 + 2, :]
                                 ).then_inc(ring2[i % RING], 16)
            sp_mlp(sp, 0)
            sp.wait_ge(v["bo"], STEP["bo.x"])
            sp.dma_start(poolw[:, :, :, :], A["pool_w_2"][0].rearrange("g (r p) n -> p g r n", p=P)).then_inc(pool_in, 16)
            sp.dma_start(psc_b, A["pool_scale_2"].to_broadcast([P, D])).then_inc(pool_in, 16)
            sp_mlp(sp, 1)
            sp.wait_ge(v["pp"], STEP["pp.x"])
            sp.dma_start(nrm_b, A["final_norm_w_2"].rearrange("(o n) -> o n", o=1).to_broadcast([P, D])).then_inc(nrm2_in, 16)
            for tt in range(TT):
                sp.wait_ge(v["z"], STEP["z.out0"] + tt)
                sp.dma_start(out[0, P * tt:P * tt + P, :], x_sb[:, tt, :]).then_inc(s_out, 16)
            sp.wait_ge(s_out, 32)

        def sp_mlp(sp, layer):
            w1 = A["mlp_w1_2"][layer].rearrange("(p t) (c n) -> c p t n", t=8, n=512)
            w2 = A["mlp_w2_2"][layer].rearrange("(c p f) n -> c p f n", p=P, f=4)
            with sp.Fori(0, 4) as m:
                for c2 in range(2):
                    s0, C = 4 * c2, 8 * layer + c2
                    sp.wait_ge(t_up, 4 * m + 2 * C + 2)
                    for r in range(2):
                        sp.dma_start(ring[:, s0 + r, :].rearrange("p (t n) -> p t n", t=4),
                                     w1[bass.ds(2 * m + c2, 1), :, 4 * r:4 * r + 4, :].rearrange("o p t n -> (o p) t n")
                                     ).then_inc(mlp_in[s0 + r], 16)
                    sp.wait_ge(t_fd, 4 * m + 2 * C + 2)
                    for r in range(2):
                        sp.dma_start(ring[:, s0 + 2 + r, :].rearrange("p (f n) -> p f n", f=2),
                                     w2[bass.ds(2 * m + c2, 1), :, 2 * r:2 * r + 2, :].rearrange("o p f n -> (o p) f n")
                                     ).then_inc(mlp_in[s0 + 2 + r], 16)

        @block.sync
        def _(sp):
            sp.dma_start(ccol[:, 0:8], A["c"].rearrange("o (p t) -> p (o t)", t=8)).then_inc(c_in, 16)
            sp.dma_start(ccol[:, 8:16], A["c_2"].rearrange("o (p t) -> p (o t)", t=8)).then_inc(c_in, 16)
            sp.dma_start(x_sb[:, :, :], A["x"].rearrange("b (a p) d -> p (b a) d", p=P)).then_inc(x_in, 16)
            for i, (kind, n) in enumerate(stream):
                if i >= RING:
                    k0, n0 = stream[i - RING]
                    if k0 == "ada":
                        sp.wait_ge(v_ada, 2 * (n0 + 1))
                    else:
                        sp.wait_ge(t_win, n0 + 1)
                dst = slot((kind, n))
                if kind == "ada":
                    vec, q = n // 4, n % 4
                    src = A["ada_w"][0].rearrange("(p t) n -> p t n", t=8)[:, 2 * q:2 * q + 2, vec * D:(vec + 1) * D]
                    sp.dma_start(dst.rearrange("p (t n) -> p t n", t=2), src).then_inc(ring_in[i % RING], 16)
                else:
                    src = A["w_in"][0].rearrange("(p t) n -> p t n", t=8)[:, :, 256 * n:256 * n + 256]
                    sp.dma_start(dst.rearrange("p (t n) -> p t n", t=8), src).then_inc(ring_in[i % RING], 16)
            sp.wait_ge(t_ada, 6)
            for i, name in enumerate(("rwkv_gn_w", "rwkv_gn_b", "mlstm_hn_w")):
                sp.dma_start(rowp[:, i, :], A[name].to_broadcast([P, 512])).then_inc(row_in, 16)
            sp_tail(sp)

        @block.gpsimd
        def _(pool):
            c = Counter(pool, g["c"])
            k = c.link
            k(nc.gpsimd.memset(ident[:, :], 0.0))
            k(nc.gpsimd.memset(ones[:, :], 1.0))
            k(nc.gpsimd.affine_select(out=ident[:, :], in_=ident[:, :], compare_op=ALU.not_equal, fill=1.0,
                                      base=0, pattern=[[-1, P]], channel_multiplier=1))
            k(nc.gpsimd.memset(nhalf[:, :], -0.5))
            k(nc.gpsimd.memset(prm[:, :], 0.0))
            k(nc.gpsimd.memset(zeros_b[:, :], 0.0))
            k(nc.gpsimd.memset(ring_zero[:, :], 0.0))
            c.at("c.ident")
            prm_rows = [("rwkv_mu", 14), ("rwkv_w0", 4), ("rwkv_a0", 4), ("rwkv_k_k", 4), ("rwkv_k_a", 4)]
            r0 = 0
            for name, n in prm_rows:
                pool.dma_start(prm[r0:r0 + n, :], A[name].rearrange("o (i p) -> (o i) p", p=P)).then_inc(prm_in, 16)
                r0 += n
            pool.dma_start(prm[30:34, :], A["rwkv_r_k"].rearrange("o (i h) j -> (o i) (h j)", h=2)).then_inc(prm_in, 16)
            pool.dma_start(prm[34:38, :], A["mlstm_conv_b"].rearrange("o (i p) -> (o i) p", p=P)).then_inc(prm_in, 16)
            pool.dma_start(prm[38:54, :], A["mlstm_conv_w"].rearrange("o j (i p) -> (o j i) p", p=P)).then_inc(prm_in, 16)
            pool.dma_start(prm[54:56, :], A["gla_b_gate_2"].rearrange("o (i p) -> (o i) p", p=P)).then_inc(prm_in, 16)
            pool.dma_start(prm[56:64, :], A["norm_w_2"][1, 0].rearrange("(i p) -> i p", p=P)).then_inc(prm_in, 16)
            pool.dma_start(prm[64:80, :], A["ada_b_2"][1, 0, 0:2048].rearrange("(i p) -> i p", p=P)).then_inc(prm_in, 16)
            pool.dma_start(adab_c[:, :, :], A["ada_b"].rearrange("o (v p t) -> p (o v) t", p=P, t=8)).then_inc(par_in, 16)
            pool.dma_start(norm_c[:, 0, :], A["mix_norm_w"].rearrange("o (p t) -> p (o t)", t=8)).then_inc(par_in, 16)
            pool.dma_start(norm_c[:, 1, :], A["ffn_norm_w"].rearrange("o (p t) -> p (o t)", t=8)).then_inc(par_in, 16)
            pool.dma_start(gate1[:, 0, :], A["ada_b"][:, 2 * D:3 * D].to_broadcast([P, D])).then_inc(par_in, 16)
            pool.dma_start(gate1[:, 1, :], A["ada_b"][:, 5 * D:6 * D].to_broadcast([P, D])).then_inc(par_in, 16)
            k(nc.gpsimd.memset(raw[:, :, :, 0:1], 0.0))
            k(nc.gpsimd.memset(convraw[:, :, 0:3], 0.0))
            k(nc.gpsimd.memset(w_if[:, :, :], 0.0))
            k(nc.gpsimd.memset(wup[:, :, :], 0.0))
            k(nc.gpsimd.memset(gate_b[:, :], 0.0))
            k(nc.gpsimd.memset(mrow[:, :, :], 0.0))
            k(nc.gpsimd.memset(ones2[:, :], 1.0))
            k(nc.gpsimd.memset(reset[:, :], 1.0))
            k(nc.gpsimd.memset(reset[:, :].rearrange("p (c s) -> p c s", s=CH)[:, :, 0:1], 0.0))
            c.at("c.zeros")
            w_in_t = A["w_in"][0].rearrange("(p t) n -> p t n", t=8)
            pool.dma_start(w_if[:, :, 0:4], w_in_t[:, :, 3328:3332]).then_inc(gate_in, 16)
            pool.dma_start(w_if[:, :, 32:36], w_in_t[:, :, 3332:3336]).then_inc(gate_in, 16)
            pool.dma_start(wup[0:64, 0, :], A["rwkv_w_up"][0]).then_inc(gate_in, 16)
            pool.dma_start(wup[64:128, 1, :], A["rwkv_a_up"][0]).then_inc(gate_in, 16)
            pool.dma_start(gup[:, :], A["rwkv_g_up"][0]).then_inc(gate_in, 16)
            pool.dma_start(gate_b[0:4, 0:1], A["mlstm_i_b"].rearrange("o h -> h o")).then_inc(gate_in, 16)
            pool.dma_start(gate_b[32:36, 0:1], A["mlstm_f_b"].rearrange("o h -> h o")).then_inc(gate_in, 16)
            for i, B in enumerate((16, 32, 64)):
                m = masks[:, i, :].rearrange("p (b f) -> p b f", f=B)
                k(nc.gpsimd.memset(masks[:, i, :], 1.0))
                k(nc.gpsimd.affine_select(out=m, in_=m, compare_op=ALU.is_ge, fill=0.0, base=0,
                                          pattern=[[-B, P // B], [0, B]], channel_multiplier=1))
                k(nc.gpsimd.affine_select(out=m, in_=m, compare_op=ALU.is_ge, fill=0.0, base=B - 1,
                                          pattern=[[B, P // B], [0, B]], channel_multiplier=-1))
            k(nc.gpsimd.tensor_copy(headblk[:, :], same64))
            k(nc.gpsimd.tensor_copy(headsel[:, :], masks[:, 2, 0:128:64]))
            k(nc.gpsimd.affine_select(out=m_causal, in_=ones[:, :], compare_op=ALU.is_ge, fill=0.0, base=0,
                                      pattern=[[1, P]], channel_multiplier=-1))
            k(nc.gpsimd.tensor_tensor(m_64, same64, same32, ALU.subtract))
            k(nc.gpsimd.tensor_tensor(same32, same32, same16, ALU.subtract))
            k(nc.gpsimd.tensor_scalar(m_n16t, same16, -1.0, None, ALU.mult))
            k(nc.gpsimd.affine_select(out=m_n16t, in_=m_n16t, compare_op=ALU.is_gt, fill=0.0, base=0,
                                      pattern=[[1, P]], channel_multiplier=-1))
            k(nc.gpsimd.tensor_scalar(masks[:, 0:2, :], masks[:, 0:2, :], -1.0, None, ALU.mult))
            k(nc.gpsimd.tensor_scalar(m_64, m_64, -1.0, None, ALU.mult))
            for m in (m_n16, m_32, m_64):
                k(nc.gpsimd.affine_select(out=m, in_=m, compare_op=ALU.is_gt, fill=0.0, base=0,
                                          pattern=[[-1, P]], channel_multiplier=1))
            k(nc.gpsimd.affine_select(out=m_ak, in_=same64, compare_op=ALU.is_gt, fill=0.0, base=0,
                                      pattern=[[1, P]], channel_multiplier=-1))
            k(nc.gpsimd.affine_select(out=m_rb, in_=same64, compare_op=ALU.is_ge, fill=0.0, base=0,
                                      pattern=[[1, P]], channel_multiplier=-1))
            c.at("c.masks")
            g_norm(pool, "n")
            c = Counter(pool, g["m"])
            pool.wait_ge(v["m"], STEP["m.ss"])
            c.link(nc.gpsimd.tensor_tensor(small[:, 8:16], small[:, 8:16], nhalf[:, 0:8], ALU.pow))
            c.at("m.rs")
            c = Counter(pool, g["r"])
            c.link(nc.gpsimd.memset(bhz[:, :, :], 0.0))
            c.link(nc.gpsimd.memset(khz[:, :, :], 0.0))
            pool.wait_ge(v["m"], STEP["m.y"])
            pool.wait_ge(v["w"], STEP["w.shift"])
            pool.wait_ge(t["n"], STEP["n.t"])
            c.link(nc.gpsimd.memset(rbuf[:, :, :], 0.0))
            c.link(nc.gpsimd.memset(ubuf[:, :, :], 0.0))
            c.link(nc.gpsimd.memset(state[:, :, :, :], 0.0))
            c.at("r.zero")
            c = Counter(pool, g["y"])
            pool.wait_ge(v["y"], STEP["y.var"])
            c.link(nc.gpsimd.tensor_tensor(small[:, 32:48], small[:, 32:48], nhalf[:, 0:16], ALU.pow))
            c.at("y.rs")
            pool.wait_ge(v["y"], STEP["y.done"])
            c.link(nc.gpsimd.iota(revi, pattern=[[-1, 8]], base=8, channel_multiplier=0))
            c.link(nc.gpsimd.tensor_copy(rev, revi))
            c.link(nc.gpsimd.memset(rel_sb[:, :], BIG))
            c.at("y.free")
            g_norm(pool, "q")
            g_norm(pool, "f")
            g_norm(pool, "bn")
            c = Counter(pool, g["bp"])
            pool.wait_ge(v["bn"], STEP["bn.v"])
            pool.wait_ge(t["bn"], STEP["bn.t"])
            c.link(nc.gpsimd.memset(ktz[:, :, :], 0.0))
            c.link(nc.gpsimd.memset(kz[:, :, :, :], 0.0))
            c.link(nc.gpsimd.memset(sg_state[:, :, :, :], 0.0))
            c.at("bp.zero")
            c = Counter(pool, g["bg"])
            pool.wait_ge(v["bg"], STEP["bg.ss"])
            c.link(nc.gpsimd.tensor_tensor(small[:, 8:16], small[:, 8:16], nhalf[:, 0:8], ALU.pow))
            c.at("bg.rs")
            g_norm(pool, "l0")
            g_norm(pool, "pn")
            c = Counter(pool, g["pp"])
            for buf in (hp, pa, pb_):
                c.link(nc.gpsimd.memset(buf[:, :, 0:PAD], 0.0))
            c.link(nc.gpsimd.iota(pcnti, pattern=[[1, SEQ]], base=1, channel_multiplier=0))
            c.link(nc.gpsimd.tensor_copy(pcnt, pcnti))
            for gi in range(4):
                c.link(nc.gpsimd.tensor_scalar(pinvc[:, gi, :], pcnt, float(2 ** (gi + 1)), None, ALU.min))
            c.at("pp.zero")
            g_norm(pool, "l1")
            g_norm(pool, "z")

        mod_of = [(mod2[:, 0, 0:8], mod2[:, 0, 8:16]), (mod2[:, 1, 0:8], mod2[:, 1, 8:16]),
                  (mod2[:, 2, 16:24], mod2[:, 2, 24:32]), (mod2[:, 3, 0:8], mod2[:, 3, 8:16])]

        def a_mlp_loop(act, layer):
            with act.Fori(0, 4) as m:
                for c2 in range(2):
                    C = 8 * layer + c2
                    for tt in range(TT):
                        act.wait_ge(t_up, 4 * m + CREDIT + 2 * C + tt + 1)
                        nc.scalar.activation(frl[:, tt, :], ps[:, 4 + tt, :], ACT.Relu).then_inc(a_mlp, 1)
                        act.wait_ge(t_ft, 4 * m + 2 * C + tt + 1)
                        nc.scalar.copy(fact_t[:, tt], ps[:, 6 + tt, :].rearrange("p (f n) -> p f n", f=4)
                                       ).then_inc(a_mlp, 1)

        def v_mlp_loop(dve, layer):
            with dve.Fori(0, 4) as m:
                for c2 in range(2):
                    C = 8 * layer + c2
                    for tt in range(TT):
                        dve.wait_ge(a_mlp, 8 * m + 4 * C + 2 * tt + 1)
                        nc.vector.tensor_tensor(fact[:, tt, :], frl[:, tt, :], ps[:, 4 + tt, :], ALU.mult).then_inc(v_mlp, 1)

        def t_mlp_loop(pe, layer):
            def up(m, c2, tt, ks):
                C, s0 = 8 * layer + c2, 4 * c2
                if ks[0] == 0:
                    pe.wait_ge(mlp_in[s0], 16 * m + 16 * (4 * layer + 1))
                    pe.wait_ge(v_mlp, 4 * m + 2 * C + tt + 1 - 2 + CREDIT)
                for k in ks:
                    if k == 4:
                        pe.wait_ge(mlp_in[s0 + 1], 16 * m + 16 * (4 * layer + 1))
                    ins = nc.tensor.matmul(ps[:, 4 + tt, :], hT[:, k, P * tt:P * tt + P],
                                           ring[:, s0 + k // 4, 512 * (k % 4):512 * (k % 4) + 512],
                                           start=k == 0, stop=k == KT - 1, skip_group_check=True)
                if ks[-1] == KT - 1:
                    ins.then_inc(t_up, 1)

            def turn(m, c2, tt):
                C = 8 * layer + c2
                pe.wait_ge(v_mlp, 4 * m + 2 * C + tt + 1 + CREDIT)
                for f in range(4):
                    ins = nc.tensor.transpose(ps[:, 6 + tt, P * f:P * f + P], fact[:, tt, f::4], ident[:, :])
                ins.then_inc(t_ft, 1)

            def down(m, c2, tt, fs):
                C, s0 = 8 * layer + c2, 4 * c2
                for f in fs:
                    if f == 0:
                        pe.wait_ge(a_mlp, 8 * m + 4 * C + 2 * tt + 2)
                    if f % 2 == 0 and tt == 0:
                        pe.wait_ge(mlp_in[s0 + 2 + f // 2], 16 * m + 16 * (4 * layer + 1))
                    for j in range(2):
                        ins = nc.tensor.matmul(ps[:, 2 * tt + j, :], fact_t[:, tt, f, :],
                                               ring[:, s0 + 2 + f // 2, D * (f % 2) + 512 * j:D * (f % 2) + 512 * j + 512],
                                               start=False, stop=False, skip_group_check=True)
                if fs[-1] == 3:
                    ins.then_inc(t_fd, 1)

            with pe.Fori(0, 4) as m:
                for c2 in range(2):
                    up(m, c2, 0, range(8))
                    up(m, c2, 1, range(5))
                    turn(m, c2, 0)
                    up(m, c2, 1, range(5, 8))
                    down(m, c2, 0, range(4))
                    turn(m, c2, 1)
                    down(m, c2, 1, range(4))

        def v_residual(dve, c, gate, base=0):
            for j in range(4):
                xs = x_sb[:, j // 2, 512 * (j % 2):512 * (j % 2) + 512]
                c.link(nc.vector.tensor_tensor(dtmp[:, :], ps[:, base + j, :], gate[:, 512 * (j % 2):512 * (j % 2) + 512], ALU.mult))
                c.link(nc.vector.tensor_tensor(xs, xs, dtmp[:, :], ALU.add))

        def t_zero(pe):
            for j in range(4):
                ins = nc.tensor.matmul(ps[:, j, :], zeros_b[:, 0:P], ring_zero, start=True, stop=True,
                                       skip_group_check=True)
            return ins

        @block.scalar
        def _(act):
            c = Counter(act, a["c"])
            act.wait_ge(c_in, 32)
            c.link(nc.scalar.activation(csig[:, :], ccol[:, :], ACT.Sigmoid))
            c.at("c.sig")
            act.wait_ge(x_in, 16)
            a_norm(act, "n", mod_c[:, 0, :], mod_c[:, 1, :])

            c = Counter(act, a["w"])
            act.wait_ge(g["c"], STEP["c.zeros"])
            act.wait_ge(t["n"], STEP["n.t"])
            for n in range(IN_SLOTS):
                act.wait_ge(t_win, n + 1)
                bank = ps[:, 4 + n % 4, :]
                if n < 7:
                    if n >= 2:
                        act.wait_ge(v["w"], STEP["w.pre"] + 3 * (n - 1))
                    c.link(nc.scalar.copy(raw[:, n % 2, :, 1:257], bank.rearrange("p (i t) -> p i t", i=2)))
                elif n < 9:
                    c.link(nc.scalar.copy(convraw[:, 2 * (n - 7):2 * (n - 7) + 2, 3:259],
                                          bank.rearrange("p (i t) -> p i t", i=2)))
                elif n < 11:
                    c.link(nc.scalar.copy(vm[:, :, 256 * (n - 9):256 * (n - 9) + 256],
                                          bank.rearrange("p (a f) -> p a f", a=2)))
                else:
                    c.link(nc.scalar.activation(om[:, :, 256 * (n - 11):256 * (n - 11) + 256],
                                                bank.rearrange("p (a f) -> p a f", a=2), ACT.Sigmoid))
            c.at("w.a")
            act.wait_ge(v["w"], STEP["w.gb"])
            act.wait_ge(t["w"], STEP["w.if"])
            c.link(nc.scalar.activation(mrow[0:4, 0, :], ps[0:4, 0, 0:256], ACT.Tanh, bias=gate_b[0:4, 1:2],
                                        scale=1 / CAP))
            c.link(nc.scalar.activation(mrow[0:4, 1, :], ps[32:36, 0, 0:256], ACT.Tanh, bias=gate_b[32:36, 1:2],
                                        scale=1 / CAP))
            c.at("w.tanh")

            c = Counter(act, a["m"])
            act.wait_ge(v["m"], STEP["m.conv"])
            c.link(nc.scalar.activation(qsig[:, :, :], qk[:, :, :], ACT.Sigmoid))
            c.at("m.sig")
            c.link(nc.scalar.activation(mrow[0:4, 1, :], mrow[0:4, 1, :], ACT.Exp, scale=-CAP))
            c.link(nc.scalar.activation(mrow[0:4, 1, :], mrow[0:4, 1, :], ACT.Ln, bias=ones[0:4, 0:1]))
            c.at("m.lf")
            act.wait_ge(v["m"], STEP["m.z"])
            c.link(nc.scalar.activation(mz[:, :, :], mz[:, :, :], ACT.Exp, scale=-1.0))
            c.link(nc.scalar.activation(mem[:, :, :], mcol[:, :, 32:36], ACT.Exp))
            c.at("m.exp")

            c = Counter(act, a["r"])
            act.wait_ge(v["w"], STEP["w.shift"])
            c.link(nc.scalar.activation(u[0:64, 12, :], u[0:64, 12, :], ACT.Tanh))
            c.link(nc.scalar.activation(u[:, 13, :], u[:, 13, :], ACT.Sigmoid))
            c.at("r.u")
            act.wait_ge(t["r"], STEP["r.wa"])
            act.wait_ge(v_ada, 2 * 24)
            for i in range(4):
                o = (i % 2) * 256
                c.link(nc.scalar.activation(lw[:, i, :], ps[:, i // 2, o:o + 256], ACT.Sigmoid, bias=w0_c[:, i:i + 1]))
                c.link(nc.scalar.activation(av[:, i, :], ps[:, 2 + i // 2, o:o + 256], ACT.Sigmoid,
                                            bias=a0_c[:, i:i + 1]))
            c.at("r.sig")
            c.link(nc.scalar.copy(gtok[:, :, :], ps[:, 4:6, :]))
            c.at("r.gtok")
            act.wait_ge(v["r"], STEP["r.scan"])
            c.link(nc.scalar.activation(pcum[:, :, :], cum[:, :, :], ACT.Exp))
            c.link(nc.scalar.activation(pinv[:, :, :], cum[:, :, :], ACT.Exp, scale=-1.0))
            c.at("r.exp")
            act.wait_ge(t["r"], STEP["r.n2"])
            c.link(nc.scalar.activation(kn[:, :, :], ps[:, 6:8, :].rearrange("p b (i t) -> p (b i) t", i=2), ACT.Sqrt))
            c.at("r.sqrt")
            act.wait_ge(v["r"], STEP["r.bh"])
            act.wait_ge(g["r"], STEP["r.zero"])
            for src, dst in ((bh, bhz), (kh, khz)):
                c.link(nc.scalar.copy(dst[0:64, 0::2, :], src[0:64, :, :]))
                c.link(nc.scalar.copy(dst[64:128, 1::2, :], src[64:128, :, :]))
            c.at("r.pad")
            for i, dst in enumerate((vtok, bend_t, kend_t)):
                act.wait_ge(t["r"], STEP["r.tr"] - 2 + i)
                c.link(nc.scalar.copy(dst[:, :, :], ps[:, 2 * i:2 * i + 2, :]))
            c.at("r.tok")

            c = Counter(act, a["i"])
            act.wait_ge(v["r"], STEP["r.bend"])
            for step, src, dst in INV_A:
                for gi in range(4):
                    act.wait_ge(t["i"], 4 * src + gi + 1)
                    c.link(nc.scalar.copy(dst[:, gi], bank4(src, gi)))
            c.at("i.a")
            c = Counter(act, a["s"])
            for ch in range(NC):
                r0 = CH * (ch % 2)
                act.wait_ge(t_u, ch + 1)
                c.link(nc.scalar.copy(ubuf[r0:r0 + CH, ch // 2, :], ps[r0:r0 + CH, 1, :]))
            c = Counter(act, a["o"])
            for k in range(0, KT, 2):
                act.wait_ge(t["o"], k // 2 + 1)
                c.link(nc.scalar.copy(hT[:, k:k + 2, :], ps[:, k // 2, :].rearrange("p (k t) -> p k t", k=2)))
            c.at("o.hT")
            act.wait_ge(v["o"], STEP["o.x"])
            a_norm(act, "q", mod_c[:, 2, :], mod_c[:, 3, :])
            c = Counter(act, a["e"])
            act.wait_ge(v["e"], STEP["e.g"])
            c.link(nc.scalar.activation(rt[:, 1, :, 0:4], rt[:, 1, :, 0:4], ACT.Exp))
            c.at("e.expg")
            act.wait_ge(v["e"], STEP["e.d"])
            c.link(nc.scalar.activation(rt[:, 9, :, 0:1], rt[:, 9, :, 0:1], ACT.Exp))
            c.at("e.expd")
            for h in range(SWA_H):
                act.wait_ge(t["e"], STEP["e.bias0"] + h)
                if h:
                    act.wait_ge(bias_out, 16 * h)
                c.link(nc.scalar.copy(ebc, ps[:, 7, 0:384]))
                act.dma_start(scratch_d[h].rearrange("(q l) -> q l", q=P), ebc).then_inc(bias_out, 16)
            c.at("e.bias")
            act.wait_ge(bias_out, 16 * SWA_H)
            for h in range(SWA_H):
                act.dma_start(bias8[:, h, :], scratch_d[h, 127:127 + P * 383].rearrange("(q l) -> q l", l=383)[:, 0:256]
                              ).then_inc(bias_in, 16)
            with act.Fori(0, NE // E_BODY) as m:
                for e8 in range(E_BODY):
                    for tt in range(TT):
                        act.wait_ge(t_gu, 2 * E_BODY * m + CREDIT + 2 * e8 + tt + 1)
                        nc.scalar.activation(sg[:, tt, :], ps[:, 4 + tt, 0:FE], ACT.Sigmoid).then_inc(a_moe, 1)
                        act.wait_ge(t_tr, 2 * E_BODY * m + 2 * e8 + tt + 1)
                        nc.scalar.copy(eact_t[:, tt], ps[:, 6, FE * tt:FE * tt + FE].rearrange("p (f n) -> p f n", f=2)
                                       ).then_inc(a_moe, 1)
            act.wait_ge(v["f"], STEP["f.moe"])
            c = Counter(act, a["f"])
            for tt in range(TT):
                c.link(nc.scalar.activation(xn[:, tt, :], x_sb[:, tt, :], ACT.Square, accum_out=small[:, tt:tt + 1]))
            c.at("f.sq")
            act.wait_ge(v["f"], STEP["f.x"])
            a_norm(act, "bn", *mod_of[0])
            c = Counter(act, a["bp"])
            act.wait_ge(v["bn"], STEP["bn.v"])
            act.wait_ge(g["bp"], STEP["bp.zero"])
            for i in range(9):
                act.wait_ge(t_bin, i + 1)
                bank = ps[:, 4 + i % 4, :]
                if i < 2:
                    c.link(nc.scalar.copy((qg, kg)[i][:, :, :], bank.rearrange("p (i t) -> p i t", i=2)))
                elif i < 4:
                    c.link(nc.scalar.copy(vg[:, :, 256 * (i - 2):256 * (i - 2) + 256], bank.rearrange("p (a n) -> p a n", a=2)))
                elif i < 6:
                    gs = ggs[:, :, 256 * (i - 4):256 * (i - 4) + 256]
                    c.link(nc.scalar.activation(gs, bank.rearrange("p (a n) -> p a n", a=2), ACT.Sigmoid))
                elif i < 8:
                    c.link(nc.scalar.copy(sq_t[:, 2 * (i - 6):2 * (i - 6) + 2, :], bank.rearrange("p (i t) -> p i t", i=2)))
                else:
                    for kv in range(2):
                        for par in range(2):
                            c.link(nc.scalar.copy(kz[64 * par:64 * par + 64, kv, par, :], bank[64 * kv:64 * kv + 64, 0:256]))
                    c.link(nc.scalar.copy(svt[:, :, :], bank[:, 256:512].rearrange("p (a n) -> p a n", a=2)))
            c.at("bp.a")
            c = Counter(act, a["bg"])
            act.wait_ge(t["bg"], STEP["bg.lr"])
            c.link(nc.scalar.copy(glr_t, ps[0:16, 0, 0:256]))
            c.at("bg.glr")
            act.wait_ge(t["bg"], STEP["bg.z"])
            for i in range(2):
                c.link(nc.scalar.activation(zb[:, i, :], ps[:, 1, 256 * i:256 * i + 256], ACT.Identity, bias=prm_c[:, 54 + i:55 + i]))
            c.at("bg.zb")
            c.link(nc.scalar.activation(az[:, :, :], zb[:, :, :], ACT.Abs))
            c.link(nc.scalar.activation(az[:, :, :], az[:, :, :], ACT.Exp, scale=-1.0))
            c.link(nc.scalar.activation(az[:, :, :], az[:, :, :], ACT.Ln, bias=ones[:, 0:1]))
            c.at("bg.ln")
            act.wait_ge(v["bg"], STEP["bg.scan"])
            c.link(nc.scalar.activation(eb[:, :, :], nb2[:, :, :], ACT.Exp, scale=-1.0 / 16))
            c.link(nc.scalar.activation(enb[:, :, :], nb2[:, :, :], ACT.Exp, scale=1.0 / 16))
            c.at("bg.exp")
            act.wait_ge(v["bg"], STEP["bg.kt"])
            act.wait_ge(g["bp"], STEP["bp.zero"])
            c.link(nc.scalar.copy(ktz[0:64, 0::2, :], kg[0:64, :, :]))
            c.link(nc.scalar.copy(ktz[64:128, 1::2, :], kg[64:128, :, :]))
            c.at("bg.pad")
            act.wait_ge(t["bg"], STEP["bg.tr"])
            c.link(nc.scalar.copy(ket[:, :, :], ps[:, 0, :].rearrange("p (a n) -> p a n", a=2)))
            c.at("bg.ket")
            c = Counter(act, a["bs"])
            act.wait_ge(v["bs"], STEP["bs.sub"])
            c.link(nc.scalar.activation(sc[:, :, :], sc[:, :, :], ACT.Exp))
            c.link(nc.scalar.activation(swm[:, 16:32], swm[:, 16:32], ACT.Exp))
            c.at("bs.exp")
            for j in range(6):
                act.wait_ge(t["bs"], STEP["bs.pt0"] + j)
                c.link(nc.scalar.copy(p_t[:, 4 * j:4 * j + 4, :], ps[:, j, :].rearrange("p (j q) -> p j q", j=4)))
            c.at("bs.pt")
            c = Counter(act, a["bo"])
            for k in range(0, KT, 2):
                act.wait_ge(t["bo"], k // 2 + 1)
                c.link(nc.scalar.copy(hT[:, k:k + 2, :], ps[:, k // 2, :].rearrange("p (k t) -> p k t", k=2)))
            c.at("bo.hT")
            act.wait_ge(v["bo"], STEP["bo.x"])
            a_norm(act, "l0", *mod_of[1])
            a_mlp_loop(act, 0)
            act.wait_ge(v["l0"], STEP["l0.x"])
            a_norm(act, "pn", *mod_of[2])
            act.wait_ge(v["pp"], STEP["pp.x"])
            a_norm(act, "l1", *mod_of[3])
            a_mlp_loop(act, 1)
            act.wait_ge(v["l1"], STEP["l1.x"])
            c = Counter(act, a["z"])
            for tt in range(TT):
                c.link(nc.scalar.activation(xn[:, tt, :], x_sb[:, tt, :], ACT.Square, accum_out=small[:, tt:tt + 1]))
            c.at("z.sq")

        @block.vector
        def _(dve):
            def ada_slot(n):
                vec, q = n // 4, n % 4
                loaded(dve, ("ada", n))
                w = slot(("ada", n)).rearrange("p (t n) -> p t n", t=2)
                acc = macc[:, vec % 3, :]
                if q == 0 and vec >= 3:
                    dve.wait_ge(t_ada, vec - 2)
                for r in range(2):
                    k = 2 * q + r
                    if k == 0:
                        ins = nc.vector.tensor_scalar(acc, w[:, r, :], ccol[:, k:k + 1], None, ALU.mult)
                    else:
                        ins = nc.vector.scalar_tensor_tensor(acc, w[:, r, :], ccol[:, k:k + 1], acc, ALU.mult, ALU.add)
                    ada.link(ins)

            ada = Counter(dve, v_ada)
            c = Counter(dve, v["c"])
            dve.wait_ge(a["c"], STEP["c.sig"])
            c.link(nc.vector.tensor_tensor(ccol[:, :], ccol[:, :], csig[:, :], ALU.mult))
            for n in range(8):
                ada_slot(n)

            def mod_mix(c):
                dve.wait_ge(t_ada, 2)
                dve.wait_ge(par_in, 16 * 5)
                c.link(nc.vector.tensor_tensor(mod_c[:, 0, :], ps[:, 6, 0:8], adab_c[:, 0, :], ALU.add))
                c.link(nc.vector.tensor_tensor(mod_c[:, 1, :], ps[:, 7, 0:8], adab_c[:, 1, :], ALU.add))
                c.link(nc.vector.scalar_tensor_tensor(mod_c[:, 1, :], mod_c[:, 1, :], 1.0, norm_c[:, 0, :],
                                                      ALU.add, ALU.mult))

            v_norm(dve, "n", mod_c[:, 0, :], mod_c[:, 1, :], mod_mix)

            c = Counter(dve, v["w"])
            dve.wait_ge(t["w"], STEP["w.prm"])
            c.link(nc.vector.tensor_copy(prm_c[:, :], ps[:, 0, 256:336]))
            c.at("w.prmc")
            dve.wait_ge(gate_in, 16 * 7)
            c.link(nc.vector.tensor_scalar(gate_b[:, 1:2], gate_b[:, 0:1], 1 / CAP, None, ALU.mult))
            c.at("w.gb")
            c.at("w.pre")
            for n in range(IN_SLOTS):
                if n < 7:
                    dve.wait_ge(a["w"], n + 1)
                    dt = dtmp[:, :].rearrange("p (i t) -> p i t", i=2)
                    c.link(nc.vector.tensor_tensor(dt, raw[:, n % 2, :, 0:256], raw[:, n % 2, :, 1:257], ALU.subtract))
                    for i in range(2):
                        c.link(nc.vector.scalar_tensor_tensor(u[:, 2 * n + i, :], dt[:, i, :], mu_c[:, 2 * n + i:2 * n + i + 1],
                                                              raw[:, n % 2, i, 1:257], ALU.mult, ALU.add))
                ada_slot(8 + n)
                if n == 6:
                    c.at("w.shift")
            for n in range(21, 24):
                ada_slot(n)
            dve.wait_ge(t_ada, 3)
            for vec, base in ((2, 1), (5, 1)):
                gt = gate1[:, vec // 3, :]
                dve.wait_ge(t_ada, {2: 3, 5: 6}[vec])
                c.link(nc.vector.tensor_tensor(gt.rearrange("p (b n) -> p b n", b=2), gt.rearrange("p (b n) -> p b n", b=2),
                                               ps[:, base:base + 2, :], ALU.add))
                c.at(f"w.gate{vec}")
            c.link(nc.vector.tensor_tensor(mod_c[:, 2, :], ps[:, 3, 0:8], adab_c[:, 3, :], ALU.add))
            c.link(nc.vector.tensor_tensor(mod_c[:, 3, :], ps[:, 3, 8:16], adab_c[:, 4, :], ALU.add))
            c.link(nc.vector.scalar_tensor_tensor(mod_c[:, 3, :], mod_c[:, 3, :], 1.0, norm_c[:, 1, :], ALU.add, ALU.mult))
            c.at("w.mod")

            c = Counter(dve, v["m"])
            dve.wait_ge(a["w"], STEP["w.a"])
            for i in range(4):
                c.link(nc.vector.tensor_scalar(qk[:, i, :], convraw[:, i, 3:259], cw_c[:, 12 + i:13 + i], cb_c[:, i:i + 1],
                                               ALU.mult, ALU.add))
                for j in range(3):
                    c.link(nc.vector.scalar_tensor_tensor(qk[:, i, :], convraw[:, i, j:j + 256],
                                                          cw_c[:, 4 * j + i:4 * j + i + 1], qk[:, i, :], ALU.mult, ALU.add))
            c.at("m.conv")
            dve.wait_ge(a["m"], STEP["m.sig"])
            c.link(nc.vector.tensor_tensor(qk[:, :, :], qk[:, :, :], qsig[:, :, :], ALU.mult))
            c.at("m.qk")
            dve.wait_ge(a["m"], STEP["m.lf"])
            one4 = ones2[0:4, :]
            c.link(nc.vector.tensor_scalar(mrow[0:4, 0, :], mrow[0:4, 0, :], CAP, None, ALU.mult))
            c.link(nc.vector.tensor_tensor_scan(mrow[0:4, 2, :], one4, mrow[0:4, 1, :], 0.0, ALU.mult, ALU.add))
            c.link(nc.vector.tensor_tensor(mrow[0:4, 4, :], mrow[0:4, 0, :], mrow[0:4, 2, :], ALU.add))
            c.link(nc.vector.tensor_tensor_scan(mrow[0:4, 5, :], one4, mrow[0:4, 4, :], 0.0, ALU.mult, ALU.max))
            c.link(nc.vector.tensor_tensor(mrow[32:36, 4, :], mrow[0:4, 2, :], mrow[0:4, 5, :], ALU.subtract))
            c.link(nc.vector.tensor_copy(sel4[:, :, :], ident[0:4, 0:4].unsqueeze(2).to_broadcast([4, 4, P])))
            c.at("m.rows")
            dve.wait_ge(t["m"], STEP["m.bc"])
            c.link(nc.vector.tensor_copy(mcol[:, :, :], ps[:, 0, 0:128].rearrange("p (a n) -> p a n", a=2)))
            for h in range(4):
                mb = ps[:, 2 + h // 2, (h % 2) * 256:(h % 2) * 256 + 256]
                c.link(nc.vector.tensor_scalar(mz[:, h, 0:256], mb, mcol[:, 0, h:h + 1], 0.0, ALU.subtract, ALU.max))
                c.link(nc.vector.tensor_scalar(mz[:, h, 256:384], mb[:, 128:256], mcol[:, 1, h:h + 1], 0.0,
                                               ALU.subtract, ALU.max))
            c.at("m.z")
            dve.wait_ge(a["m"], STEP["m.exp"])
            dve.wait_ge(g["c"], STEP["c.masks"])
            cmask = m_causal.unsqueeze(1).to_broadcast([P, 4, P])
            c.link(nc.vector.tensor_tensor(mz[:, :, 0:128], mz[:, :, 0:128], cmask, ALU.mult))
            c.link(nc.vector.tensor_tensor(mz[:, :, 256:384], mz[:, :, 256:384], cmask, ALU.mult))
            dve.wait_ge(t["m"], STEP["m.sc"])
            for h in range(4):
                c.link(nc.vector.scalar_tensor_tensor(mz[:, h, :], ps[:, 4 + h, 0:384], 0.125, mz[:, h, :],
                                                      ALU.mult, ALU.mult))
            c.at("m.pt")
            dve.wait_ge(t["m"], STEP["m.num"])
            den, rec = small[:, 16:24], small[:, 24:32]
            c.link(nc.vector.tensor_copy(den, ps[:, 2, 0:8]))
            c.link(nc.vector.scalar_tensor_tensor(den, den, -1.0, den, ALU.mult, ALU.max))
            c.link(nc.vector.tensor_tensor(den, den, mem[:, :, :].rearrange("p a h -> p (a h)"), ALU.max))
            c.link(nc.vector.reciprocal(rec, den))
            ym = ytok[:, :, 512:1024]
            for tt in range(TT):
                c.link(nc.vector.tensor_tensor(ym[:, tt, :].rearrange("p (h n) -> p h n", h=4),
                                               ps[:, tt, :].rearrange("p (h n) -> p h n", h=4),
                                               rec[:, 4 * tt:4 * tt + 4].unsqueeze(2).to_broadcast([P, 4, P]), ALU.mult))
            c.link(nc.vector.tensor_tensor(msq[:, :, :], ym, ym, ALU.mult))
            for tt in range(TT):
                c.link(nc.vector.tensor_reduce(small[:, 8 + 4 * tt:12 + 4 * tt], msq[:, tt, :].rearrange("p (h n) -> p h n", h=4),
                                               AX_X, ALU.add))
            c.link(nc.vector.tensor_scalar(small[:, 8:16], small[:, 8:16], 1 / P, EPS, ALU.mult, ALU.add))
            c.at("m.ss")
            dve.wait_ge(g["m"], STEP["m.rs"])
            dve.wait_ge(row_in, 48)
            for tt in range(TT):
                yv = ym[:, tt, :].rearrange("p (h n) -> p h n", h=4)
                c.link(nc.vector.tensor_tensor(yv, yv, small[:, 8 + 4 * tt:12 + 4 * tt].unsqueeze(2).to_broadcast([P, 4, P]),
                                               ALU.mult))
            c.link(nc.vector.tensor_tensor(ym, ym, rowp[:, 2, :].unsqueeze(1).to_broadcast([P, TT, 512]), ALU.mult))
            c.link(nc.vector.tensor_tensor(ym, ym, om[:, :, :], ALU.mult))
            c.at("m.y")

            c = Counter(dve, v["r"])
            r_, k_ = u[:, 0:4, :], u[:, 4:8, :]

            def col4(x, n=SEQ):
                return x.unsqueeze(2).to_broadcast([P, 4, n])

            c.link(nc.vector.tensor_tensor(kx[:, :, :], k_, col4(kk_c), ALU.mult))
            c.link(nc.vector.tensor_tensor(sq[:, :, :], kx[:, :, :], kx[:, :, :], ALU.mult))
            c.at("r.sq")
            dve.wait_ge(a["r"], STEP["r.sig"])
            c.link(nc.vector.tensor_scalar(lw[:, :, :], lw[:, :, :], -DECAY, None, ALU.mult))
            for i in range(4):
                c.link(nc.vector.tensor_tensor_scan(cum[:, i, :], reset[:, :], lw[:, i, :], 0.0, ALU.mult, ALU.add))
            c.at("r.scan")
            c.link(nc.vector.scalar_tensor_tensor(kmod[:, :, :], av[:, :, :], 1.0, col4(ka_c), ALU.subtract, ALU.mult))
            c.link(nc.vector.scalar_tensor_tensor(kmod[:, :, :], kmod[:, :, :], 1.0, k_, ALU.add, ALU.mult))
            c.link(nc.vector.tensor_tensor(rkp[:, :, :], r_, kmod[:, :, :], ALU.mult))
            c.link(nc.vector.tensor_tensor(rkp[:, :, :], rkp[:, :, :], col4(rk_c), ALU.mult))
            c.at("r.rkp")
            dve.wait_ge(a["r"], STEP["r.sqrt"])
            c.link(nc.vector.tensor_scalar(kn[:, :, :], kn[:, :, :], 1e-12, None, ALU.max))
            c.link(nc.vector.reciprocal(kn[:, :, :], kn[:, :, :]))
            c.link(nc.vector.tensor_tensor(kx[:, :, :], kx[:, :, :], kn[:, :, :], ALU.mult))
            chunk = lambda x: x.rearrange("p i (c s) -> p i c s", s=CH)
            aq, kxc, pcc = chunk(ar[:, :, 0, :]), chunk(kx), chunk(pcum)
            c.link(nc.vector.tensor_tensor(aq[:, :, :, 1:CH], kxc[:, :, :, 1:CH], pcc[:, :, :, 0:CH - 1], ALU.mult))
            c.link(nc.vector.tensor_copy(aq[:, :, :, 0:1], kxc[:, :, :, 0:1]))
            c.link(nc.vector.tensor_tensor(ar[:, :, 1, :], r_, pcum[:, :, :], ALU.mult))
            c.link(nc.vector.tensor_tensor(sq[:, :, :], kx[:, :, :], av[:, :, :], ALU.mult))
            c.link(nc.vector.tensor_tensor(bh[:, :, :], sq[:, :, :], pinv[:, :, :], ALU.mult))
            c.link(nc.vector.tensor_tensor(kh[:, :, :], kmod[:, :, :], pinv[:, :, :], ALU.mult))
            c.at("r.bh")
            c.link(nc.vector.tensor_copy(pend[:, :, :], pcc[:, :, :, CH - 1]))
            pb = pend[:, :, :].unsqueeze(3).to_broadcast([P, 4, NC, CH])
            c.link(nc.vector.tensor_tensor(chunk(bend), chunk(bh), pb, ALU.mult))
            c.link(nc.vector.tensor_tensor(chunk(kend), chunk(kh), pb, ALU.mult))
            c.at("r.bend")
            dve.wait_ge(t["r"], STEP["r.bonus"])
            c.link(nc.vector.tensor_copy(bon[:, :, :], ps[:, 6, 0:16].rearrange("p (a h) -> p a h", a=2)))
            c.at("r.bon")

            c = Counter(dve, v["i"])

            def m4(m):
                return m.unsqueeze(1).to_broadcast([P, 4, P])

            dve.wait_ge(a["r"], STEP["r.tok"])
            for step, (kind, src, arg, dst) in enumerate(INV_V):
                for gi in range(4):
                    if src is not None:
                        dve.wait_ge(t["i"], 4 * src + gi + 1)
                    if kind == "mask":
                        ins = nc.vector.tensor_tensor(dst[:, gi], bank4(src, gi), m4(arg), ALU.mult)
                    elif kind == "maskF":
                        if step == V_A16:
                            dve.wait_ge(a["i"], gi + 1)
                        ins = nc.vector.tensor_tensor(dst[:, gi], iF[:, gi], m4(arg), ALU.mult)
                    elif kind == "ident":
                        ins = nc.vector.tensor_tensor(dst[:, gi], iB[:, gi], m4(ident[:, :]), ALU.add)
                    elif kind == "lakv":
                        ins = nc.vector.tensor_copy(lakv[:, gi // 2, 256 * (gi % 2):256 * (gi % 2) + 256],
                                                    ps[:, bank_of(src, gi), 0:256])
                    else:
                        ins = nc.vector.tensor_tensor(dst[:, gi], dst[:, gi], bank4(src, gi), ALU.add)
                    c.link(ins)
            c.at("i.done")

            c = Counter(dve, v["s"])
            dve.wait_ge(g["r"], STEP["r.zero"])
            for ch in range(NC):
                r0, tt = CH * (ch % 2), ch // 2
                rr, lk = rbuf[r0:r0 + CH, tt, :], lakv[r0:r0 + CH, tt, :]
                if ch == 0:
                    c.link(nc.vector.tensor_scalar(rr, lk, -1.0, None, ALU.mult))
                else:
                    dve.wait_ge(t_as, ch)
                    c.link(nc.vector.scalar_tensor_tensor(rr, ps[r0:r0 + CH, 0, :], -1.0, lk, ALU.mult, ALU.subtract))
                assert c.n == 5 * ch + 1
                if ch < NC - 1:
                    for hh in range(2):
                        q = slice(64 * hh, 64 * hh + 64)
                        c.link(nc.vector.tensor_tensor(state[q, ch + 1, :, q], state[q, ch, :, q],
                                                       pend[q, :, ch].unsqueeze(2).to_broadcast([64, 4, 64]), ALU.mult))
                    dve.wait_ge(t_ds, ch + 1)
                    for hh in range(2):
                        q = slice(64 * hh, 64 * hh + 64)
                        dl = ps[q, 2, :].rearrange("p (i n) -> p i n", i=4)[:, :, q]
                        c.link(nc.vector.tensor_tensor(state[q, ch + 1, :, q], state[q, ch + 1, :, q], dl, ALU.add))
            c = Counter(dve, v["y"])
            sm, sv = small[:, 32:48], small[:, 48:64]
            for tt in range(TT):
                dve.wait_ge(t_y, tt + 1)
                pv = ps[:, 4 + tt, :].rearrange("p (h n) -> p h n", h=8)
                s8 = sm[:, 8 * tt:8 * tt + 8]
                c.link(nc.vector.tensor_reduce(s8, pv, AX_X, ALU.add))
                c.link(nc.vector.tensor_scalar(s8, s8, 1 / 64, None, ALU.mult))
                c.link(nc.vector.tensor_tensor(ytok[:, tt, 0:512].rearrange("p (h n) -> p h n", h=8), pv,
                                               s8.unsqueeze(2).to_broadcast([P, 8, 64]), ALU.subtract))
            yr = ytok[:, :, 0:512]
            c.link(nc.vector.tensor_tensor(ysq[:, :, :], yr, yr, ALU.mult))
            for tt in range(TT):
                c.link(nc.vector.tensor_reduce(sm[:, 8 * tt:8 * tt + 8], ysq[:, tt, :].rearrange("p (h n) -> p h n", h=8),
                                               AX_X, ALU.add))
            c.link(nc.vector.tensor_scalar(sm, sm, 1 / 64, GN_EPS, ALU.mult, ALU.add))
            c.at("y.var")
            dve.wait_ge(g["y"], STEP["y.rs"])

            def h8(x):
                return x.rearrange("p a (h n) -> p (a h) n", h=8)

            for tt in range(TT):
                yv = ytok[:, tt, 0:512].rearrange("p (h n) -> p h n", h=8)
                c.link(nc.vector.tensor_tensor(yv, yv, sm[:, 8 * tt:8 * tt + 8].unsqueeze(2).to_broadcast([P, 8, 64]), ALU.mult))
            c.link(nc.vector.tensor_tensor(yr, yr, rowp[:, 0, :].unsqueeze(1).to_broadcast([P, TT, 512]), ALU.mult))
            c.link(nc.vector.tensor_tensor(yr, yr, rowp[:, 1, :].unsqueeze(1).to_broadcast([P, TT, 512]), ALU.add))
            c.link(nc.vector.tensor_tensor(h8(ysq), h8(vtok), bon[:, :, :].rearrange("p a h -> p (a h)").unsqueeze(2)
                                           .to_broadcast([P, 16, 64]), ALU.mult))
            c.link(nc.vector.tensor_tensor(yr, yr, ysq[:, :, :], ALU.add))
            c.link(nc.vector.tensor_tensor(yr, yr, gtok[:, :, :], ALU.mult))
            c.at("y.done")
            c = Counter(dve, v["o"])
            dve.wait_ge(par_in, 16 * 5)
            for j in range(4):
                dve.wait_ge(t_out, j + 1)
                xs = x_sb[:, j // 2, 512 * (j % 2):512 * (j % 2) + 512]
                c.link(nc.vector.tensor_tensor(dtmp[:, :], ps[:, 4 + j, :], gate1[:, 0, 512 * (j % 2):512 * (j % 2) + 512], ALU.mult))
                c.link(nc.vector.tensor_tensor(xs, xs, dtmp[:, :], ALU.add))
            c.at("o.x")
            nc.vector.memset(dtmp[:, :], 0.0).then_inc(v_ada2, CREDIT)
            dve.wait_ge(v_ada2, CREDIT)
            nc.vector.memset(dtmp[:, :], 0.0).then_inc(v_moe, CREDIT)
            dve.wait_ge(v_moe, CREDIT)
            nc.vector.memset(dtmp[:, :], 0.0).then_inc(v_mod, CREDIT)
            v_norm(dve, "q", mod_c[:, 2, :], mod_c[:, 3, :])

            c = Counter(dve, v["e"])
            R = lambda i, n: rt[:, i, :, 0:n]
            b8 = lambda x, n: x.to_broadcast([P, TT, n])
            rv = lambda n: rev[:, 8 - n:8].unsqueeze(1).to_broadcast([P, TT, n])
            dve.wait_ge(t["e"], STEP["e.rt"])
            dve.wait_ge(rt_in, 64)
            c.link(nc.vector.tensor_tensor(lg[:, :, :], ps[:, 4, 0:128].rearrange("p (a n) -> p a n", a=2)[:, :, 0:36],
                                           b_rt.unsqueeze(1).to_broadcast([P, TT, 36]), ALU.add))
            gl = lg[:, :, 32:36]
            c.link(nc.vector.tensor_reduce(R(0, 1), gl, AX_X, ALU.max))
            c.link(nc.vector.tensor_tensor(R(1, 4), gl, b8(R(0, 1), 4), ALU.subtract))
            c.at("e.g")

            def first_max(vals, top, n, onehot, key):
                c.link(nc.vector.tensor_tensor(onehot, vals, b8(top, n), ALU.is_equal))
                c.link(nc.vector.tensor_tensor(onehot, onehot, rv(n), ALU.mult))
                c.link(nc.vector.tensor_reduce(key, onehot, AX_X, ALU.max))
                c.link(nc.vector.tensor_tensor(onehot, rv(n), b8(key, n), ALU.is_equal))

            first_max(gl, R(0, 1), 4, R(2, 4), R(3, 1))
            prod = rt[:, 10:11].rearrange("p o a n -> p (o a) n")
            c.link(nc.vector.tensor_tensor(prod.rearrange("p a (g e) -> p a g e", g=NG),
                                           lg[:, :, 0:32].rearrange("p a (g e) -> p a g e", g=NG),
                                           R(2, 4).unsqueeze(3).to_broadcast([P, TT, NG, EG]), ALU.mult))
            sel = R(4, 8)
            c.link(nc.vector.tensor_reduce(sel, prod.rearrange("p a (g e) -> p a e g", g=NG), AX_X, ALU.add))
            c.link(nc.vector.tensor_reduce(R(5, 1), sel, AX_X, ALU.max))
            first_max(sel, R(5, 1), 8, R(6, 8), R(3, 1))
            c.link(nc.vector.scalar_tensor_tensor(sel, R(6, 8), -3e38, sel, ALU.mult, ALU.add))
            c.link(nc.vector.tensor_reduce(R(7, 1), sel, AX_X, ALU.max))
            first_max(sel, R(7, 1), 8, R(8, 8), R(3, 1))
            c.link(nc.vector.tensor_tensor(R(9, 1), R(7, 1), R(5, 1), ALU.subtract))
            c.at("e.d")
            dve.wait_ge(a["e"], STEP["e.expg"])
            c.link(nc.vector.tensor_reduce(R(0, 1), R(1, 4), AX_X, ALU.add))
            dve.wait_ge(a["e"], STEP["e.expd"])
            c.link(nc.vector.tensor_scalar(R(11, 1), R(9, 1), 1.0, None, ALU.add))
            c.link(nc.vector.tensor_tensor(R(11, 1), R(11, 1), R(0, 1), ALU.mult))
            c.link(nc.vector.reciprocal(R(11, 1), R(11, 1)))
            c.link(nc.vector.tensor_tensor(R(9, 1), R(9, 1), R(11, 1), ALU.mult))
            c.link(nc.vector.tensor_tensor(R(6, 8), R(6, 8), b8(R(11, 1), 8), ALU.mult))
            c.link(nc.vector.tensor_tensor(R(8, 8), R(8, 8), b8(R(9, 1), 8), ALU.mult))
            c.link(nc.vector.tensor_tensor(R(6, 8), R(6, 8), R(8, 8), ALU.add))
            c.link(nc.vector.tensor_tensor(cw[:, :, :].rearrange("p a (g e) -> p a g e", g=NG),
                                           R(2, 4).unsqueeze(3).to_broadcast([P, TT, NG, EG]),
                                           R(6, 8).unsqueeze(2).to_broadcast([P, TT, NG, EG]), ALU.mult))
            c.at("e.cw")
            dve.wait_ge(hot_in, 32)
            for h in range(SWA_H):
                if h:
                    dve.wait_ge(t["e"], STEP["e.bias0"] + h - 1)
                c.link(nc.vector.tensor_copy(relx[0:33, :], rel_sb[0:33, h:h + 1].to_broadcast([33, P])))
                if h == 0:
                    c.at("e.relx0")
            with dve.Fori(0, NE // E_BODY) as m:
                for e8 in range(E_BODY):
                    for tt in range(TT):
                        n = 4 * e8 + 2 * tt
                        dve.wait_ge(a_moe, 4 * E_BODY * m + 4 * e8 + 2 * tt + 1)
                        nc.vector.tensor_tensor(gact[:, tt, :], sg[:, tt, :], ps[:, 4 + tt, 0:FE], ALU.mult).then_inc(v_moe, 1)
                        dve.wait_ge(v_moe, 4 * E_BODY * m + CREDIT + n + 1)
                        nc.vector.scalar_tensor_tensor(eact[:, tt, :], ps[:, 4 + tt, FE:2 * FE],
                                                       cw[:, tt, bass.ds(m * E_BODY + e8, 1)], gact[:, tt, :],
                                                       ALU.mult, ALU.mult).then_inc(v_moe, 1)
                        if e8 < 6:
                            k = 2 * e8 + tt
                            vec, q = k // 4, k % 4
                            acc = macc[:, vec, :]
                            dve.wait_ge(ada2_in[k % 2], 16 * 6 * m + 16 * (k // 2 + 1))
                            for r in range(2):
                                w = ring[:, 6 + k % 2, D * r:D * r + D]
                                cc = ccol[:, 8 + 2 * q + r:9 + 2 * q + r]
                                if 2 * q + r == 0:
                                    ins = nc.vector.tensor_scalar(acc, w, cc, None, ALU.mult)
                                else:
                                    ins = nc.vector.scalar_tensor_tensor(acc, w, cc, acc, ALU.mult, ALU.add)
                                ins.then_inc(v_ada2, 1)
                                dve.wait_ge(v_ada2, 24 * m + CREDIT + 2 * k + r + 1)
                        if (e8, tt) == (6, 1):
                            dve.wait_ge(t_mod, 3 * m + 1)
                            nc.vector.tensor_copy(mod2[:, bass.ds(m, 1), :].rearrange("p o n -> p (o n)"),
                                                  ps[:, 7, 0:32]).then_inc(v_mod, 1)
                        if e8 == 7:
                            dve.wait_ge(t_mod, 3 * m + 2 + tt)
                            gv = gate2[:, bass.ds(m, 1), 512 * tt:512 * tt + 512].rearrange("p o n -> p (o n)")
                            nc.vector.tensor_tensor(gv, gv, ps[:, 7, :], ALU.add).then_inc(v_mod, 1)
            c = Counter(dve, v["f"])
            dve.wait_ge(t_dn, CREDIT + 2 * NE)
            v_residual(dve, c, gate1[:, 1, :])
            c.at("f.moe")
            v_rstd(dve, c, "f")
            dve.wait_ge(nrm_in, 16)
            for tt in range(TT):
                c.link(nc.vector.scalar_tensor_tensor(x_sb[:, tt, :], x_sb[:, tt, :], small[:, tt:tt + 1], nrm_b,
                                                      ALU.mult, ALU.mult))
            c.at("f.x")
            for m in range(4):
                if m == 2:
                    c.link(nc.vector.tensor_tensor(mod2[:, 2, 16:32], mod2[:, 2, 16:32], prm_c[:, 64:80], ALU.add))
                    c.link(nc.vector.scalar_tensor_tensor(mod2[:, 2, 24:32], mod2[:, 2, 24:32], 1.0, prm_c[:, 56:64],
                                                          ALU.add, ALU.mult))
                else:
                    c.link(nc.vector.tensor_tensor(mod2[:, m, 0:16], mod2[:, m, 0:16],
                                                   adab2_c[:, 2 * m:2 * m + 2, :].rearrange("p v t -> p (v t)"), ALU.add))
                    c.link(nc.vector.scalar_tensor_tensor(mod2[:, m, 8:16], mod2[:, m, 8:16], 1.0, norm2_c[:, m, :],
                                                          ALU.add, ALU.mult))
            c.at("f.mod")
            v_norm(dve, "bn", *mod_of[0])
            c = Counter(dve, v["bp"])
            for i in (4, 5):
                dve.wait_ge(a["bp"], i + 1)
                gs = ggs[:, :, 256 * (i - 4):256 * (i - 4) + 256]
                c.link(nc.vector.tensor_tensor(gs, gs, ps[:, 4 + i % 4, :].rearrange("p (a n) -> p a n", a=2), ALU.mult))
            c = Counter(dve, v["bg"])
            dve.wait_ge(a["bg"], STEP["bg.ln"])
            c.link(nc.vector.tensor_scalar(zb[:, :, :], zb[:, :, :], -1.0, 0.0, ALU.mult, ALU.max))
            c.link(nc.vector.tensor_tensor(zb[:, :, :], zb[:, :, :], az[:, :, :], ALU.add))
            for i in range(2):
                c.link(nc.vector.tensor_tensor_scan(nb2[:, i, :], reset[:, :], zb[:, i, :], 0.0, ALU.mult, ALU.add))
            c.at("bg.scan")
            dve.wait_ge(a["bg"], STEP["bg.exp"])
            dve.wait_ge(a["bp"], STEP["bp.a"])
            c.link(nc.vector.scalar_tensor_tensor(qg[:, :, :], qg[:, :, :], 0.125, eb[:, :, :], ALU.mult, ALU.mult))
            c.link(nc.vector.tensor_tensor(kg[:, :, :], kg[:, :, :], enb[:, :, :], ALU.mult))
            c.at("bg.kt")
            c.link(nc.vector.tensor_copy(gdec[:, :, :], chunk2(eb)[:, :, :, CH - 1]))
            c.link(nc.vector.tensor_tensor(chunk2(kend2), chunk2(kg), gdec[:, :, :].unsqueeze(3).to_broadcast([P, 2, NC, CH]),
                                           ALU.mult))
            c.at("bg.kend")
            for tt in range(TT):
                dve.wait_ge(t["bg"], STEP["bg.at0"] + tt)
                c.link(nc.vector.tensor_tensor(at[:, tt], ps[:, 2 + tt, :].rearrange("p (h t) -> p h t", h=4),
                                               m_rb.unsqueeze(1).to_broadcast([P, 4, P]), ALU.mult))
            c.at("bg.at")
            dve.wait_ge(t["bg"], STEP["bg.ds"])
            dve.wait_ge(g["bp"], STEP["bp.zero"])
            for ch in range(NC - 1):
                for hh in range(2):
                    q, e = slice(64 * hh, 64 * hh + 64), slice(P * hh, P * hh + P)
                    st, nx = sg_state[q, ch, :, e], sg_state[q, ch + 1, :, e]
                    c.link(nc.vector.tensor_tensor(nx, st, gdec[q, :, ch].unsqueeze(2).to_broadcast([64, 2, P]), ALU.mult))
                    c.link(nc.vector.tensor_tensor(nx, nx, ps[q, 4 + ch, :].rearrange("p (i n) -> p i n", i=2)[:, :, e], ALU.add))
            c.at("bg.state")
            dve.wait_ge(t["bg"], STEP["bg.o"])
            og = y2[:, :, 0:512]
            c.link(nc.vector.tensor_copy(og, ps[:, 0:2, :]))
            c.link(nc.vector.tensor_tensor(gsq[:, :, :], og, og, ALU.mult))
            c.link(nc.vector.tensor_reduce(small[:, 8:16], gsq[:, :, :].rearrange("p a (h n) -> p (a h) n", h=4), AX_X, ALU.add))
            c.link(nc.vector.tensor_scalar(small[:, 8:16], small[:, 8:16], 1 / P, EPS, ALU.mult, ALU.add))
            c.at("bg.ss")
            dve.wait_ge(g["bg"], STEP["bg.rs"])
            for tt in range(TT):
                ov = og[:, tt, :].rearrange("p (h n) -> p h n", h=4)
                c.link(nc.vector.tensor_tensor(ov, ov, small[:, 8 + 4 * tt:12 + 4 * tt].unsqueeze(2).to_broadcast([P, 4, P]), ALU.mult))
                c.link(nc.vector.tensor_tensor(ov, ov, ggn.unsqueeze(1).to_broadcast([P, 4, P]), ALU.mult))
            c.link(nc.vector.tensor_tensor(og, og, ggs[:, :, :], ALU.mult))
            c.at("bg.y")
            c = Counter(dve, v["bs"])
            dve.wait_ge(bias_in, 16 * SWA_H)
            for j in range(6):
                dve.wait_ge(t["bs"], STEP["bs.s0"] + j)
                if j < 2:
                    c.link(nc.vector.scalar_tensor_tensor(sc[:, 4 * j:4 * j + 4, 0:P], ps[:, j, :].rearrange("p (h k) -> p h k", h=4),
                                                          0.125, bias8[:, 4 * j:4 * j + 4, P:2 * P], ALU.mult, ALU.add))
                else:
                    hs = slice(2 * (j - 2), 2 * (j - 2) + 2)
                    c.link(nc.vector.scalar_tensor_tensor(sc[:, hs, P:3 * P], ps[:, j, :].rearrange("p (h k) -> p h k", h=2),
                                                          0.125, bias8[:, hs, :], ALU.mult, ALU.add))
            mx, es, dn = swm[:, 0:16], swm[:, 16:32], swm[:, 32:48]
            parts = ((0, sc[:, :, 0:P], P), (8, sc[:, :, P:3 * P], 2 * P))
            for o, s_, n in parts:
                c.link(nc.vector.tensor_reduce(mx[:, o:o + 8], s_, AX_X, ALU.max))
                c.link(nc.vector.tensor_tensor(mx[:, o:o + 8], mx[:, o:o + 8], sink_b, ALU.max))
                c.link(nc.vector.tensor_tensor(es[:, o:o + 8], sink_b, mx[:, o:o + 8], ALU.subtract))
                c.link(nc.vector.tensor_tensor(s_, s_, mx[:, o:o + 8].unsqueeze(2).to_broadcast([P, 8, n]), ALU.subtract))
            c.at("bs.sub")
            dve.wait_ge(a["bs"], STEP["bs.exp"])
            for o, s_, n in parts:
                c.link(nc.vector.tensor_reduce(dn[:, o:o + 8], s_, AX_X, ALU.add))
            c.link(nc.vector.tensor_tensor(dn, dn, es, ALU.add))
            c.link(nc.vector.reciprocal(dn, dn))
            c.at("bs.den")
            for tt in range(TT):
                dve.wait_ge(t["bs"], STEP["bs.o"])
                c.link(nc.vector.tensor_tensor(y2[:, tt, 512:1024].rearrange("p (h n) -> p h n", h=8),
                                               ps[:, 6 + tt, :].rearrange("p (h n) -> p h n", h=8),
                                               dn[:, 8 * tt:8 * tt + 8].unsqueeze(2).to_broadcast([P, 8, 64]), ALU.mult))
            c.at("bs.y")
            c = Counter(dve, v["bo"])
            nc.vector.memset(dtmp[:, :], 0.0).then_inc(v_mlp, CREDIT)
            dve.wait_ge(v_mlp, CREDIT)
            dve.wait_ge(t_bout, 4)
            v_residual(dve, c, gate2[:, 0, :], 4)
            c.at("bo.x")
            v_norm(dve, "l0", *mod_of[1])
            v_mlp_loop(dve, 0)
            dve.wait_ge(t_fd, CREDIT + 16)
            c = Counter(dve, v["l0"], STEP["l0.v"])
            v_residual(dve, c, gate2[:, 1, :])
            c.at("l0.x")
            v_norm(dve, "pn", *mod_of[2])
            c = Counter(dve, v["pp"])
            dve.wait_ge(a["pn"], STEP["pn.a"])
            dve.wait_ge(g["pp"], STEP["pp.zero"])
            c.link(nc.vector.tensor_copy(hp[:, :, PAD:], hT[:, :, :]))
            c.link(nc.vector.reciprocal(pinvc[:, :, :], pinvc[:, :, :]))
            c.link(nc.vector.tensor_tensor(pa[:, :, PAD:], hp[:, :, PAD:], hp[:, :, PAD - 1:PAD + 255], ALU.add))
            c.link(nc.vector.tensor_tensor(pb_[:, :, PAD:], pa[:, 2:8, PAD:], pa[:, 2:8, PAD - 2:PAD + 254], ALU.add))
            c.link(nc.vector.tensor_tensor(pa[:, 4:8, PAD:], pb_[:, 2:6, PAD:], pb_[:, 2:6, PAD - 4:PAD + 252], ALU.add))
            c.link(nc.vector.tensor_tensor(pb_[:, 4:6, PAD:], pa[:, 6:8, PAD:], pa[:, 6:8, PAD - 8:PAD + 248], ALU.add))
            for gi, src in enumerate((pa[:, 0:2], pb_[:, 0:2], pa[:, 4:6], pb_[:, 4:6])):
                o = hT[:, 2 * gi:2 * gi + 2, :]
                c.link(nc.vector.tensor_tensor(src[:, :, PAD:], src[:, :, PAD:],
                                               pinvc[:, gi, :].unsqueeze(1).to_broadcast([P, 2, SEQ]), ALU.mult))
                c.link(nc.vector.tensor_tensor(o, src[:, :, PAD:], hp[:, 2 * gi:2 * gi + 2, PAD:], ALU.subtract))
            c.at("pp.h")
            dve.wait_ge(pool_in, 32)
            c.link(nc.vector.tensor_tensor(gate2[:, 2, :], gate2[:, 2, :], psc_b, ALU.mult))
            dve.wait_ge(t["pp"], STEP["pp.mm"])
            v_residual(dve, c, gate2[:, 2, :], 4)
            c.at("pp.x")
            v_norm(dve, "l1", *mod_of[3])
            v_mlp_loop(dve, 1)
            dve.wait_ge(t_fd, CREDIT + 32)
            c = Counter(dve, v["l1"], STEP["l1.v"])
            v_residual(dve, c, gate2[:, 3, :])
            c.at("l1.x")
            c = Counter(dve, v["z"])
            v_rstd(dve, c, "z")
            dve.wait_ge(nrm2_in, 16)
            for tt in range(TT):
                c.link(nc.vector.scalar_tensor_tensor(x_sb[:, tt, :], x_sb[:, tt, :], small[:, tt:tt + 1], nrm_b,
                                                      ALU.mult, ALU.mult))
                if tt == 0:
                    c.at("z.out0")

        @block.tensor
        def _(pe):
            pe.wait_ge(g["c"], STEP["c.ident"])
            for vec in range(2):
                pe.wait_ge(v_ada, 8 * (vec + 1))
                t_columns(macc[:, vec, :], ps[:, 6 + vec, :]).then_inc(t_ada, 1)
            t_norm(pe, "n")

            c = Counter(pe, t["w"])
            pe.wait_ge(prm_in, 16 * 10)
            pe.wait_ge(a["n"], STEP["n.a"])
            pe.wait_ge(v["n"], STEP["n.v"])
            c.mark(nc.tensor.transpose(ps[:, 0, 256:336], prm[0:80, :], ident[0:80, 0:80]))
            c.at("w.prm")
            for n in range(IN_SLOTS):
                loaded(pe, ("win", n))
                if n >= 4:
                    pe.wait_ge(a["w"], n - 3)
                w = slot(("win", n)).rearrange("p (t n) -> p t n", t=8)
                for j in range(2):
                    for k in range(KT):
                        if n < 9:
                            ins = nc.tensor.matmul(ps[:, 4 + n % 4, 256 * j:256 * j + 256], w[:, k, P * j:P * j + P],
                                                   hT[:, k, :], start=k == 0, stop=k == KT - 1)
                        else:
                            ins = nc.tensor.matmul(ps[:, 4 + n % 4, 256 * j:256 * j + 256], hT[:, k, P * j:P * j + P],
                                                   w[:, k, :], start=k == 0, stop=k == KT - 1)
                ins.then_inc(t_win, 1)
            pe.wait_ge(gate_in, 16 * 7)
            pe.wait_ge(v["w"], STEP["w.prmc"])
            for k in range(KT):
                ins = nc.tensor.matmul(ps[0:36, 0, 0:256], w_if[:, k, :], hT[:, k, :], start=k == 0, stop=k == KT - 1)
            c.mark(ins)
            c.at("w.if")
            for vec in range(2, 6):
                pe.wait_ge(v_ada, 8 * (vec + 1))
                if vec in (2, 5):
                    if vec == 5:
                        pe.wait_ge(v["w"], STEP["w.gate2"])
                    for j in range(2):
                        ins = nc.tensor.matmul(ps[:, 1 + j, :], ones[:, :], macc[:, vec % 3, 512 * j:512 * j + 512],
                                               start=True, stop=True)
                else:
                    ins = t_columns(macc[:, vec % 3, :], ps[:, 3, 8 * (vec - 3):8 * (vec - 3) + 8])
                ins.then_inc(t_ada, 1)

            c = Counter(pe, t["m"])
            pe.wait_ge(v["m"], STEP["m.rows"])
            pe.wait_ge(v["w"], STEP["w.mod"])
            for tt in range(TT):
                nc.tensor.transpose(ps[:, 0, 64 * tt:64 * tt + 64], mrow[:, 4, P * tt:P * tt + P], ident[0:64, 0:64])
            for h in range(4):
                ins = nc.tensor.matmul(ps[:, 2 + h // 2, (h % 2) * 256:(h % 2) * 256 + 256], sel4[:, h, :], mrow[0:4, 5, :],
                                       start=True, stop=True)
            c.mark(ins)
            c.at("m.bc")
            pe.wait_ge(a["w"], STEP["w.a"])
            for h in range(4):
                q = slice(64 * (h % 2), 64 * (h % 2) + 64)
                nc.tensor.matmul(ps[:, 4 + h, 0:256], qk[q, 2 + h // 2, 0:P], qk[q, h // 2, :], start=True, stop=True)
                ins = nc.tensor.matmul(ps[:, 4 + h, 256:384], qk[q, 2 + h // 2, P:2 * P], qk[q, h // 2, P:2 * P],
                                       start=True, stop=True)
            c.mark(ins)
            c.at("m.sc")
            pe.wait_ge(v["m"], STEP["m.pt"])
            for tt in range(TT):
                for h in range(4):
                    parts = [(0, 0)] if tt == 0 else [(0, 128), (1, 256)]
                    for i, (s_, o) in enumerate(parts):
                        nc.tensor.matmul(ps[:, tt, P * h:P * h + P], mz[:, h, o:o + P], vm[:, s_, P * h:P * h + P],
                                         start=i == 0, stop=i == len(parts) - 1)
                    for i, (s_, o) in enumerate(parts):
                        ins = nc.tensor.matmul(ps[:, 2, 4 * tt + h:4 * tt + h + 1], mz[:, h, o:o + P], ones[:, 0:1],
                                               start=i == 0, stop=i == len(parts) - 1)
            c.mark(ins)
            c.at("m.num")

            c = Counter(pe, t["r"])
            pe.wait_ge(a["r"], STEP["r.u"])
            pe.wait_ge(v["m"], STEP["m.y"])
            for j in range(2):
                for i in range(4):
                    o = (i % 2) * 256
                    nc.tensor.matmul(ps[:, 2 * j + i // 2, o:o + 256], wup[:, j, P * i:P * i + P], u[:, 12, :],
                                     start=True, stop=True)
            for tt in range(TT):
                ins = nc.tensor.matmul(ps[:, 4 + tt, :], u[:, 13, P * tt:P * tt + P], gup[:, :], start=True, stop=True)
            c.mark(ins)
            c.at("r.wa")
            pe.wait_ge(v["r"], STEP["r.sq"])
            for i in range(4):
                ins = nc.tensor.matmul(ps[:, 6 + i // 2, (i % 2) * 256:(i % 2) * 256 + 256], headblk[:, :], sq[:, i, :],
                                       start=True, stop=True)
            c.mark(ins)
            c.at("r.n2")
            pe.wait_ge(a["r"], STEP["r.sqrt"])
            pe.wait_ge(v["r"], STEP["r.rkp"])
            for tt in range(TT):
                for i in range(4):
                    ins = nc.tensor.matmul(ps[:, 6, 8 * tt + 2 * i:8 * tt + 2 * i + 2], rkp[:, i, P * tt:P * tt + P],
                                           headsel[:, :], start=True, stop=True)
            c.mark(ins)
            c.at("r.bonus")
            pe.wait_ge(v["r"], STEP["r.bend"])
            for b, src in enumerate((u[:, 8:12, :], bend, kend)):
                for tt in range(TT):
                    for i in range(4):
                        ins = nc.tensor.transpose(ps[:, 2 * b + tt, P * i:P * i + P], src[:, i, P * tt:P * tt + P], ident[:, :])
                c.mark(ins)
            c.at("r.tr")

            c = Counter(pe, t["i"])
            pe.wait_ge(a["r"], STEP["r.tok"])
            pe.wait_ge(v["r"], STEP["r.bon"])
            for step, (kind, lhs, rhs, need_a, need_v, free) in enumerate(INV_T):
                for gi in range(4):
                    tt, hf = gi // 2, gi % 2
                    if need_a is not None:
                        pe.wait_ge(a["i"], 4 * need_a + gi + 1)
                    if need_v is not None:
                        pe.wait_ge(v["i"], 4 * need_v + gi + 1)
                    if free is not None:
                        pe.wait_ge({"a": a, "v": v}[free[0]]["i"], 4 * free[1] + gi + 1)
                    tok = slice(P * tt, P * tt + P)
                    for hh in range(4):
                        h = 4 * hf + hh
                        o = bank4(step, gi)[:, hh]
                        if kind == "F":
                            ins = nc.tensor.matmul(o, ar[:, h // 2, 0, tok], bhz[:, h, tok], start=True, stop=True)
                        elif kind == "G":
                            ins = nc.tensor.matmul(o, lhs[:, h, tok], ar[:, h // 2, rhs, tok], start=True, stop=True)
                        elif kind == "T":
                            ins = nc.tensor.transpose(o, lhs[:, gi, hh], ident[:, :])
                        elif kind == "V":
                            ins = nc.tensor.matmul(ps[:, bank_of(step, gi), 64 * hh:64 * hh + 64], lhs[:, gi, hh],
                                                   vtok[:, tt, 64 * h:64 * h + 64], start=True, stop=True)
                        else:
                            ins = nc.tensor.matmul(o, lhs[:, gi, hh], rhs[:, gi, hh], start=True, stop=True)
                    c.mark(ins)

            pe.wait_ge(v["i"], STEP["i.done"])
            pe.wait_ge(g["r"], STEP["r.zero"])
            for ch in range(NC):
                r0, tt = CH * (ch % 2), ch // 2
                rows, toks = slice(r0, r0 + CH), slice(CH * ch, CH * ch + CH)
                if ch:
                    pe.wait_ge(v["s"], 5 * ch)
                    for i in range(4):
                        ins = nc.tensor.matmul(ps[rows, 0, P * i:P * i + P], ar[:, i, 0, toks], state[:, ch, i, :],
                                               start=True, stop=True)
                    ins.then_inc(t_as, 1)
                pe.wait_ge(v["s"], 5 * ch + 1)
                for h in range(8):
                    ins = nc.tensor.matmul(ps[rows, 1, 64 * h:64 * h + 64], iQ[:, 2 * tt + h // 4, h % 4, rows],
                                           rbuf[:, tt, 64 * h:64 * h + 64], start=True, stop=True)
                ins.then_inc(t_u, 1)
                if ch < NC - 1:
                    pe.wait_ge(a["s"], ch + 1)
                    for i in range(4):
                        cols = slice(P * i, P * i + P)
                        nc.tensor.matmul(ps[:, 2, cols], bend_t[rows, tt, cols], ubuf[rows, tt, cols], start=True, stop=False)
                        ins = nc.tensor.matmul(ps[:, 2, cols], kend_t[rows, tt, cols], vtok[rows, tt, cols],
                                               start=False, stop=True)
                    ins.then_inc(t_ds, 1)
            pe.wait_ge(a["s"], NC)
            for tt in range(TT):
                for i in range(4):
                    cols = slice(P * i, P * i + P)
                    for hf in range(2):
                        ch = 2 * tt + hf
                        nc.tensor.matmul(ps[CH * hf:CH * hf + CH, 4 + tt, cols], ar[:, i, 1, CH * ch:CH * ch + CH],
                                         state[:, ch, i, :], start=True, stop=False, skip_group_check=True)
                    for h in (2 * i, 2 * i + 1):
                        hc = slice(64 * h, 64 * h + 64)
                        nc.tensor.matmul(ps[:, 4 + tt, hc], grb[:, 2 * tt + h // 4, h % 4, :], ubuf[:, tt, hc],
                                         start=False, stop=False, skip_group_check=True)
                        ins = nc.tensor.matmul(ps[:, 4 + tt, hc], grk[:, 2 * tt + h // 4, h % 4, :], vtok[:, tt, hc],
                                               start=False, stop=True, skip_group_check=True)
                ins.then_inc(t_y, 1)

            c = Counter(pe, t["o"])
            pe.wait_ge(v["y"], STEP["y.done"])
            for k in range(KT):
                for tt in range(TT):
                    o = (k % 2) * 256 + tt * P
                    ins = nc.tensor.transpose(ps[:, k // 2, o:o + P], ytok[:, tt, k::8], ident[:, :])
                if k % 2:
                    c.mark(ins)
            pe.wait_ge(wout_in, 64)
            pe.wait_ge(a["o"], STEP["o.hT"])
            for j in range(4):
                for k in range(KT):
                    w = ring[:, k // 2, :].rearrange("p (t n) -> p t n", t=2)[:, k % 2, 512 * (j % 2):512 * (j % 2) + 512]
                    ins = nc.tensor.matmul(ps[:, 4 + j, :], hT[:, k, P * (j // 2):P * (j // 2) + P], w,
                                           start=k == 0, stop=k == KT - 1)
                ins.then_inc(t_out, 1)
            nc.tensor.matmul(ps[0:1, 0, 0:1], ones[:, 0:1], ones[:, 0:1], start=True, stop=True).then_inc(t_gu, CREDIT)
            nc.tensor.matmul(ps[0:1, 0, 0:1], ones[:, 0:1], ones[:, 0:1], start=True, stop=True).then_inc(t_dn, CREDIT)
            t_norm(pe, "q")
            c = Counter(pe, t["e"])
            pe.wait_ge(rt_in, 64)
            pe.wait_ge(a["q"], STEP["q.a"])
            pe.wait_ge(v["q"], STEP["q.v"])
            for tt in range(TT):
                for k in range(KT):
                    ins = nc.tensor.matmul(ps[:, 4, 64 * tt:64 * tt + 36], hT[:, k, P * tt:P * tt + P], w_rt[:, k, :],
                                           start=k == 0, stop=k == KT - 1)
            c.mark(ins)
            c.at("e.rt")
            for h in range(SWA_H):
                pe.wait_ge(v["e"], STEP["e.relx0"] + h)
                if h:
                    pe.wait_ge(a["e"], STEP["e.expd"] + h)
                c.mark(nc.tensor.matmul(ps[:, 7, 0:384], relx[0:33, :], hots[0:33, :], start=True, stop=True))
                if h == 0:
                    c.at("e.bias0")
            pe.wait_ge(a["e"], STEP["e.bias"])
            t_zero(pe)

            def gate_up(m, e8, tt, ks):
                s0 = 3 * (e8 % 2)
                if ks[0] == 0:
                    if tt == 0:
                        for j in range(2):
                            pe.wait_ge(moe_in[s0 + j], 16 * (E_BODY // 2) * m + 16 * (e8 // 2 + 1))
                    pe.wait_ge(v_moe, 4 * E_BODY * m + 4 * e8 + 2 * tt + 2)
                for k in ks:
                    ins = nc.tensor.matmul(ps[:, 4 + tt, :].rearrange("p (j n) -> p j n", j=2), hT[:, k, P * tt:P * tt + P],
                                           ring[:, s0:s0 + 2, FE * k:FE * k + FE], start=k == 0, stop=k == KT - 1,
                                           skip_group_check=True)
                if ks[-1] == KT - 1:
                    ins.then_inc(t_gu, 1)

            def turn(m, e8, tt):
                pe.wait_ge(v_moe, 4 * E_BODY * m + 4 * e8 + 2 * tt + 2 + CREDIT)
                for f in range(2):
                    ins = nc.tensor.transpose(ps[:, 6, FE * tt + P * f:FE * tt + P * f + P], eact[:, tt, f::2], ident[:, :])
                ins.then_inc(t_tr, 1)

            def down(m, e8, tt):
                s0 = 3 * (e8 % 2)
                if tt == 0:
                    pe.wait_ge(moe_in[s0 + 2], 16 * (E_BODY // 2) * m + 16 * (e8 // 2 + 1))
                pe.wait_ge(a_moe, 4 * E_BODY * m + 4 * e8 + 2 * tt + 2)
                for f in range(2):
                    for j in range(2):
                        ins = nc.tensor.matmul(ps[:, 2 * tt + j, :], eact_t[:, tt, f, :],
                                               ring[:, s0 + 2, D * f + 512 * j:D * f + 512 * j + 512],
                                               start=False, stop=False, skip_group_check=True)
                ins.then_inc(t_dn, 1)

            def gate_row(m, j):
                pe.wait_ge(v_mod, 3 * m + 1 + j + CREDIT)
                nc.tensor.matmul(ps[:, 7, :], ones[:, :], macc[:, 2, 512 * j:512 * j + 512], start=True, stop=True
                                 ).then_inc(t_mod, 1)

            with pe.Fori(0, NE // E_BODY) as m:
                for e8 in range(E_BODY):
                    gate_up(m, e8, 0, range(8))
                    gate_up(m, e8, 1, range(6))
                    turn(m, e8, 0)
                    gate_up(m, e8, 1, range(6, 8))
                    if e8 == 6:
                        pe.wait_ge(v_ada2, 24 * m + 24 + CREDIT)
                        pe.wait_ge(v_mod, 3 * m + CREDIT)
                        for vec in range(2):
                            t_columns(macc[:, vec, :], ps[:, 7, 8 * vec:8 * vec + 8])
                            for k in range(KT):
                                ins = nc.tensor.matmul(ps[:, 7, 16 + 8 * vec + k:17 + 8 * vec + k],
                                                       macc[:, vec, P * k:P * k + P], ones[:, 0:1], start=True, stop=True)
                        ins.then_inc(t_mod, 1)
                    if e8 == 7:
                        gate_row(m, 0)
                    down(m, e8, 0)
                    turn(m, e8, 1)
                    if e8 == 7:
                        gate_row(m, 1)
                    down(m, e8, 1)
            pe.wait_ge(v["f"], STEP["f.mod"])
            t_norm(pe, "bn")
            pe.wait_ge(v["bn"], STEP["bn.v"])
            pe.wait_ge(a["bn"], STEP["bn.a"])
            pe.wait_ge(v_mod, 12 + CREDIT)
            for i in range(9):
                pe.wait_ge(ring2[i % RING], 16 * (i // RING + 1))
                if i >= 4:
                    pe.wait_ge(a["bp"], i - 3)
                if i >= 8:
                    pe.wait_ge(v["bp"], i - 7)
                w = ring[:, i % RING, :].rearrange("p (t n) -> p t n", t=8)
                for j in range(2):
                    for k in range(KT):
                        o = ps[:, 4 + i % 4, 256 * j:256 * j + 256]
                        if i in (0, 1, 6, 7) or (i, j) == (8, 0):
                            ins = nc.tensor.matmul(o, w[:, k, P * j:P * j + P], hT[:, k, :], start=k == 0, stop=k == KT - 1)
                        elif i < 8:
                            ins = nc.tensor.matmul(o, hT[:, k, P * j:P * j + P], w[:, k, :], start=k == 0, stop=k == KT - 1)
                if i == 8:
                    for tt in range(TT):
                        for k in range(KT):
                            ins = nc.tensor.matmul(ps[:, 4, 256 + P * tt:256 + P * tt + P], hT[:, k, P * tt:P * tt + P],
                                                   w[:, k, P:2 * P], start=k == 0, stop=k == KT - 1)
                ins.then_inc(t_bin, 1)
            c = Counter(pe, t["bg"])
            for k in range(KT):
                ins = nc.tensor.matmul(ps[0:16, 0, 0:256], w_glr[:, k, :], hT[:, k, :], start=k == 0, stop=k == KT - 1)
            c.mark(ins)
            c.at("bg.lr")
            pe.wait_ge(a["bg"], STEP["bg.glr"])
            for i in range(2):
                ins = nc.tensor.matmul(ps[:, 1, 256 * i:256 * i + 256], w_gg[:, P * i:P * i + P], glr_t, start=True, stop=True)
            c.mark(ins)
            c.at("bg.z")
            pe.wait_ge(a["bg"], STEP["bg.pad"])
            for tt in range(TT):
                tok = slice(P * tt, P * tt + P)
                for h in range(GLA_H):
                    ins = nc.tensor.matmul(ps[:, 2 + tt, P * h:P * h + P], ktz[:, h, tok], qg[:, h // 2, tok], start=True, stop=True)
                c.mark(ins)
                if tt == 0:
                    c.at("bg.at0")
            pe.wait_ge(v["bg"], STEP["bg.kend"])
            for tt in range(TT):
                for i in range(2):
                    ins = nc.tensor.transpose(ps[:, 0, 256 * tt + P * i:256 * tt + P * i + P], kend2[:, i, P * tt:P * tt + P], ident[:, :])
            c.mark(ins)
            c.at("bg.tr")
            pe.wait_ge(a["bg"], STEP["bg.ket"])
            pe.wait_ge(a["bp"], STEP["bp.a"])
            for ch in range(NC - 1):
                rows, tt = slice(CH * (ch % 2), CH * (ch % 2) + CH), ch // 2
                for i in range(2):
                    ins = nc.tensor.matmul(ps[:, 4 + ch, 256 * i:256 * i + 256], ket[rows, tt, P * i:P * i + P],
                                           vg[rows, tt, 256 * i:256 * i + 256], start=True, stop=True)
            c.mark(ins)
            c.at("bg.ds")
            pe.wait_ge(v["bg"], STEP["bg.state"])
            for tt in range(TT):
                for i in range(2):
                    for hf in range(2):
                        ch = 2 * tt + hf
                        nc.tensor.matmul(ps[CH * hf:CH * hf + CH, tt, 256 * i:256 * i + 256], qg[:, i, CH * ch:CH * ch + CH],
                                         sg_state[:, ch, i, :], start=True, stop=False, skip_group_check=True)
                    for h in (2 * i, 2 * i + 1):
                        ins = nc.tensor.matmul(ps[:, tt, P * h:P * h + P], at[:, tt, h, :], vg[:, tt, P * h:P * h + P],
                                               start=False, stop=True, skip_group_check=True)
            c.mark(ins)
            c.at("bg.o")
            c = Counter(pe, t["bs"])
            pe.wait_ge(v["bg"], STEP["bg.y"])
            for j in range(6):
                hs = range(4 * j, 4 * j + 4) if j < 2 else range(2 * (j - 2), 2 * (j - 2) + 2)
                n = P if j < 2 else 2 * P
                for i, h in enumerate(hs):
                    q = slice(0, P) if j < 2 else slice(P, 2 * P)
                    ins = nc.tensor.matmul(ps[:, j, n * i:n * i + n], sq_t[:, h // 2, q], kz[:, h // 4, h % 2, 0:n],
                                           start=True, stop=True)
                c.mark(ins)
                if j == 0:
                    c.at("bs.s0")
            pe.wait_ge(a["bs"], STEP["bs.exp"])
            for j in range(6):
                for i in range(4):
                    n = 4 * j + i
                    h, o = (n, 0) if n < 8 else ((n - 8) // 2, P + P * (n % 2))
                    ins = nc.tensor.transpose(ps[:, j, P * i:P * i + P], sc[:, h, o:o + P], ident[:, :])
                c.mark(ins)
                if j == 0:
                    c.at("bs.pt0")
            pe.wait_ge(a["bs"], STEP["bs.pt"])
            for h in range(SWA_H):
                kv = slice(64 * (h // 4), 64 * (h // 4) + 64)
                nc.tensor.matmul(ps[:, 6, 64 * h:64 * h + 64], p_t[:, h, :], svt[:, 0, kv], start=True, stop=True)
                for r in range(2):
                    ins = nc.tensor.matmul(ps[:, 7, 64 * h:64 * h + 64], p_t[:, 8 + 2 * h + r, :], svt[:, r, kv],
                                           start=r == 0, stop=r == 1)
            c.mark(ins)
            c.at("bs.o")
            c = Counter(pe, t["bo"])
            pe.wait_ge(v["bs"], STEP["bs.y"])
            for k in range(KT):
                for tt in range(TT):
                    o = (k % 2) * 256 + tt * P
                    ins = nc.tensor.transpose(ps[:, k // 2, o:o + P], y2[:, tt, k::8], ident[:, :])
                if k % 2:
                    c.mark(ins)
            pe.wait_ge(a["bo"], STEP["bo.hT"])
            for q in range(4):
                pe.wait_ge(ring2[(9 + q) % RING], 32)
            for j in range(4):
                for k in range(KT):
                    w = ring[:, (9 + k // 2) % RING, D * (k % 2) + 512 * (j % 2):D * (k % 2) + 512 * (j % 2) + 512]
                    ins = nc.tensor.matmul(ps[:, 4 + j, :], hT[:, k, P * (j // 2):P * (j // 2) + P], w,
                                           start=k == 0, stop=k == KT - 1)
                ins.then_inc(t_bout, 1)
            nc.tensor.matmul(ps[0:1, 0, 0:1], ones[:, 0:1], ones[:, 0:1], start=True, stop=True).then_inc(t_up, CREDIT)
            nc.tensor.matmul(ps[0:1, 0, 0:1], ones[:, 0:1], ones[:, 0:1], start=True, stop=True).then_inc(t_fd, CREDIT)
            t_norm(pe, "l0")
            pe.wait_ge(a["l0"], STEP["l0.a"])
            pe.wait_ge(v["l0"], STEP["l0.v"])
            t_zero(pe)
            t_mlp_loop(pe, 0)
            t_norm(pe, "pn", tiles=True)
            c = Counter(pe, t["pp"])
            pe.wait_ge(v["pp"], STEP["pp.h"])
            pe.wait_ge(pool_in, 32)
            for j in range(4):
                for i in range(2):
                    gi = 2 * (j % 2) + i
                    for r in range(2):
                        ins = nc.tensor.matmul(ps[:, 4 + j, 256 * i:256 * i + 256], hT[:, 2 * gi + r, P * (j // 2):P * (j // 2) + P],
                                               poolw[:, gi, r, :], start=r == 0, stop=r == 1)
            c.mark(ins)
            c.at("pp.mm")
            t_norm(pe, "l1")
            pe.wait_ge(a["l1"], STEP["l1.a"])
            pe.wait_ge(v["l1"], STEP["l1.v"])
            t_zero(pe)
            t_mlp_loop(pe, 1)


_INS = [
    "x", "c", "ada_w", "ada_b", "mix_norm_w", "w_in", "rwkv_mu", "rwkv_w0", "rwkv_w_up", "rwkv_a0",
    "rwkv_a_up", "rwkv_g_up", "rwkv_k_k", "rwkv_k_a", "rwkv_r_k", "rwkv_gn_w", "rwkv_gn_b", "mlstm_conv_w",
    "mlstm_conv_b", "mlstm_i_b", "mlstm_f_b", "mlstm_hn_w", "w_out", "ffn_norm_w", "moe_w_group",
    "moe_b_group", "moe_w_router", "moe_b_router", "moe_w_gate", "moe_w_up", "moe_w_down", "final_norm_w",
    "c_2", "norm_w_2", "ada_w_2", "ada_b_2", "attn_w_in_2", "gla_w_gate_2", "gla_b_gate_2", "gla_norm_w_2",
    "attn_sinks_2", "attn_w_out_2", "rel_bias_2", "pool_w_2", "pool_scale_2", "mlp_w1_2", "mlp_w2_2",
    "final_norm_w_2",
]


def distance_buckets():
    import numpy as np

    half = N_BUCKETS // 2
    dist = 2 * WINDOW - 1 - np.arange(3 * P)
    far = half + (np.log(np.maximum(dist, 1) / half) / np.log(MAX_DIST / half) * half).astype(np.int32)
    bucket = np.where(dist < half, dist, np.minimum(far, N_BUCKETS - 1))
    row = np.where((dist >= 0) & (dist < WINDOW), bucket, N_BUCKETS)
    return (np.arange(N_BUCKETS + 1)[:, None] == row[None, :]).astype(np.float32)


def kernel(**inputs):
    import numpy as _np
    import concourse.bacc as _bacc
    from concourse import mybir as _mybir
    from concourse.bass_utils import run_bass_kernel_spmd as _run

    nc = _bacc.Bacc("TRN2", target_bir_lowering=False, num_devices=1)
    arrays, A = {}, {}
    for name in _INS + ["hots"]:
        a = distance_buckets() if name == "hots" else _np.ascontiguousarray(inputs[name])
        arrays[f"in_{name}_dram"] = a
        A[name] = nc.dram_tensor(f"in_{name}_dram", a.shape, _mybir.dt.from_np(a.dtype), kind="ExternalInput").ap()
    out = nc.dram_tensor("out_0_dram", (1, SEQ, D), F32, kind="ExternalOutput").ap()
    program(nc, A, out)
    r = _run(nc, [arrays], core_ids=[0])
    return r.results[0]["out_0_dram"]
```

```python
from contextlib import ExitStack

import concourse.bass as bass
from concourse import mybir

F32 = mybir.dt.float32
BF16 = mybir.dt.bfloat16
F32R = mybir.dt.float32r
I32 = mybir.dt.int32
ALU = mybir.AluOpType
ACT = mybir.ActivationFunctionType
AX_X = mybir.AxisListType.X

P = 128
D = 1024
SEQ = 256
TT = SEQ // P
KT = D // P
CH = 64
NC = SEQ // CH
EPS = 1e-6
GN_EPS = 64e-5
DECAY = 0.6065306597126334
RW_TILES = 14
IN_SLOTS = 13
NE = 32
FE = 256
SLOT = 2048
RING = 8
CAP = 15.0
NG, EG = 4, 8
E_BODY = 8
LAST_PASS = NE // E_BODY - 1
FF_SLOTS = 4
GLA_H, GLA_DV = 4, 128
SWA_H = 8
N_BUCKETS, MAX_DIST, WINDOW = 32, 128, 128
BIG = -1e30

STEP = {
    "c.ident": 8, "c.zeros": 17, "c.masks": 40, "n.rstd": 1, "m.rs": 1, "r.zero": 5, "y.rs": 1, "y.free": 3,
    "q.rstd": 1, "f.rstd": 1, "bn.rstd": 1, "bp.zero": 3, "bg.rs": 1, "l0.rstd": 1, "pn.rstd": 1, "pp.zero":
    9, "l1.rstd": 1, "z.rstd": 1, "c.sig": 1, "n.sq": 2, "n.a": 6, "w.a": 13, "w.tanh": 15, "m.sig": 1,
    "m.lf": 3, "m.exp": 5, "r.u": 2, "r.sig": 10, "r.gtok": 11, "r.exp": 13, "r.sqrt": 14, "r.pad": 18,
    "r.tok": 21, "i.a": 40, "o.hT": 4, "q.sq": 2, "q.a": 6, "e.expg": 1, "e.expd": 2, "f.sq": 2, "bn.sq": 2,
    "bn.a": 6, "bp.a": 13, "bg.glr": 1, "bg.zb": 3, "bg.ln": 6, "bg.exp": 8, "bg.pad": 10, "bg.ket": 11,
    "bs.exp": 2, "bs.pt": 8, "bo.hT": 4, "l0.sq": 2, "l0.a": 6, "pn.sq": 2, "pn.a": 6, "l1.sq": 2, "l1.a": 6,
    "z.sq": 2, "n.ss": 1, "n.xn": 3, "n.mod": 6, "n.v": 10, "w.prmc": 1, "w.gb": 2, "w.pre": 2, "w.shift": 23,
    "w.gate2": 24, "w.gate5": 25, "w.mod": 28, "m.conv": 16, "m.qk": 17, "m.rows": 23, "m.z": 32, "m.pt": 38,
    "m.ss": 48, "m.y": 52, "r.sq": 2, "r.scan": 7, "r.rkp": 11, "r.bh": 20, "r.bend": 23, "r.bon": 24,
    "i.done": 56, "y.var": 10, "y.done": 17, "o.x": 8, "q.ss": 1, "q.xn": 3, "q.mod": 3, "q.v": 7, "e.g": 3,
    "e.d": 21, "e.cw": 30, "f.moe": 8, "f.ss": 9, "f.x": 11, "f.mod": 19, "bn.ss": 1, "bn.xn": 3, "bn.mod": 3,
    "bn.v": 7, "bg.scan": 4, "bg.kt": 6, "bg.kend": 8, "bg.at": 10, "bg.state": 22, "bg.ss": 26, "bg.y": 31,
    "bs.sub": 14, "bs.den": 18, "bs.y": 20, "bo.x": 8, "l0.ss": 1, "l0.xn": 3, "l0.mod": 3, "l0.v": 7, "l0.x":
    15, "pn.ss": 1, "pn.xn": 3, "pn.mod": 3, "pn.v": 7, "pp.h": 14, "pp.x": 23, "l1.ss": 1, "l1.xn": 3,
    "l1.mod": 3, "l1.v": 7, "l1.x": 15, "z.ss": 1, "z.out0": 2, "n.t": 4, "w.prm": 1, "w.if": 2, "m.bc": 1,
    "m.sc": 2, "m.num": 3, "r.wa": 1, "r.n2": 2, "r.bonus": 3, "r.tr": 6, "q.t": 4, "e.rt": 1, "bn.t": 4,
    "bg.lr": 1, "bg.z": 2, "bg.at0": 3, "bg.tr": 5, "bg.ds": 6, "bg.o": 7, "bs.s0": 1, "bs.pt0": 7, "bs.o":
    13, "l0.t": 4, "pn.t": 4, "pp.mm": 1, "l1.t": 4,
}


class Counter:

    def __init__(self, eng, sem, n=0):
        self.eng, self.sem, self.n = eng, sem, n

    def link(self, ins):
        self.n += 1
        ins.then_inc(self.sem, 1)
        self.eng.wait_ge(self.sem, self.n)

    def mark(self, ins):
        self.n += 1
        ins.then_inc(self.sem, 1)

    def at(self, name):
        assert STEP[name] == self.n, (name, self.n)


def program(nc, A, out):
    ctx = ExitStack()
    with ctx:
        def sb(name, shape, dt=F32):
            return ctx.enter_context(nc.sbuf_tensor(name, shape, dt))

        def sem(name):
            return ctx.enter_context(nc.semaphore(name))

        ps = ctx.enter_context(nc.psum_tensor("ps", [P, 8, 512], F32))

        x_sb = sb("x_sb", [P, TT, D])

        def sb_twice(name, shape):
            whole = sb(name, shape)
            end = nc.sbuf_base
            words = 1
            for n in shape[1:]:
                words *= n
            return whole, nc.alloc_sbuf_tensor_at(name + "_parts", shape, F32R, offset=end - 4 * words)

        hT, hT_lo = sb_twice("hT", [P, KT, SEQ])
        ring, ring_lo = sb_twice("ring", [P, RING, SLOT])
        macc, macc_r = sb_twice("macc", [P, 3, D])
        gate1, gate1_r = sb_twice("gate1", [P, 2, D])
        KB = 256
        arena, arena_r = sb_twice("arena", [P, 91 * KB])

        def area(kb, words):
            return arena[:, int(kb * KB):int(kb * KB) + words]

        def area_r(kb, words):
            return arena_r[:, int(kb * KB):int(kb * KB) + words]

        u = area(0, 14 * 256).rearrange("p (i t) -> p i t", t=SEQ)
        grb = area(0, 16 * 128).rearrange("p (g h s) -> p g h s", g=4, h=4)
        lakv = area(8, 1024).rearrange("p (a n) -> p a n", a=TT)
        ar = area(14, 2048).rearrange("p (i k t) -> p i k t", i=4, k=2)
        bhz = area(22, 2048).rearrange("p (h t) -> p h t", h=8)
        khz = area(30, 2048).rearrange("p (h t) -> p h t", h=8)
        vtok = area(38, 1024).rearrange("p (a n) -> p a n", a=TT)
        bend_t = area(42, 1024).rearrange("p (a n) -> p a n", a=TT)
        kend_t = area(46, 1024).rearrange("p (a n) -> p a n", a=TT)
        convraw = area(42, 4 * 259).rearrange("p (i t) -> p i t", i=4)
        rbuf = area(50, 1024).rearrange("p (a n) -> p a n", a=TT)
        ubuf = area(54, 1024).rearrange("p (a n) -> p a n", a=TT)
        xn = area(50, 2048).rearrange("p (a n) -> p a n", a=TT)
        state = area(58, 2048).rearrange("p (c i v) -> p c i v", c=4, i=4)
        raw = area(58, 4 * 257).rearrange("p (b i t) -> p b i t", b=2, i=2)
        gtok = area(66, 1024).rearrange("p (a n) -> p a n", a=TT)
        ytok = area(70, 2048).rearrange("p (a n) -> p a n", a=TT)
        qk = area(78, 1024).rearrange("p (i t) -> p i t", i=4)
        vm = area(82, 1024).rearrange("p (a n) -> p a n", a=TT)
        om = area(87, 1024).rearrange("p (a n) -> p a n", a=TT)
        grk = hT[:, :, :].rearrange("p k t -> p (k t)").rearrange("p (g h s) -> p g h s", g=4, h=4)
        dtmp = sb("dtmp", [P, 512])

        ident = sb("ident", [P, P])
        ones = sb("ones", [P, P])
        headblk = sb("headblk", [P, P])
        headsel = sb("headsel", [P, 2])
        masks = sb("masks", [P, 7, P])
        same16, same32, same64 = masks[:, 0, :], masks[:, 1, :], masks[:, 2, :]
        m_n16t, m_n16 = masks[:, 3, :], masks[:, 0, :]
        m_32, m_64 = masks[:, 1, :], masks[:, 4, :]
        m_ak, m_rb, m_causal = masks[:, 5, :], masks[:, 2, :], masks[:, 6, :]
        reset = sb("reset", [P, SEQ])
        prm = sb("prm", [P, P])
        prm_c = sb("prm_c", [P, 80])
        mu_c, w0_c, a0_c, kk_c = prm_c[:, 0:14], prm_c[:, 14:18], prm_c[:, 18:22], prm_c[:, 22:26]
        ka_c, rk_c, cb_c, cw_c = prm_c[:, 26:30], prm_c[:, 30:34], prm_c[:, 34:38], prm_c[:, 38:54]
        ccol = sb("ccol", [P, 16])
        csig = sb("csig", [P, 16])
        adab_c = sb("adab_c", [P, 6, 8])
        norm_c = sb("norm_c", [P, 2, 8])
        mod_c = sb("mod_c", [P, 4, 8])
        small = sb("small", [P, 64])
        nhalf = sb("nhalf", [P, 16])
        wup = sb("wup", [P, 2, 512])
        gup = area(47, 512)
        w_if = sb("w_if", [P, 8, 36])
        rowp = macc[:, 0:2, :].rearrange("p v n -> p (v n)")[:, 0:1536].rearrange("p (i n) -> p i n", i=3)
        gate_b = sb("gate_b", [36, 2])
        bon = sb("bon", [P, TT, 8])
        mrow = arena[0:64, 14 * KB:20 * KB].rearrange("p (i t) -> p i t", i=6)
        sel4 = arena[0:4, 20 * KB:22 * KB].rearrange("p (h n) -> p h n", h=4)

        v = {s: sem("v_" + s) for s in "c n w m r i s y o q e f bn bp bg bs bo l0 pn pp l1 z".split()}
        a = {s: sem("a_" + s) for s in "c n w m r i s o q e f bn bp bg bs bo l0 pn l1 z".split()}
        g = {s: sem("g_" + s) for s in "c n m r y q f bn bp bg l0 pn pp l1 z".split()}
        t = {s: sem("t_" + s) for s in "n w m r i o q e bn bg bs bo l0 pn pp l1".split()}
        ring_in = [sem(f"ring_in{i}") for i in range(RING)]
        x_in, c_in, prm_in, par_in, gate_in, row_in = (
            sem(n) for n in ("x_in", "c_in", "prm_in", "par_in", "gate_in", "row_in"))
        v_ada = sem("v_ada")
        t_win = sem("t_win")
        s_out = sem("s_out")

        wout_in = sem("wout_in")
        t_ada, t_as, t_u, t_ds, t_y, t_out = (sem(n) for n in ("t_ada", "t_as", "t_u", "t_ds", "t_y", "t_out"))

        def tmp(i):
            return ring[:, i // 2, 1024 * (i % 2):1024 * (i % 2) + 1024].rearrange("p (i t) -> p i t", i=4)

        lw, cum, av, pcum, pinv, kn, kx, sq, kmod, bh, kh, bend, kend, rkp = (tmp(i) for i in range(14))
        ysq = ring[:, 6, 0:1024].rearrange("p (a n) -> p a n", a=TT)
        mz = ring[:, 0, 0:4 * 384].rearrange("p (h n) -> p h n", h=4)
        msq = ring[:, 1, 0:1024].rearrange("p (a n) -> p a n", a=TT)
        mcol = ring[:, 2, 0:128].rearrange("p (a n) -> p a n", a=TT)
        mem = ring[:, 2, 128:136].rearrange("p (a n) -> p a n", a=TT)
        qsig = area(50, 1024).rearrange("p (i t) -> p i t", i=4)
        pend = sb("pend", [P, 4, NC])

        w_rt = area(0, KT * 36).rearrange("p (t n) -> p t n", t=KT)
        b_rt = area(2, 36)
        lg = area(3, 2 * 36).rearrange("p (a n) -> p a n", a=TT)
        rt = area(4, 16 * 64).rearrange("p (i a n) -> p i a n", i=16, a=TT)
        cw = area(8, TT * NE).rearrange("p (a e) -> p a e", a=TT)
        rev = area(9, 8)
        revi = area(9.5, 8).bitcast(mybir.dt.int32)
        gact = area(12, TT * FE).rearrange("p (a n) -> p a n", a=TT)
        eact = area(14, TT * FE).rearrange("p (a n) -> p a n", a=TT)
        eact_hi, eact_lo = (area_r(kb, TT * FE).rearrange("p (a f n) -> p a f n", a=TT, f=2) for kb in (16, 18))
        moe_hi = [area_r(kb, SLOT) for kb in (40, 64, 0, 48, 56, 72)]
        gate_up_hi = [area_r(kb, n).rearrange("p (i n) -> p i n", i=2)[:, :, 0:SLOT] for kb, n in ((40, 48 * KB), (48, 16 * KB))]
        hT_hi = area_r(80, KT * SEQ).rearrange("p (k t) -> p k t", k=KT)
        gate2 = area(20, 4 * D).rearrange("p (m n) -> p m n", m=4)
        mod2 = area(36, 4 * 32).rearrange("p (m n) -> p m n", m=4)
        adab2_c = area(37, 64).rearrange("p (m n) -> p m n", m=8)
        norm2_c = area(37.5, 32).rearrange("p (m n) -> p m n", m=4)
        sink_b = area(37.75, 8)
        w_glr = area(38.5, KT * 16).rearrange("p (t n) -> p t n", t=KT)
        w_gg = arena[0:16, 39 * KB:40 * KB]
        vg = area(0, 1024).rearrange("p (a n) -> p a n", a=TT)
        ggs = area(4, 1024).rearrange("p (a n) -> p a n", a=TT)
        sq_t = area(8, 1024).rearrange("p (i t) -> p i t", i=4)
        kz = area(12, 1024).rearrange("p (k h t) -> p k h t", k=2, h=2)
        svt = area(16, 256).rearrange("p (a n) -> p a n", a=TT)
        glr_t = arena[0:16, 17 * KB:18 * KB]
        swm = area(18, 64)
        f2 = lambda kb: area(kb, 512).rearrange("p (i t) -> p i t", i=2)
        zb, az, nb2, eb, enb, kend2 = (f2(kb) for kb in (40, 42, 44, 46, 48, 50))
        ket = area(52, 512).rearrange("p (a n) -> p a n", a=TT)
        at = area(54, 1024).rearrange("p (a h t) -> p a h t", a=TT, h=4)
        ktz = area(58, 1024).rearrange("p (h t) -> p h t", h=4)
        sg_state = area(64, 2048).rearrange("p (c i v) -> p c i v", c=4, i=2)
        qg, kg = f2(72), f2(74)
        gdec = area(76, 8).rearrange("p (i c) -> p i c", i=2)
        ggn = area(38, GLA_DV)
        gsq = area(78, 1024).rearrange("p (a n) -> p a n", a=TT)
        sc = area(40, 8 * 384).rearrange("p (h k) -> p h k", h=8)
        p_t = area(52, 24 * P).rearrange("p (j q) -> p j q", j=24)
        bias8 = area(83, 8 * 256).rearrange("p (h k) -> p h k", h=8)
        hots = arena[0:64, 30 * KB:30 * KB + 384]
        rel_sb = arena[0:64, 32 * KB:32 * KB + 8]
        ebc = arena[0:SWA_H, 34 * KB:34 * KB + 384]
        y2 = macc[:, 0:2, :]
        PAD = 16
        hp = area(0, 8 * 272).rearrange("p (k t) -> p k t", k=KT)
        pa = area(9, 8 * 272).rearrange("p (k t) -> p k t", k=KT)
        pb_ = area(40, 6 * 272).rearrange("p (k t) -> p k t", k=6)
        pinvc = area(58, 4 * 256).rearrange("p (g t) -> p g t", g=4)
        pcnt = area(62, 256)
        pcnti = area(63, 256).bitcast(mybir.dt.int32)
        poolw = area(64, 2048).rearrange("p (g r n) -> p g r n", g=4, r=2)
        psc_b = area(72, 1024)
        frl = area(16, 1024).rearrange("p (a n) -> p a n", a=TT)
        fact, fact_hi, fact_lo = macc[:, 0, :], macc_r[:, 1, :], macc_r[:, 2, :]
        fact = fact.rearrange("p (a n) -> p a n", a=TT)
        fact_hi, fact_lo = (x.rearrange("p (a f n) -> p a f n", a=TT, f=4) for x in (fact_hi, fact_lo))
        mlp_hi = [area_r(kb, SLOT) for kb in (0, 8, 40, 48, 56, 64, 72, 80)]
        gT_hi = gate1_r[:, :, :].rearrange("p v n -> p (v n)").rearrange("p (k t) -> p k t", k=KT)
        nrm_b = area(0, D)
        zeros_b = sb("zeros_b", [P, P], BF16)[:, :]
        ring_zero = sb("ring_zero", [P, 512], BF16)[:, :]

        moe_in = [sem(f"moe_in{i}") for i in range(6)]
        ada2_in = [sem(f"ada2_in{i}") for i in range(2)]
        rt_in, par2_in, bias_out, bias_in, nrm_in, pool_in = (
            sem(n) for n in ("rt_in", "par2_in", "bias_out", "bias_in", "nrm_in", "pool_in"))
        t_gu, t_tr, t_dn, a_silu, v_eact, v_eact_t, a_gu, g_gate, v_gate_up, a_dn, v_dn, v_ada2, v_mod, t_mod = (
            sem(n) for n in ("t_gu", "t_tr", "t_dn", "a_silu", "v_eact", "v_eact_t", "a_gu", "g_gate", "v_gate_up", "a_dn", "v_dn", "v_ada2",
                             "v_mod", "t_mod"))
        ring2 = [sem(f"ring2_{i}") for i in range(RING)]
        t_bin, t_bout, nrm2_in, hot_in = (sem(n) for n in ("t_bin", "t_bout", "nrm2_in", "hot_in"))
        mlp_in = ring2
        ring2_n = [16 * len(range(i, 13, RING)) for i in range(RING)]
        t_up, t_ft, t_fd, a_fact, v_fact_t, a_w1, g_w1, v_w1, a_w2, v_w2 = (
            sem(n) for n in ("t_up", "t_ft", "t_fd", "a_fact", "v_fact_t", "a_w1", "g_w1", "v_w1", "a_w2", "v_w2"))
        t_bias, a_bias, a_hi, v_lo = (sem(n) for n in ("t_bias", "a_bias", "a_hi", "v_lo"))
        scratch_d = nc.dram_tensor("bias_rows", (SWA_H, P * 384), F32, kind="Internal").ap()
        CREDIT = 4
        in2_cols = [0, 256, 512, 768, 1024, 1280, 1552, 1808, 2064]
        stream2 = [("in", c0) for c0 in in2_cols] + [("out", q) for q in range(4)]
        ones2 = arena[0:4, 86 * KB:87 * KB]

        def scratch(i):
            return ring[:, i, :].rearrange("p (g h s) -> p g h s", g=4, h=4)

        iF, iA, iB, iC, iD, iQ = (scratch(i) for i in range(6))

        def chunk2(x):
            return x.rearrange("p i (c s) -> p i c s", s=CH)

        def bank_of(step, gi):
            return (4 * step + gi) % 8

        def bank4(step, gi):
            return ps[:, bank_of(step, gi), :].rearrange("p (h s) -> p h s", h=4)

        INV_T = [
            ("F", None, None, None, None, None),
            ("G", bhz, 0, None, None, None),
            ("G", khz, 0, None, None, ("a", 0)),
            ("G", bhz, 1, None, None, ("v", 0)),
            ("G", khz, 1, None, None, ("v", 1)),
            ("V", iD, None, None, 1, ("v", 4)),
            ("M", iB, iA, None, 2, ("v", 5)),
            ("M", iA, iB, None, 2, ("v", 6)),
            ("M", iC, iQ, 1, 3, ("a", 1)),
            ("M", iD, iC, 2, None, ("a", 2)),
            ("M", iC, iD, None, None, ("v", 7)),
            ("M", iA, iQ, 3, 7, ("a", 3)),
            ("M", iB, iA, 4, None, ("a", 4)),
            ("M", iC, iQ, 5, 8, ("v", 8)),
            ("T", iQ, None, None, 9, ("a", 5)),
            ("M", iA, iQ, None, 10, ("v", 9)),
            ("M", iD, iB, 7, None, ("a", 6)),
            ("T", iQ, None, None, 11, ("a", 7)),
            ("M", iA, iQ, None, 12, ("v", 11)),
            ("M", iD, iB, 9, None, ("a", 8)),
        ]
        INV_A = [(i, s_, d_) for i, (s_, d_) in enumerate(
            [(0, iF), (6, iC), (7, iD), (9, iA), (10, iB), (12, iC), (14, iD), (15, iB), (17, iD), (18, iB)])]
        INV_V = [
            ("mask", 1, m_n16t, iB),
            ("mask", 2, m_ak, iD),
            ("maskF", None, m_n16, iA),
            ("ident", None, None, iQ),
            ("mask", 3, m_rb, grb),
            ("mask", 4, m_rb, grk),
            ("lakv", 5, None, None),
            ("add", 8, None, iQ),
            ("add", 11, None, iQ),
            ("add", 13, None, iQ),
            ("maskF", None, m_32, iA),
            ("add", 16, None, iQ),
            ("maskF", None, m_64, iA),
            ("add", 19, None, iQ),
        ]
        V_A16 = 2

        block = ctx.enter_context(nc.Block())

        stream = [("ada", n) for n in range(8)]
        for n in range(IN_SLOTS):
            stream += [("win", n), ("ada", 8 + n)]
        stream += [("ada", n) for n in range(21, 24)]
        place = {key: i for i, key in enumerate(stream)}

        def loaded(eng, key):
            eng.wait_ge(ring_in[place[key] % RING], 16 * (place[key] // RING + 1))

        def slot(key):
            return ring[:, place[key] % RING, :]

        def g_norm(pool, st):
            c = Counter(pool, g[st])
            pool.wait_ge(v[st], STEP[st + ".ss"])
            c.link(nc.gpsimd.tensor_tensor(small[:, 0:2], small[:, 0:2], nhalf[:, 0:2], ALU.pow))
            c.at(st + ".rstd")

        def a_norm(act, st, shift, scale, meanwhile=None):
            c = Counter(act, a[st])
            for tt in range(TT):
                c.link(nc.scalar.activation(xn[:, tt, :], x_sb[:, tt, :], ACT.Square, accum_out=small[:, tt:tt + 1]))
            c.at(st + ".sq")
            if meanwhile:
                meanwhile()
            act.wait_ge(v[st], STEP[st + ".mod"])
            for k in (2, 3, 6, 7):
                act.wait_ge(t[st], k // 2 + 1)
                c.link(nc.scalar.activation(hT[:, k, :], ps[:, k // 2, 256 * (k % 2):256 * (k % 2) + 256], ACT.Identity,
                                            bias=shift[:, k:k + 1], scale=scale[:, k:k + 1]))
            c.at(st + ".a")

        def v_rstd(dve, c, st):
            dve.wait_ge(a[st], STEP[st + ".sq"])
            c.link(nc.vector.tensor_scalar(small[:, 0:2], small[:, 0:2], 1.0 / D, EPS, ALU.mult, ALU.add))
            c.at(st + ".ss")
            dve.wait_ge(g[st], STEP[st + ".rstd"])

        def v_norm(dve, st, shift, scale, mod=None):
            c = Counter(dve, v[st])
            v_rstd(dve, c, st)
            for tt in range(TT):
                c.link(nc.vector.tensor_scalar(xn[:, tt, :], x_sb[:, tt, :], small[:, tt:tt + 1], None, ALU.mult))
            c.at(st + ".xn")
            if mod:
                mod(c)
            c.at(st + ".mod")
            for k in (0, 1, 4, 5):
                dve.wait_ge(t[st], k // 2 + 1)
                c.link(nc.vector.tensor_scalar(hT[:, k, :], ps[:, k // 2, 256 * (k % 2):256 * (k % 2) + 256],
                                               scale[:, k:k + 1], shift[:, k:k + 1], ALU.mult, ALU.add))
            c.at(st + ".v")

        def mm3(o, x_hi, x_lo, w_hi, w_lo, start=False, stop=False):
            for i, (l, r) in enumerate(((x_hi, w_hi), (x_hi, w_lo), (x_lo, w_hi))):
                ins = nc.tensor.matmul(o, l, r, start=start and i == 0, stop=stop and i == 2, skip_group_check=True)
            return ins

        def trailing(eng, lo, x, hi):
            return eng.tensor_tensor(lo, x, hi.bitcast(F32), ALU.subtract)

        def t_norm(pe, st, tiles=False):
            c = Counter(pe, t[st])
            pe.wait_ge(v[st], STEP[st + ".xn"])
            for k in range(KT):
                for tt in range(TT):
                    o = (k % 2) * 256 + tt * P
                    src = xn[:, tt, P * k:P * k + P] if tiles else xn[:, tt, k::8]
                    ins = nc.tensor.transpose(ps[:, k // 2, o:o + P], src, ident[:, :])
                if k % 2:
                    c.mark(ins)
            c.at(st + ".t")

        def t_columns(acc, dst):
            for k in range(KT):
                ins = nc.tensor.matmul(dst[:, k:k + 1], acc[:, k::8], ones[:, 0:1], start=True, stop=True)
            return ins

        def gate_up_in(sp, m, e):
            for i, name in enumerate(("moe_w_gate", "moe_w_up")):
                s_ = 3 * (e % 2) + i
                sp.dma_start(ring[:, s_, :], A[name][0, bass.ds(m * E_BODY + e, 1)]
                             .rearrange("o (p t) n -> (o p) (t n)", t=8)).then_inc(moe_in[s_], 16)

        def down_in(eng, m, e):
            s_ = 3 * (e % 2) + 2
            eng.dma_start(ring[:, s_, :], A["moe_w_down"][0, bass.ds(m * E_BODY + e, 1)]
                          .rearrange("o (p t) n -> (o p) (t n)", t=2)).then_inc(moe_in[s_], 16)

        def sp_expert(sp, m, j):
            last = isinstance(m, int) and j == E_BODY - 1
            if not last:
                sp.wait_ge(t_gu, 2 * (E_BODY * m + j))
                gate_up_in(sp, m, j + 1)
            if 1 <= j <= 6:
                w_ada2 = A["ada_w_2"].rearrange("l j (p t) n -> (l j) p t n", t=8)
                for k in (2 * j - 2, 2 * j - 1):
                    vec, q = k // 4, k % 4
                    sp.wait_ge(v_ada2, 24 * m + 2 * k + 2)
                    sp.dma_start(ring[:, 6 + k % 2, :].rearrange("p (t n) -> p t n", t=2),
                                 w_ada2[bass.ds(m, 1), :, 2 * q:2 * q + 2, vec * D:(vec + 1) * D]
                                 .rearrange("o p t n -> (o p) t n")).then_inc(ada2_in[k % 2], 16)

        def sp_tail(sp):
            sp.wait_ge(v["i"], STEP["i.done"])
            for q in range(4):
                sp.dma_start(ring[:, q, :].rearrange("p (t n) -> p t n", t=2),
                             A["w_out"][0].rearrange("(p t) n -> p t n", t=8)[:, 2 * q:2 * q + 2, :]
                             ).then_inc(wout_in, 16)
            sp.wait_ge(v["y"], STEP["y.done"])
            sp.wait_ge(g["y"], STEP["y.free"])
            sp.dma_start(w_rt[:, :, 0:32], A["moe_w_router"][0].rearrange("(p t) n -> p t n", t=8)).then_inc(rt_in, 16)
            sp.dma_start(w_rt[:, :, 32:36], A["moe_w_group"][0].rearrange("(p t) n -> p t n", t=8)).then_inc(rt_in, 16)
            sp.dma_start(b_rt[:, 0:32], A["moe_b_router"].to_broadcast([P, NE])).then_inc(rt_in, 16)
            sp.dma_start(b_rt[:, 32:36], A["moe_b_group"].to_broadcast([P, NG])).then_inc(rt_in, 16)
            for m in range(4):
                sp.dma_start(gate2[:, m, :], A["ada_b_2"][m // 2, m % 2:m % 2 + 1, 2 * D:3 * D].to_broadcast([P, D])
                             ).then_inc(par2_in, 16)
                sp.dma_start(adab2_c[:, 2 * m:2 * m + 2, :],
                             A["ada_b_2"][m // 2, m % 2, 0:2 * D].rearrange("(v p t) -> p v t", p=P, t=8)
                             ).then_inc(par2_in, 16)
                sp.dma_start(norm2_c[:, m, :], A["norm_w_2"][m // 2, m % 2].rearrange("(p t) -> p t", t=8)
                             ).then_inc(par2_in, 16)
            sp.dma_start(sink_b, A["attn_sinks_2"].to_broadcast([P, SWA_H])).then_inc(par2_in, 16)
            sp.dma_start(w_glr[:, :, :], A["attn_w_in_2"][0].rearrange("(p t) n -> p t n", t=8)[:, :, 1536:1552]
                         ).then_inc(par2_in, 16)
            sp.dma_start(w_gg, A["gla_w_gate_2"][0]).then_inc(par2_in, 16)
            sp.wait_ge(t["o"], KT // 2)
            sp.dma_start(ggn, A["gla_norm_w_2"].to_broadcast([P, GLA_DV])).then_inc(par2_in, 16)

            sp.wait_ge(t_out, 4)
            for e in range(2):
                gate_up_in(sp, 0, e)
                down_in(sp, 0, e)
            with sp.Fori(0, LAST_PASS) as m:
                for j in range(1, E_BODY + 1):
                    sp_expert(sp, m, j)
            for j in range(1, E_BODY):
                sp_expert(sp, LAST_PASS, j)
            sp.wait_ge(t_dn, 2 * NE)
            sp.wait_ge(bias_out, 16)
            sp.dma_start(bias8[:, :, :], scratch_d[:, 127:127 + P * 383].rearrange("h (q l) -> q h l", l=383)[:, :, 0:256]
                         ).then_inc(bias_in, 16)
            sp.dma_start(nrm_b, A["final_norm_w"].rearrange("(o n) -> o n", o=1).to_broadcast([P, D])).then_inc(nrm_in, 16)
            sp_block2(sp)

        def sp_block2(sp):
            for i, (kind, c0) in enumerate(stream2):
                if i < RING:
                    if i == 6:
                        sp.wait_ge(v_ada2, CREDIT + 24 * 4)
                else:
                    sp.wait_ge(t_bin, i - RING + 1)
                if kind == "in":
                    sp.dma_start(ring[:, i % RING, :].rearrange("p (t n) -> p t n", t=8),
                                 A["attn_w_in_2"][0].rearrange("(p t) n -> p t n", t=8)[:, :, c0:c0 + 256]
                                 ).then_inc(ring2[i % RING], 16)
                else:
                    sp.dma_start(ring[:, i % RING, :].rearrange("p (t n) -> p t n", t=2),
                                 A["attn_w_out_2"][0].rearrange("(p t) n -> p t n", t=8)[:, 2 * c0:2 * c0 + 2, :]
                                 ).then_inc(ring2[i % RING], 16)
            sp.wait_ge(t_bin, 9)
            first_chunks_in(sp, 0, (0, 5, 6, 7))
            sp.wait_ge(t_bout, 4)
            first_chunks_in(sp, 0, (1, 2, 3, 4))
            sp_mlp(sp, 0)
            sp.wait_ge(t_fd, 16)
            sp.dma_start(poolw[:, :, :, :], A["pool_w_2"][0].rearrange("g (r p) n -> p g r n", p=P)).then_inc(pool_in, 16)
            sp.dma_start(psc_b, A["pool_scale_2"].to_broadcast([P, D])).then_inc(pool_in, 16)
            first_chunks_in(sp, 1, (0, 1, 2, 3, 4, 5, 6, 7))
            sp_mlp(sp, 1)
            sp.wait_ge(v["pp"], STEP["pp.x"])
            sp.dma_start(gate2[:, 0, :], A["final_norm_w_2"].rearrange("(o n) -> o n", o=1).to_broadcast([P, D])).then_inc(nrm2_in, 16)
            for tt in range(TT):
                sp.wait_ge(v["z"], STEP["z.out0"] + tt)
                sp.dma_start(out[0, P * tt:P * tt + P, :], x_sb[:, tt, :]).then_inc(s_out, 16)
            sp.wait_ge(s_out, 32)

        def w1_in(sp, layer, m, j, r):
            s_ = 4 * (j % 2) + r
            sp.dma_start(ring[:, s_, :].rearrange("p (t n) -> p t n", t=4),
                         A["mlp_w1_2"][layer].rearrange("(p t) (c n) -> c p t n", t=8, n=512)
                         [bass.ds(2 * m + j, 1), :, 4 * r:4 * r + 4, :].rearrange("o p t n -> (o p) t n")
                         ).then_inc(mlp_in[s_], 16)

        def w2_in(eng, layer, m, j, r):
            s_ = 4 * (j % 2) + 2 + r
            eng.dma_start(ring[:, s_, :].rearrange("p (f n) -> p f n", f=2),
                          A["mlp_w2_2"][layer].rearrange("(c p f) n -> c p f n", p=P, f=4)
                          [bass.ds(2 * m + j, 1), :, 2 * r:2 * r + 2, :].rearrange("o p f n -> (o p) f n")
                          ).then_inc(mlp_in[s_], 16)

        def sp_mlp(sp, layer):
            def chunk_in(m, j):
                sp.wait_ge(t_up, 16 * layer + 2 * (2 * m + j))
                for r in range(2):
                    w1_in(sp, layer, m, j + 1, r)

            with sp.Fori(0, 3) as m:
                for j in (1, 2):
                    chunk_in(m, j)

        def first_chunks_in(sp, layer, slots):
            for s_ in slots:
                (w1_in if s_ % 4 < 2 else w2_in)(sp, layer, 0, s_ // 4, s_ % 2)

        @block.sync
        def _(sp):
            sp.dma_start(ccol[:, 0:8], A["c"].rearrange("o (p t) -> p (o t)", t=8)).then_inc(c_in, 16)
            sp.dma_start(ccol[:, 8:16], A["c_2"].rearrange("o (p t) -> p (o t)", t=8)).then_inc(c_in, 16)
            sp.dma_start(x_sb[:, :, :], A["x"].rearrange("b (a p) d -> p (b a) d", p=P)).then_inc(x_in, 16)
            for i, (kind, n) in enumerate(stream):
                if i >= RING:
                    k0, n0 = stream[i - RING]
                    if k0 == "ada":
                        sp.wait_ge(v_ada, 2 * (n0 + 1))
                    else:
                        sp.wait_ge(t_win, n0 + 1)
                dst = slot((kind, n))
                if kind == "ada":
                    vec, q = n // 4, n % 4
                    src = A["ada_w"][0].rearrange("(p t) n -> p t n", t=8)[:, 2 * q:2 * q + 2, vec * D:(vec + 1) * D]
                    sp.dma_start(dst.rearrange("p (t n) -> p t n", t=2), src).then_inc(ring_in[i % RING], 16)
                else:
                    src = A["w_in"][0].rearrange("(p t) n -> p t n", t=8)[:, :, 256 * n:256 * n + 256]
                    sp.dma_start(dst.rearrange("p (t n) -> p t n", t=8), src).then_inc(ring_in[i % RING], 16)
            sp.wait_ge(t_ada, 6)
            for i, name in enumerate(("rwkv_gn_w", "rwkv_gn_b", "mlstm_hn_w")):
                sp.dma_start(rowp[:, i, :], A[name].to_broadcast([P, 512])).then_inc(row_in, 16)
            sp_tail(sp)

        def g_mlp_loop(pool, layer):
            with pool.Fori(0, 4) as m:
                for j in range(2):
                    pool.wait_ge(a_w1, 16 * layer + 4 * m + 2 * j + 1)
                    trailing(nc.gpsimd, ring_lo[:, 4 * j, :], ring[:, 4 * j, :], mlp_hi[4 * j]).then_inc(g_w1, 1)

        @block.gpsimd
        def _(pool):
            c = Counter(pool, g["c"])
            k = c.link
            k(nc.gpsimd.memset(ident[:, :], 0.0))
            k(nc.gpsimd.memset(ones[:, :], 1.0))
            k(nc.gpsimd.affine_select(out=ident[:, :], in_=ident[:, :], compare_op=ALU.not_equal, fill=1.0,
                                      base=0, pattern=[[-1, P]], channel_multiplier=1))
            k(nc.gpsimd.memset(nhalf[:, :], -0.5))
            k(nc.gpsimd.memset(prm[:, :], 0.0))
            k(nc.gpsimd.memset(rel_sb[:, :], BIG))
            pool.dma_start(rel_sb[0:32, :], A["rel_bias_2"]).then_inc(hot_in, 16)
            pool.dma_start(hots[0:33, :], A["hots"]).then_inc(hot_in, 16)
            k(nc.gpsimd.memset(zeros_b[:, :], 0.0))
            k(nc.gpsimd.memset(ring_zero[:, :], 0.0))
            c.at("c.ident")
            prm_rows = [("rwkv_mu", 14), ("rwkv_w0", 4), ("rwkv_a0", 4), ("rwkv_k_k", 4), ("rwkv_k_a", 4)]
            r0 = 0
            for name, n in prm_rows:
                pool.dma_start(prm[r0:r0 + n, :], A[name].rearrange("o (i p) -> (o i) p", p=P)).then_inc(prm_in, 16)
                r0 += n
            pool.dma_start(prm[30:34, :], A["rwkv_r_k"].rearrange("o (i h) j -> (o i) (h j)", h=2)).then_inc(prm_in, 16)
            pool.dma_start(prm[34:38, :], A["mlstm_conv_b"].rearrange("o (i p) -> (o i) p", p=P)).then_inc(prm_in, 16)
            pool.dma_start(prm[38:54, :], A["mlstm_conv_w"].rearrange("o j (i p) -> (o j i) p", p=P)).then_inc(prm_in, 16)
            pool.dma_start(prm[54:56, :], A["gla_b_gate_2"].rearrange("o (i p) -> (o i) p", p=P)).then_inc(prm_in, 16)
            pool.dma_start(prm[56:64, :], A["norm_w_2"][1, 0].rearrange("(i p) -> i p", p=P)).then_inc(prm_in, 16)
            pool.dma_start(prm[64:80, :], A["ada_b_2"][1, 0, 0:2048].rearrange("(i p) -> i p", p=P)).then_inc(prm_in, 16)
            pool.dma_start(adab_c[:, :, :], A["ada_b"].rearrange("o (v p t) -> p (o v) t", p=P, t=8)).then_inc(par_in, 16)
            pool.dma_start(norm_c[:, 0, :], A["mix_norm_w"].rearrange("o (p t) -> p (o t)", t=8)).then_inc(par_in, 16)
            pool.dma_start(norm_c[:, 1, :], A["ffn_norm_w"].rearrange("o (p t) -> p (o t)", t=8)).then_inc(par_in, 16)
            pool.dma_start(gate1[:, 0, :], A["ada_b"][:, 2 * D:3 * D].to_broadcast([P, D])).then_inc(par_in, 16)
            pool.dma_start(gate1[:, 1, :], A["ada_b"][:, 5 * D:6 * D].to_broadcast([P, D])).then_inc(par_in, 16)
            k(nc.gpsimd.memset(raw[:, :, :, 0:1], 0.0))
            k(nc.gpsimd.memset(convraw[:, :, 0:3], 0.0))
            k(nc.gpsimd.memset(w_if[:, :, :], 0.0))
            k(nc.gpsimd.memset(wup[:, :, :], 0.0))
            k(nc.gpsimd.memset(gate_b[:, :], 0.0))
            k(nc.gpsimd.memset(mrow[:, :, :], 0.0))
            k(nc.gpsimd.memset(ones2[:, :], 1.0))
            k(nc.gpsimd.memset(reset[:, :], 1.0))
            k(nc.gpsimd.memset(reset[:, :].rearrange("p (c s) -> p c s", s=CH)[:, :, 0:1], 0.0))
            c.at("c.zeros")
            w_in_t = A["w_in"][0].rearrange("(p t) n -> p t n", t=8)
            pool.dma_start(w_if[:, :, 0:4], w_in_t[:, :, 3328:3332]).then_inc(gate_in, 16)
            pool.dma_start(w_if[:, :, 32:36], w_in_t[:, :, 3332:3336]).then_inc(gate_in, 16)
            pool.dma_start(wup[0:64, 0, :], A["rwkv_w_up"][0]).then_inc(gate_in, 16)
            pool.dma_start(wup[64:128, 1, :], A["rwkv_a_up"][0]).then_inc(gate_in, 16)
            pool.dma_start(gup[:, :], A["rwkv_g_up"][0]).then_inc(gate_in, 16)
            pool.dma_start(gate_b[0:4, 0:1], A["mlstm_i_b"].rearrange("o h -> h o")).then_inc(gate_in, 16)
            pool.dma_start(gate_b[32:36, 0:1], A["mlstm_f_b"].rearrange("o h -> h o")).then_inc(gate_in, 16)
            for i, B in enumerate((16, 32, 64)):
                m = masks[:, i, :].rearrange("p (b f) -> p b f", f=B)
                k(nc.gpsimd.memset(masks[:, i, :], 1.0))
                k(nc.gpsimd.affine_select(out=m, in_=m, compare_op=ALU.is_ge, fill=0.0, base=0,
                                          pattern=[[-B, P // B], [0, B]], channel_multiplier=1))
                k(nc.gpsimd.affine_select(out=m, in_=m, compare_op=ALU.is_ge, fill=0.0, base=B - 1,
                                          pattern=[[B, P // B], [0, B]], channel_multiplier=-1))
            k(nc.gpsimd.tensor_copy(headblk[:, :], same64))
            k(nc.gpsimd.tensor_copy(headsel[:, :], masks[:, 2, 0:128:64]))
            k(nc.gpsimd.affine_select(out=m_causal, in_=ones[:, :], compare_op=ALU.is_ge, fill=0.0, base=0,
                                      pattern=[[1, P]], channel_multiplier=-1))
            k(nc.gpsimd.tensor_tensor(m_64, same64, same32, ALU.subtract))
            k(nc.gpsimd.tensor_tensor(same32, same32, same16, ALU.subtract))
            k(nc.gpsimd.tensor_scalar(m_n16t, same16, -1.0, None, ALU.mult))
            k(nc.gpsimd.affine_select(out=m_n16t, in_=m_n16t, compare_op=ALU.is_gt, fill=0.0, base=0,
                                      pattern=[[1, P]], channel_multiplier=-1))
            k(nc.gpsimd.tensor_scalar(masks[:, 0:2, :], masks[:, 0:2, :], -1.0, None, ALU.mult))
            k(nc.gpsimd.tensor_scalar(m_64, m_64, -1.0, None, ALU.mult))
            for m in (m_n16, m_32, m_64):
                k(nc.gpsimd.affine_select(out=m, in_=m, compare_op=ALU.is_gt, fill=0.0, base=0,
                                          pattern=[[-1, P]], channel_multiplier=1))
            k(nc.gpsimd.affine_select(out=m_ak, in_=same64, compare_op=ALU.is_gt, fill=0.0, base=0,
                                      pattern=[[1, P]], channel_multiplier=-1))
            k(nc.gpsimd.affine_select(out=m_rb, in_=same64, compare_op=ALU.is_ge, fill=0.0, base=0,
                                      pattern=[[1, P]], channel_multiplier=-1))
            c.at("c.masks")
            g_norm(pool, "n")
            c = Counter(pool, g["m"])
            pool.wait_ge(v["m"], STEP["m.ss"])
            c.link(nc.gpsimd.tensor_tensor(small[:, 8:16], small[:, 8:16], nhalf[:, 0:8], ALU.pow))
            c.at("m.rs")
            c = Counter(pool, g["r"])
            pool.wait_ge(bias_out, 16)
            c.link(nc.gpsimd.memset(bhz[:, :, :], 0.0))
            c.link(nc.gpsimd.memset(khz[:, :, :], 0.0))
            pool.wait_ge(v["m"], STEP["m.y"])
            pool.wait_ge(v["w"], STEP["w.shift"])
            pool.wait_ge(t["n"], STEP["n.t"])
            c.link(nc.gpsimd.memset(rbuf[:, :, :], 0.0))
            c.link(nc.gpsimd.memset(ubuf[:, :, :], 0.0))
            c.link(nc.gpsimd.memset(state[:, :, :, :], 0.0))
            c.at("r.zero")
            c = Counter(pool, g["y"])
            pool.wait_ge(v["y"], STEP["y.var"])
            c.link(nc.gpsimd.tensor_tensor(small[:, 32:48], small[:, 32:48], nhalf[:, 0:16], ALU.pow))
            c.at("y.rs")
            pool.wait_ge(v["y"], STEP["y.done"])
            c.link(nc.gpsimd.iota(revi, pattern=[[-1, 8]], base=8, channel_multiplier=0))
            c.link(nc.gpsimd.tensor_copy(rev, revi))
            c.at("y.free")
            g_norm(pool, "q")
            with pool.Fori(0, NE // E_BODY) as m:
                for e in range(E_BODY):
                    s_ = 3 * (e % 2)
                    pool.wait_ge(a_gu, 2 * E_BODY * m + 2 * e + 1)
                    trailing(nc.gpsimd, ring_lo[:, s_, :], ring[:, s_, :], moe_hi[s_]).then_inc(g_gate, 1)
            g_norm(pool, "f")
            g_norm(pool, "bn")
            c = Counter(pool, g["bp"])
            pool.wait_ge(v["bn"], STEP["bn.v"])
            pool.wait_ge(t["bn"], STEP["bn.t"])
            c.link(nc.gpsimd.memset(ktz[:, :, :], 0.0))
            c.link(nc.gpsimd.memset(kz[:, :, :, :], 0.0))
            c.link(nc.gpsimd.memset(sg_state[:, :, :, :], 0.0))
            c.at("bp.zero")
            c = Counter(pool, g["bg"])
            pool.wait_ge(v["bg"], STEP["bg.ss"])
            c.link(nc.gpsimd.tensor_tensor(small[:, 8:16], small[:, 8:16], nhalf[:, 0:8], ALU.pow))
            c.at("bg.rs")
            g_norm(pool, "l0")
            g_mlp_loop(pool, 0)
            g_norm(pool, "pn")
            c = Counter(pool, g["pp"])
            for buf in (hp, pa, pb_):
                c.link(nc.gpsimd.memset(buf[:, :, 0:PAD], 0.0))
            c.link(nc.gpsimd.iota(pcnti, pattern=[[1, SEQ]], base=1, channel_multiplier=0))
            c.link(nc.gpsimd.tensor_copy(pcnt, pcnti))
            for gi in range(4):
                c.link(nc.gpsimd.tensor_scalar(pinvc[:, gi, :], pcnt, float(2 ** (gi + 1)), None, ALU.min))
            c.at("pp.zero")
            g_norm(pool, "l1")
            g_mlp_loop(pool, 1)
            g_norm(pool, "z")

        mod_of = [(mod2[:, 0, 0:8], mod2[:, 0, 8:16]), (mod2[:, 1, 0:8], mod2[:, 1, 8:16]),
                  (mod2[:, 2, 16:24], mod2[:, 2, 24:32]), (mod2[:, 3, 0:8], mod2[:, 3, 8:16])]

        def a_mlp_loop(act, layer):
            def squares(m, j, tt, first=False):
                n = 16 * layer + 4 * m + 2 * j + tt + 1
                act.wait_ge(t_up, n)
                nc.scalar.activation(frl[:, tt, :], ps[:, 4 + tt, :], ACT.Relu).then_inc(a_fact, 1)
                act.wait_ge(a_fact, 2 * n - 1)
                if not first:
                    act.wait_ge(t_ft, n - 2)
                nc.scalar.activation(fact[:, tt, :], frl[:, tt, :], ACT.Square).then_inc(a_fact, 1)

            def chunk(m, j, first=False, last=False):
                if not last:
                    a_w1_hi(act, layer, m, j + 1)
                squares(m, j, 0, first)
                for r in range(2):
                    s_ = 4 * (j % 2) + 2 + r
                    act.wait_ge(mlp_in[s_], ring2_n[s_] + 64 * layer + 16 * (m + j // 2) + 16)
                    nc.scalar.copy(mlp_hi[s_], ring[:, s_, :]).then_inc(a_w2, 1)
                squares(m, j, 1, first)
                if not first and not last:
                    act.wait_ge(t_fd, 16 * layer + 2 * (2 * m + j))
                    for r in range(2):
                        w2_in(act, layer, m, j + 1, r)

            chunk(0, 0, first=True)
            with act.Fori(0, 3) as m:
                for j in (1, 2):
                    chunk(m, j)
            chunk(3, 1, last=True)

        def a_w1_hi(act, layer, m, j):
            for r in range(2):
                s_ = 4 * (j % 2) + r
                act.wait_ge(mlp_in[s_], ring2_n[s_] + 64 * layer + 16 * (m + j // 2) + 16)
                nc.scalar.copy(mlp_hi[s_], ring[:, s_, :]).then_inc(a_w1, 1)

        def a_hT_hi(act, st, hi):
            act.wait_ge(v[st], STEP[st + ".v"])
            for k in (0, 4):
                nc.scalar.copy(hi[:, k:k + 4, :], hT[:, k:k + 4, :]).then_inc(a_hi, 1)

        def v_hT_lo(dve, st, hi, n):
            dve.wait_ge(a[st], STEP[st + ".a"])
            for i, k in enumerate((0, 4)):
                dve.wait_ge(a_hi, 2 * n + i + 1)
                trailing(nc.vector, hT_lo[:, k:k + 4, :], hT[:, k:k + 4, :], hi[:, k:k + 4, :]).then_inc(v_lo, 1)

        def v_w1_lo(dve, layer, m, j):
            s_ = 4 * (j % 2) + 1
            dve.wait_ge(a_w1, 16 * layer + 4 * m + 2 * j + 2)
            trailing(nc.vector, ring_lo[:, s_, :], ring[:, s_, :], mlp_hi[s_]).then_inc(v_w1, 1)

        def v_squares_t(dve, layer, m, j, tt):
            n = 16 * layer + 4 * m + 2 * j + tt + 1
            dve.wait_ge(t_ft, n)
            if not (isinstance(m, int) and m == 0 and j == 0):
                dve.wait_ge(t_fd, n - 2)
            src = ps[:, 6 + tt, :].rearrange("p (f n) -> p f n", f=4)
            nc.vector.tensor_copy(fact_hi[:, tt], src).then_inc(v_fact_t, 1)
            dve.wait_ge(v_fact_t, 2 * n - 1)
            trailing(nc.vector, fact_lo[:, tt], src, fact_hi[:, tt]).then_inc(v_fact_t, 1)

        def v_w2_lo(dve, layer, m, j):
            for r in range(2):
                s_ = 4 * (j % 2) + 2 + r
                dve.wait_ge(a_w2, 16 * layer + 4 * m + 2 * j + r + 1)
                trailing(nc.vector, ring_lo[:, s_, :], ring[:, s_, :], mlp_hi[s_]).then_inc(v_w2, 1)

        def v_chunk(dve, layer, m, j, first=False, last=False):
            if not last:
                v_w1_lo(dve, layer, m, j + 1)
            if not first:
                v_squares_t(dve, layer, m, j - 1, 1)
            v_w2_lo(dve, layer, m, j)
            v_squares_t(dve, layer, m, j, 0)

        def v_mlp_loop(dve, layer):
            v_chunk(dve, layer, 0, 0, first=True)
            with dve.Fori(0, 3) as m:
                for j in (1, 2):
                    v_chunk(dve, layer, m, j)
            v_chunk(dve, layer, 3, 1, last=True)
            v_squares_t(dve, layer, 3, 1, 1)

        def a_gate_up_hi(act, m, e, i):
            s_ = 3 * (e % 2) + i
            act.wait_ge(moe_in[s_], 16 * (E_BODY // 2) * m + 16 * (e // 2 + 1))
            nc.scalar.copy(moe_hi[s_], ring[:, s_, :]).then_inc(a_gu, 1)

        def v_up_lo(dve, m, e):
            s_ = 3 * (e % 2) + 1
            dve.wait_ge(a_gu, 2 * (E_BODY * m + e) + 2)
            trailing(nc.vector, ring_lo[:, s_, :], ring[:, s_, :], moe_hi[s_]).then_inc(v_gate_up, 1)

        def v_down_lo(dve, m, e):
            s_ = 3 * (e % 2) + 2
            dve.wait_ge(a_dn, E_BODY * m + e + 1)
            trailing(nc.vector, ring_lo[:, s_, :], ring[:, s_, :], moe_hi[s_]).then_inc(v_dn, 1)

        def t_mlp_loop(pe, layer):
            def up(m, j, tt, first=False):
                s0 = 4 * (j % 2)
                if not first:
                    pe.wait_ge(a_fact, 32 * layer + 8 * m + 4 * j + 2 * tt - 2)
                for k in range(KT):
                    if tt == 0 and k % 4 == 0:
                        pe.wait_ge((g_w1, v_w1)[k // 4], 8 * layer + 2 * m + j + 1)
                    tok, cols = slice(P * tt, P * tt + P), slice(512 * (k % 4), 512 * (k % 4) + 512)
                    ins = mm3(ps[:, 4 + tt, :], gT_hi[:, k, tok], hT_lo[:, k, tok], mlp_hi[s0 + k // 4][:, cols],
                              ring_lo[:, s0 + k // 4, cols], start=k == 0, stop=k == KT - 1)
                ins.then_inc(t_up, 1)

            def turn(m, j, tt, first=False):
                pe.wait_ge(a_fact, 32 * layer + 8 * m + 4 * j + 2 * tt + 2)
                if not first:
                    pe.wait_ge(v_fact_t, 32 * layer + 8 * m + 4 * j + 2 * tt - 2)
                for f in range(4):
                    ins = nc.tensor.transpose(ps[:, 6 + tt, P * f:P * f + P], fact[:, tt, f::4], ident[:, :])
                ins.then_inc(t_ft, 1)

            def down(m, j, tt):
                s0 = 4 * (j % 2) + 2
                pe.wait_ge(v_fact_t, 32 * layer + 8 * m + 4 * j + 2 * tt + 2)
                for f in range(4):
                    if tt == 0 and f % 2 == 0:
                        pe.wait_ge(v_w2, 16 * layer + 4 * m + 2 * j + f // 2 + 1)
                    for h in range(2):
                        cols = slice(D * (f % 2) + 512 * h, D * (f % 2) + 512 * h + 512)
                        ins = mm3(ps[:, 2 * tt + h, :], fact_hi[:, tt, f, :], fact_lo[:, tt, f, :],
                                  mlp_hi[s0 + f // 2][:, cols], ring_lo[:, s0 + f // 2, cols])
                ins.then_inc(t_fd, 1)

            def chunk(m, j):
                up(m, j, 0)
                turn(m, j - 1, 1, first=isinstance(m, int) and m == 0 and j == 1)
                down(m, j - 1, 0)
                up(m, j, 1)
                turn(m, j, 0)
                down(m, j - 1, 1)

            up(0, 0, 0, first=True)
            up(0, 0, 1, first=True)
            turn(0, 0, 0, first=True)
            with pe.Fori(0, 3) as m:
                for j in (1, 2):
                    chunk(m, j)
            chunk(3, 1)
            turn(3, 1, 1)
            down(3, 1, 0)
            down(3, 1, 1)

        def v_residual(dve, c, gate, base=0):
            for j in range(4):
                xs = x_sb[:, j // 2, 512 * (j % 2):512 * (j % 2) + 512]
                c.link(nc.vector.tensor_tensor(dtmp[:, :], ps[:, base + j, :], gate[:, 512 * (j % 2):512 * (j % 2) + 512], ALU.mult))
                c.link(nc.vector.tensor_tensor(xs, xs, dtmp[:, :], ALU.add))

        def t_zero(pe):
            for j in range(4):
                ins = nc.tensor.matmul(ps[:, j, :], zeros_b[:, 0:P], ring_zero, start=True, stop=True,
                                       skip_group_check=True)
            return ins

        @block.scalar
        def _(act):
            c = Counter(act, a["c"])
            act.wait_ge(c_in, 32)
            c.link(nc.scalar.activation(csig[:, :], ccol[:, :], ACT.Sigmoid))
            c.at("c.sig")
            act.wait_ge(t_bias, 1)
            nc.scalar.copy(ebc, ps[0:SWA_H, 4, 0:384]).then_inc(a_bias, 1)
            act.wait_ge(a_bias, 1)
            act.dma_start(scratch_d.rearrange("h (q l) -> h q l", q=P), ebc.unsqueeze(1).to_broadcast([SWA_H, P, 384])
                          ).then_inc(bias_out, 16)
            act.wait_ge(x_in, 16)
            a_norm(act, "n", mod_c[:, 0, :], mod_c[:, 1, :])

            c = Counter(act, a["w"])
            act.wait_ge(g["c"], STEP["c.zeros"])
            act.wait_ge(t["n"], STEP["n.t"])
            for n in range(IN_SLOTS):
                act.wait_ge(t_win, n + 1)
                bank = ps[:, 4 + n % 4, :]
                if n < 7:
                    if n >= 2:
                        act.wait_ge(v["w"], STEP["w.pre"] + 3 * (n - 1))
                    c.link(nc.scalar.copy(raw[:, n % 2, :, 1:257], bank.rearrange("p (i t) -> p i t", i=2)))
                elif n < 9:
                    c.link(nc.scalar.copy(convraw[:, 2 * (n - 7):2 * (n - 7) + 2, 3:259],
                                          bank.rearrange("p (i t) -> p i t", i=2)))
                elif n < 11:
                    c.link(nc.scalar.copy(vm[:, :, 256 * (n - 9):256 * (n - 9) + 256],
                                          bank.rearrange("p (a f) -> p a f", a=2)))
                else:
                    c.link(nc.scalar.activation(om[:, :, 256 * (n - 11):256 * (n - 11) + 256],
                                                bank.rearrange("p (a f) -> p a f", a=2), ACT.Sigmoid))
            c.at("w.a")
            act.wait_ge(v["w"], STEP["w.gb"])
            act.wait_ge(t["w"], STEP["w.if"])
            c.link(nc.scalar.activation(mrow[0:4, 0, :], ps[0:4, 0, 0:256], ACT.Tanh, bias=gate_b[0:4, 1:2],
                                        scale=1 / CAP))
            c.link(nc.scalar.activation(mrow[0:4, 1, :], ps[32:36, 0, 0:256], ACT.Tanh, bias=gate_b[32:36, 1:2],
                                        scale=1 / CAP))
            c.at("w.tanh")

            c = Counter(act, a["m"])
            act.wait_ge(v["m"], STEP["m.conv"])
            c.link(nc.scalar.activation(qsig[:, :, :], qk[:, :, :], ACT.Sigmoid))
            c.at("m.sig")
            c.link(nc.scalar.activation(mrow[0:4, 1, :], mrow[0:4, 1, :], ACT.Exp, scale=-CAP))
            c.link(nc.scalar.activation(mrow[0:4, 1, :], mrow[0:4, 1, :], ACT.Ln, bias=ones[0:4, 0:1]))
            c.at("m.lf")
            act.wait_ge(v["m"], STEP["m.z"])
            c.link(nc.scalar.activation(mz[:, :, :], mz[:, :, :], ACT.Exp, scale=-1.0))
            c.link(nc.scalar.activation(mem[:, :, :], mcol[:, :, 32:36], ACT.Exp))
            c.at("m.exp")

            c = Counter(act, a["r"])
            act.wait_ge(v["w"], STEP["w.shift"])
            c.link(nc.scalar.activation(u[0:64, 12, :], u[0:64, 12, :], ACT.Tanh))
            c.link(nc.scalar.activation(u[:, 13, :], u[:, 13, :], ACT.Sigmoid))
            c.at("r.u")
            act.wait_ge(t["r"], STEP["r.wa"])
            act.wait_ge(v_ada, 2 * 24)
            for i in range(4):
                o = (i % 2) * 256
                c.link(nc.scalar.activation(lw[:, i, :], ps[:, i // 2, o:o + 256], ACT.Sigmoid, bias=w0_c[:, i:i + 1]))
                c.link(nc.scalar.activation(av[:, i, :], ps[:, 2 + i // 2, o:o + 256], ACT.Sigmoid,
                                            bias=a0_c[:, i:i + 1]))
            c.at("r.sig")
            c.link(nc.scalar.copy(gtok[:, :, :], ps[:, 4:6, :]))
            c.at("r.gtok")
            act.wait_ge(v["r"], STEP["r.scan"])
            c.link(nc.scalar.activation(pcum[:, :, :], cum[:, :, :], ACT.Exp))
            c.link(nc.scalar.activation(pinv[:, :, :], cum[:, :, :], ACT.Exp, scale=-1.0))
            c.at("r.exp")
            act.wait_ge(t["r"], STEP["r.n2"])
            c.link(nc.scalar.activation(kn[:, :, :], ps[:, 6:8, :].rearrange("p b (i t) -> p (b i) t", i=2), ACT.Sqrt))
            c.at("r.sqrt")
            act.wait_ge(v["r"], STEP["r.bh"])
            act.wait_ge(g["r"], STEP["r.zero"])
            for src, dst in ((bh, bhz), (kh, khz)):
                c.link(nc.scalar.copy(dst[0:64, 0::2, :], src[0:64, :, :]))
                c.link(nc.scalar.copy(dst[64:128, 1::2, :], src[64:128, :, :]))
            c.at("r.pad")
            for i, dst in enumerate((vtok, bend_t, kend_t)):
                act.wait_ge(t["r"], STEP["r.tr"] - 2 + i)
                c.link(nc.scalar.copy(dst[:, :, :], ps[:, 2 * i:2 * i + 2, :]))
            c.at("r.tok")

            c = Counter(act, a["i"])
            act.wait_ge(v["r"], STEP["r.bend"])
            for step, src, dst in INV_A:
                for gi in range(4):
                    act.wait_ge(t["i"], 4 * src + gi + 1)
                    c.link(nc.scalar.copy(dst[:, gi], bank4(src, gi)))
            c.at("i.a")
            c = Counter(act, a["s"])
            for ch in range(NC):
                r0 = CH * (ch % 2)
                act.wait_ge(t_u, ch + 1)
                c.link(nc.scalar.copy(ubuf[r0:r0 + CH, ch // 2, :], ps[r0:r0 + CH, 1, :]))
            c = Counter(act, a["o"])
            for k in range(0, KT, 2):
                act.wait_ge(t["o"], k // 2 + 1)
                c.link(nc.scalar.copy(hT[:, k:k + 2, :], ps[:, k // 2, :].rearrange("p (k t) -> p k t", k=2)))
            c.at("o.hT")
            act.wait_ge(v["o"], STEP["o.x"])
            a_norm(act, "q", mod_c[:, 2, :], mod_c[:, 3, :],
                   meanwhile=lambda: [a_gate_up_hi(act, 0, 0, i) for i in range(2)])
            a_hT_hi(act, "q", hT_hi)
            c = Counter(act, a["e"])
            act.wait_ge(v["e"], STEP["e.g"])
            c.link(nc.scalar.activation(rt[:, 1, :, 0:4], rt[:, 1, :, 0:4], ACT.Exp))
            c.at("e.expg")
            act.wait_ge(v["e"], STEP["e.d"])
            c.link(nc.scalar.activation(rt[:, 9, :, 0:1], rt[:, 9, :, 0:1], ACT.Exp))
            c.at("e.expd")
            def silu(m, j, tt, first=False):
                n = 2 * (E_BODY * m + j) + tt + 1
                act.wait_ge(t_gu, n)
                if not first:
                    act.wait_ge(v_eact, n - 2)
                nc.scalar.activation(gact[:, tt, :], ps[:, 4 + tt, 0:FE], ACT.Silu).then_inc(a_silu, 1)

            def expert(m, j, first=False, last=False):
                act.wait_ge(moe_in[3 * (j % 2) + 2], 16 * (E_BODY // 2) * m + 16 * (j // 2 + 1))
                nc.scalar.copy(moe_hi[3 * (j % 2) + 2], ring[:, 3 * (j % 2) + 2, :]).then_inc(a_dn, 1)
                if not last:
                    a_gate_up_hi(act, m, j + 1, 0)
                silu(m, j, 0, first)
                if not last:
                    a_gate_up_hi(act, m, j + 1, 1)
                silu(m, j, 1, first)
                if not first and not last:
                    act.wait_ge(t_dn, 2 * (E_BODY * m + j))
                    down_in(act, m, j + 1)

            act.wait_ge(v["e"], STEP["e.cw"])
            expert(0, 0, first=True)
            with act.Fori(0, LAST_PASS) as m:
                for j in range(1, E_BODY + 1):
                    expert(m, j)
            for j in range(1, E_BODY):
                expert(LAST_PASS, j, last=j == E_BODY - 1)
            act.wait_ge(v["f"], STEP["f.moe"])
            c = Counter(act, a["f"])
            for tt in range(TT):
                c.link(nc.scalar.activation(xn[:, tt, :], x_sb[:, tt, :], ACT.Square, accum_out=small[:, tt:tt + 1]))
            c.at("f.sq")
            act.wait_ge(v["f"], STEP["f.x"])
            a_norm(act, "bn", *mod_of[0])
            c = Counter(act, a["bp"])
            act.wait_ge(v["bn"], STEP["bn.v"])
            act.wait_ge(g["bp"], STEP["bp.zero"])
            for i in range(9):
                act.wait_ge(t_bin, i + 1)
                bank = ps[:, 4 + i % 4, :]
                if i < 2:
                    c.link(nc.scalar.copy((qg, kg)[i][:, :, :], bank.rearrange("p (i t) -> p i t", i=2)))
                elif i < 4:
                    c.link(nc.scalar.copy(vg[:, :, 256 * (i - 2):256 * (i - 2) + 256], bank.rearrange("p (a n) -> p a n", a=2)))
                elif i < 6:
                    gs = ggs[:, :, 256 * (i - 4):256 * (i - 4) + 256]
                    c.link(nc.scalar.activation(gs, bank.rearrange("p (a n) -> p a n", a=2), ACT.Sigmoid))
                elif i < 8:
                    c.link(nc.scalar.copy(sq_t[:, 2 * (i - 6):2 * (i - 6) + 2, :], bank.rearrange("p (i t) -> p i t", i=2)))
                else:
                    for kv in range(2):
                        for par in range(2):
                            c.link(nc.scalar.copy(kz[64 * par:64 * par + 64, kv, par, :], bank[64 * kv:64 * kv + 64, 0:256]))
                    c.link(nc.scalar.copy(svt[:, :, :], bank[:, 256:512].rearrange("p (a n) -> p a n", a=2)))
            c.at("bp.a")
            c = Counter(act, a["bg"])
            act.wait_ge(t["bg"], STEP["bg.lr"])
            c.link(nc.scalar.copy(glr_t, ps[0:16, 0, 0:256]))
            c.at("bg.glr")
            act.wait_ge(t["bg"], STEP["bg.z"])
            for i in range(2):
                c.link(nc.scalar.activation(zb[:, i, :], ps[:, 1, 256 * i:256 * i + 256], ACT.Identity, bias=prm_c[:, 54 + i:55 + i]))
            c.at("bg.zb")
            c.link(nc.scalar.activation(az[:, :, :], zb[:, :, :], ACT.Abs))
            c.link(nc.scalar.activation(az[:, :, :], az[:, :, :], ACT.Exp, scale=-1.0))
            c.link(nc.scalar.activation(az[:, :, :], az[:, :, :], ACT.Ln, bias=ones[:, 0:1]))
            c.at("bg.ln")
            act.wait_ge(v["bg"], STEP["bg.scan"])
            c.link(nc.scalar.activation(eb[:, :, :], nb2[:, :, :], ACT.Exp, scale=-1.0 / 16))
            c.link(nc.scalar.activation(enb[:, :, :], nb2[:, :, :], ACT.Exp, scale=1.0 / 16))
            c.at("bg.exp")
            act.wait_ge(v["bg"], STEP["bg.kt"])
            act.wait_ge(g["bp"], STEP["bp.zero"])
            c.link(nc.scalar.copy(ktz[0:64, 0::2, :], kg[0:64, :, :]))
            c.link(nc.scalar.copy(ktz[64:128, 1::2, :], kg[64:128, :, :]))
            c.at("bg.pad")
            act.wait_ge(t["bg"], STEP["bg.tr"])
            c.link(nc.scalar.copy(ket[:, :, :], ps[:, 0, :].rearrange("p (a n) -> p a n", a=2)))
            c.at("bg.ket")
            c = Counter(act, a["bs"])
            act.wait_ge(v["bs"], STEP["bs.sub"])
            c.link(nc.scalar.activation(sc[:, :, :], sc[:, :, :], ACT.Exp))
            c.link(nc.scalar.activation(swm[:, 16:32], swm[:, 16:32], ACT.Exp))
            c.at("bs.exp")
            for j in range(6):
                act.wait_ge(t["bs"], STEP["bs.pt0"] + j)
                c.link(nc.scalar.copy(p_t[:, 4 * j:4 * j + 4, :], ps[:, j, :].rearrange("p (j q) -> p j q", j=4)))
            c.at("bs.pt")
            c = Counter(act, a["bo"])
            for k in range(0, KT, 2):
                act.wait_ge(t["bo"], k // 2 + 1)
                c.link(nc.scalar.copy(hT[:, k:k + 2, :], ps[:, k // 2, :].rearrange("p (k t) -> p k t", k=2)))
            c.at("bo.hT")
            act.wait_ge(v["bo"], STEP["bo.x"])
            a_norm(act, "l0", *mod_of[1], meanwhile=lambda: a_w1_hi(act, 0, 0, 0))
            a_hT_hi(act, "l0", gT_hi)
            a_mlp_loop(act, 0)
            act.wait_ge(v["l0"], STEP["l0.x"])
            a_norm(act, "pn", *mod_of[2])
            act.wait_ge(v["pp"], STEP["pp.x"])
            a_norm(act, "l1", *mod_of[3], meanwhile=lambda: a_w1_hi(act, 1, 0, 0))
            a_hT_hi(act, "l1", gT_hi)
            a_mlp_loop(act, 1)
            act.wait_ge(v["l1"], STEP["l1.x"])
            c = Counter(act, a["z"])
            for tt in range(TT):
                c.link(nc.scalar.activation(xn[:, tt, :], x_sb[:, tt, :], ACT.Square, accum_out=small[:, tt:tt + 1]))
            c.at("z.sq")

        @block.vector
        def _(dve):
            def ada_slot(n):
                vec, q = n // 4, n % 4
                loaded(dve, ("ada", n))
                w = slot(("ada", n)).rearrange("p (t n) -> p t n", t=2)
                acc = macc[:, vec % 3, :]
                if q == 0 and vec >= 3:
                    dve.wait_ge(t_ada, vec - 2)
                for r in range(2):
                    k = 2 * q + r
                    if k == 0:
                        ins = nc.vector.tensor_scalar(acc, w[:, r, :], ccol[:, k:k + 1], None, ALU.mult)
                    else:
                        ins = nc.vector.scalar_tensor_tensor(acc, w[:, r, :], ccol[:, k:k + 1], acc, ALU.mult, ALU.add)
                    ada.link(ins)

            ada = Counter(dve, v_ada)
            c = Counter(dve, v["c"])
            dve.wait_ge(a["c"], STEP["c.sig"])
            c.link(nc.vector.tensor_tensor(ccol[:, :], ccol[:, :], csig[:, :], ALU.mult))
            for n in range(8):
                ada_slot(n)

            def mod_mix(c):
                dve.wait_ge(t_ada, 2)
                dve.wait_ge(par_in, 16 * 5)
                c.link(nc.vector.tensor_tensor(mod_c[:, 0, :], ps[:, 6, 0:8], adab_c[:, 0, :], ALU.add))
                c.link(nc.vector.tensor_tensor(mod_c[:, 1, :], ps[:, 7, 0:8], adab_c[:, 1, :], ALU.add))
                c.link(nc.vector.scalar_tensor_tensor(mod_c[:, 1, :], mod_c[:, 1, :], 1.0, norm_c[:, 0, :],
                                                      ALU.add, ALU.mult))

            v_norm(dve, "n", mod_c[:, 0, :], mod_c[:, 1, :], mod_mix)

            c = Counter(dve, v["w"])
            dve.wait_ge(t["w"], STEP["w.prm"])
            c.link(nc.vector.tensor_copy(prm_c[:, :], ps[:, 0, 256:336]))
            c.at("w.prmc")
            dve.wait_ge(gate_in, 16 * 7)
            c.link(nc.vector.tensor_scalar(gate_b[:, 1:2], gate_b[:, 0:1], 1 / CAP, None, ALU.mult))
            c.at("w.gb")
            c.at("w.pre")
            for n in range(IN_SLOTS):
                if n < 7:
                    dve.wait_ge(a["w"], n + 1)
                    dt = dtmp[:, :].rearrange("p (i t) -> p i t", i=2)
                    c.link(nc.vector.tensor_tensor(dt, raw[:, n % 2, :, 0:256], raw[:, n % 2, :, 1:257], ALU.subtract))
                    for i in range(2):
                        c.link(nc.vector.scalar_tensor_tensor(u[:, 2 * n + i, :], dt[:, i, :], mu_c[:, 2 * n + i:2 * n + i + 1],
                                                              raw[:, n % 2, i, 1:257], ALU.mult, ALU.add))
                ada_slot(8 + n)
                if n == 6:
                    c.at("w.shift")
            for n in range(21, 24):
                ada_slot(n)
            dve.wait_ge(t_ada, 3)
            for vec, base in ((2, 1), (5, 1)):
                gt = gate1[:, vec // 3, :]
                dve.wait_ge(t_ada, {2: 3, 5: 6}[vec])
                c.link(nc.vector.tensor_tensor(gt.rearrange("p (b n) -> p b n", b=2), gt.rearrange("p (b n) -> p b n", b=2),
                                               ps[:, base:base + 2, :], ALU.add))
                c.at(f"w.gate{vec}")
            c.link(nc.vector.tensor_tensor(mod_c[:, 2, :], ps[:, 3, 0:8], adab_c[:, 3, :], ALU.add))
            c.link(nc.vector.tensor_tensor(mod_c[:, 3, :], ps[:, 3, 8:16], adab_c[:, 4, :], ALU.add))
            c.link(nc.vector.scalar_tensor_tensor(mod_c[:, 3, :], mod_c[:, 3, :], 1.0, norm_c[:, 1, :], ALU.add, ALU.mult))
            c.at("w.mod")

            c = Counter(dve, v["m"])
            dve.wait_ge(a["w"], STEP["w.a"])
            for i in range(4):
                c.link(nc.vector.tensor_scalar(qk[:, i, :], convraw[:, i, 3:259], cw_c[:, 12 + i:13 + i], cb_c[:, i:i + 1],
                                               ALU.mult, ALU.add))
                for j in range(3):
                    c.link(nc.vector.scalar_tensor_tensor(qk[:, i, :], convraw[:, i, j:j + 256],
                                                          cw_c[:, 4 * j + i:4 * j + i + 1], qk[:, i, :], ALU.mult, ALU.add))
            c.at("m.conv")
            dve.wait_ge(a["m"], STEP["m.sig"])
            c.link(nc.vector.tensor_tensor(qk[:, :, :], qk[:, :, :], qsig[:, :, :], ALU.mult))
            c.at("m.qk")
            dve.wait_ge(a["m"], STEP["m.lf"])
            one4 = ones2[0:4, :]
            c.link(nc.vector.tensor_scalar(mrow[0:4, 0, :], mrow[0:4, 0, :], CAP, None, ALU.mult))
            c.link(nc.vector.tensor_tensor_scan(mrow[0:4, 2, :], one4, mrow[0:4, 1, :], 0.0, ALU.mult, ALU.add))
            c.link(nc.vector.tensor_tensor(mrow[0:4, 4, :], mrow[0:4, 0, :], mrow[0:4, 2, :], ALU.add))
            c.link(nc.vector.tensor_tensor_scan(mrow[0:4, 5, :], one4, mrow[0:4, 4, :], 0.0, ALU.mult, ALU.max))
            c.link(nc.vector.tensor_tensor(mrow[32:36, 4, :], mrow[0:4, 2, :], mrow[0:4, 5, :], ALU.subtract))
            c.link(nc.vector.tensor_copy(sel4[:, :, :], ident[0:4, 0:4].unsqueeze(2).to_broadcast([4, 4, P])))
            c.at("m.rows")
            dve.wait_ge(t["m"], STEP["m.bc"])
            c.link(nc.vector.tensor_copy(mcol[:, :, :], ps[:, 0, 0:128].rearrange("p (a n) -> p a n", a=2)))
            for h in range(4):
                mb = ps[:, 2 + h // 2, (h % 2) * 256:(h % 2) * 256 + 256]
                c.link(nc.vector.tensor_scalar(mz[:, h, 0:256], mb, mcol[:, 0, h:h + 1], 0.0, ALU.subtract, ALU.max))
                c.link(nc.vector.tensor_scalar(mz[:, h, 256:384], mb[:, 128:256], mcol[:, 1, h:h + 1], 0.0,
                                               ALU.subtract, ALU.max))
            c.at("m.z")
            dve.wait_ge(a["m"], STEP["m.exp"])
            dve.wait_ge(g["c"], STEP["c.masks"])
            cmask = m_causal.unsqueeze(1).to_broadcast([P, 4, P])
            c.link(nc.vector.tensor_tensor(mz[:, :, 0:128], mz[:, :, 0:128], cmask, ALU.mult))
            c.link(nc.vector.tensor_tensor(mz[:, :, 256:384], mz[:, :, 256:384], cmask, ALU.mult))
            dve.wait_ge(t["m"], STEP["m.sc"])
            for h in range(4):
                c.link(nc.vector.scalar_tensor_tensor(mz[:, h, :], ps[:, 4 + h, 0:384], 0.125, mz[:, h, :],
                                                      ALU.mult, ALU.mult))
            c.at("m.pt")
            dve.wait_ge(t["m"], STEP["m.num"])
            den, rec = small[:, 16:24], small[:, 24:32]
            c.link(nc.vector.tensor_copy(den, ps[:, 2, 0:8]))
            c.link(nc.vector.scalar_tensor_tensor(den, den, -1.0, den, ALU.mult, ALU.max))
            c.link(nc.vector.tensor_tensor(den, den, mem[:, :, :].rearrange("p a h -> p (a h)"), ALU.max))
            c.link(nc.vector.reciprocal(rec, den))
            ym = ytok[:, :, 512:1024]
            for tt in range(TT):
                c.link(nc.vector.tensor_tensor(ym[:, tt, :].rearrange("p (h n) -> p h n", h=4),
                                               ps[:, tt, :].rearrange("p (h n) -> p h n", h=4),
                                               rec[:, 4 * tt:4 * tt + 4].unsqueeze(2).to_broadcast([P, 4, P]), ALU.mult))
            c.link(nc.vector.tensor_tensor(msq[:, :, :], ym, ym, ALU.mult))
            for tt in range(TT):
                c.link(nc.vector.tensor_reduce(small[:, 8 + 4 * tt:12 + 4 * tt], msq[:, tt, :].rearrange("p (h n) -> p h n", h=4),
                                               AX_X, ALU.add))
            c.link(nc.vector.tensor_scalar(small[:, 8:16], small[:, 8:16], 1 / P, EPS, ALU.mult, ALU.add))
            c.at("m.ss")
            dve.wait_ge(g["m"], STEP["m.rs"])
            dve.wait_ge(row_in, 48)
            for tt in range(TT):
                yv = ym[:, tt, :].rearrange("p (h n) -> p h n", h=4)
                c.link(nc.vector.tensor_tensor(yv, yv, small[:, 8 + 4 * tt:12 + 4 * tt].unsqueeze(2).to_broadcast([P, 4, P]),
                                               ALU.mult))
            c.link(nc.vector.tensor_tensor(ym, ym, rowp[:, 2, :].unsqueeze(1).to_broadcast([P, TT, 512]), ALU.mult))
            c.link(nc.vector.tensor_tensor(ym, ym, om[:, :, :], ALU.mult))
            c.at("m.y")

            c = Counter(dve, v["r"])
            r_, k_ = u[:, 0:4, :], u[:, 4:8, :]

            def col4(x, n=SEQ):
                return x.unsqueeze(2).to_broadcast([P, 4, n])

            c.link(nc.vector.tensor_tensor(kx[:, :, :], k_, col4(kk_c), ALU.mult))
            c.link(nc.vector.tensor_tensor(sq[:, :, :], kx[:, :, :], kx[:, :, :], ALU.mult))
            c.at("r.sq")
            dve.wait_ge(a["r"], STEP["r.sig"])
            c.link(nc.vector.tensor_scalar(lw[:, :, :], lw[:, :, :], -DECAY, None, ALU.mult))
            for i in range(4):
                c.link(nc.vector.tensor_tensor_scan(cum[:, i, :], reset[:, :], lw[:, i, :], 0.0, ALU.mult, ALU.add))
            c.at("r.scan")
            c.link(nc.vector.scalar_tensor_tensor(kmod[:, :, :], av[:, :, :], 1.0, col4(ka_c), ALU.subtract, ALU.mult))
            c.link(nc.vector.scalar_tensor_tensor(kmod[:, :, :], kmod[:, :, :], 1.0, k_, ALU.add, ALU.mult))
            c.link(nc.vector.tensor_tensor(rkp[:, :, :], r_, kmod[:, :, :], ALU.mult))
            c.link(nc.vector.tensor_tensor(rkp[:, :, :], rkp[:, :, :], col4(rk_c), ALU.mult))
            c.at("r.rkp")
            dve.wait_ge(a["r"], STEP["r.sqrt"])
            c.link(nc.vector.tensor_scalar(kn[:, :, :], kn[:, :, :], 1e-12, None, ALU.max))
            c.link(nc.vector.reciprocal(kn[:, :, :], kn[:, :, :]))
            c.link(nc.vector.tensor_tensor(kx[:, :, :], kx[:, :, :], kn[:, :, :], ALU.mult))
            chunk = lambda x: x.rearrange("p i (c s) -> p i c s", s=CH)
            aq, kxc, pcc = chunk(ar[:, :, 0, :]), chunk(kx), chunk(pcum)
            c.link(nc.vector.tensor_tensor(aq[:, :, :, 1:CH], kxc[:, :, :, 1:CH], pcc[:, :, :, 0:CH - 1], ALU.mult))
            c.link(nc.vector.tensor_copy(aq[:, :, :, 0:1], kxc[:, :, :, 0:1]))
            c.link(nc.vector.tensor_tensor(ar[:, :, 1, :], r_, pcum[:, :, :], ALU.mult))
            c.link(nc.vector.tensor_tensor(sq[:, :, :], kx[:, :, :], av[:, :, :], ALU.mult))
            c.link(nc.vector.tensor_tensor(bh[:, :, :], sq[:, :, :], pinv[:, :, :], ALU.mult))
            c.link(nc.vector.tensor_tensor(kh[:, :, :], kmod[:, :, :], pinv[:, :, :], ALU.mult))
            c.at("r.bh")
            c.link(nc.vector.tensor_copy(pend[:, :, :], pcc[:, :, :, CH - 1]))
            pb = pend[:, :, :].unsqueeze(3).to_broadcast([P, 4, NC, CH])
            c.link(nc.vector.tensor_tensor(chunk(bend), chunk(bh), pb, ALU.mult))
            c.link(nc.vector.tensor_tensor(chunk(kend), chunk(kh), pb, ALU.mult))
            c.at("r.bend")
            dve.wait_ge(t["r"], STEP["r.bonus"])
            c.link(nc.vector.tensor_copy(bon[:, :, :], ps[:, 6, 0:16].rearrange("p (a h) -> p a h", a=2)))
            c.at("r.bon")

            c = Counter(dve, v["i"])

            def m4(m):
                return m.unsqueeze(1).to_broadcast([P, 4, P])

            dve.wait_ge(a["r"], STEP["r.tok"])
            for step, (kind, src, arg, dst) in enumerate(INV_V):
                for gi in range(4):
                    if src is not None:
                        dve.wait_ge(t["i"], 4 * src + gi + 1)
                    if kind == "mask":
                        ins = nc.vector.tensor_tensor(dst[:, gi], bank4(src, gi), m4(arg), ALU.mult)
                    elif kind == "maskF":
                        if step == V_A16:
                            dve.wait_ge(a["i"], gi + 1)
                        ins = nc.vector.tensor_tensor(dst[:, gi], iF[:, gi], m4(arg), ALU.mult)
                    elif kind == "ident":
                        ins = nc.vector.tensor_tensor(dst[:, gi], iB[:, gi], m4(ident[:, :]), ALU.add)
                    elif kind == "lakv":
                        ins = nc.vector.tensor_copy(lakv[:, gi // 2, 256 * (gi % 2):256 * (gi % 2) + 256],
                                                    ps[:, bank_of(src, gi), 0:256])
                    else:
                        ins = nc.vector.tensor_tensor(dst[:, gi], dst[:, gi], bank4(src, gi), ALU.add)
                    c.link(ins)
            c.at("i.done")

            c = Counter(dve, v["s"])
            dve.wait_ge(g["r"], STEP["r.zero"])
            for ch in range(NC):
                r0, tt = CH * (ch % 2), ch // 2
                rr, lk = rbuf[r0:r0 + CH, tt, :], lakv[r0:r0 + CH, tt, :]
                if ch == 0:
                    c.link(nc.vector.tensor_scalar(rr, lk, -1.0, None, ALU.mult))
                else:
                    dve.wait_ge(t_as, ch)
                    c.link(nc.vector.scalar_tensor_tensor(rr, ps[r0:r0 + CH, 0, :], -1.0, lk, ALU.mult, ALU.subtract))
                assert c.n == 5 * ch + 1
                if ch < NC - 1:
                    for hh in range(2):
                        q = slice(64 * hh, 64 * hh + 64)
                        c.link(nc.vector.tensor_tensor(state[q, ch + 1, :, q], state[q, ch, :, q],
                                                       pend[q, :, ch].unsqueeze(2).to_broadcast([64, 4, 64]), ALU.mult))
                    dve.wait_ge(t_ds, ch + 1)
                    for hh in range(2):
                        q = slice(64 * hh, 64 * hh + 64)
                        dl = ps[q, 2, :].rearrange("p (i n) -> p i n", i=4)[:, :, q]
                        c.link(nc.vector.tensor_tensor(state[q, ch + 1, :, q], state[q, ch + 1, :, q], dl, ALU.add))
            c = Counter(dve, v["y"])
            sm, sv = small[:, 32:48], small[:, 48:64]
            for tt in range(TT):
                dve.wait_ge(t_y, tt + 1)
                pv = ps[:, 4 + tt, :].rearrange("p (h n) -> p h n", h=8)
                s8 = sm[:, 8 * tt:8 * tt + 8]
                c.link(nc.vector.tensor_reduce(s8, pv, AX_X, ALU.add))
                c.link(nc.vector.tensor_scalar(s8, s8, 1 / 64, None, ALU.mult))
                c.link(nc.vector.tensor_tensor(ytok[:, tt, 0:512].rearrange("p (h n) -> p h n", h=8), pv,
                                               s8.unsqueeze(2).to_broadcast([P, 8, 64]), ALU.subtract))
            yr = ytok[:, :, 0:512]
            c.link(nc.vector.tensor_tensor(ysq[:, :, :], yr, yr, ALU.mult))
            for tt in range(TT):
                c.link(nc.vector.tensor_reduce(sm[:, 8 * tt:8 * tt + 8], ysq[:, tt, :].rearrange("p (h n) -> p h n", h=8),
                                               AX_X, ALU.add))
            c.link(nc.vector.tensor_scalar(sm, sm, 1 / 64, GN_EPS, ALU.mult, ALU.add))
            c.at("y.var")
            dve.wait_ge(g["y"], STEP["y.rs"])

            def h8(x):
                return x.rearrange("p a (h n) -> p (a h) n", h=8)

            for tt in range(TT):
                yv = ytok[:, tt, 0:512].rearrange("p (h n) -> p h n", h=8)
                c.link(nc.vector.tensor_tensor(yv, yv, sm[:, 8 * tt:8 * tt + 8].unsqueeze(2).to_broadcast([P, 8, 64]), ALU.mult))
            c.link(nc.vector.tensor_tensor(yr, yr, rowp[:, 0, :].unsqueeze(1).to_broadcast([P, TT, 512]), ALU.mult))
            c.link(nc.vector.tensor_tensor(yr, yr, rowp[:, 1, :].unsqueeze(1).to_broadcast([P, TT, 512]), ALU.add))
            c.link(nc.vector.tensor_tensor(h8(ysq), h8(vtok), bon[:, :, :].rearrange("p a h -> p (a h)").unsqueeze(2)
                                           .to_broadcast([P, 16, 64]), ALU.mult))
            c.link(nc.vector.tensor_tensor(yr, yr, ysq[:, :, :], ALU.add))
            c.link(nc.vector.tensor_tensor(yr, yr, gtok[:, :, :], ALU.mult))
            c.at("y.done")
            c = Counter(dve, v["o"])
            dve.wait_ge(par_in, 16 * 5)
            for j in range(4):
                dve.wait_ge(t_out, j + 1)
                xs = x_sb[:, j // 2, 512 * (j % 2):512 * (j % 2) + 512]
                c.link(nc.vector.tensor_tensor(dtmp[:, :], ps[:, 4 + j, :], gate1[:, 0, 512 * (j % 2):512 * (j % 2) + 512], ALU.mult))
                c.link(nc.vector.tensor_tensor(xs, xs, dtmp[:, :], ALU.add))
            c.at("o.x")
            nc.vector.memset(dtmp[:, :], 0.0).then_inc(v_ada2, CREDIT)
            dve.wait_ge(v_ada2, CREDIT)
            nc.vector.memset(dtmp[:, :], 0.0).then_inc(v_mod, CREDIT)
            v_norm(dve, "q", mod_c[:, 2, :], mod_c[:, 3, :])
            dve.wait_ge(t["e"], STEP["e.rt"])
            v_hT_lo(dve, "q", hT_hi, 0)
            v_up_lo(dve, 0, 0)

            c = Counter(dve, v["e"])
            R = lambda i, n: rt[:, i, :, 0:n]
            b8 = lambda x, n: x.to_broadcast([P, TT, n])
            rv = lambda n: rev[:, 8 - n:8].unsqueeze(1).to_broadcast([P, TT, n])
            dve.wait_ge(t["e"], STEP["e.rt"])
            dve.wait_ge(rt_in, 64)
            c.link(nc.vector.tensor_tensor(lg[:, :, :], ps[:, 7, 0:128].rearrange("p (a n) -> p a n", a=2)[:, :, 0:36],
                                           b_rt.unsqueeze(1).to_broadcast([P, TT, 36]), ALU.add))
            gl = lg[:, :, 32:36]
            c.link(nc.vector.tensor_reduce(R(0, 1), gl, AX_X, ALU.max))
            c.link(nc.vector.tensor_tensor(R(1, 4), gl, b8(R(0, 1), 4), ALU.subtract))
            c.at("e.g")

            def first_max(vals, top, n, onehot, key):
                c.link(nc.vector.tensor_tensor(onehot, vals, b8(top, n), ALU.is_equal))
                c.link(nc.vector.tensor_tensor(onehot, onehot, rv(n), ALU.mult))
                c.link(nc.vector.tensor_reduce(key, onehot, AX_X, ALU.max))
                c.link(nc.vector.tensor_tensor(onehot, rv(n), b8(key, n), ALU.is_equal))

            first_max(gl, R(0, 1), 4, R(2, 4), R(3, 1))
            prod = rt[:, 10:11].rearrange("p o a n -> p (o a) n")
            c.link(nc.vector.tensor_tensor(prod.rearrange("p a (g e) -> p a g e", g=NG),
                                           lg[:, :, 0:32].rearrange("p a (g e) -> p a g e", g=NG),
                                           R(2, 4).unsqueeze(3).to_broadcast([P, TT, NG, EG]), ALU.mult))
            sel = R(4, 8)
            c.link(nc.vector.tensor_reduce(sel, prod.rearrange("p a (g e) -> p a e g", g=NG), AX_X, ALU.add))
            c.link(nc.vector.tensor_reduce(R(5, 1), sel, AX_X, ALU.max))
            first_max(sel, R(5, 1), 8, R(6, 8), R(3, 1))
            c.link(nc.vector.scalar_tensor_tensor(sel, R(6, 8), -3e38, sel, ALU.mult, ALU.add))
            c.link(nc.vector.tensor_reduce(R(7, 1), sel, AX_X, ALU.max))
            first_max(sel, R(7, 1), 8, R(8, 8), R(3, 1))
            c.link(nc.vector.tensor_tensor(R(9, 1), R(7, 1), R(5, 1), ALU.subtract))
            c.at("e.d")
            dve.wait_ge(a["e"], STEP["e.expg"])
            c.link(nc.vector.tensor_reduce(R(0, 1), R(1, 4), AX_X, ALU.add))
            dve.wait_ge(a["e"], STEP["e.expd"])
            c.link(nc.vector.tensor_scalar(R(11, 1), R(9, 1), 1.0, None, ALU.add))
            c.link(nc.vector.tensor_tensor(R(11, 1), R(11, 1), R(0, 1), ALU.mult))
            c.link(nc.vector.reciprocal(R(11, 1), R(11, 1)))
            c.link(nc.vector.tensor_tensor(R(9, 1), R(9, 1), R(11, 1), ALU.mult))
            c.link(nc.vector.tensor_tensor(R(6, 8), R(6, 8), b8(R(11, 1), 8), ALU.mult))
            c.link(nc.vector.tensor_tensor(R(8, 8), R(8, 8), b8(R(9, 1), 8), ALU.mult))
            c.link(nc.vector.tensor_tensor(R(6, 8), R(6, 8), R(8, 8), ALU.add))
            c.link(nc.vector.tensor_tensor(cw[:, :, :].rearrange("p a (g e) -> p a g e", g=NG),
                                           R(2, 4).unsqueeze(3).to_broadcast([P, TT, NG, EG]),
                                           R(6, 8).unsqueeze(2).to_broadcast([P, TT, NG, EG]), ALU.mult))
            c.at("e.cw")
            def products(m, e, tt, first=False):
                n = 2 * (E_BODY * m + e) + tt + 1
                dve.wait_ge(a_silu, n)
                if not first:
                    dve.wait_ge(t_tr, n - 2)
                nc.vector.scalar_tensor_tensor(eact[:, tt, :], ps[:, 4 + tt, FE:2 * FE],
                                               cw[:, tt, bass.ds(m * E_BODY + e, 1)], gact[:, tt, :],
                                               ALU.mult, ALU.mult).then_inc(v_eact, 1)

            def products_t(m, e, tt, first=False):
                n = 2 * (E_BODY * m + e) + tt + 1
                dve.wait_ge(t_tr, n)
                if not first:
                    dve.wait_ge(t_dn, n - 2)
                src = ps[:, 6, FE * tt:FE * tt + FE].rearrange("p (f n) -> p f n", f=2)
                nc.vector.tensor_copy(eact_hi[:, tt], src).then_inc(v_eact_t, 1)
                dve.wait_ge(v_eact_t, 2 * n - 1)
                trailing(nc.vector, eact_lo[:, tt], src, eact_hi[:, tt]).then_inc(v_eact_t, 1)

            def modulation(m, k):
                vec, q = k // 4, k % 4
                acc = macc[:, vec, :]
                dve.wait_ge(ada2_in[k % 2], 16 * 6 * m + 16 * (k // 2 + 1))
                for r in range(2):
                    w = ring[:, 6 + k % 2, D * r:D * r + D]
                    cc = ccol[:, 8 + 2 * q + r:9 + 2 * q + r]
                    if 2 * q + r == 0:
                        ins = nc.vector.tensor_scalar(acc, w, cc, None, ALU.mult)
                    else:
                        ins = nc.vector.scalar_tensor_tensor(acc, w, cc, acc, ALU.mult, ALU.add)
                    ins.then_inc(v_ada2, 1)
                    dve.wait_ge(v_ada2, 24 * m + CREDIT + 2 * k + r + 1)

            def gate_row(m, h):
                dve.wait_ge(t_mod, 3 * m + 2 + h)
                gv = gate2[:, bass.ds(m, 1), 512 * h:512 * h + 512].rearrange("p o n -> p (o n)")
                nc.vector.tensor_tensor(gv, gv, ps[:, 7, :], ALU.add).then_inc(v_mod, 1)

            def expert(m, j, first=False, last=False):
                if 1 <= j <= 6:
                    modulation(m, 2 * j - 2)
                if not first:
                    products_t(m, j - 1, 1, first=isinstance(m, int) and m == 0 and j == 1)
                products(m, j, 0, first=first)
                if j == 7:
                    dve.wait_ge(t_mod, 3 * m + 1)
                    nc.vector.tensor_copy(mod2[:, bass.ds(m, 1), :].rearrange("p o n -> p (o n)"),
                                          ps[:, 7, 0:32]).then_inc(v_mod, 1)
                v_down_lo(dve, m, j)
                if not last:
                    v_up_lo(dve, m, j + 1)
                if 1 <= j <= 6:
                    modulation(m, 2 * j - 1)
                products_t(m, j, 0, first=first)
                if j == 7:
                    gate_row(m, 0)
                products(m, j, 1, first=first)
                if j == 7:
                    gate_row(m, 1)

            expert(0, 0, first=True)
            with dve.Fori(0, LAST_PASS) as m:
                for j in range(1, E_BODY + 1):
                    expert(m, j)
            for j in range(1, E_BODY):
                expert(LAST_PASS, j, last=j == E_BODY - 1)
            products_t(LAST_PASS, E_BODY - 1, 1)
            c = Counter(dve, v["f"])
            dve.wait_ge(t_dn, 2 * NE)
            v_residual(dve, c, gate1[:, 1, :])
            c.at("f.moe")
            v_rstd(dve, c, "f")
            dve.wait_ge(nrm_in, 16)
            for tt in range(TT):
                c.link(nc.vector.scalar_tensor_tensor(x_sb[:, tt, :], x_sb[:, tt, :], small[:, tt:tt + 1], nrm_b,
                                                      ALU.mult, ALU.mult))
            c.at("f.x")
            for m in range(4):
                if m == 2:
                    c.link(nc.vector.tensor_tensor(mod2[:, 2, 16:32], mod2[:, 2, 16:32], prm_c[:, 64:80], ALU.add))
                    c.link(nc.vector.scalar_tensor_tensor(mod2[:, 2, 24:32], mod2[:, 2, 24:32], 1.0, prm_c[:, 56:64],
                                                          ALU.add, ALU.mult))
                else:
                    c.link(nc.vector.tensor_tensor(mod2[:, m, 0:16], mod2[:, m, 0:16],
                                                   adab2_c[:, 2 * m:2 * m + 2, :].rearrange("p v t -> p (v t)"), ALU.add))
                    c.link(nc.vector.scalar_tensor_tensor(mod2[:, m, 8:16], mod2[:, m, 8:16], 1.0, norm2_c[:, m, :],
                                                          ALU.add, ALU.mult))
            c.at("f.mod")
            v_norm(dve, "bn", *mod_of[0])
            c = Counter(dve, v["bp"])
            for i in (4, 5):
                dve.wait_ge(a["bp"], i + 1)
                gs = ggs[:, :, 256 * (i - 4):256 * (i - 4) + 256]
                c.link(nc.vector.tensor_tensor(gs, gs, ps[:, 4 + i % 4, :].rearrange("p (a n) -> p a n", a=2), ALU.mult))
            c = Counter(dve, v["bg"])
            dve.wait_ge(a["bg"], STEP["bg.ln"])
            c.link(nc.vector.tensor_scalar(zb[:, :, :], zb[:, :, :], -1.0, 0.0, ALU.mult, ALU.max))
            c.link(nc.vector.tensor_tensor(zb[:, :, :], zb[:, :, :], az[:, :, :], ALU.add))
            for i in range(2):
                c.link(nc.vector.tensor_tensor_scan(nb2[:, i, :], reset[:, :], zb[:, i, :], 0.0, ALU.mult, ALU.add))
            c.at("bg.scan")
            dve.wait_ge(a["bg"], STEP["bg.exp"])
            dve.wait_ge(a["bp"], STEP["bp.a"])
            c.link(nc.vector.scalar_tensor_tensor(qg[:, :, :], qg[:, :, :], 0.125, eb[:, :, :], ALU.mult, ALU.mult))
            c.link(nc.vector.tensor_tensor(kg[:, :, :], kg[:, :, :], enb[:, :, :], ALU.mult))
            c.at("bg.kt")
            c.link(nc.vector.tensor_copy(gdec[:, :, :], chunk2(eb)[:, :, :, CH - 1]))
            c.link(nc.vector.tensor_tensor(chunk2(kend2), chunk2(kg), gdec[:, :, :].unsqueeze(3).to_broadcast([P, 2, NC, CH]),
                                           ALU.mult))
            c.at("bg.kend")
            for tt in range(TT):
                dve.wait_ge(t["bg"], STEP["bg.at0"] + tt)
                c.link(nc.vector.tensor_tensor(at[:, tt], ps[:, 2 + tt, :].rearrange("p (h t) -> p h t", h=4),
                                               m_rb.unsqueeze(1).to_broadcast([P, 4, P]), ALU.mult))
            c.at("bg.at")
            dve.wait_ge(t["bg"], STEP["bg.ds"])
            dve.wait_ge(g["bp"], STEP["bp.zero"])
            for ch in range(NC - 1):
                for hh in range(2):
                    q, e = slice(64 * hh, 64 * hh + 64), slice(P * hh, P * hh + P)
                    st, nx = sg_state[q, ch, :, e], sg_state[q, ch + 1, :, e]
                    c.link(nc.vector.tensor_tensor(nx, st, gdec[q, :, ch].unsqueeze(2).to_broadcast([64, 2, P]), ALU.mult))
                    c.link(nc.vector.tensor_tensor(nx, nx, ps[q, 4 + ch, :].rearrange("p (i n) -> p i n", i=2)[:, :, e], ALU.add))
            c.at("bg.state")
            dve.wait_ge(t["bg"], STEP["bg.o"])
            og = y2[:, :, 0:512]
            c.link(nc.vector.tensor_copy(og, ps[:, 0:2, :]))
            c.link(nc.vector.tensor_tensor(gsq[:, :, :], og, og, ALU.mult))
            c.link(nc.vector.tensor_reduce(small[:, 8:16], gsq[:, :, :].rearrange("p a (h n) -> p (a h) n", h=4), AX_X, ALU.add))
            c.link(nc.vector.tensor_scalar(small[:, 8:16], small[:, 8:16], 1 / P, EPS, ALU.mult, ALU.add))
            c.at("bg.ss")
            dve.wait_ge(g["bg"], STEP["bg.rs"])
            for tt in range(TT):
                ov = og[:, tt, :].rearrange("p (h n) -> p h n", h=4)
                c.link(nc.vector.tensor_tensor(ov, ov, small[:, 8 + 4 * tt:12 + 4 * tt].unsqueeze(2).to_broadcast([P, 4, P]), ALU.mult))
                c.link(nc.vector.tensor_tensor(ov, ov, ggn.unsqueeze(1).to_broadcast([P, 4, P]), ALU.mult))
            c.link(nc.vector.tensor_tensor(og, og, ggs[:, :, :], ALU.mult))
            c.at("bg.y")
            c = Counter(dve, v["bs"])
            dve.wait_ge(bias_in, 16)
            for j in range(6):
                dve.wait_ge(t["bs"], STEP["bs.s0"] + j)
                if j < 2:
                    c.link(nc.vector.scalar_tensor_tensor(sc[:, 4 * j:4 * j + 4, 0:P], ps[:, j, :].rearrange("p (h k) -> p h k", h=4),
                                                          0.125, bias8[:, 4 * j:4 * j + 4, P:2 * P], ALU.mult, ALU.add))
                else:
                    hs = slice(2 * (j - 2), 2 * (j - 2) + 2)
                    c.link(nc.vector.scalar_tensor_tensor(sc[:, hs, P:3 * P], ps[:, j, :].rearrange("p (h k) -> p h k", h=2),
                                                          0.125, bias8[:, hs, :], ALU.mult, ALU.add))
            mx, es, dn = swm[:, 0:16], swm[:, 16:32], swm[:, 32:48]
            parts = ((0, sc[:, :, 0:P], P), (8, sc[:, :, P:3 * P], 2 * P))
            for o, s_, n in parts:
                c.link(nc.vector.tensor_reduce(mx[:, o:o + 8], s_, AX_X, ALU.max))
                c.link(nc.vector.tensor_tensor(mx[:, o:o + 8], mx[:, o:o + 8], sink_b, ALU.max))
                c.link(nc.vector.tensor_tensor(es[:, o:o + 8], sink_b, mx[:, o:o + 8], ALU.subtract))
                c.link(nc.vector.tensor_tensor(s_, s_, mx[:, o:o + 8].unsqueeze(2).to_broadcast([P, 8, n]), ALU.subtract))
            c.at("bs.sub")
            dve.wait_ge(a["bs"], STEP["bs.exp"])
            for o, s_, n in parts:
                c.link(nc.vector.tensor_reduce(dn[:, o:o + 8], s_, AX_X, ALU.add))
            c.link(nc.vector.tensor_tensor(dn, dn, es, ALU.add))
            c.link(nc.vector.reciprocal(dn, dn))
            c.at("bs.den")
            for tt in range(TT):
                dve.wait_ge(t["bs"], STEP["bs.o"])
                c.link(nc.vector.tensor_tensor(y2[:, tt, 512:1024].rearrange("p (h n) -> p h n", h=8),
                                               ps[:, 6 + tt, :].rearrange("p (h n) -> p h n", h=8),
                                               dn[:, 8 * tt:8 * tt + 8].unsqueeze(2).to_broadcast([P, 8, 64]), ALU.mult))
            c.at("bs.y")
            c = Counter(dve, v["bo"])
            dve.wait_ge(t_bout, 4)
            v_residual(dve, c, gate2[:, 0, :], 4)
            c.at("bo.x")
            v_norm(dve, "l0", *mod_of[1])
            v_hT_lo(dve, "l0", gT_hi, 1)
            v_w1_lo(dve, 0, 0, 0)
            v_mlp_loop(dve, 0)
            dve.wait_ge(t_fd, 16)
            c = Counter(dve, v["l0"], STEP["l0.v"])
            v_residual(dve, c, gate2[:, 1, :])
            c.at("l0.x")
            v_norm(dve, "pn", *mod_of[2])
            c = Counter(dve, v["pp"])
            dve.wait_ge(a["pn"], STEP["pn.a"])
            dve.wait_ge(g["pp"], STEP["pp.zero"])
            c.link(nc.vector.tensor_copy(hp[:, :, PAD:], hT[:, :, :]))
            c.link(nc.vector.reciprocal(pinvc[:, :, :], pinvc[:, :, :]))
            c.link(nc.vector.tensor_tensor(pa[:, :, PAD:], hp[:, :, PAD:], hp[:, :, PAD - 1:PAD + 255], ALU.add))
            c.link(nc.vector.tensor_tensor(pb_[:, :, PAD:], pa[:, 2:8, PAD:], pa[:, 2:8, PAD - 2:PAD + 254], ALU.add))
            c.link(nc.vector.tensor_tensor(pa[:, 4:8, PAD:], pb_[:, 2:6, PAD:], pb_[:, 2:6, PAD - 4:PAD + 252], ALU.add))
            c.link(nc.vector.tensor_tensor(pb_[:, 4:6, PAD:], pa[:, 6:8, PAD:], pa[:, 6:8, PAD - 8:PAD + 248], ALU.add))
            for gi, src in enumerate((pa[:, 0:2], pb_[:, 0:2], pa[:, 4:6], pb_[:, 4:6])):
                o = hT[:, 2 * gi:2 * gi + 2, :]
                c.link(nc.vector.tensor_tensor(src[:, :, PAD:], src[:, :, PAD:],
                                               pinvc[:, gi, :].unsqueeze(1).to_broadcast([P, 2, SEQ]), ALU.mult))
                c.link(nc.vector.tensor_tensor(o, src[:, :, PAD:], hp[:, 2 * gi:2 * gi + 2, PAD:], ALU.subtract))
            c.at("pp.h")
            dve.wait_ge(pool_in, 32)
            c.link(nc.vector.tensor_tensor(gate2[:, 2, :], gate2[:, 2, :], psc_b, ALU.mult))
            dve.wait_ge(t["pp"], STEP["pp.mm"])
            v_residual(dve, c, gate2[:, 2, :], 4)
            c.at("pp.x")
            v_norm(dve, "l1", *mod_of[3])
            v_hT_lo(dve, "l1", gT_hi, 2)
            v_w1_lo(dve, 1, 0, 0)
            v_mlp_loop(dve, 1)
            dve.wait_ge(t_fd, 32)
            c = Counter(dve, v["l1"], STEP["l1.v"])
            v_residual(dve, c, gate2[:, 3, :])
            c.at("l1.x")
            c = Counter(dve, v["z"])
            v_rstd(dve, c, "z")
            dve.wait_ge(nrm2_in, 16)
            for tt in range(TT):
                c.link(nc.vector.scalar_tensor_tensor(x_sb[:, tt, :], x_sb[:, tt, :], small[:, tt:tt + 1], gate2[:, 0, :],
                                                      ALU.mult, ALU.mult))
                if tt == 0:
                    c.at("z.out0")

        @block.tensor
        def _(pe):
            pe.wait_ge(hot_in, 32)
            nc.tensor.matmul(ps[0:SWA_H, 4, 0:384], rel_sb[0:33, :], hots[0:33, :], start=True, stop=True).then_inc(t_bias, 1)
            pe.wait_ge(g["c"], STEP["c.ident"])
            for vec in range(2):
                pe.wait_ge(v_ada, 8 * (vec + 1))
                t_columns(macc[:, vec, :], ps[:, 6 + vec, :]).then_inc(t_ada, 1)
            t_norm(pe, "n")

            c = Counter(pe, t["w"])
            pe.wait_ge(prm_in, 16 * 10)
            pe.wait_ge(a["n"], STEP["n.a"])
            pe.wait_ge(v["n"], STEP["n.v"])
            c.mark(nc.tensor.transpose(ps[:, 0, 256:336], prm[0:80, :], ident[0:80, 0:80]))
            c.at("w.prm")
            pe.wait_ge(a_bias, 1)
            for n in range(IN_SLOTS):
                loaded(pe, ("win", n))
                if n >= 4:
                    pe.wait_ge(a["w"], n - 3)
                w = slot(("win", n)).rearrange("p (t n) -> p t n", t=8)
                for j in range(2):
                    for k in range(KT):
                        if n < 9:
                            ins = nc.tensor.matmul(ps[:, 4 + n % 4, 256 * j:256 * j + 256], w[:, k, P * j:P * j + P],
                                                   hT[:, k, :], start=k == 0, stop=k == KT - 1)
                        else:
                            ins = nc.tensor.matmul(ps[:, 4 + n % 4, 256 * j:256 * j + 256], hT[:, k, P * j:P * j + P],
                                                   w[:, k, :], start=k == 0, stop=k == KT - 1)
                ins.then_inc(t_win, 1)
            pe.wait_ge(gate_in, 16 * 7)
            pe.wait_ge(v["w"], STEP["w.prmc"])
            for k in range(KT):
                ins = nc.tensor.matmul(ps[0:36, 0, 0:256], w_if[:, k, :], hT[:, k, :], start=k == 0, stop=k == KT - 1)
            c.mark(ins)
            c.at("w.if")
            for vec in range(2, 6):
                pe.wait_ge(v_ada, 8 * (vec + 1))
                if vec in (2, 5):
                    if vec == 5:
                        pe.wait_ge(v["w"], STEP["w.gate2"])
                    for j in range(2):
                        ins = nc.tensor.matmul(ps[:, 1 + j, :], ones[:, :], macc[:, vec % 3, 512 * j:512 * j + 512],
                                               start=True, stop=True)
                else:
                    ins = t_columns(macc[:, vec % 3, :], ps[:, 3, 8 * (vec - 3):8 * (vec - 3) + 8])
                ins.then_inc(t_ada, 1)

            c = Counter(pe, t["m"])
            pe.wait_ge(v["m"], STEP["m.rows"])
            pe.wait_ge(v["w"], STEP["w.mod"])
            for tt in range(TT):
                nc.tensor.transpose(ps[:, 0, 64 * tt:64 * tt + 64], mrow[:, 4, P * tt:P * tt + P], ident[0:64, 0:64])
            for h in range(4):
                ins = nc.tensor.matmul(ps[:, 2 + h // 2, (h % 2) * 256:(h % 2) * 256 + 256], sel4[:, h, :], mrow[0:4, 5, :],
                                       start=True, stop=True)
            c.mark(ins)
            c.at("m.bc")
            pe.wait_ge(a["w"], STEP["w.a"])
            for h in range(4):
                q = slice(64 * (h % 2), 64 * (h % 2) + 64)
                nc.tensor.matmul(ps[:, 4 + h, 0:256], qk[q, 2 + h // 2, 0:P], qk[q, h // 2, :], start=True, stop=True)
                ins = nc.tensor.matmul(ps[:, 4 + h, 256:384], qk[q, 2 + h // 2, P:2 * P], qk[q, h // 2, P:2 * P],
                                       start=True, stop=True)
            c.mark(ins)
            c.at("m.sc")
            pe.wait_ge(v["m"], STEP["m.pt"])
            for tt in range(TT):
                for h in range(4):
                    parts = [(0, 0)] if tt == 0 else [(0, 128), (1, 256)]
                    for i, (s_, o) in enumerate(parts):
                        nc.tensor.matmul(ps[:, tt, P * h:P * h + P], mz[:, h, o:o + P], vm[:, s_, P * h:P * h + P],
                                         start=i == 0, stop=i == len(parts) - 1)
                    for i, (s_, o) in enumerate(parts):
                        ins = nc.tensor.matmul(ps[:, 2, 4 * tt + h:4 * tt + h + 1], mz[:, h, o:o + P], ones[:, 0:1],
                                               start=i == 0, stop=i == len(parts) - 1)
            c.mark(ins)
            c.at("m.num")

            c = Counter(pe, t["r"])
            pe.wait_ge(a["r"], STEP["r.u"])
            pe.wait_ge(v["m"], STEP["m.y"])
            for j in range(2):
                for i in range(4):
                    o = (i % 2) * 256
                    nc.tensor.matmul(ps[:, 2 * j + i // 2, o:o + 256], wup[:, j, P * i:P * i + P], u[:, 12, :],
                                     start=True, stop=True)
            for tt in range(TT):
                ins = nc.tensor.matmul(ps[:, 4 + tt, :], u[:, 13, P * tt:P * tt + P], gup[:, :], start=True, stop=True)
            c.mark(ins)
            c.at("r.wa")
            pe.wait_ge(v["r"], STEP["r.sq"])
            for i in range(4):
                ins = nc.tensor.matmul(ps[:, 6 + i // 2, (i % 2) * 256:(i % 2) * 256 + 256], headblk[:, :], sq[:, i, :],
                                       start=True, stop=True)
            c.mark(ins)
            c.at("r.n2")
            pe.wait_ge(a["r"], STEP["r.sqrt"])
            pe.wait_ge(v["r"], STEP["r.rkp"])
            for tt in range(TT):
                for i in range(4):
                    ins = nc.tensor.matmul(ps[:, 6, 8 * tt + 2 * i:8 * tt + 2 * i + 2], rkp[:, i, P * tt:P * tt + P],
                                           headsel[:, :], start=True, stop=True)
            c.mark(ins)
            c.at("r.bonus")
            pe.wait_ge(v["r"], STEP["r.bend"])
            for b, src in enumerate((u[:, 8:12, :], bend, kend)):
                for tt in range(TT):
                    for i in range(4):
                        ins = nc.tensor.transpose(ps[:, 2 * b + tt, P * i:P * i + P], src[:, i, P * tt:P * tt + P], ident[:, :])
                c.mark(ins)
            c.at("r.tr")

            c = Counter(pe, t["i"])
            pe.wait_ge(a["r"], STEP["r.tok"])
            pe.wait_ge(v["r"], STEP["r.bon"])
            for step, (kind, lhs, rhs, need_a, need_v, free) in enumerate(INV_T):
                for gi in range(4):
                    tt, hf = gi // 2, gi % 2
                    if need_a is not None:
                        pe.wait_ge(a["i"], 4 * need_a + gi + 1)
                    if need_v is not None:
                        pe.wait_ge(v["i"], 4 * need_v + gi + 1)
                    if free is not None:
                        pe.wait_ge({"a": a, "v": v}[free[0]]["i"], 4 * free[1] + gi + 1)
                    tok = slice(P * tt, P * tt + P)
                    for hh in range(4):
                        h = 4 * hf + hh
                        o = bank4(step, gi)[:, hh]
                        if kind == "F":
                            ins = nc.tensor.matmul(o, ar[:, h // 2, 0, tok], bhz[:, h, tok], start=True, stop=True)
                        elif kind == "G":
                            ins = nc.tensor.matmul(o, lhs[:, h, tok], ar[:, h // 2, rhs, tok], start=True, stop=True)
                        elif kind == "T":
                            ins = nc.tensor.transpose(o, lhs[:, gi, hh], ident[:, :])
                        elif kind == "V":
                            ins = nc.tensor.matmul(ps[:, bank_of(step, gi), 64 * hh:64 * hh + 64], lhs[:, gi, hh],
                                                   vtok[:, tt, 64 * h:64 * h + 64], start=True, stop=True)
                        else:
                            ins = nc.tensor.matmul(o, lhs[:, gi, hh], rhs[:, gi, hh], start=True, stop=True)
                    c.mark(ins)

            pe.wait_ge(v["i"], STEP["i.done"])
            pe.wait_ge(g["r"], STEP["r.zero"])
            for ch in range(NC):
                r0, tt = CH * (ch % 2), ch // 2
                rows, toks = slice(r0, r0 + CH), slice(CH * ch, CH * ch + CH)
                if ch:
                    pe.wait_ge(v["s"], 5 * ch)
                    for i in range(4):
                        ins = nc.tensor.matmul(ps[rows, 0, P * i:P * i + P], ar[:, i, 0, toks], state[:, ch, i, :],
                                               start=True, stop=True)
                    ins.then_inc(t_as, 1)
                pe.wait_ge(v["s"], 5 * ch + 1)
                for h in range(8):
                    ins = nc.tensor.matmul(ps[rows, 1, 64 * h:64 * h + 64], iQ[:, 2 * tt + h // 4, h % 4, rows],
                                           rbuf[:, tt, 64 * h:64 * h + 64], start=True, stop=True)
                ins.then_inc(t_u, 1)
                if ch < NC - 1:
                    pe.wait_ge(a["s"], ch + 1)
                    for i in range(4):
                        cols = slice(P * i, P * i + P)
                        nc.tensor.matmul(ps[:, 2, cols], bend_t[rows, tt, cols], ubuf[rows, tt, cols], start=True, stop=False)
                        ins = nc.tensor.matmul(ps[:, 2, cols], kend_t[rows, tt, cols], vtok[rows, tt, cols],
                                               start=False, stop=True)
                    ins.then_inc(t_ds, 1)
            pe.wait_ge(a["s"], NC)
            for tt in range(TT):
                for i in range(4):
                    cols = slice(P * i, P * i + P)
                    for hf in range(2):
                        ch = 2 * tt + hf
                        nc.tensor.matmul(ps[CH * hf:CH * hf + CH, 4 + tt, cols], ar[:, i, 1, CH * ch:CH * ch + CH],
                                         state[:, ch, i, :], start=True, stop=False, skip_group_check=True)
                    for h in (2 * i, 2 * i + 1):
                        hc = slice(64 * h, 64 * h + 64)
                        nc.tensor.matmul(ps[:, 4 + tt, hc], grb[:, 2 * tt + h // 4, h % 4, :], ubuf[:, tt, hc],
                                         start=False, stop=False, skip_group_check=True)
                        ins = nc.tensor.matmul(ps[:, 4 + tt, hc], grk[:, 2 * tt + h // 4, h % 4, :], vtok[:, tt, hc],
                                               start=False, stop=True, skip_group_check=True)
                ins.then_inc(t_y, 1)

            c = Counter(pe, t["o"])
            pe.wait_ge(v["y"], STEP["y.done"])
            for k in range(KT):
                for tt in range(TT):
                    o = (k % 2) * 256 + tt * P
                    ins = nc.tensor.transpose(ps[:, k // 2, o:o + P], ytok[:, tt, k::8], ident[:, :])
                if k % 2:
                    c.mark(ins)
            pe.wait_ge(wout_in, 64)
            pe.wait_ge(a["o"], STEP["o.hT"])
            for j in range(4):
                for k in range(KT):
                    w = ring[:, k // 2, :].rearrange("p (t n) -> p t n", t=2)[:, k % 2, 512 * (j % 2):512 * (j % 2) + 512]
                    ins = nc.tensor.matmul(ps[:, 4 + j, :], hT[:, k, P * (j // 2):P * (j // 2) + P], w,
                                           start=k == 0, stop=k == KT - 1)
                ins.then_inc(t_out, 1)
            t_norm(pe, "q")
            c = Counter(pe, t["e"])
            pe.wait_ge(rt_in, 64)
            pe.wait_ge(a["q"], STEP["q.a"])
            pe.wait_ge(v["q"], STEP["q.v"])
            for tt in range(TT):
                for k in range(KT):
                    ins = nc.tensor.matmul(ps[:, 7, 64 * tt:64 * tt + 36], hT[:, k, P * tt:P * tt + P], w_rt[:, k, :],
                                           start=k == 0, stop=k == KT - 1)
            c.mark(ins)
            c.at("e.rt")
            t_zero(pe)
            pe.wait_ge(v_lo, 2)

            def gate_up(m, e, tt, first=False):
                s0 = 3 * (e % 2)
                x2 = 2 * (E_BODY * m + e)
                if tt == 0:
                    pe.wait_ge(g_gate, E_BODY * m + e + 1)
                    pe.wait_ge(v_gate_up, E_BODY * m + e + 1)
                if not first:
                    pe.wait_ge(v_eact, x2 + tt - 1)
                o = ps[:, 4 + tt, :].rearrange("p (i n) -> p i n", i=2)
                tok = slice(P * tt, P * tt + P)
                for k in range(KT):
                    cols = slice(FE * k, FE * k + FE)
                    ins = mm3(o, hT_hi[:, k, tok], hT_lo[:, k, tok], gate_up_hi[e % 2][:, :, cols],
                              ring_lo[:, s0:s0 + 2, cols], start=k == 0, stop=k == KT - 1)
                ins.then_inc(t_gu, 1)

            def turn(m, e, tt, first=False):
                x4 = 4 * (E_BODY * m + e)
                pe.wait_ge(v_eact, 2 * (E_BODY * m + e) + tt + 1)
                if not first:
                    pe.wait_ge(v_eact_t, x4 + 2 * tt)
                for f in range(2):
                    ins = nc.tensor.transpose(ps[:, 6, FE * tt + P * f:FE * tt + P * f + P], eact[:, tt, f::2], ident[:, :])
                ins.then_inc(t_tr, 1)

            def down(m, e, tt):
                s_ = 3 * (e % 2) + 2
                if tt == 0:
                    pe.wait_ge(v_dn, E_BODY * m + e + 1)
                pe.wait_ge(v_eact_t, 4 * (E_BODY * m + e) + 2 * tt + 2)
                for f in range(2):
                    for h in range(2):
                        cols = slice(D * f + 512 * h, D * f + 512 * h + 512)
                        ins = mm3(ps[:, 2 * tt + h, :], eact_hi[:, tt, f, :], eact_lo[:, tt, f, :], moe_hi[s_][:, cols],
                                  ring_lo[:, s_, cols])
                ins.then_inc(t_dn, 1)

            def gate_row(m, h):
                pe.wait_ge(v_mod, 3 * m + 1 + h + CREDIT)
                nc.tensor.matmul(ps[:, 7, :], ones[:, :], macc[:, 2, 512 * h:512 * h + 512], start=True, stop=True
                                 ).then_inc(t_mod, 1)

            def expert(m, j):
                gate_up(m, j, 0)
                if j == 7:
                    pe.wait_ge(v_ada2, 24 * m + 24 + CREDIT)
                    pe.wait_ge(v_mod, 3 * m + CREDIT)
                    for vec in range(2):
                        t_columns(macc[:, vec, :], ps[:, 7, 8 * vec:8 * vec + 8])
                        for k in range(KT):
                            ins = nc.tensor.matmul(ps[:, 7, 16 + 8 * vec + k:17 + 8 * vec + k],
                                                   macc[:, vec, P * k:P * k + P], ones[:, 0:1], start=True, stop=True)
                    ins.then_inc(t_mod, 1)
                turn(m, j - 1, 1)
                down(m, j - 1, 0)
                gate_up(m, j, 1)
                turn(m, j, 0)
                if j == 7:
                    gate_row(m, 0)
                down(m, j - 1, 1)
                if j == 7:
                    gate_row(m, 1)

            gate_up(0, 0, 0, first=True)
            gate_up(0, 0, 1, first=True)
            turn(0, 0, 0, first=True)
            with pe.Fori(0, LAST_PASS) as m:
                for j in range(1, E_BODY + 1):
                    expert(m, j)
            for j in range(1, E_BODY):
                expert(LAST_PASS, j)
            turn(LAST_PASS, E_BODY - 1, 1)
            down(LAST_PASS, E_BODY - 1, 0)
            down(LAST_PASS, E_BODY - 1, 1)
            pe.wait_ge(v["f"], STEP["f.mod"])
            t_norm(pe, "bn")
            pe.wait_ge(v["bn"], STEP["bn.v"])
            pe.wait_ge(a["bn"], STEP["bn.a"])
            pe.wait_ge(v_mod, 12 + CREDIT)
            for i in range(9):
                pe.wait_ge(ring2[i % RING], 16 * (i // RING + 1))
                if i >= 4:
                    pe.wait_ge(a["bp"], i - 3)
                if i >= 8:
                    pe.wait_ge(v["bp"], i - 7)
                w = ring[:, i % RING, :].rearrange("p (t n) -> p t n", t=8)
                for j in range(2):
                    for k in range(KT):
                        o = ps[:, 4 + i % 4, 256 * j:256 * j + 256]
                        if i in (0, 1, 6, 7) or (i, j) == (8, 0):
                            ins = nc.tensor.matmul(o, w[:, k, P * j:P * j + P], hT[:, k, :], start=k == 0, stop=k == KT - 1)
                        elif i < 8:
                            ins = nc.tensor.matmul(o, hT[:, k, P * j:P * j + P], w[:, k, :], start=k == 0, stop=k == KT - 1)
                if i == 8:
                    for tt in range(TT):
                        for k in range(KT):
                            ins = nc.tensor.matmul(ps[:, 4, 256 + P * tt:256 + P * tt + P], hT[:, k, P * tt:P * tt + P],
                                                   w[:, k, P:2 * P], start=k == 0, stop=k == KT - 1)
                ins.then_inc(t_bin, 1)
            c = Counter(pe, t["bg"])
            for k in range(KT):
                ins = nc.tensor.matmul(ps[0:16, 0, 0:256], w_glr[:, k, :], hT[:, k, :], start=k == 0, stop=k == KT - 1)
            c.mark(ins)
            c.at("bg.lr")
            pe.wait_ge(a["bg"], STEP["bg.glr"])
            for i in range(2):
                ins = nc.tensor.matmul(ps[:, 1, 256 * i:256 * i + 256], w_gg[:, P * i:P * i + P], glr_t, start=True, stop=True)
            c.mark(ins)
            c.at("bg.z")
            pe.wait_ge(a["bg"], STEP["bg.pad"])
            for tt in range(TT):
                tok = slice(P * tt, P * tt + P)
                for h in range(GLA_H):
                    ins = nc.tensor.matmul(ps[:, 2 + tt, P * h:P * h + P], ktz[:, h, tok], qg[:, h // 2, tok], start=True, stop=True)
                c.mark(ins)
                if tt == 0:
                    c.at("bg.at0")
            pe.wait_ge(v["bg"], STEP["bg.kend"])
            for tt in range(TT):
                for i in range(2):
                    ins = nc.tensor.transpose(ps[:, 0, 256 * tt + P * i:256 * tt + P * i + P], kend2[:, i, P * tt:P * tt + P], ident[:, :])
            c.mark(ins)
            c.at("bg.tr")
            pe.wait_ge(a["bg"], STEP["bg.ket"])
            pe.wait_ge(a["bp"], STEP["bp.a"])
            for ch in range(NC - 1):
                rows, tt = slice(CH * (ch % 2), CH * (ch % 2) + CH), ch // 2
                for i in range(2):
                    ins = nc.tensor.matmul(ps[:, 4 + ch, 256 * i:256 * i + 256], ket[rows, tt, P * i:P * i + P],
                                           vg[rows, tt, 256 * i:256 * i + 256], start=True, stop=True)
            c.mark(ins)
            c.at("bg.ds")
            pe.wait_ge(v["bg"], STEP["bg.state"])
            for tt in range(TT):
                for i in range(2):
                    for hf in range(2):
                        ch = 2 * tt + hf
                        nc.tensor.matmul(ps[CH * hf:CH * hf + CH, tt, 256 * i:256 * i + 256], qg[:, i, CH * ch:CH * ch + CH],
                                         sg_state[:, ch, i, :], start=True, stop=False, skip_group_check=True)
                    for h in (2 * i, 2 * i + 1):
                        ins = nc.tensor.matmul(ps[:, tt, P * h:P * h + P], at[:, tt, h, :], vg[:, tt, P * h:P * h + P],
                                               start=False, stop=True, skip_group_check=True)
            c.mark(ins)
            c.at("bg.o")
            c = Counter(pe, t["bs"])
            pe.wait_ge(v["bg"], STEP["bg.y"])
            for j in range(6):
                hs = range(4 * j, 4 * j + 4) if j < 2 else range(2 * (j - 2), 2 * (j - 2) + 2)
                n = P if j < 2 else 2 * P
                for i, h in enumerate(hs):
                    q = slice(0, P) if j < 2 else slice(P, 2 * P)
                    ins = nc.tensor.matmul(ps[:, j, n * i:n * i + n], sq_t[:, h // 2, q], kz[:, h // 4, h % 2, 0:n],
                                           start=True, stop=True)
                c.mark(ins)
                if j == 0:
                    c.at("bs.s0")
            pe.wait_ge(a["bs"], STEP["bs.exp"])
            for j in range(6):
                for i in range(4):
                    n = 4 * j + i
                    h, o = (n, 0) if n < 8 else ((n - 8) // 2, P + P * (n % 2))
                    ins = nc.tensor.transpose(ps[:, j, P * i:P * i + P], sc[:, h, o:o + P], ident[:, :])
                c.mark(ins)
                if j == 0:
                    c.at("bs.pt0")
            pe.wait_ge(a["bs"], STEP["bs.pt"])
            for h in range(SWA_H):
                kv = slice(64 * (h // 4), 64 * (h // 4) + 64)
                nc.tensor.matmul(ps[:, 6, 64 * h:64 * h + 64], p_t[:, h, :], svt[:, 0, kv], start=True, stop=True)
                for r in range(2):
                    ins = nc.tensor.matmul(ps[:, 7, 64 * h:64 * h + 64], p_t[:, 8 + 2 * h + r, :], svt[:, r, kv],
                                           start=r == 0, stop=r == 1)
            c.mark(ins)
            c.at("bs.o")
            c = Counter(pe, t["bo"])
            pe.wait_ge(v["bs"], STEP["bs.y"])
            for k in range(KT):
                for tt in range(TT):
                    o = (k % 2) * 256 + tt * P
                    ins = nc.tensor.transpose(ps[:, k // 2, o:o + P], y2[:, tt, k::8], ident[:, :])
                if k % 2:
                    c.mark(ins)
            pe.wait_ge(a["bo"], STEP["bo.hT"])
            for q in range(4):
                pe.wait_ge(ring2[(9 + q) % RING], 32)
            for j in range(4):
                for k in range(KT):
                    w = ring[:, (9 + k // 2) % RING, D * (k % 2) + 512 * (j % 2):D * (k % 2) + 512 * (j % 2) + 512]
                    ins = nc.tensor.matmul(ps[:, 4 + j, :], hT[:, k, P * (j // 2):P * (j // 2) + P], w,
                                           start=k == 0, stop=k == KT - 1)
                ins.then_inc(t_bout, 1)
            t_norm(pe, "l0")
            pe.wait_ge(a["l0"], STEP["l0.a"])
            pe.wait_ge(v["l0"], STEP["l0.v"])
            t_zero(pe)
            pe.wait_ge(v_lo, 4)
            t_mlp_loop(pe, 0)
            t_norm(pe, "pn", tiles=True)
            c = Counter(pe, t["pp"])
            pe.wait_ge(v["pp"], STEP["pp.h"])
            pe.wait_ge(pool_in, 32)
            for j in range(4):
                for i in range(2):
                    gi = 2 * (j % 2) + i
                    for r in range(2):
                        ins = nc.tensor.matmul(ps[:, 4 + j, 256 * i:256 * i + 256], hT[:, 2 * gi + r, P * (j // 2):P * (j // 2) + P],
                                               poolw[:, gi, r, :], start=r == 0, stop=r == 1)
            c.mark(ins)
            c.at("pp.mm")
            t_norm(pe, "l1")
            pe.wait_ge(a["l1"], STEP["l1.a"])
            pe.wait_ge(v["l1"], STEP["l1.v"])
            t_zero(pe)
            pe.wait_ge(v_lo, 6)
            t_mlp_loop(pe, 1)


_INS = [
    "x", "c", "ada_w", "ada_b", "mix_norm_w", "w_in", "rwkv_mu", "rwkv_w0", "rwkv_w_up", "rwkv_a0",
    "rwkv_a_up", "rwkv_g_up", "rwkv_k_k", "rwkv_k_a", "rwkv_r_k", "rwkv_gn_w", "rwkv_gn_b", "mlstm_conv_w",
    "mlstm_conv_b", "mlstm_i_b", "mlstm_f_b", "mlstm_hn_w", "w_out", "ffn_norm_w", "moe_w_group",
    "moe_b_group", "moe_w_router", "moe_b_router", "moe_w_gate", "moe_w_up", "moe_w_down", "final_norm_w",
    "c_2", "norm_w_2", "ada_w_2", "ada_b_2", "attn_w_in_2", "gla_w_gate_2", "gla_b_gate_2", "gla_norm_w_2",
    "attn_sinks_2", "attn_w_out_2", "rel_bias_2", "pool_w_2", "pool_scale_2", "mlp_w1_2", "mlp_w2_2",
    "final_norm_w_2",
]


def distance_buckets():
    import numpy as np

    half = N_BUCKETS // 2
    dist = 2 * WINDOW - 1 - np.arange(3 * P)
    far = half + (np.log(np.maximum(dist, 1) / half) / np.log(MAX_DIST / half) * half).astype(np.int32)
    bucket = np.where(dist < half, dist, np.minimum(far, N_BUCKETS - 1))
    row = np.where((dist >= 0) & (dist < WINDOW), bucket, N_BUCKETS)
    return (np.arange(N_BUCKETS + 1)[:, None] == row[None, :]).astype(np.float32)


def kernel(**inputs):
    import numpy as _np
    import concourse.bacc as _bacc
    from concourse import mybir as _mybir
    from concourse.bass_utils import run_bass_kernel_spmd as _run

    nc = _bacc.Bacc("TRN2", target_bir_lowering=False, num_devices=1)
    arrays, A = {}, {}
    for name in _INS + ["hots"]:
        a = distance_buckets() if name == "hots" else _np.ascontiguousarray(inputs[name])
        arrays[f"in_{name}_dram"] = a
        A[name] = nc.dram_tensor(f"in_{name}_dram", a.shape, _mybir.dt.from_np(a.dtype), kind="ExternalInput").ap()
    out = nc.dram_tensor("out_0_dram", (1, SEQ, D), F32, kind="ExternalOutput").ap()
    program(nc, A, out)
    r = _run(nc, [arrays], core_ids=[0])
    return r.results[0]["out_0_dram"]
```

```python
from contextlib import ExitStack

import concourse.bass as bass
from concourse import mybir

F32 = mybir.dt.float32
BF16 = mybir.dt.bfloat16
F32R = mybir.dt.float32r
I32 = mybir.dt.int32
ALU = mybir.AluOpType
ACT = mybir.ActivationFunctionType
AX_X = mybir.AxisListType.X

P = 128
D = 1024
SEQ = 256
TT = SEQ // P
KT = D // P
CH = 64
NC = SEQ // CH
EPS = 1e-6
GN_EPS = 64e-5
DECAY = 0.6065306597126334
RW_TILES = 14
IN_SLOTS = 13
NE = 32
FE = 256
SLOT = 2048
RING = 8
CAP = 15.0
NG, EG = 4, 8
E_BODY = 8
LAST_PASS = NE // E_BODY - 1
FF_SLOTS = 4
GLA_H, GLA_DV = 4, 128
SWA_H = 8
N_BUCKETS, MAX_DIST, WINDOW = 32, 128, 128
BIG = -1e30

STEP = {
    "c.ident": 8, "c.zeros": 17, "n.rstd0": 1, "n.rstd1": 2, "c.masks": 40, "m.rs": 1, "r.zero": 5, "r.rkp":
    7, "r.kh": 8, "r.kend": 9, "y.rs0": 1, "y.rs1": 2, "y.free": 4, "q.rstd0": 1, "q.rstd1": 2, "f.rstd0": 1,
    "bn.rstd0": 1, "f.rstd1": 2, "bn.rstd1": 2, "bp.zero": 3, "bp.len": 9, "bg.rs": 1, "bg.lo": 4, "l0.rstd0":
    1, "l0.rstd1": 2, "pn.rstd0": 1, "pn.rstd1": 2, "pp.zero": 3, "pp.g": 9, "l1.rstd0": 1, "l1.rstd1": 2,
    "z.rstd0": 1, "z.rstd1": 2, "c.sig": 1, "n.sq0": 1, "n.sq1": 2, "n.a": 6, "w.col7": 1, "w.col8": 2,
    "m.lf": 4, "w.col9": 3, "m.sig": 5, "w.col10": 4, "w.col11": 5, "m.exp": 7, "w.col12": 6, "w.col0": 7,
    "w.col1": 8, "w.col2": 9, "w.col3": 10, "w.col4": 11, "w.col5": 12, "w.col6": 13, "r.u": 2, "r.sqrt": 3,
    "r.sig": 11, "r.gtok": 12, "r.exp": 15, "r.pad": 19, "r.tok": 21, "i.a": 40, "o.hT0": 4, "o.hT1": 8,
    "q.sq0": 1, "q.sq1": 2, "q.a": 6, "e.expg": 1, "e.expd": 2, "f.sq0": 1, "bn.sq0": 1, "f.sq1": 2, "bn.sq1":
    2, "bn.a": 6, "bg.glr": 1, "bg.zb": 3, "bg.ln": 6, "bg.exp": 8, "bg.pad": 10, "bg.ket": 11, "bp.a": 13,
    "bs.hi0": 1, "bs.hi1": 2, "bs.exp0": 3, "bs.hi2": 6, "bs.exp1": 8, "bs.pt": 12, "bs.hi3": 13, "bo.hT": 4,
    "l0.sq0": 1, "l0.sq1": 2, "l0.a": 6, "pn.sq0": 1, "pn.sq1": 2, "pn.a": 6, "l1.sq0": 1, "l1.sq1": 2,
    "l1.a": 6, "z.sq0": 1, "z.sq1": 2, "n.ss0": 1, "n.ss1": 2, "n.xn0": 3, "n.xn1": 4, "n.mod": 7, "n.vh": 9,
    "n.v": 11, "w.prmc": 1, "w.gb": 2, "w.pre": 2, "m.conv": 16, "m.rows": 23, "m.z": 32, "m.pt": 38, "m.ss":
    48, "m.s": 50, "w.shift": 23, "r.sq": 2, "w.mod": 27, "r.kmod": 6, "r.scan": 10, "r.pend": 13, "r.bh": 14,
    "r.bend": 15, "r.q": 18, "r.bon": 19, "i.done": 56, "y.sub0": 3, "y.var0": 6, "y.done0": 9, "y.sub1": 12,
    "y.var1": 15, "y.done1": 18, "o.gate": 1, "o.x0": 5, "q.ss0": 1, "q.xn0": 2, "o.x1": 9, "q.ss1": 3,
    "q.xn1": 4, "q.mod": 4, "q.vh": 6, "q.v": 8, "e.g": 3, "e.d": 21, "e.cw": 30, "f.mod": 6, "f.x0": 10,
    "f.ss0": 11, "f.n0": 12, "f.x1": 16, "bn.ss0": 1, "f.ss1": 17, "bn.xn0": 2, "f.n1": 18, "bn.ss1": 3,
    "bn.xn1": 4, "bn.mod": 4, "bn.vh": 6, "bn.v": 8, "bg.scan": 4, "bg.kt": 6, "bg.kend": 8, "bg.at": 10,
    "bg.state": 22, "bg.ss": 26, "bg.y": 31, "bs.sub0": 6, "bs.sub1": 14, "bs.den": 18, "bs.y": 21, "bo.lo":
    4, "bo.len": 5, "bo.x0": 9, "l0.ss0": 1, "l0.xn0": 2, "bo.x1": 13, "l0.ss1": 3, "l0.xn1": 4, "l0.mod": 4,
    "l0.vh": 6, "l0.v": 8, "l0.x0": 12, "pn.ss0": 1, "pn.xn0": 2, "l0.x1": 16, "pn.ss1": 3, "pn.xn1": 4,
    "pn.mod": 6, "pn.vh": 8, "pn.v": 10, "pp.h": 9, "pp.x0": 14, "l1.ss0": 1, "l1.xn0": 2, "pp.x1": 18,
    "l1.ss1": 3, "l1.xn1": 4, "l1.mod": 4, "l1.vh": 6, "l1.v": 8, "l1.x0": 12, "z.ss0": 1, "z.out0": 2,
    "l1.x1": 16, "z.ss1": 3, "z.out1": 4, "n.t": 4, "w.prm": 1, "w.if": 2, "m.bc": 1, "m.sc0": 2, "m.sc1": 3,
    "m.num": 4, "r.n2": 1, "r.wa": 2, "r.vt": 3, "r.bonus": 4, "r.bt": 5, "r.kt": 6, "o.t": 8, "q.t": 4,
    "e.rt": 1, "bn.t": 4, "bg.lr": 1, "bg.z": 2, "bg.at0": 3, "bg.tr": 5, "bg.ds": 6, "bg.o": 7, "bs.s0": 1,
    "bs.pt0": 7, "bs.o": 13, "l0.t": 4, "pn.t": 4, "pp.mm": 4, "l1.t": 4,
}


class Counter:

    def __init__(self, eng, sem, n=0):
        self.eng, self.sem, self.n = eng, sem, n

    def link(self, ins):
        self.n += 1
        ins.then_inc(self.sem, 1)
        self.eng.wait_ge(self.sem, self.n)

    def mark(self, ins):
        self.n += 1
        ins.then_inc(self.sem, 1)

    def at(self, name):
        assert STEP[name] == self.n, (name, self.n)


def program(nc, A, out):
    ctx = ExitStack()
    with ctx:
        def sb(name, shape, dt=F32):
            return ctx.enter_context(nc.sbuf_tensor(name, shape, dt))

        def sem(name):
            return ctx.enter_context(nc.semaphore(name))

        ps = ctx.enter_context(nc.psum_tensor("ps", [P, 8, 512], F32))

        x_sb = sb("x_sb", [P, TT, D])

        def sb_twice(name, shape):
            whole = sb(name, shape)
            end = nc.sbuf_base
            words = 1
            for n in shape[1:]:
                words *= n
            return whole, nc.alloc_sbuf_tensor_at(name + "_parts", shape, F32R, offset=end - 4 * words)

        hT, hT_lo = sb_twice("hT", [P, KT, SEQ])
        ring, ring_lo = sb_twice("ring", [P, RING, SLOT])
        macc, macc_r = sb_twice("macc", [P, 3, D])
        gate1, gate1_r = sb_twice("gate1", [P, 2, D])
        KB = 256
        arena, arena_r = sb_twice("arena", [P, 91 * KB])

        def area(kb, words):
            return arena[:, int(kb * KB):int(kb * KB) + words]

        def area_r(kb, words):
            return arena_r[:, int(kb * KB):int(kb * KB) + words]

        u = area(0, 14 * 256).rearrange("p (i t) -> p i t", t=SEQ)
        grb = area(0, 16 * 128).rearrange("p (g h s) -> p g h s", g=4, h=4)
        lakv = area(8, 1024).rearrange("p (a n) -> p a n", a=TT)
        ar = area(14, 2048).rearrange("p (i k t) -> p i k t", i=4, k=2)
        bhz = area(22, 2048).rearrange("p (h t) -> p h t", h=8)
        khz = area(30, 2048).rearrange("p (h t) -> p h t", h=8)
        vtok = area(38, 1024).rearrange("p (a n) -> p a n", a=TT)
        bend_t = area(42, 1024).rearrange("p (a n) -> p a n", a=TT)
        kend_t = area(46, 1024).rearrange("p (a n) -> p a n", a=TT)
        convraw = area(42, 4 * 259).rearrange("p (i t) -> p i t", i=4)
        rbuf = area(50, 1024).rearrange("p (a n) -> p a n", a=TT)
        ubuf = area(54, 1024).rearrange("p (a n) -> p a n", a=TT)
        xn = area(50, 2048).rearrange("p (a n) -> p a n", a=TT)
        state = area(58, 2048).rearrange("p (c i v) -> p c i v", c=4, i=4)
        raw = area(58, 4 * 257).rearrange("p (b i t) -> p b i t", b=2, i=2)
        gtok = area(66, 1024).rearrange("p (a n) -> p a n", a=TT)
        ytok = area(70, 2048).rearrange("p (a n) -> p a n", a=TT)
        qk = area(78, 1024).rearrange("p (i t) -> p i t", i=4)
        vm = area(82, 1024).rearrange("p (a n) -> p a n", a=TT)
        om = area(87, 1024).rearrange("p (a n) -> p a n", a=TT)
        grk = hT[:, :, :].rearrange("p k t -> p (k t)").rearrange("p (g h s) -> p g h s", g=4, h=4)
        dtmp = sb("dtmp", [P, 512])

        ident = sb("ident", [P, P])
        ones = sb("ones", [P, P])
        headblk = sb("headblk", [P, P])
        headsel = sb("headsel", [P, 2])
        masks = sb("masks", [P, 7, P])
        same16, same32, same64 = masks[:, 0, :], masks[:, 1, :], masks[:, 2, :]
        m_n16t, m_n16 = masks[:, 3, :], masks[:, 0, :]
        m_32, m_64 = masks[:, 1, :], masks[:, 4, :]
        m_ak, m_rb, m_causal = masks[:, 5, :], masks[:, 2, :], masks[:, 6, :]
        reset = sb("reset", [P, SEQ])
        prm = sb("prm", [P, P])
        prm_c = sb("prm_c", [P, 80])
        mu_c, w0_c, a0_c, kk_c = prm_c[:, 0:14], prm_c[:, 14:18], prm_c[:, 18:22], prm_c[:, 22:26]
        ka_c, rk_c, cb_c, cw_c = prm_c[:, 26:30], prm_c[:, 30:34], prm_c[:, 34:38], prm_c[:, 38:54]
        ccol = sb("ccol", [P, 16])
        csig = sb("csig", [P, 16])
        adab_c = sb("adab_c", [P, 6, 8])
        norm_c = sb("norm_c", [P, 2, 8])
        mod_c = sb("mod_c", [P, 4, 8])
        small = sb("small", [P, 64])
        nhalf = sb("nhalf", [P, 16])
        wup = sb("wup", [P, 2, 512])
        gup = area(47, 512)
        w_if = sb("w_if", [P, 8, 36])
        rowp = macc[:, 0:2, :].rearrange("p v n -> p (v n)")[:, 0:1536].rearrange("p (i n) -> p i n", i=3)
        gate_b = sb("gate_b", [36, 2])
        bon = sb("bon", [P, TT, 8])
        mrow = arena[0:64, 14 * KB:20 * KB].rearrange("p (i t) -> p i t", i=6)
        sel4 = arena[0:4, 20 * KB:22 * KB].rearrange("p (h n) -> p h n", h=4)

        v = {s: sem("v_" + s) for s in "c n w m r i s p y o q e f bn bp bg bs bo l0 pn pp l1 z".split()}
        a = {s: sem("a_" + s) for s in "c n w m r i s o q e f bn bp bg bs bo l0 pn l1 z".split()}
        g = {s: sem("g_" + s) for s in "c n m r y q f bn bp bg l0 pn pp l1 z".split()}
        t = {s: sem("t_" + s) for s in "n w m r i o q e bn bg bs bo l0 pn pp l1".split()}
        ring_in = [sem(f"ring_in{i}") for i in range(RING)]
        x_in, c_in, prm_in, col_in, par_in, gate_in, row_in = (
            sem(n) for n in ("x_in", "c_in", "prm_in", "col_in", "par_in", "gate_in", "row_in"))
        v_ada = sem("v_ada")
        t_win = sem("t_win")
        s_out = sem("s_out")

        wout_in = sem("wout_in")
        t_ada, t_as, t_u, t_ds, t_y, t_out = (sem(n) for n in ("t_ada", "t_as", "t_u", "t_ds", "t_y", "t_out"))

        tmp_slot = (6, 7, 0, 5, 1, 4, 3)

        def tmp(i):
            s_ = tmp_slot[i // 2]
            return ring[:, s_, 1024 * (i % 2):1024 * (i % 2) + 1024].rearrange("p (i t) -> p i t", i=4)

        lw, cum, av, pcum, pinv, kn, kx, sq, kmod, bh, kh, bend, kend, rkp = (tmp(i) for i in range(14))
        ysq = ring[:, 6, 0:1024].rearrange("p (a n) -> p a n", a=TT)
        yterm = ring[:, 7, 0:1024].rearrange("p (a n) -> p a n", a=TT)
        mz = area(22, 4 * 384).rearrange("p (h n) -> p h n", h=4)
        mcol = area(28, 128).rearrange("p (a n) -> p a n", a=TT)
        mem = area(28.5, 8).rearrange("p (a n) -> p a n", a=TT)
        msq = area(30, 1024).rearrange("p (a n) -> p a n", a=TT)
        qsig = area(50, 1024).rearrange("p (i t) -> p i t", i=4)
        pend = sb("pend", [P, 4, NC])
        halves = small[:, 16:48].rearrange("p (i t) -> p i t", i=4)

        w_rt = area(0, KT * 36).rearrange("p (t n) -> p t n", t=KT)
        b_rt = area(2, 36)
        lg = area(3, 2 * 36).rearrange("p (a n) -> p a n", a=TT)
        rt = area(4, 16 * 64).rearrange("p (i a n) -> p i a n", i=16, a=TT)
        cw = area(8, TT * NE).rearrange("p (a e) -> p a e", a=TT)
        rev = area(9, 8)
        revi = area(9.5, 8).bitcast(mybir.dt.int32)
        gact = area(12, TT * FE).rearrange("p (a n) -> p a n", a=TT)
        eact = area(14, TT * FE).rearrange("p (a n) -> p a n", a=TT)
        eact_hi, eact_lo = (area_r(kb, TT * FE).rearrange("p (a f n) -> p a f n", a=TT, f=2) for kb in (16, 18))
        moe_hi = [area_r(kb, SLOT) for kb in (40, 64, 0, 48, 56, 72)]
        gate_up_hi = [area_r(kb, n).rearrange("p (i n) -> p i n", i=2)[:, :, 0:SLOT] for kb, n in ((40, 48 * KB), (48, 16 * KB))]
        hT_hi = area_r(80, KT * SEQ).rearrange("p (k t) -> p k t", k=KT)
        gate2 = area(20, 4 * D).rearrange("p (m n) -> p m n", m=4)
        mod2 = area(36, 4 * 32).rearrange("p (m n) -> p m n", m=4)
        adab2_c = area(37, 64).rearrange("p (m n) -> p m n", m=8)
        norm2_c = area(37.5, 32).rearrange("p (m n) -> p m n", m=4)
        sink_b = area(37.75, 8)
        w_glr = area(38.5, KT * 16).rearrange("p (t n) -> p t n", t=KT)
        w_gg = arena[0:16, 39 * KB:40 * KB]
        vg = area(0, 1024).rearrange("p (a n) -> p a n", a=TT)
        ggs = area(4, 1024).rearrange("p (a n) -> p a n", a=TT)
        sq_t = area(8, 1024).rearrange("p (i t) -> p i t", i=4)
        kz = area(12, 1024).rearrange("p (k h t) -> p k h t", k=2, h=2)
        svt = area(16, 256).rearrange("p (a n) -> p a n", a=TT)
        glr_t = arena[0:16, 17 * KB:18 * KB]
        swm = area(18, 64)
        f2 = lambda kb: area(kb, 512).rearrange("p (i t) -> p i t", i=2)
        zb, az, nb2, eb, enb, kend2 = (f2(kb) for kb in (40, 42, 44, 46, 48, 50))
        ket = area(52, 512).rearrange("p (a n) -> p a n", a=TT)
        at = area(54, 1024).rearrange("p (a h t) -> p a h t", a=TT, h=4)
        ktz = area(58, 1024).rearrange("p (h t) -> p h t", h=4)
        sg_state = area(64, 2048).rearrange("p (c i v) -> p c i v", c=4, i=2)
        qg, kg = f2(72), f2(74)
        gdec = area(76, 8).rearrange("p (i c) -> p i c", i=2)
        ggn = area(38, GLA_DV)
        gsq = area(78, 1024).rearrange("p (a n) -> p a n", a=TT)
        sc = area(40, 8 * 384).rearrange("p (h k) -> p h k", h=8)
        p_t = area(52, 24 * P).rearrange("p (j q) -> p j q", j=24)
        bias8 = area(83, 8 * 256).rearrange("p (h k) -> p h k", h=8)
        hots = arena[0:64, 30 * KB:30 * KB + 384]
        rel_sb = arena[0:64, 32 * KB:32 * KB + 8]
        ebc = arena[0:SWA_H, 34 * KB:34 * KB + 384]
        y2 = macc[:, 0:2, :]
        dlen = area(56, 512)
        PAD = 16
        hp = area(0, 8 * 272).rearrange("p (k t) -> p k t", k=KT)
        hp_tok = hp[:, :, PAD:]
        pa = area(9, 8 * 272).rearrange("p (k t) -> p k t", k=KT)
        pb_ = area(40, 6 * 272).rearrange("p (k t) -> p k t", k=6)
        pinvc = wup[:, :, :].rearrange("p j n -> p (j n)").rearrange("p (g t) -> p g t", g=4)
        pcnt = dlen[:, 0:256]
        pcnti = dlen[:, 256:512].bitcast(mybir.dt.int32)
        poolw = area(64, 2048).rearrange("p (g r n) -> p g r n", g=4, r=2)
        psc_b = area(72, 1024)
        frl = area(16, 1024).rearrange("p (a n) -> p a n", a=TT)
        fact, fact_hi, fact_lo = macc[:, 0, :], macc_r[:, 1, :], macc_r[:, 2, :]
        fact = fact.rearrange("p (a n) -> p a n", a=TT)
        fact_hi, fact_lo = (x.rearrange("p (a f n) -> p a f n", a=TT, f=4) for x in (fact_hi, fact_lo))
        mlp_hi = [area_r(kb, SLOT) for kb in (0, 8, 40, 48, 56, 64, 72, 80)]
        gT_hi = gate1_r[:, :, :].rearrange("p v n -> p (v n)").rearrange("p (k t) -> p k t", k=KT)
        nrm_b = wup[:, :, :].rearrange("p j n -> p (j n)")
        zeros_b = sb("zeros_b", [P, P], BF16)[:, :]
        ring_zero = sb("ring_zero", [P, 512], BF16)[:, :]

        moe_in = [sem(f"moe_in{i}") for i in range(6)]
        ada2_in = [sem(f"ada2_in{i}") for i in range(2)]
        rt_in, par2_in, bias_out, bias_in, nrm_in, pool_in = (
            sem(n) for n in ("rt_in", "par2_in", "bias_out", "bias_in", "nrm_in", "pool_in"))
        t_gu, t_tr, t_dn, a_silu, v_eact, v_eact_t, a_gu, g_gate, v_gate_up, a_dn, v_dn, v_ada2, v_mod, v_cols, t_mod = (
            sem(n) for n in ("t_gu", "t_tr", "t_dn", "a_silu", "v_eact", "v_eact_t", "a_gu", "g_gate", "v_gate_up", "a_dn", "v_dn", "v_ada2",
                             "v_mod", "v_cols", "t_mod"))
        ring2 = [sem(f"ring2_{i}") for i in range(RING)]
        t_bin, t_bout, nrm2_in, hot_in = (sem(n) for n in ("t_bin", "t_bout", "nrm2_in", "hot_in"))
        mlp_in = ring2
        ring2_n = [16 * len(range(i, 13, RING)) for i in range(RING)]
        t_up, t_ft, t_fd, a_fact, v_fact_t, a_w1, g_w1, v_w1, a_w2, v_w2 = (
            sem(n) for n in ("t_up", "t_ft", "t_fd", "a_fact", "v_fact_t", "a_w1", "g_w1", "v_w1", "a_w2", "v_w2"))
        t_bias, a_bias, a_hi, v_lo, cols_out, cols_in, t_cols = (
            sem(n) for n in ("t_bias", "a_bias", "a_hi", "v_lo", "cols_out", "cols_in", "t_cols"))
        cols_d = nc.dram_tensor("pool_columns", (2, D), F32, kind="Internal").ap()
        scratch_d = nc.dram_tensor("bias_rows", (SWA_H, P * 384), F32, kind="Internal").ap()
        CREDIT = 4
        in2_cols = [0, 256, 512, 768, 1024, 1280, 1552, 1808, 2064]
        stream2 = [("in", c0) for c0 in in2_cols] + [("out", q) for q in range(4)]
        ones2 = arena[0:4, 86 * KB:87 * KB]

        def scratch(i):
            return ring[:, tmp_slot[i], :].rearrange("p (g h s) -> p g h s", g=4, h=4)

        iF, iA, iB, iC, iD, iQ = (scratch(i) for i in range(6))

        def chunk(x):
            return x.rearrange("p i (c s) -> p i c s", s=CH)

        def to_end():
            return pend[:, :, :].unsqueeze(3).to_broadcast([P, 4, NC, CH])

        def chunk2(x):
            return x.rearrange("p i (c s) -> p i c s", s=CH)

        def bank_of(step, gi):
            return (4 * step + gi) % 8

        def bank4(step, gi):
            return ps[:, bank_of(step, gi), :].rearrange("p (h s) -> p h s", h=4)

        INV_T = [
            ("F", None, None, None, None, None),
            ("G", bhz, 0, None, None, None),
            ("G", khz, 0, None, None, ("a", 0)),
            ("G", bhz, 1, None, None, ("v", 0)),
            ("G", khz, 1, None, None, ("v", 1)),
            ("V", iD, None, None, 1, ("v", 4)),
            ("M", iB, iA, None, 2, ("v", 5)),
            ("M", iA, iB, None, 2, ("v", 6)),
            ("M", iC, iQ, 1, 3, ("a", 1)),
            ("M", iD, iC, 2, None, ("a", 2)),
            ("M", iC, iD, None, None, ("v", 7)),
            ("M", iA, iQ, 3, 7, ("a", 3)),
            ("M", iB, iA, 4, None, ("a", 4)),
            ("M", iC, iQ, 5, 8, ("v", 8)),
            ("T", iQ, None, None, 9, ("a", 5)),
            ("M", iA, iQ, None, 10, ("v", 9)),
            ("M", iD, iB, 7, None, ("a", 6)),
            ("T", iQ, None, None, 11, ("a", 7)),
            ("M", iA, iQ, None, 12, ("v", 11)),
            ("M", iD, iB, 9, None, ("a", 8)),
        ]
        INV_A = [(i, s_, d_) for i, (s_, d_) in enumerate(
            [(0, iF), (6, iC), (7, iD), (9, iA), (10, iB), (12, iC), (14, iD), (15, iB), (17, iD), (18, iB)])]
        INV_V = [
            ("mask", 1, m_n16t, iB),
            ("mask", 2, m_ak, iD),
            ("maskF", None, m_n16, iA),
            ("ident", None, None, iQ),
            ("mask", 3, m_rb, grb),
            ("mask", 4, m_rb, grk),
            ("lakv", 5, None, None),
            ("add", 8, None, iQ),
            ("add", 11, None, iQ),
            ("add", 13, None, iQ),
            ("maskF", None, m_32, iA),
            ("add", 16, None, iQ),
            ("maskF", None, m_64, iA),
            ("add", 19, None, iQ),
        ]
        V_A16 = 2
        out_hi = [mlp_hi[i] for i in (5, 6, 0, 1)]
        ds_bank = (4, 5, 2)
        bs_bank = (2, 3, 4, 5, 7, 6)

        def bin_bank(i):
            return ps[:, 6 + i % 2, :]

        sc_bank = (4, 5, 2, 3)

        block = ctx.enter_context(nc.Block())

        win_order = [7, 8, 9, 10, 11, 12, 0, 1, 2, 3, 4, 5, 6]
        stream = [("ada", n) for n in range(8)]
        for i, n in enumerate(win_order):
            stream += [("win", n)] + [("ada", 8 + i)]
        stream += [("ada", n) for n in range(21, 24)]
        place = {key: i for i, key in enumerate(stream)}

        def loaded(eng, key):
            eng.wait_ge(ring_in[place[key] % RING], 16 * (place[key] // RING + 1))

        def slot(key):
            return ring[:, place[key] % RING, :]

        def g_norm(pool, st):
            c = Counter(pool, g[st])
            for tt in range(TT):
                g_rstd(pool, c, st, tt)

        def g_rstd(pool, c, st, tt):
            pool.wait_ge(v[st], STEP[f"{st}.ss{tt}"])
            c.link(nc.gpsimd.tensor_tensor(small[:, tt:tt + 1], small[:, tt:tt + 1], nhalf[:, 0:1], ALU.pow))
            c.at(f"{st}.rstd{tt}")

        def a_square(c, st, tt):
            c.link(nc.scalar.activation(xn[:, tt, :], x_sb[:, tt, :], ACT.Square, accum_out=small[:, tt:tt + 1]))
            c.at(f"{st}.sq{tt}")

        def a_norm(act, st, shift, scale, after=None, between=None, meanwhile=None, out=hT, hi=None):
            c = Counter(act, a[st])
            for tt in range(TT):
                if after:
                    act.wait_ge(v[after], STEP[f"{after}.x{tt}"])
                a_square(c, st, tt)
                if between and tt == 0:
                    between()
            a_norm_out(act, c, st, shift, scale, meanwhile, out, hi)

        def a_norm_out(act, c, st, shift, scale, meanwhile=None, out=hT, hi=None):
            if meanwhile:
                meanwhile()
            act.wait_ge(v[st], STEP[st + ".mod"])
            for k in (2, 3, 6, 7):
                act.wait_ge(t[st], k // 2 + 1)
                c.link(nc.scalar.activation(out[:, k, :], ps[:, k // 2, 256 * (k % 2):256 * (k % 2) + 256], ACT.Identity,
                                            bias=shift[:, k:k + 1], scale=scale[:, k:k + 1]))
                if hi is not None and k == 3:
                    a_hT_hi(act, st, hi, 0)
            c.at(st + ".a")
            if hi is not None:
                a_hT_hi(act, st, hi, 1)

        def v_mean(dve, c, st, tt):
            dve.wait_ge(a[st], STEP[f"{st}.sq{tt}"])
            c.link(nc.vector.tensor_scalar(small[:, tt:tt + 1], small[:, tt:tt + 1], 1.0 / D, EPS, ALU.mult, ALU.add))
            c.at(f"{st}.ss{tt}")

        def v_xn(dve, c, st, tt):
            dve.wait_ge(g[st], STEP[f"{st}.rstd{tt}"])
            c.link(nc.vector.tensor_scalar(xn[:, tt, :], x_sb[:, tt, :], small[:, tt:tt + 1], None, ALU.mult))
            c.at(f"{st}.xn{tt}")

        def v_residual(dve, c, st, gate, base, tt, ready):
            for j in (2 * tt, 2 * tt + 1):
                ready(j)
                xs = x_sb[:, tt, 512 * (j % 2):512 * (j % 2) + 512]
                c.link(nc.vector.tensor_tensor(dtmp[:, :], ps[:, base + j, :], gate[:, 512 * (j % 2):512 * (j % 2) + 512], ALU.mult))
                c.link(nc.vector.tensor_tensor(xs, xs, dtmp[:, :], ALU.add))
            c.at(f"{st}.x{tt}")

        def v_residual_norm(dve, c, st, gate, base, ready, nst, shift, scale, mod=None, out=hT):
            cn = Counter(dve, v[nst])
            for tt in range(TT):
                v_residual(dve, c, st, gate, base, tt, ready)
                v_mean(dve, cn, nst, tt)
                v_xn(dve, cn, nst, tt)
            v_norm_out(dve, cn, nst, shift, scale, mod, out)

        def v_norm(dve, st, shift, scale, mod=None, meanwhile=None):
            c = Counter(dve, v[st])
            for tt in range(TT):
                v_mean(dve, c, st, tt)
            if meanwhile:
                meanwhile()
            for tt in range(TT):
                v_xn(dve, c, st, tt)
            v_norm_out(dve, c, st, shift, scale, mod)

        def v_norm_out(dve, c, st, shift, scale, mod=None, out=hT):
            if mod:
                mod(c)
            c.at(st + ".mod")
            for k in (0, 1, 4, 5):
                dve.wait_ge(t[st], k // 2 + 1)
                c.link(nc.vector.tensor_scalar(out[:, k, :], ps[:, k // 2, 256 * (k % 2):256 * (k % 2) + 256],
                                               scale[:, k:k + 1], shift[:, k:k + 1], ALU.mult, ALU.add))
                if k == 1:
                    c.at(st + ".vh")
            c.at(st + ".v")

        def window_sum(c, eng, dst, src, k0, k1, w):
            rows = lambda buf: buf[:, k0 - (2 if buf is pb_ else 0):k1 - (2 if buf is pb_ else 0)]
            c.link(eng.tensor_tensor(rows(dst)[:, :, PAD:], rows(src)[:, :, PAD:], rows(src)[:, :, PAD - w:PAD + SEQ - w], ALU.add))

        def mean(c, eng, gi, buf):
            k = 2 * gi - (2 if buf is pb_ else 0)
            sums = buf[:, k:k + 2, PAD:]
            c.link(eng.tensor_tensor(sums, sums, pinvc[:, gi, :].unsqueeze(1).to_broadcast([P, 2, SEQ]), ALU.mult))
            return sums

        def less_input(c, eng, gi, sums):
            c.link(eng.tensor_tensor(hT[:, 2 * gi:2 * gi + 2, :], sums, hp[:, 2 * gi:2 * gi + 2, PAD:], ALU.subtract))

        def mean_less_input(c, eng, gi, buf):
            less_input(c, eng, gi, mean(c, eng, gi, buf))

        def mm3(o, x_hi, x_lo, w_hi, w_lo, start=False, stop=False):
            for i, (l, r) in enumerate(((x_hi, w_hi), (x_hi, w_lo), (x_lo, w_hi))):
                ins = nc.tensor.matmul(o, l, r, start=start and i == 0, stop=stop and i == 2, skip_group_check=True)
            return ins

        def trailing(eng, lo, x, hi):
            return eng.tensor_tensor(lo, x, hi.bitcast(F32), ALU.subtract)

        def t_norm(pe, st, tiles=False, after=None):
            c = Counter(pe, t[st])
            if after:
                pe.wait_ge(v[after], STEP[after + ".x1"])
            for tt in range(TT):
                pe.wait_ge(v[st], STEP[f"{st}.xn{tt}"])
                for k in range(KT):
                    o = (k % 2) * 256 + tt * P
                    src = xn[:, tt, P * k:P * k + P] if tiles else xn[:, tt, k::8]
                    ins = nc.tensor.transpose(ps[:, k // 2, o:o + P], src, ident[:, :])
                    if tt == 1 and k % 2:
                        c.mark(ins)
            c.at(st + ".t")

        def t_columns(acc, dst):
            for k in range(KT):
                ins = nc.tensor.matmul(dst[:, k:k + 1], acc[:, k::8], ones[:, 0:1], start=True, stop=True)
            return ins

        def gate_up_in(sp, m, e):
            for i, name in enumerate(("moe_w_gate", "moe_w_up")):
                s_ = 3 * (e % 2) + i
                sp.dma_start(ring[:, s_, :], A[name][0, bass.ds(m * E_BODY + e, 1)]
                             .rearrange("o (p t) n -> (o p) (t n)", t=8)).then_inc(moe_in[s_], 16)

        def down_in(eng, m, e):
            s_ = 3 * (e % 2) + 2
            eng.dma_start(ring[:, s_, :], A["moe_w_down"][0, bass.ds(m * E_BODY + e, 1)]
                          .rearrange("o (p t) n -> (o p) (t n)", t=2)).then_inc(moe_in[s_], 16)

        def sp_expert(sp, m, j):
            last = isinstance(m, int) and j == E_BODY - 1
            if not last:
                sp.wait_ge(t_gu, 2 * (E_BODY * m + j))
                gate_up_in(sp, m, j + 1)
            if j <= 5 or j == E_BODY:
                ada2_next(sp, m + j // E_BODY, j % E_BODY, 0)

        def ada2_next(eng, m, j, i):
            k = 2 * j + i
            vec, q = k // 4, k % 4
            eng.wait_ge(v_ada2, 24 * m + 2 * k + 2)
            eng.dma_start(ring[:, 6 + i, :].rearrange("p (t n) -> p t n", t=2),
                          A["ada_w_2"].rearrange("l j (p t) n -> (l j) p t n", t=8)
                          [bass.ds(m, 1), :, 2 * q:2 * q + 2, vec * D:(vec + 1) * D]
                          .rearrange("o p t n -> (o p) t n")).then_inc(ada2_in[i], 16)

        def sp_tail(sp):
            sp.wait_ge(v["i"], STEP["i.done"])
            for q in range(4):
                sp.dma_start(ring[:, q, :].rearrange("p (t n) -> p t n", t=2),
                             A["w_out"][0].rearrange("(p t) n -> p t n", t=8)[:, 2 * q:2 * q + 2, :]
                             ).then_inc(wout_in, 16)
            sp.wait_ge(v["y"], STEP["y.done1"])
            sp.wait_ge(g["y"], STEP["y.free"])
            sp.dma_start(w_rt[:, :, 0:32], A["moe_w_router"][0].rearrange("(p t) n -> p t n", t=8)).then_inc(rt_in, 16)
            sp.dma_start(w_rt[:, :, 32:36], A["moe_w_group"][0].rearrange("(p t) n -> p t n", t=8)).then_inc(rt_in, 16)
            sp.dma_start(b_rt[:, 0:32], A["moe_b_router"].to_broadcast([P, NE])).then_inc(rt_in, 16)
            sp.dma_start(b_rt[:, 32:36], A["moe_b_group"].to_broadcast([P, NG])).then_inc(rt_in, 16)
            sp.dma_start(nrm_b, A["final_norm_w"].rearrange("(o n) -> o n", o=1).to_broadcast([P, D])).then_inc(nrm_in, 16)
            for m in range(4):
                sp.dma_start(gate2[:, m, :], A["ada_b_2"][m // 2, m % 2:m % 2 + 1, 2 * D:3 * D].to_broadcast([P, D])
                             ).then_inc(par2_in, 16)
                sp.dma_start(adab2_c[:, 2 * m:2 * m + 2, :],
                             A["ada_b_2"][m // 2, m % 2, 0:2 * D].rearrange("(v p t) -> p v t", p=P, t=8)
                             ).then_inc(par2_in, 16)
                sp.dma_start(norm2_c[:, m, :], A["norm_w_2"][m // 2, m % 2].rearrange("(p t) -> p t", t=8)
                             ).then_inc(par2_in, 16)
            sp.dma_start(sink_b, A["attn_sinks_2"].to_broadcast([P, SWA_H])).then_inc(par2_in, 16)
            sp.dma_start(w_glr[:, :, :], A["attn_w_in_2"][0].rearrange("(p t) n -> p t n", t=8)[:, :, 1536:1552]
                         ).then_inc(par2_in, 16)
            sp.dma_start(w_gg, A["gla_w_gate_2"][0]).then_inc(par2_in, 16)
            sp.wait_ge(t["o"], STEP["o.t"])
            sp.dma_start(ggn, A["gla_norm_w_2"].to_broadcast([P, GLA_DV])).then_inc(par2_in, 16)

            sp.wait_ge(t_out, 4)
            for e in range(2):
                gate_up_in(sp, 0, e)
                down_in(sp, 0, e)
            for i in range(2):
                ada2_next(sp, 0, 0, i)
            with sp.Fori(0, LAST_PASS) as m:
                for j in range(1, E_BODY + 1):
                    sp_expert(sp, m, j)
            for j in range(1, E_BODY):
                sp_expert(sp, LAST_PASS, j)
            sp.wait_ge(v_cols, 5 * 3)
            sp.dma_start(cols_d.rearrange("v (p t) -> p v t", t=8), mod2[:, 2, 0:16].rearrange("p (v t) -> p v t", v=2)
                         ).then_inc(cols_out, 16)
            sp.wait_ge(cols_out, 16)
            sp.dma_start(prm[0:16, :], cols_d.rearrange("v (k p) -> (v k) p", p=P)).then_inc(cols_in, 16)
            sp.wait_ge(t_dn, 2 * NE)
            sp.wait_ge(bias_out, 16)
            sp.dma_start(bias8[:, :, :], scratch_d[:, 127:127 + P * 383].rearrange("h (q l) -> q h l", l=383)[:, :, 0:256]
                         ).then_inc(bias_in, 16)
            sp_block2(sp)

        def sp_block2(sp):
            for i, (kind, c0) in enumerate(stream2):
                if i < RING:
                    if i == 6:
                        sp.wait_ge(v_ada2, CREDIT + 24 * 4)
                else:
                    sp.wait_ge(t_bin, i - RING + 1)
                if kind == "in":
                    sp.dma_start(ring[:, i % RING, :].rearrange("p (t n) -> p t n", t=8),
                                 A["attn_w_in_2"][0].rearrange("(p t) n -> p t n", t=8)[:, :, c0:c0 + 256]
                                 ).then_inc(ring2[i % RING], 16)
                else:
                    sp.dma_start(ring[:, i % RING, :].rearrange("p (t n) -> p t n", t=2),
                                 A["attn_w_out_2"][0].rearrange("(p t) n -> p t n", t=8)[:, 2 * c0:2 * c0 + 2, :]
                                 ).then_inc(ring2[i % RING], 16)
            sp.wait_ge(t_bin, 9)
            first_chunks_in(sp, 0, (0, 5, 6, 7))
            sp.wait_ge(t_bout, 4)
            first_chunks_in(sp, 0, (1, 2, 3, 4))
            sp_mlp(sp, 0)
            sp.wait_ge(t_fd, 16)
            sp.dma_start(poolw[:, :, :, :], A["pool_w_2"][0].rearrange("g (r p) n -> p g r n", p=P)).then_inc(pool_in, 16)
            sp.dma_start(psc_b, A["pool_scale_2"].to_broadcast([P, D])).then_inc(pool_in, 16)
            first_chunks_in(sp, 1, (0, 1, 2, 3, 4, 5, 6, 7))
            sp_mlp(sp, 1)
            sp.wait_ge(v["pp"], STEP["pp.x1"])
            sp.dma_start(gate2[:, 0, :], A["final_norm_w_2"].rearrange("(o n) -> o n", o=1).to_broadcast([P, D])).then_inc(nrm2_in, 16)
            for tt in range(TT):
                sp.wait_ge(v["z"], STEP[f"z.out{tt}"])
                sp.dma_start(out[0, P * tt:P * tt + P, :], x_sb[:, tt, :]).then_inc(s_out, 16)
            sp.wait_ge(s_out, 32)

        def w1_in(sp, layer, m, j, r):
            s_ = 4 * (j % 2) + r
            sp.dma_start(ring[:, s_, :].rearrange("p (t n) -> p t n", t=4),
                         A["mlp_w1_2"][layer].rearrange("(p t) (c n) -> c p t n", t=8, n=512)
                         [bass.ds(2 * m + j, 1), :, 4 * r:4 * r + 4, :].rearrange("o p t n -> (o p) t n")
                         ).then_inc(mlp_in[s_], 16)

        def w2_in(eng, layer, m, j, r):
            s_ = 4 * (j % 2) + 2 + r
            eng.dma_start(ring[:, s_, :].rearrange("p (f n) -> p f n", f=2),
                          A["mlp_w2_2"][layer].rearrange("(c p f) n -> c p f n", p=P, f=4)
                          [bass.ds(2 * m + j, 1), :, 2 * r:2 * r + 2, :].rearrange("o p f n -> (o p) f n")
                          ).then_inc(mlp_in[s_], 16)

        def sp_mlp(sp, layer):
            def chunk_in(m, j):
                sp.wait_ge(t_up, 16 * layer + 2 * (2 * m + j))
                for r in range(2):
                    w1_in(sp, layer, m, j + 1, r)

            with sp.Fori(0, 3) as m:
                for j in (1, 2):
                    chunk_in(m, j)

        def first_chunks_in(sp, layer, slots):
            for s_ in slots:
                (w1_in if s_ % 4 < 2 else w2_in)(sp, layer, 0, s_ // 4, s_ % 2)

        @block.sync
        def _(sp):
            sp.dma_start(ccol[:, 0:8], A["c"].rearrange("o (p t) -> p (o t)", t=8)).then_inc(c_in, 16)
            sp.dma_start(ccol[:, 8:16], A["c_2"].rearrange("o (p t) -> p (o t)", t=8)).then_inc(c_in, 16)
            sp.dma_start(x_sb[:, :, :], A["x"].rearrange("b (a p) d -> p (b a) d", p=P)).then_inc(x_in, 16)
            for i, (kind, n) in enumerate(stream):
                if i >= RING:
                    k0, n0 = stream[i - RING]
                    if k0 == "ada":
                        sp.wait_ge(v_ada, 2 * (n0 + 1))
                    else:
                        sp.wait_ge(t_win, win_order.index(n0) + 1)
                dst = slot((kind, n))
                if kind == "ada":
                    vec, q = n // 4, n % 4
                    src = A["ada_w"][0].rearrange("(p t) n -> p t n", t=8)[:, 2 * q:2 * q + 2, vec * D:(vec + 1) * D]
                    sp.dma_start(dst.rearrange("p (t n) -> p t n", t=2), src).then_inc(ring_in[i % RING], 16)
                else:
                    src = A["w_in"][0].rearrange("(p t) n -> p t n", t=8)[:, :, 256 * n:256 * n + 256]
                    sp.dma_start(dst.rearrange("p (t n) -> p t n", t=8), src).then_inc(ring_in[i % RING], 16)
            sp.wait_ge(t_ada, 5)
            for i, name in enumerate(("rwkv_gn_w", "rwkv_gn_b", "mlstm_hn_w")):
                sp.dma_start(rowp[:, i, :], A[name].to_broadcast([P, 512])).then_inc(row_in, 16)
            sp_tail(sp)

        def g_mlp_loop(pool, layer):
            with pool.Fori(0, 4) as m:
                for j in range(2):
                    pool.wait_ge(a_w1, 16 * layer + 4 * m + 2 * j + 1)
                    trailing(nc.gpsimd, ring_lo[:, 4 * j, :], ring[:, 4 * j, :], mlp_hi[4 * j]).then_inc(g_w1, 1)

        @block.gpsimd
        def _(pool):
            c = Counter(pool, g["c"])
            k = c.link
            k(nc.gpsimd.memset(ident[:, :], 0.0))
            k(nc.gpsimd.memset(ones[:, :], 1.0))
            k(nc.gpsimd.affine_select(out=ident[:, :], in_=ident[:, :], compare_op=ALU.not_equal, fill=1.0,
                                      base=0, pattern=[[-1, P]], channel_multiplier=1))
            k(nc.gpsimd.memset(nhalf[:, :], -0.5))
            k(nc.gpsimd.memset(prm[:, :], 0.0))
            k(nc.gpsimd.memset(rel_sb[:, :], BIG))
            k(nc.gpsimd.memset(zeros_b[:, :], 0.0))
            k(nc.gpsimd.memset(ring_zero[:, :], 0.0))
            c.at("c.ident")
            k(nc.gpsimd.memset(raw[:, :, :, 0:1], 0.0))
            k(nc.gpsimd.memset(convraw[:, :, 0:3], 0.0))
            k(nc.gpsimd.memset(w_if[:, :, :], 0.0))
            k(nc.gpsimd.memset(wup[:, :, :], 0.0))
            k(nc.gpsimd.memset(gate_b[:, :], 0.0))
            k(nc.gpsimd.memset(mrow[:, :, :], 0.0))
            k(nc.gpsimd.memset(ones2[:, :], 1.0))
            k(nc.gpsimd.memset(reset[:, :], 1.0))
            k(nc.gpsimd.memset(reset[:, :].rearrange("p (c s) -> p c s", s=CH)[:, :, 0:1], 0.0))
            c.at("c.zeros")
            pool.dma_start(rel_sb[0:32, :], A["rel_bias_2"]).then_inc(hot_in, 16)
            pool.dma_start(hots[0:33, :], A["hots"]).then_inc(hot_in, 16)
            prm_rows = [("rwkv_mu", 14), ("rwkv_w0", 4), ("rwkv_a0", 4), ("rwkv_k_k", 4), ("rwkv_k_a", 4)]
            r0 = 0
            for name, n in prm_rows:
                pool.dma_start(prm[r0:r0 + n, :], A[name].rearrange("o (i p) -> (o i) p", p=P)).then_inc(prm_in, 16)
                r0 += n
            pool.dma_start(prm[30:34, :], A["rwkv_r_k"].rearrange("o (i h) j -> (o i) (h j)", h=2)).then_inc(prm_in, 16)
            pool.dma_start(prm[34:38, :], A["mlstm_conv_b"].rearrange("o (i p) -> (o i) p", p=P)).then_inc(prm_in, 16)
            pool.dma_start(prm[38:54, :], A["mlstm_conv_w"].rearrange("o j (i p) -> (o j i) p", p=P)).then_inc(prm_in, 16)
            pool.dma_start(prm[54:56, :], A["gla_b_gate_2"].rearrange("o (i p) -> (o i) p", p=P)).then_inc(prm_in, 16)
            pool.dma_start(prm[56:64, :], A["norm_w_2"][1, 0].rearrange("(i p) -> i p", p=P)).then_inc(prm_in, 16)
            pool.dma_start(prm[64:80, :], A["ada_b_2"][1, 0, 0:2048].rearrange("(i p) -> i p", p=P)).then_inc(prm_in, 16)
            pool.dma_start(gate1[:, 0, :], A["ada_b"][:, 2 * D:3 * D].to_broadcast([P, D])).then_inc(par_in, 16)
            pool.dma_start(gate1[:, 1, :], A["ada_b"][:, 5 * D:6 * D].to_broadcast([P, D])).then_inc(par_in, 16)
            g_norm(pool, "n")
            c = Counter(pool, g["c"], STEP["c.zeros"])
            k = c.link
            for i, B in enumerate((16, 32, 64)):
                m = masks[:, i, :].rearrange("p (b f) -> p b f", f=B)
                k(nc.gpsimd.memset(masks[:, i, :], 1.0))
                k(nc.gpsimd.affine_select(out=m, in_=m, compare_op=ALU.is_ge, fill=0.0, base=0,
                                          pattern=[[-B, P // B], [0, B]], channel_multiplier=1))
                k(nc.gpsimd.affine_select(out=m, in_=m, compare_op=ALU.is_ge, fill=0.0, base=B - 1,
                                          pattern=[[B, P // B], [0, B]], channel_multiplier=-1))
            k(nc.gpsimd.tensor_copy(headblk[:, :], same64))
            k(nc.gpsimd.tensor_copy(headsel[:, :], masks[:, 2, 0:128:64]))
            k(nc.gpsimd.affine_select(out=m_causal, in_=ones[:, :], compare_op=ALU.is_ge, fill=0.0, base=0,
                                      pattern=[[1, P]], channel_multiplier=-1))
            k(nc.gpsimd.tensor_tensor(m_64, same64, same32, ALU.subtract))
            k(nc.gpsimd.tensor_tensor(same32, same32, same16, ALU.subtract))
            k(nc.gpsimd.tensor_scalar(m_n16t, same16, -1.0, None, ALU.mult))
            k(nc.gpsimd.affine_select(out=m_n16t, in_=m_n16t, compare_op=ALU.is_gt, fill=0.0, base=0,
                                      pattern=[[1, P]], channel_multiplier=-1))
            k(nc.gpsimd.tensor_scalar(masks[:, 0:2, :], masks[:, 0:2, :], -1.0, None, ALU.mult))
            k(nc.gpsimd.tensor_scalar(m_64, m_64, -1.0, None, ALU.mult))
            for m in (m_n16, m_32, m_64):
                k(nc.gpsimd.affine_select(out=m, in_=m, compare_op=ALU.is_gt, fill=0.0, base=0,
                                          pattern=[[-1, P]], channel_multiplier=1))
            k(nc.gpsimd.affine_select(out=m_ak, in_=same64, compare_op=ALU.is_gt, fill=0.0, base=0,
                                      pattern=[[1, P]], channel_multiplier=-1))
            k(nc.gpsimd.affine_select(out=m_rb, in_=same64, compare_op=ALU.is_ge, fill=0.0, base=0,
                                      pattern=[[1, P]], channel_multiplier=-1))
            c.at("c.masks")
            c = Counter(pool, g["m"])
            pool.wait_ge(v["m"], STEP["m.ss"])
            c.link(nc.gpsimd.tensor_tensor(small[:, 8:16], small[:, 8:16], nhalf[:, 0:8], ALU.pow))
            c.at("m.rs")
            c = Counter(pool, g["r"])
            pool.wait_ge(bias_out, 16)
            pool.wait_ge(v["m"], STEP["m.s"])
            c.link(nc.gpsimd.memset(bhz[:, :, :], 0.0))
            c.link(nc.gpsimd.memset(khz[:, :, :], 0.0))
            pool.wait_ge(v["w"], STEP["w.shift"])
            pool.wait_ge(t["n"], STEP["n.t"])
            c.link(nc.gpsimd.memset(rbuf[:, :, :], 0.0))
            c.link(nc.gpsimd.memset(ubuf[:, :, :], 0.0))
            c.link(nc.gpsimd.memset(state[:, :, :, :], 0.0))
            c.at("r.zero")
            pool.wait_ge(v_ada, 48)
            pool.wait_ge(v["r"], STEP["r.kmod"])
            c.link(nc.gpsimd.tensor_tensor(rkp[:, :, :], u[:, 0:4, :], kmod[:, :, :], ALU.mult))
            c.link(nc.gpsimd.tensor_tensor(rkp[:, :, :], rkp[:, :, :], rk_c.unsqueeze(2).to_broadcast([P, 4, SEQ]), ALU.mult))
            c.at("r.rkp")
            pool.wait_ge(a["r"], STEP["r.exp"])
            c.link(nc.gpsimd.tensor_tensor(kh[:, :, :], kmod[:, :, :], pinv[:, :, :], ALU.mult))
            c.at("r.kh")
            pool.wait_ge(v["r"], STEP["r.pend"])
            c.link(nc.gpsimd.tensor_tensor(chunk(kend), chunk(kh), to_end(), ALU.mult))
            c.at("r.kend")
            c = Counter(pool, g["y"])
            for tt in range(TT):
                pool.wait_ge(v["y"], STEP[f"y.var{tt}"])
                s8 = small[:, 32 + 8 * tt:40 + 8 * tt]
                c.link(nc.gpsimd.tensor_tensor(s8, s8, nhalf[:, 0:8], ALU.pow))
                c.at(f"y.rs{tt}")
            pool.wait_ge(v["y"], STEP["y.done1"])
            c.link(nc.gpsimd.iota(revi, pattern=[[-1, 8]], base=8, channel_multiplier=0))
            c.link(nc.gpsimd.tensor_copy(rev, revi))
            c.at("y.free")
            g_norm(pool, "q")
            with pool.Fori(0, NE // E_BODY) as m:
                for e in range(E_BODY):
                    s_ = 3 * (e % 2)
                    pool.wait_ge(a_gu, 2 * E_BODY * m + 2 * e + 1)
                    trailing(nc.gpsimd, ring_lo[:, s_, :], ring[:, s_, :], moe_hi[s_]).then_inc(g_gate, 1)
            cf, cn = Counter(pool, g["f"]), Counter(pool, g["bn"])
            for tt in range(TT):
                g_rstd(pool, cf, "f", tt)
                g_rstd(pool, cn, "bn", tt)
            c = Counter(pool, g["bp"])
            pool.wait_ge(v["bn"], STEP["bn.v"])
            pool.wait_ge(t["bn"], STEP["bn.t"])
            c.link(nc.gpsimd.memset(ktz[:, :, :], 0.0))
            c.link(nc.gpsimd.memset(kz[:, :, :, :], 0.0))
            c.link(nc.gpsimd.memset(sg_state[:, :, :, :], 0.0))
            c.at("bp.zero")
            c.link(nc.gpsimd.iota(pcnti, pattern=[[1, SEQ]], base=1, channel_multiplier=0))
            c.link(nc.gpsimd.tensor_copy(pcnt, pcnti))
            for gi in range(4):
                c.link(nc.gpsimd.tensor_scalar(pinvc[:, gi, :], pcnt, float(2 ** (gi + 1)), None, ALU.min))
            c.at("bp.len")
            c = Counter(pool, g["bg"])
            pool.wait_ge(v["bg"], STEP["bg.ss"])
            c.link(nc.gpsimd.tensor_tensor(small[:, 8:16], small[:, 8:16], nhalf[:, 0:8], ALU.pow))
            c.at("bg.rs")
            for q in range(3):
                pool.wait_ge(a["bs"], STEP[f"bs.hi{q}"])
                c.link(trailing(nc.gpsimd, ring_lo[:, (9 + q) % RING, :], ring[:, (9 + q) % RING, :], out_hi[q]))
            c.at("bg.lo")
            g_norm(pool, "l0")
            g_mlp_loop(pool, 0)
            g_norm(pool, "pn")
            c = Counter(pool, g["pp"])
            for buf in (hp, pa, pb_):
                c.link(nc.gpsimd.memset(buf[:, :, 0:PAD], 0.0))
            c.at("pp.zero")
            pool.wait_ge(v["pn"], STEP["pn.v"])
            pool.wait_ge(a["pn"], STEP["pn.a"])
            window_sum(c, nc.gpsimd, pa, hp, 0, 2, 1)
            pool.wait_ge(v["bo"], STEP["bo.len"])
            mean_less_input(c, nc.gpsimd, 0, pa)
            window_sum(c, nc.gpsimd, pa, hp, 2, 4, 1)
            window_sum(c, nc.gpsimd, pb_, pa, 2, 4, 2)
            mean(c, nc.gpsimd, 1, pb_)
            c.at("pp.g")
            g_norm(pool, "l1")
            g_mlp_loop(pool, 1)
            g_norm(pool, "z")

        mod_of = [(mod2[:, 0, 0:8], mod2[:, 0, 8:16]), (mod2[:, 1, 0:8], mod2[:, 1, 8:16]),
                  (mod2[:, 2, 16:24], mod2[:, 2, 24:32]), (mod2[:, 3, 0:8], mod2[:, 3, 8:16])]

        def a_mlp_loop(act, layer):
            def squares(m, j, tt, first=False):
                n = 16 * layer + 4 * m + 2 * j + tt + 1
                act.wait_ge(t_up, n)
                nc.scalar.activation(frl[:, tt, :], ps[:, 4 + tt, :], ACT.Relu).then_inc(a_fact, 1)
                act.wait_ge(a_fact, 2 * n - 1)
                if not first:
                    act.wait_ge(t_ft, n - 2)
                nc.scalar.activation(fact[:, tt, :], frl[:, tt, :], ACT.Square).then_inc(a_fact, 1)

            def chunk(m, j, first=False, last=False):
                if not last:
                    a_w1_hi(act, layer, m, j + 1)
                squares(m, j, 0, first)
                for r in range(2):
                    s_ = 4 * (j % 2) + 2 + r
                    act.wait_ge(mlp_in[s_], ring2_n[s_] + 64 * layer + 16 * (m + j // 2) + 16)
                    nc.scalar.copy(mlp_hi[s_], ring[:, s_, :]).then_inc(a_w2, 1)
                squares(m, j, 1, first)
                if not first and not last:
                    act.wait_ge(t_fd, 16 * layer + 2 * (2 * m + j))
                    for r in range(2):
                        w2_in(act, layer, m, j + 1, r)

            chunk(0, 0, first=True)
            with act.Fori(0, 3) as m:
                for j in (1, 2):
                    chunk(m, j)
            chunk(3, 1, last=True)

        def a_w1_hi(act, layer, m, j, parts=(0, 1)):
            for r in parts:
                s_ = 4 * (j % 2) + r
                act.wait_ge(mlp_in[s_], ring2_n[s_] + 64 * layer + 16 * (m + j // 2) + 16)
                nc.scalar.copy(mlp_hi[s_], ring[:, s_, :]).then_inc(a_w1, 1)

        def a_hT_hi(act, st, hi, half):
            act.wait_ge(v[st], STEP[st + (".vh", ".v")[half]])
            k = 4 * half
            nc.scalar.copy(hi[:, k:k + 4, :], hT[:, k:k + 4, :]).then_inc(a_hi, 1)

        def v_hT_lo(dve, st, hi, n):
            for i, k in enumerate((0, 4)):
                dve.wait_ge(a_hi, 2 * n + i + 1)
                trailing(nc.vector, hT_lo[:, k:k + 4, :], hT[:, k:k + 4, :], hi[:, k:k + 4, :]).then_inc(v_lo, 1)

        def v_w1_lo(dve, layer, m, j):
            s_ = 4 * (j % 2) + 1
            dve.wait_ge(a_w1, 16 * layer + 4 * m + 2 * j + 2)
            trailing(nc.vector, ring_lo[:, s_, :], ring[:, s_, :], mlp_hi[s_]).then_inc(v_w1, 1)

        def v_squares_t(dve, layer, m, j, tt):
            n = 16 * layer + 4 * m + 2 * j + tt + 1
            dve.wait_ge(t_ft, n)
            if not (isinstance(m, int) and m == 0 and j == 0):
                dve.wait_ge(t_fd, n - 2)
            src = ps[:, 6 + tt, :].rearrange("p (f n) -> p f n", f=4)
            nc.vector.tensor_copy(fact_hi[:, tt], src).then_inc(v_fact_t, 1)
            dve.wait_ge(v_fact_t, 2 * n - 1)
            trailing(nc.vector, fact_lo[:, tt], src, fact_hi[:, tt]).then_inc(v_fact_t, 1)

        def v_w2_lo(dve, layer, m, j):
            for r in range(2):
                s_ = 4 * (j % 2) + 2 + r
                dve.wait_ge(a_w2, 16 * layer + 4 * m + 2 * j + r + 1)
                trailing(nc.vector, ring_lo[:, s_, :], ring[:, s_, :], mlp_hi[s_]).then_inc(v_w2, 1)

        def v_chunk(dve, layer, m, j, first=False, last=False):
            if not last:
                v_w1_lo(dve, layer, m, j + 1)
            if not first:
                v_squares_t(dve, layer, m, j - 1, 1)
            v_w2_lo(dve, layer, m, j)
            v_squares_t(dve, layer, m, j, 0)

        def v_mlp_loop(dve, layer):
            v_chunk(dve, layer, 0, 0, first=True)
            with dve.Fori(0, 3) as m:
                for j in (1, 2):
                    v_chunk(dve, layer, m, j)
            v_chunk(dve, layer, 3, 1, last=True)
            v_squares_t(dve, layer, 3, 1, 1)

        def a_gate_up_hi(act, m, e, i):
            s_ = 3 * (e % 2) + i
            act.wait_ge(moe_in[s_], 16 * (E_BODY // 2) * m + 16 * (e // 2 + 1))
            nc.scalar.copy(moe_hi[s_], ring[:, s_, :]).then_inc(a_gu, 1)

        def v_up_lo(dve, m, e):
            s_ = 3 * (e % 2) + 1
            dve.wait_ge(a_gu, 2 * (E_BODY * m + e) + 2)
            trailing(nc.vector, ring_lo[:, s_, :], ring[:, s_, :], moe_hi[s_]).then_inc(v_gate_up, 1)

        def v_down_lo(dve, m, e):
            s_ = 3 * (e % 2) + 2
            dve.wait_ge(a_dn, E_BODY * m + e + 1)
            trailing(nc.vector, ring_lo[:, s_, :], ring[:, s_, :], moe_hi[s_]).then_inc(v_dn, 1)

        def t_mlp_loop(pe, layer):
            def up(m, j, tt, first=False):
                s0 = 4 * (j % 2)
                if not first:
                    pe.wait_ge(a_fact, 32 * layer + 8 * m + 4 * j + 2 * tt - 2)
                for k in range(KT):
                    if first and tt == 0 and k % 4 == 0:
                        pe.wait_ge(v_lo, 2 * layer + 3 + k // 4)
                    if tt == 0 and k % 4 == 0:
                        pe.wait_ge((g_w1, v_w1)[k // 4], 8 * layer + 2 * m + j + 1)
                    tok, cols = slice(P * tt, P * tt + P), slice(512 * (k % 4), 512 * (k % 4) + 512)
                    ins = mm3(ps[:, 4 + tt, :], gT_hi[:, k, tok], hT_lo[:, k, tok], mlp_hi[s0 + k // 4][:, cols],
                              ring_lo[:, s0 + k // 4, cols], start=k == 0, stop=k == KT - 1)
                ins.then_inc(t_up, 1)

            def turn(m, j, tt, first=False):
                pe.wait_ge(a_fact, 32 * layer + 8 * m + 4 * j + 2 * tt + 2)
                if not first:
                    pe.wait_ge(v_fact_t, 32 * layer + 8 * m + 4 * j + 2 * tt - 2)
                for f in range(4):
                    ins = nc.tensor.transpose(ps[:, 6 + tt, P * f:P * f + P], fact[:, tt, f::4], ident[:, :])
                ins.then_inc(t_ft, 1)

            def down(m, j, tt):
                s0 = 4 * (j % 2) + 2
                pe.wait_ge(v_fact_t, 32 * layer + 8 * m + 4 * j + 2 * tt + 2)
                for f in range(4):
                    if tt == 0 and f % 2 == 0:
                        pe.wait_ge(v_w2, 16 * layer + 4 * m + 2 * j + f // 2 + 1)
                    for h in range(2):
                        cols = slice(D * (f % 2) + 512 * h, D * (f % 2) + 512 * h + 512)
                        ins = mm3(ps[:, 2 * tt + h, :], fact_hi[:, tt, f, :], fact_lo[:, tt, f, :],
                                  mlp_hi[s0 + f // 2][:, cols], ring_lo[:, s0 + f // 2, cols])
                ins.then_inc(t_fd, 1)

            def chunk(m, j):
                up(m, j, 0)
                turn(m, j - 1, 1, first=isinstance(m, int) and m == 0 and j == 1)
                down(m, j - 1, 0)
                up(m, j, 1)
                turn(m, j, 0)
                down(m, j - 1, 1)

            up(0, 0, 0, first=True)
            pe.wait_ge(a[f"l{layer}"], STEP[f"l{layer}.a"])
            pe.wait_ge(v[f"l{layer}"], STEP[f"l{layer}.v"])
            t_zero(pe)
            up(0, 0, 1, first=True)
            turn(0, 0, 0, first=True)
            with pe.Fori(0, 3) as m:
                for j in (1, 2):
                    chunk(m, j)
            chunk(3, 1)
            turn(3, 1, 1)
            down(3, 1, 0)
            down(3, 1, 1)

        def t_zero(pe):
            for j in range(4):
                ins = nc.tensor.matmul(ps[:, j, :], zeros_b[:, 0:P], ring_zero, start=True, stop=True,
                                       skip_group_check=True)
            return ins

        @block.scalar
        def _(act):
            c = Counter(act, a["c"])
            act.wait_ge(c_in, 32)
            c.link(nc.scalar.activation(csig[:, :], ccol[:, :], ACT.Sigmoid))
            c.at("c.sig")
            act.dma_start(adab_c[:, :, :], A["ada_b"].rearrange("o (v p t) -> p (o v) t", p=P, t=8)).then_inc(col_in, 16)
            act.dma_start(norm_c[:, 0, :], A["mix_norm_w"].rearrange("o (p t) -> p (o t)", t=8)).then_inc(col_in, 16)
            act.dma_start(norm_c[:, 1, :], A["ffn_norm_w"].rearrange("o (p t) -> p (o t)", t=8)).then_inc(col_in, 16)
            act.wait_ge(g["c"], STEP["c.zeros"])
            w_in_t = A["w_in"][0].rearrange("(p t) n -> p t n", t=8)
            act.dma_start(w_if[:, :, 0:4], w_in_t[:, :, 3328:3332]).then_inc(gate_in, 16)
            act.dma_start(w_if[:, :, 32:36], w_in_t[:, :, 3332:3336]).then_inc(gate_in, 16)
            act.dma_start(wup[0:64, 0, :], A["rwkv_w_up"][0]).then_inc(gate_in, 16)
            act.dma_start(wup[64:128, 1, :], A["rwkv_a_up"][0]).then_inc(gate_in, 16)
            act.dma_start(gup[:, :], A["rwkv_g_up"][0]).then_inc(gate_in, 16)
            act.dma_start(gate_b[0:4, 0:1], A["mlstm_i_b"].rearrange("o h -> h o")).then_inc(gate_in, 16)
            act.dma_start(gate_b[32:36, 0:1], A["mlstm_f_b"].rearrange("o h -> h o")).then_inc(gate_in, 16)
            act.wait_ge(t_bias, 1)
            nc.scalar.copy(ebc, ps[0:SWA_H, 4, 0:384]).then_inc(a_bias, 1)
            act.wait_ge(a_bias, 1)
            act.dma_start(scratch_d.rearrange("h (q l) -> h q l", q=P), ebc.unsqueeze(1).to_broadcast([SWA_H, P, 384])
                          ).then_inc(bias_out, 16)
            act.wait_ge(x_in, 16)
            a_norm(act, "n", mod_c[:, 0, :], mod_c[:, 1, :])

            c = Counter(act, a["w"])
            cm = Counter(act, a["m"])
            act.wait_ge(g["c"], STEP["c.zeros"])
            act.wait_ge(t["n"], STEP["n.t"])

            def columns(n):
                i = win_order.index(n)
                act.wait_ge(t_win, i + 1)
                bank = ps[:, 6 + i % 2, :]
                if n < 7:
                    if n >= 2:
                        act.wait_ge(v["w"], STEP["w.pre"] + 3 * (n - 1))
                    c.link(nc.scalar.copy(raw[:, n % 2, :, 1:257], bank.rearrange("p (i t) -> p i t", i=2)))
                elif n < 9:
                    c.link(nc.scalar.copy(convraw[:, 2 * (n - 7):2 * (n - 7) + 2, 3:259],
                                          bank.rearrange("p (i t) -> p i t", i=2)))
                elif n < 11:
                    c.link(nc.scalar.copy(vm[:, :, 256 * (n - 9):256 * (n - 9) + 256],
                                          bank.rearrange("p (a f) -> p a f", a=2)))
                else:
                    c.link(nc.scalar.activation(om[:, :, 256 * (n - 11):256 * (n - 11) + 256],
                                                bank.rearrange("p (a f) -> p a f", a=2), ACT.Sigmoid))
                c.at(f"w.col{n}")

            for n in (7, 8):
                columns(n)
            act.wait_ge(v["w"], STEP["w.gb"])
            act.wait_ge(t["w"], STEP["w.if"])
            cm.link(nc.scalar.activation(mrow[0:4, 0, :], ps[0:4, 0, 0:256], ACT.Tanh, bias=gate_b[0:4, 1:2],
                                         scale=1 / CAP))
            cm.link(nc.scalar.activation(mrow[0:4, 1, :], ps[32:36, 0, 0:256], ACT.Tanh, bias=gate_b[32:36, 1:2],
                                         scale=1 / CAP))
            cm.link(nc.scalar.activation(mrow[0:4, 1, :], mrow[0:4, 1, :], ACT.Exp, scale=-CAP))
            cm.link(nc.scalar.activation(mrow[0:4, 1, :], mrow[0:4, 1, :], ACT.Ln, bias=ones[0:4, 0:1]))
            cm.at("m.lf")
            columns(9)
            act.wait_ge(v["m"], STEP["m.conv"])
            cm.link(nc.scalar.activation(qsig[:, :, :], qk[:, :, :], ACT.Sigmoid))
            cm.at("m.sig")
            columns(10)
            columns(11)
            act.wait_ge(v["m"], STEP["m.z"])
            cm.link(nc.scalar.activation(mz[:, :, :], mz[:, :, :], ACT.Exp, scale=-1.0))
            cm.link(nc.scalar.activation(mem[:, :, :], mcol[:, :, 32:36], ACT.Exp))
            cm.at("m.exp")
            columns(12)
            for n in range(7):
                columns(n)

            c = Counter(act, a["r"])
            act.wait_ge(v["w"], STEP["w.shift"])
            c.link(nc.scalar.activation(u[0:64, 12, :], u[0:64, 12, :], ACT.Tanh))
            c.link(nc.scalar.activation(u[:, 13, :], u[:, 13, :], ACT.Sigmoid))
            c.at("r.u")
            act.wait_ge(t["r"], STEP["r.n2"])
            c.link(nc.scalar.activation(kn[:, :, :], ps[:, 6:8, :].rearrange("p b (i t) -> p (b i) t", i=2), ACT.Sqrt))
            c.at("r.sqrt")
            act.wait_ge(t["r"], STEP["r.wa"])
            for i in range(4):
                o = (i % 2) * 256
                c.link(nc.scalar.activation(av[:, i, :], ps[:, 2 + i // 2, o:o + 256], ACT.Sigmoid,
                                            bias=a0_c[:, i:i + 1]))
                c.link(nc.scalar.activation(lw[:, i, :], ps[:, i // 2, o:o + 256], ACT.Sigmoid, bias=w0_c[:, i:i + 1]))
            c.at("r.sig")
            c.link(nc.scalar.copy(gtok[:, :, :], ps[:, 4:6, :]))
            c.at("r.gtok")
            act.wait_ge(t["r"], STEP["r.vt"])
            c.link(nc.scalar.copy(vtok[:, :, :], ps[:, 0:2, :]))
            act.wait_ge(v["r"], STEP["r.scan"])
            c.link(nc.scalar.activation(pcum[:, :, :], cum[:, :, :], ACT.Exp, scale=-DECAY))
            c.link(nc.scalar.activation(pinv[:, :, :], cum[:, :, :], ACT.Exp, scale=DECAY))
            c.at("r.exp")
            act.wait_ge(g["r"], STEP["r.kh"])
            c.link(nc.scalar.copy(khz[0:64, 0::2, :], kh[0:64, :, :]))
            c.link(nc.scalar.copy(khz[64:128, 1::2, :], kh[64:128, :, :]))
            act.wait_ge(v["r"], STEP["r.bh"])
            c.link(nc.scalar.copy(bhz[0:64, 0::2, :], bh[0:64, :, :]))
            c.link(nc.scalar.copy(bhz[64:128, 1::2, :], bh[64:128, :, :]))
            c.at("r.pad")
            act.wait_ge(t["r"], STEP["r.bt"])
            c.link(nc.scalar.copy(bend_t[:, :, :], ps[:, 4:6, :]))
            act.wait_ge(t["r"], STEP["r.kt"])
            c.link(nc.scalar.copy(kend_t[:, :, :], ps[:, 6:8, :]))
            c.at("r.tok")

            c = Counter(act, a["i"])
            for step, src, dst in INV_A:
                for gi in range(4):
                    act.wait_ge(t["i"], 4 * src + gi + 1)
                    c.link(nc.scalar.copy(dst[:, gi], bank4(src, gi)))
            c.at("i.a")
            c = Counter(act, a["s"])
            for ch in range(NC):
                r0 = CH * (ch % 2)
                act.wait_ge(t_u, ch + 1)
                c.link(nc.scalar.copy(ubuf[r0:r0 + CH, ch // 2, :], ps[r0:r0 + CH, 1, :]))
            c = Counter(act, a["o"])
            for tt in range(TT):
                tok = slice(P * tt, P * tt + P)
                for k in range(0, KT, 2):
                    act.wait_ge(t["o"], 4 * tt + k // 2 + 1)
                    c.link(nc.scalar.copy(hT[:, k:k + 2, tok], ps[:, k // 2, :].rearrange("p (k t) -> p k t", k=2)[:, :, tok]))
                c.at(f"o.hT{tt}")
            a_norm(act, "q", mod_c[:, 2, :], mod_c[:, 3, :], after="o", hi=hT_hi)
            for i in range(2):
                a_gate_up_hi(act, 0, 0, i)
            c = Counter(act, a["e"])
            act.wait_ge(v["e"], STEP["e.g"])
            c.link(nc.scalar.activation(rt[:, 1, :, 0:4], rt[:, 1, :, 0:4], ACT.Exp))
            c.at("e.expg")
            act.wait_ge(v["e"], STEP["e.d"])
            c.link(nc.scalar.activation(rt[:, 9, :, 0:1], rt[:, 9, :, 0:1], ACT.Exp))
            c.at("e.expd")
            def silu(m, j, tt, first=False):
                n = 2 * (E_BODY * m + j) + tt + 1
                act.wait_ge(t_gu, n)
                if not first:
                    act.wait_ge(v_eact, n - 2)
                nc.scalar.activation(gact[:, tt, :], ps[:, 4 + tt, 0:FE], ACT.Silu).then_inc(a_silu, 1)

            def expert(m, j, first=False, last=False):
                if not last:
                    a_gate_up_hi(act, m, j + 1, 0)
                silu(m, j, 0, first)
                if not last:
                    a_gate_up_hi(act, m, j + 1, 1)
                act.wait_ge(moe_in[3 * (j % 2) + 2], 16 * (E_BODY // 2) * m + 16 * (j // 2 + 1))
                nc.scalar.copy(moe_hi[3 * (j % 2) + 2], ring[:, 3 * (j % 2) + 2, :]).then_inc(a_dn, 1)
                silu(m, j, 1, first)
                if not first and not last:
                    act.wait_ge(t_dn, 2 * (E_BODY * m + j))
                    down_in(act, m, j + 1)
                if not first and (j <= 5 or j == E_BODY):
                    ada2_next(act, m + j // E_BODY, j % E_BODY, 1)

            act.wait_ge(v["e"], STEP["e.cw"])
            expert(0, 0, first=True)
            with act.Fori(0, LAST_PASS) as m:
                for j in range(1, E_BODY + 1):
                    expert(m, j)
            for j in range(1, E_BODY):
                expert(LAST_PASS, j, last=j == E_BODY - 1)
            cf, cn = Counter(act, a["f"]), Counter(act, a["bn"])
            for tt in range(TT):
                act.wait_ge(v["f"], STEP[f"f.x{tt}"])
                a_square(cf, "f", tt)
                act.wait_ge(v["f"], STEP[f"f.n{tt}"])
                a_square(cn, "bn", tt)
            a_norm_out(act, cn, "bn", *mod_of[0])
            cp = Counter(act, a["bp"])
            act.wait_ge(v["bn"], STEP["bn.v"])
            act.wait_ge(g["bp"], STEP["bp.zero"])
            def copied(i):
                act.wait_ge(t_bin, i + 1)
                bank = bin_bank(i)
                if i < 2:
                    cp.link(nc.scalar.copy((qg, kg)[i][:, :, :], bank.rearrange("p (i t) -> p i t", i=2)))
                elif i < 4:
                    cp.link(nc.scalar.copy(vg[:, :, 256 * (i - 2):256 * (i - 2) + 256], bank.rearrange("p (a n) -> p a n", a=2)))
                elif i < 6:
                    gs = ggs[:, :, 256 * (i - 4):256 * (i - 4) + 256]
                    cp.link(nc.scalar.activation(gs, bank.rearrange("p (a n) -> p a n", a=2), ACT.Sigmoid))
                elif i < 8:
                    cp.link(nc.scalar.copy(sq_t[:, 2 * (i - 6):2 * (i - 6) + 2, :], bank.rearrange("p (i t) -> p i t", i=2)))
                else:
                    for kv in range(2):
                        for par in range(2):
                            cp.link(nc.scalar.copy(kz[64 * par:64 * par + 64, kv, par, :], bank[64 * kv:64 * kv + 64, 0:256]))
                    cp.link(nc.scalar.copy(svt[:, :, :], bank[:, 256:512].rearrange("p (a n) -> p a n", a=2)))

            c = Counter(act, a["bg"])
            act.wait_ge(t["bg"], STEP["bg.lr"])
            c.link(nc.scalar.copy(glr_t, ps[0:16, 0, 0:256]))
            c.at("bg.glr")
            copied(0)
            act.wait_ge(t["bg"], STEP["bg.z"])
            for i in range(2):
                c.link(nc.scalar.activation(zb[:, i, :], ps[:, 1, 256 * i:256 * i + 256], ACT.Identity, bias=prm_c[:, 54 + i:55 + i]))
            c.at("bg.zb")
            c.link(nc.scalar.activation(az[:, :, :], zb[:, :, :], ACT.Abs))
            c.link(nc.scalar.activation(az[:, :, :], az[:, :, :], ACT.Exp, scale=-1.0))
            c.link(nc.scalar.activation(az[:, :, :], az[:, :, :], ACT.Ln, bias=ones[:, 0:1]))
            c.at("bg.ln")
            copied(1)
            act.wait_ge(v["bg"], STEP["bg.scan"])
            c.link(nc.scalar.activation(eb[:, :, :], nb2[:, :, :], ACT.Exp, scale=-1.0 / 16))
            c.link(nc.scalar.activation(enb[:, :, :], nb2[:, :, :], ACT.Exp, scale=1.0 / 16))
            c.at("bg.exp")
            copied(2)
            act.wait_ge(v["bg"], STEP["bg.kt"])
            c.link(nc.scalar.copy(ktz[0:64, 0::2, :], kg[0:64, :, :]))
            c.link(nc.scalar.copy(ktz[64:128, 1::2, :], kg[64:128, :, :]))
            c.at("bg.pad")
            copied(3)
            act.wait_ge(t["bg"], STEP["bg.tr"])
            c.link(nc.scalar.copy(ket[:, :, :], ps[:, 0, :].rearrange("p (a n) -> p a n", a=2)))
            c.at("bg.ket")
            for i in range(4, 9):
                copied(i)
            cp.at("bp.a")
            c = Counter(act, a["bs"])

            def out_hi_copy(q):
                act.wait_ge(ring2[(9 + q) % RING], 32)
                c.link(nc.scalar.copy(out_hi[q], ring[:, (9 + q) % RING, :]))
                c.at(f"bs.hi{q}")

            def exp_part(part):
                act.wait_ge(v["bs"], STEP[f"bs.sub{part}"])
                s_ = sc[:, :, P * part:P + 2 * P * part]
                c.link(nc.scalar.activation(s_, s_, ACT.Exp))

            def weights_t(j):
                act.wait_ge(t["bs"], STEP["bs.pt0"] + j)
                c.link(nc.scalar.copy(p_t[:, 4 * j:4 * j + 4, :], ps[:, bs_bank[j], :].rearrange("p (j q) -> p j q", j=4)))

            act.wait_ge(v["bg"], STEP["bg.y"])
            out_hi_copy(0)
            out_hi_copy(1)
            exp_part(0)
            c.at("bs.exp0")
            for j in range(2):
                weights_t(j)
            out_hi_copy(2)
            exp_part(1)
            c.link(nc.scalar.activation(swm[:, 16:32], swm[:, 16:32], ACT.Exp))
            c.at("bs.exp1")
            for j in range(2, 6):
                weights_t(j)
            c.at("bs.pt")
            out_hi_copy(3)
            c = Counter(act, a["bo"])
            for k in range(0, KT, 2):
                act.wait_ge(t["bo"], k // 2 + 1)
                c.link(nc.scalar.copy(gT_hi[:, k:k + 2, :], ps[:, k // 2, :].rearrange("p (k t) -> p k t", k=2)))
            c.at("bo.hT")
            def w1_first(layer, done, n):
                act.wait_ge(done, n)
                a_w1_hi(act, layer, 0, 0, (0,))

            a_norm(act, "l0", *mod_of[1], after="bo", between=lambda: w1_first(0, t_bout, 4),
                   meanwhile=lambda: a_w1_hi(act, 0, 0, 0, (1,)), hi=gT_hi)
            a_mlp_loop(act, 0)
            a_norm(act, "pn", *mod_of[2], after="l0", out=hp_tok)
            a_norm(act, "l1", *mod_of[3], after="pp", between=lambda: w1_first(1, t["pp"], 4),
                   meanwhile=lambda: a_w1_hi(act, 1, 0, 0, (1,)), hi=gT_hi)
            a_mlp_loop(act, 1)
            c = Counter(act, a["z"])
            for tt in range(TT):
                act.wait_ge(v["l1"], STEP[f"l1.x{tt}"])
                a_square(c, "z", tt)

        @block.vector
        def _(dve):
            def ada_slot(n):
                vec, q = n // 4, n % 4
                loaded(dve, ("ada", n))
                w = slot(("ada", n)).rearrange("p (t n) -> p t n", t=2)
                acc = macc[:, vec % 3, :]
                if q == 0 and vec >= 3:
                    dve.wait_ge(t_ada, vec - 2)
                for r in range(2):
                    k = 2 * q + r
                    if k == 0:
                        ins = nc.vector.tensor_scalar(acc, w[:, r, :], ccol[:, k:k + 1], None, ALU.mult)
                    else:
                        ins = nc.vector.scalar_tensor_tensor(acc, w[:, r, :], ccol[:, k:k + 1], acc, ALU.mult, ALU.add)
                    ada.link(ins)

            ada = Counter(dve, v_ada)
            c = Counter(dve, v["c"])
            dve.wait_ge(a["c"], STEP["c.sig"])
            c.link(nc.vector.tensor_tensor(ccol[:, :], ccol[:, :], csig[:, :], ALU.mult))
            for n in range(6):
                ada_slot(n)

            def mod_mix(c):
                ada_slot(7)
                dve.wait_ge(t_ada, 2)
                dve.wait_ge(col_in, 16 * 3)
                c.link(nc.vector.tensor_tensor(mod_c[:, 0, :], ps[:, 6, 0:8], adab_c[:, 0, :], ALU.add))
                c.link(nc.vector.tensor_tensor(mod_c[:, 1, :], ps[:, 7, 0:8], adab_c[:, 1, :], ALU.add))
                c.link(nc.vector.scalar_tensor_tensor(mod_c[:, 1, :], mod_c[:, 1, :], 1.0, norm_c[:, 0, :],
                                                      ALU.add, ALU.mult))

            v_norm(dve, "n", mod_c[:, 0, :], mod_c[:, 1, :], mod_mix, meanwhile=lambda: ada_slot(6))

            c = Counter(dve, v["w"])
            dve.wait_ge(t["w"], STEP["w.prm"])
            c.link(nc.vector.tensor_copy(prm_c[:, :], ps[:, 0, 256:336]))
            c.at("w.prmc")
            dve.wait_ge(gate_in, 16 * 7)
            c.link(nc.vector.tensor_scalar(gate_b[:, 1:2], gate_b[:, 0:1], 1 / CAP, None, ALU.mult))
            c.at("w.gb")
            c.at("w.pre")

            def shift(n):
                dve.wait_ge(a["w"], STEP[f"w.col{n}"])
                dt = dtmp[:, :].rearrange("p (i t) -> p i t", i=2)
                c.link(nc.vector.tensor_tensor(dt, raw[:, n % 2, :, 0:256], raw[:, n % 2, :, 1:257], ALU.subtract))
                for i in range(2):
                    c.link(nc.vector.scalar_tensor_tensor(u[:, 2 * n + i, :], dt[:, i, :], mu_c[:, 2 * n + i:2 * n + i + 1],
                                                          raw[:, n % 2, i, 1:257], ALU.mult, ALU.add))

            cm = Counter(dve, v["m"])
            ada_slot(8)
            ada_slot(9)
            for i in range(4):
                dve.wait_ge(a["w"], STEP[f"w.col{7 + i // 2}"])
                cm.link(nc.vector.tensor_scalar(qk[:, i, :], convraw[:, i, 3:259], cw_c[:, 12 + i:13 + i], cb_c[:, i:i + 1],
                                                ALU.mult, ALU.add))
                for j in range(3):
                    cm.link(nc.vector.scalar_tensor_tensor(qk[:, i, :], convraw[:, i, j:j + 256],
                                                           cw_c[:, 4 * j + i:4 * j + i + 1], qk[:, i, :], ALU.mult, ALU.add))
            cm.at("m.conv")
            dve.wait_ge(a["m"], STEP["m.lf"])
            one4 = ones2[0:4, :]
            cm.link(nc.vector.tensor_scalar(mrow[0:4, 0, :], mrow[0:4, 0, :], CAP, None, ALU.mult))
            cm.link(nc.vector.tensor_tensor_scan(mrow[0:4, 2, :], one4, mrow[0:4, 1, :], 0.0, ALU.mult, ALU.add))
            cm.link(nc.vector.tensor_tensor(mrow[0:4, 4, :], mrow[0:4, 0, :], mrow[0:4, 2, :], ALU.add))
            cm.link(nc.vector.tensor_tensor_scan(mrow[0:4, 5, :], one4, mrow[0:4, 4, :], 0.0, ALU.mult, ALU.max))
            cm.link(nc.vector.tensor_tensor(mrow[32:36, 4, :], mrow[0:4, 2, :], mrow[0:4, 5, :], ALU.subtract))
            cm.link(nc.vector.tensor_copy(sel4[:, :, :], ident[0:4, 0:4].unsqueeze(2).to_broadcast([4, 4, P])))
            dve.wait_ge(a["m"], STEP["m.sig"])
            cm.link(nc.vector.tensor_tensor(qk[:, :, :], qk[:, :, :], qsig[:, :, :], ALU.mult))
            cm.at("m.rows")
            ada_slot(10)
            dve.wait_ge(t["m"], STEP["m.bc"])
            cm.link(nc.vector.tensor_copy(mcol[:, :, :], ps[:, 0, 0:128].rearrange("p (a n) -> p a n", a=2)))
            for h in range(4):
                mb = ps[:, 2 + h // 2, (h % 2) * 256:(h % 2) * 256 + 256]
                cm.link(nc.vector.tensor_scalar(mz[:, h, 0:256], mb, mcol[:, 0, h:h + 1], 0.0, ALU.subtract, ALU.max))
                cm.link(nc.vector.tensor_scalar(mz[:, h, 256:384], mb[:, 128:256], mcol[:, 1, h:h + 1], 0.0,
                                                ALU.subtract, ALU.max))
            cm.at("m.z")
            ada_slot(11)
            ada_slot(12)
            dve.wait_ge(a["m"], STEP["m.exp"])
            dve.wait_ge(g["c"], STEP["c.masks"])
            cmask = m_causal.unsqueeze(1).to_broadcast([P, 4, P])
            cm.link(nc.vector.tensor_tensor(mz[:, :, 0:128], mz[:, :, 0:128], cmask, ALU.mult))
            cm.link(nc.vector.tensor_tensor(mz[:, :, 256:384], mz[:, :, 256:384], cmask, ALU.mult))
            for h in range(4):
                dve.wait_ge(t["m"], STEP[f"m.sc{h // 2}"])
                cm.link(nc.vector.scalar_tensor_tensor(mz[:, h, :], ps[:, sc_bank[h], 0:384], 0.125, mz[:, h, :],
                                                       ALU.mult, ALU.mult))
            cm.at("m.pt")
            ada_slot(13)
            ada_slot(14)
            shift(0)
            dve.wait_ge(t["m"], STEP["m.num"])
            den, rec = small[:, 16:24], small[:, 24:32]
            cm.link(nc.vector.tensor_copy(den, ps[:, 2, 0:8]))
            cm.link(nc.vector.scalar_tensor_tensor(den, den, -1.0, den, ALU.mult, ALU.max))
            cm.link(nc.vector.tensor_tensor(den, den, mem[:, :, :].rearrange("p a h -> p (a h)"), ALU.max))
            cm.link(nc.vector.reciprocal(rec, den))
            ym = ytok[:, :, 512:1024]
            for tt in range(TT):
                cm.link(nc.vector.tensor_tensor(ym[:, tt, :].rearrange("p (h n) -> p h n", h=4),
                                                ps[:, tt, :].rearrange("p (h n) -> p h n", h=4),
                                                rec[:, 4 * tt:4 * tt + 4].unsqueeze(2).to_broadcast([P, 4, P]), ALU.mult))
            dve.wait_ge(bias_out, 16)
            cm.link(nc.vector.tensor_tensor(msq[:, :, :], ym, ym, ALU.mult))
            for tt in range(TT):
                cm.link(nc.vector.tensor_reduce(small[:, 8 + 4 * tt:12 + 4 * tt], msq[:, tt, :].rearrange("p (h n) -> p h n", h=4),
                                                AX_X, ALU.add))
            cm.link(nc.vector.tensor_scalar(small[:, 8:16], small[:, 8:16], 1 / P, EPS, ALU.mult, ALU.add))
            cm.at("m.ss")
            ada_slot(15)
            dve.wait_ge(g["m"], STEP["m.rs"])
            for tt in range(TT):
                yv = ym[:, tt, :].rearrange("p (h n) -> p h n", h=4)
                cm.link(nc.vector.tensor_tensor(yv, yv, small[:, 8 + 4 * tt:12 + 4 * tt].unsqueeze(2).to_broadcast([P, 4, P]),
                                                ALU.mult))
            cm.at("m.s")
            for n in range(1, 7):
                shift(n)
                ada_slot(15 + n)
            c.at("w.shift")
            cr = Counter(dve, v["r"])
            cr.link(nc.vector.tensor_tensor(kx[:, :, :], u[:, 4:8, :], kk_c.unsqueeze(2).to_broadcast([P, 4, SEQ]), ALU.mult))
            cr.link(nc.vector.tensor_tensor(sq[:, :, :], kx[:, :, :], kx[:, :, :], ALU.mult))
            cr.at("r.sq")
            dve.wait_ge(t_ada, 5)
            dve.wait_ge(par_in, 16 * 2)
            gt = gate1[:, 0, :].rearrange("p (b n) -> p b n", b=2)
            c.link(nc.vector.tensor_tensor(gt, gt, ps[:, 1:3, :], ALU.add))
            c.link(nc.vector.tensor_tensor(mod_c[:, 2, :], ps[:, 3, 0:8], adab_c[:, 3, :], ALU.add))
            c.link(nc.vector.tensor_tensor(mod_c[:, 3, :], ps[:, 3, 8:16], adab_c[:, 4, :], ALU.add))
            c.link(nc.vector.scalar_tensor_tensor(mod_c[:, 3, :], mod_c[:, 3, :], 1.0, norm_c[:, 1, :], ALU.add, ALU.mult))
            c.at("w.mod")

            c = cr
            r_, k_ = u[:, 0:4, :], u[:, 4:8, :]

            def col4(x, n=SEQ):
                return x.unsqueeze(2).to_broadcast([P, 4, n])

            for n in (22, 23):
                ada_slot(n)
            dve.wait_ge(a["r"], STEP["r.sqrt"])
            c.link(nc.vector.tensor_scalar(kn[:, :, :], kn[:, :, :], 1e-12, None, ALU.max))
            c.link(nc.vector.reciprocal(kn[:, :, :], kn[:, :, :]))
            dve.wait_ge(a["r"], STEP["r.sig"])
            c.link(nc.vector.scalar_tensor_tensor(kmod[:, :, :], av[:, :, :], 1.0, col4(ka_c), ALU.subtract, ALU.mult))
            c.link(nc.vector.scalar_tensor_tensor(kmod[:, :, :], kmod[:, :, :], 1.0, k_, ALU.add, ALU.mult))
            c.at("r.kmod")
            for i in range(4):
                c.link(nc.vector.tensor_tensor_scan(cum[:, i, :], reset[:, :], lw[:, i, :], 0.0, ALU.mult, ALU.add))
            c.at("r.scan")
            c.link(nc.vector.tensor_tensor(kx[:, :, :], kx[:, :, :], kn[:, :, :], ALU.mult))
            c.link(nc.vector.tensor_tensor(sq[:, :, :], kx[:, :, :], av[:, :, :], ALU.mult))
            dve.wait_ge(a["r"], STEP["r.exp"])
            aq, kxc, pcc = chunk(ar[:, :, 0, :]), chunk(kx), chunk(pcum)
            c.link(nc.vector.tensor_copy(pend[:, :, :], pcc[:, :, :, CH - 1]))
            c.at("r.pend")
            c.link(nc.vector.tensor_tensor(bh[:, :, :], sq[:, :, :], pinv[:, :, :], ALU.mult))
            c.at("r.bh")
            c.link(nc.vector.tensor_tensor(chunk(bend), chunk(bh), to_end(), ALU.mult))
            c.at("r.bend")
            c.link(nc.vector.tensor_tensor(aq[:, :, :, 1:CH], kxc[:, :, :, 1:CH], pcc[:, :, :, 0:CH - 1], ALU.mult))
            c.link(nc.vector.tensor_copy(aq[:, :, :, 0:1], kxc[:, :, :, 0:1]))
            c.link(nc.vector.tensor_tensor(ar[:, :, 1, :], r_, pcum[:, :, :], ALU.mult))
            c.at("r.q")
            dve.wait_ge(t["r"], STEP["r.bonus"])
            c.link(nc.vector.tensor_copy(bon[:, :, :], ps[:, 3, 0:16].rearrange("p (a h) -> p a h", a=2)))
            c.at("r.bon")

            c = Counter(dve, v["i"])

            def m4(m):
                return m.unsqueeze(1).to_broadcast([P, 4, P])

            dve.wait_ge(a["r"], STEP["r.tok"])
            for step, (kind, src, arg, dst) in enumerate(INV_V):
                for gi in range(4):
                    if src is not None:
                        dve.wait_ge(t["i"], 4 * src + gi + 1)
                    if kind == "mask":
                        ins = nc.vector.tensor_tensor(dst[:, gi], bank4(src, gi), m4(arg), ALU.mult)
                    elif kind == "maskF":
                        if step == V_A16:
                            dve.wait_ge(a["i"], gi + 1)
                        ins = nc.vector.tensor_tensor(dst[:, gi], iF[:, gi], m4(arg), ALU.mult)
                    elif kind == "ident":
                        ins = nc.vector.tensor_tensor(dst[:, gi], iB[:, gi], m4(ident[:, :]), ALU.add)
                    elif kind == "lakv":
                        ins = nc.vector.tensor_copy(lakv[:, gi // 2, 256 * (gi % 2):256 * (gi % 2) + 256],
                                                    ps[:, bank_of(src, gi), 0:256])
                    else:
                        ins = nc.vector.tensor_tensor(dst[:, gi], dst[:, gi], bank4(src, gi), ALU.add)
                    c.link(ins)
            c.at("i.done")

            c = Counter(dve, v["s"])
            dve.wait_ge(g["r"], STEP["r.zero"])

            def h8(x):
                return x.rearrange("p a (h n) -> p (a h) n", h=8)

            p = Counter(dve, v["p"])

            def pieces(ch):
                def row(i):
                    return rowp[:, i, :].unsqueeze(1).to_broadcast([P, TT, 512])

                if ch == 0:
                    dve.wait_ge(row_in, 48)
                    p.link(nc.vector.tensor_tensor(ym, ym, row(2), ALU.mult))
                    p.link(nc.vector.tensor_tensor(ym, ym, om[:, :, :], ALU.mult))
                elif ch == 1:
                    p.link(nc.vector.tensor_tensor(h8(yterm), h8(vtok), bon[:, :, :].rearrange("p a h -> p (a h)").unsqueeze(2)
                                                   .to_broadcast([P, 16, 64]), ALU.mult))
                    p.link(nc.vector.tensor_tensor(yterm[:, :, :], yterm[:, :, :], row(1), ALU.add))
                elif ch == 2:
                    p.link(nc.vector.tensor_tensor(yterm[:, :, :], yterm[:, :, :], gtok[:, :, :], ALU.mult))
                    p.link(nc.vector.tensor_tensor(gtok[:, :, :], gtok[:, :, :], row(0), ALU.mult))

            for ch in range(NC):
                r0, tt = CH * (ch % 2), ch // 2
                rr, lk = rbuf[r0:r0 + CH, tt, :], lakv[r0:r0 + CH, tt, :]
                if ch == 0:
                    c.link(nc.vector.tensor_scalar(rr, lk, -1.0, None, ALU.mult))
                else:
                    dve.wait_ge(t_as, ch)
                    c.link(nc.vector.scalar_tensor_tensor(rr, ps[r0:r0 + CH, 0, :], -1.0, lk, ALU.mult, ALU.subtract))
                assert c.n == 5 * ch + 1
                if ch < NC - 1:
                    pieces(ch)
                    for hh in range(2):
                        q = slice(64 * hh, 64 * hh + 64)
                        c.link(nc.vector.tensor_tensor(state[q, ch + 1, :, q], state[q, ch, :, q],
                                                       pend[q, :, ch].unsqueeze(2).to_broadcast([64, 4, 64]), ALU.mult))
                    dve.wait_ge(t_ds, ch + 1)
                    for hh in range(2):
                        q = slice(64 * hh, 64 * hh + 64)
                        dl = ps[q, 2, :].rearrange("p (i n) -> p i n", i=4)[:, :, q]
                        c.link(nc.vector.tensor_tensor(state[q, ch + 1, :, q], state[q, ch + 1, :, q], dl, ALU.add))
            c = Counter(dve, v["y"])
            sm = small[:, 32:48]
            for tt in range(TT):
                dve.wait_ge(t_y, tt + 1)
                heads = lambda x: x.rearrange("p (h n) -> p h n", h=8)
                s8 = sm[:, 8 * tt:8 * tt + 8]
                yr = ytok[:, tt, 0:512]
                c.link(nc.vector.tensor_reduce(s8, heads(ps[:, 4 + tt, :]), AX_X, ALU.add))
                c.link(nc.vector.tensor_scalar(s8, s8, 1 / 64, None, ALU.mult))
                c.link(nc.vector.tensor_tensor(heads(yr), heads(ps[:, 4 + tt, :]), s8.unsqueeze(2).to_broadcast([P, 8, 64]),
                                               ALU.subtract))
                c.at(f"y.sub{tt}")
                c.link(nc.vector.tensor_tensor(ysq[:, tt, :], yr, yr, ALU.mult))
                c.link(nc.vector.tensor_reduce(s8, heads(ysq[:, tt, :]), AX_X, ALU.add))
                c.link(nc.vector.tensor_scalar(s8, s8, 1 / 64, GN_EPS, ALU.mult, ALU.add))
                c.at(f"y.var{tt}")
                dve.wait_ge(g["y"], STEP[f"y.rs{tt}"])
                c.link(nc.vector.tensor_tensor(heads(yr), heads(yr), s8.unsqueeze(2).to_broadcast([P, 8, 64]), ALU.mult))
                c.link(nc.vector.tensor_tensor(yr, yr, gtok[:, tt, :], ALU.mult))
                c.link(nc.vector.tensor_tensor(yr, yr, yterm[:, tt, :], ALU.add))
                c.at(f"y.done{tt}")
            c = Counter(dve, v["o"])
            dve.wait_ge(par_in, 16 * 2)
            dve.wait_ge(t_ada, 6)
            gt = gate1[:, 1, :].rearrange("p (b n) -> p b n", b=2)
            c.link(nc.vector.tensor_tensor(gt, gt, ps[:, 6:8, :], ALU.add))
            c.at("o.gate")
            nc.vector.memset(dtmp[:, :], 0.0).then_inc(v_ada2, CREDIT)
            dve.wait_ge(v_ada2, CREDIT)
            nc.vector.memset(dtmp[:, :], 0.0).then_inc(v_mod, CREDIT)
            dve.wait_ge(v_mod, CREDIT)
            v_residual_norm(dve, c, "o", gate1[:, 0, :], 4, lambda j: dve.wait_ge(t_out, j + 1),
                            "q", mod_c[:, 2, :], mod_c[:, 3, :])
            dve.wait_ge(t["e"], STEP["e.rt"])
            v_hT_lo(dve, "q", hT_hi, 0)
            v_up_lo(dve, 0, 0)

            c = Counter(dve, v["e"])
            R = lambda i, n: rt[:, i, :, 0:n]
            b8 = lambda x, n: x.to_broadcast([P, TT, n])
            rv = lambda n: rev[:, 8 - n:8].unsqueeze(1).to_broadcast([P, TT, n])
            dve.wait_ge(t["e"], STEP["e.rt"])
            dve.wait_ge(rt_in, 64)
            c.link(nc.vector.tensor_tensor(lg[:, :, :], ps[:, 7, 0:128].rearrange("p (a n) -> p a n", a=2)[:, :, 0:36],
                                           b_rt.unsqueeze(1).to_broadcast([P, TT, 36]), ALU.add))
            gl = lg[:, :, 32:36]
            c.link(nc.vector.tensor_reduce(R(0, 1), gl, AX_X, ALU.max))
            c.link(nc.vector.tensor_tensor(R(1, 4), gl, b8(R(0, 1), 4), ALU.subtract))
            c.at("e.g")

            def first_max(vals, top, n, onehot, key):
                c.link(nc.vector.tensor_tensor(onehot, vals, b8(top, n), ALU.is_equal))
                c.link(nc.vector.tensor_tensor(onehot, onehot, rv(n), ALU.mult))
                c.link(nc.vector.tensor_reduce(key, onehot, AX_X, ALU.max))
                c.link(nc.vector.tensor_tensor(onehot, rv(n), b8(key, n), ALU.is_equal))

            first_max(gl, R(0, 1), 4, R(2, 4), R(3, 1))
            prod = rt[:, 10:11].rearrange("p o a n -> p (o a) n")
            c.link(nc.vector.tensor_tensor(prod.rearrange("p a (g e) -> p a g e", g=NG),
                                           lg[:, :, 0:32].rearrange("p a (g e) -> p a g e", g=NG),
                                           R(2, 4).unsqueeze(3).to_broadcast([P, TT, NG, EG]), ALU.mult))
            sel = R(4, 8)
            c.link(nc.vector.tensor_reduce(sel, prod.rearrange("p a (g e) -> p a e g", g=NG), AX_X, ALU.add))
            c.link(nc.vector.tensor_reduce(R(5, 1), sel, AX_X, ALU.max))
            first_max(sel, R(5, 1), 8, R(6, 8), R(3, 1))
            c.link(nc.vector.scalar_tensor_tensor(sel, R(6, 8), -3e38, sel, ALU.mult, ALU.add))
            c.link(nc.vector.tensor_reduce(R(7, 1), sel, AX_X, ALU.max))
            first_max(sel, R(7, 1), 8, R(8, 8), R(3, 1))
            c.link(nc.vector.tensor_tensor(R(9, 1), R(7, 1), R(5, 1), ALU.subtract))
            c.at("e.d")
            dve.wait_ge(a["e"], STEP["e.expg"])
            c.link(nc.vector.tensor_reduce(R(0, 1), R(1, 4), AX_X, ALU.add))
            dve.wait_ge(a["e"], STEP["e.expd"])
            c.link(nc.vector.tensor_scalar(R(11, 1), R(9, 1), 1.0, None, ALU.add))
            c.link(nc.vector.tensor_tensor(R(11, 1), R(11, 1), R(0, 1), ALU.mult))
            c.link(nc.vector.reciprocal(R(11, 1), R(11, 1)))
            c.link(nc.vector.tensor_tensor(R(9, 1), R(9, 1), R(11, 1), ALU.mult))
            c.link(nc.vector.tensor_tensor(R(6, 8), R(6, 8), b8(R(11, 1), 8), ALU.mult))
            c.link(nc.vector.tensor_tensor(R(8, 8), R(8, 8), b8(R(9, 1), 8), ALU.mult))
            c.link(nc.vector.tensor_tensor(R(6, 8), R(6, 8), R(8, 8), ALU.add))
            c.link(nc.vector.tensor_tensor(cw[:, :, :].rearrange("p a (g e) -> p a g e", g=NG),
                                           R(2, 4).unsqueeze(3).to_broadcast([P, TT, NG, EG]),
                                           R(6, 8).unsqueeze(2).to_broadcast([P, TT, NG, EG]), ALU.mult))
            c.at("e.cw")
            def products(m, e, tt, first=False):
                n = 2 * (E_BODY * m + e) + tt + 1
                dve.wait_ge(a_silu, n)
                if not first:
                    dve.wait_ge(t_tr, n - 2)
                nc.vector.scalar_tensor_tensor(eact[:, tt, :], ps[:, 4 + tt, FE:2 * FE],
                                               cw[:, tt, bass.ds(m * E_BODY + e, 1)], gact[:, tt, :],
                                               ALU.mult, ALU.mult).then_inc(v_eact, 1)

            def products_t(m, e, tt, first=False):
                n = 2 * (E_BODY * m + e) + tt + 1
                dve.wait_ge(t_tr, n)
                if not first:
                    dve.wait_ge(t_dn, n - 2)
                src = ps[:, 6, FE * tt:FE * tt + FE].rearrange("p (f n) -> p f n", f=2)
                nc.vector.tensor_copy(eact_hi[:, tt], src).then_inc(v_eact_t, 1)
                dve.wait_ge(v_eact_t, 2 * n - 1)
                trailing(nc.vector, eact_lo[:, tt], src, eact_hi[:, tt]).then_inc(v_eact_t, 1)

            def modulation(m, k):
                vec, q = k // 4, k % 4
                acc = macc[:, vec, :]
                dve.wait_ge(ada2_in[k % 2], 16 * 6 * m + 16 * (k // 2 + 1))
                for r in range(2):
                    w = ring[:, 6 + k % 2, D * r:D * r + D]
                    cc = ccol[:, 8 + 2 * q + r:9 + 2 * q + r]
                    if 2 * q + r == 0:
                        ins = nc.vector.tensor_scalar(acc, w, cc, None, ALU.mult)
                    else:
                        ins = nc.vector.scalar_tensor_tensor(acc, w, cc, acc, ALU.mult, ALU.add)
                    ins.then_inc(v_ada2, 1)
                    dve.wait_ge(v_ada2, 24 * m + CREDIT + 2 * k + r + 1)

            def modulation_row(m, i):
                dve.wait_ge(t_mod, 6 * m + i + 1)
                if i < 4:
                    half = i % 2
                    own = ident[:, 64 * half:64 * half + 64].unsqueeze(2).to_broadcast([P, 64, 8])
                    picked = dtmp[:, :].rearrange("p (q t) -> p q t", t=8)
                    dve.wait_ge(v_mod, 6 * m + i + CREDIT)
                    nc.vector.tensor_tensor(picked, ps[:, 7, :].rearrange("p (q t) -> p q t", t=8), own, ALU.mult
                                            ).then_inc(v_cols, 1)
                    dve.wait_ge(v_cols, 5 * m + i + 1)
                    nc.vector.tensor_reduce(halves[:, i, :], picked.rearrange("p q t -> p t q"), AX_X, ALU.add
                                            ).then_inc(v_mod, 1)
                    if i == 3:
                        h4 = halves[:, :, :].rearrange("p (v h) t -> p v h t", h=2)
                        dve.wait_ge(v_mod, 6 * m + 4 + CREDIT)
                        nc.vector.tensor_tensor(mod2[:, bass.ds(m, 1), 0:16].rearrange("p o (v t) -> p (o v) t", v=2),
                                                h4[:, :, 0, :], h4[:, :, 1, :], ALU.add).then_inc(v_cols, 1)
                else:
                    h = i - 4
                    gv = gate2[:, bass.ds(m, 1), 512 * h:512 * h + 512].rearrange("p o n -> p (o n)")
                    nc.vector.tensor_tensor(gv, gv, ps[:, 7, :], ALU.add).then_inc(v_mod, 1)

            def expert(m, j, first=False, last=False):
                if 1 <= j <= 6:
                    modulation(m, 2 * j - 2)
                if not first:
                    products_t(m, j - 1, 1, first=isinstance(m, int) and m == 0 and j == 1)
                products(m, j, 0, first=first)
                if j in (7, 8):
                    modulation_row(m, {7: 0, 8: 4}[j])
                if not last:
                    v_up_lo(dve, m, j + 1)
                v_down_lo(dve, m, j)
                if j == 7:
                    modulation_row(m, 1)
                if j == 8:
                    modulation_row(m, 5)
                if 1 <= j <= 6:
                    modulation(m, 2 * j - 1)
                products_t(m, j, 0, first=first)
                if j == 7:
                    modulation_row(m, 2)
                products(m, j, 1, first=first)
                if j == 7:
                    modulation_row(m, 3)

            expert(0, 0, first=True)
            with dve.Fori(0, LAST_PASS) as m:
                for j in range(1, E_BODY + 1):
                    expert(m, j)
            for j in range(1, E_BODY):
                expert(LAST_PASS, j, last=j == E_BODY - 1)
            products_t(LAST_PASS, E_BODY - 1, 1)
            modulation_row(LAST_PASS, 4)
            modulation_row(LAST_PASS, 5)
            c = Counter(dve, v["f"])
            for m in range(4):
                if m != 2:
                    c.link(nc.vector.tensor_tensor(mod2[:, m, 0:16], mod2[:, m, 0:16],
                                                   adab2_c[:, 2 * m:2 * m + 2, :].rearrange("p v t -> p (v t)"), ALU.add))
                    c.link(nc.vector.scalar_tensor_tensor(mod2[:, m, 8:16], mod2[:, m, 8:16], 1.0, norm2_c[:, m, :],
                                                          ALU.add, ALU.mult))
            c.at("f.mod")
            def final(tt):
                dve.wait_ge(g["f"], STEP[f"f.rstd{tt}"])
                c.link(nc.vector.scalar_tensor_tensor(x_sb[:, tt, :], x_sb[:, tt, :], small[:, tt:tt + 1], nrm_b,
                                                      ALU.mult, ALU.mult))
                c.at(f"f.n{tt}")

            cn = Counter(dve, v["bn"])
            experts_of = lambda j: dve.wait_ge(t_dn, 2 * NE - 1 + j // 2)
            v_residual(dve, c, "f", gate1[:, 1, :], 0, 0, experts_of)
            v_mean(dve, c, "f", 0)
            dve.wait_ge(nrm_in, 16)
            final(0)
            v_residual(dve, c, "f", gate1[:, 1, :], 0, 1, experts_of)
            v_mean(dve, cn, "bn", 0)
            v_mean(dve, c, "f", 1)
            v_xn(dve, cn, "bn", 0)
            final(1)
            v_mean(dve, cn, "bn", 1)
            v_xn(dve, cn, "bn", 1)
            v_norm_out(dve, cn, "bn", *mod_of[0])
            c = Counter(dve, v["bg"])
            dve.wait_ge(a["bg"], STEP["bg.ln"])
            c.link(nc.vector.tensor_scalar(zb[:, :, :], zb[:, :, :], -1.0, 0.0, ALU.mult, ALU.max))
            c.link(nc.vector.tensor_tensor(zb[:, :, :], zb[:, :, :], az[:, :, :], ALU.add))
            for i in range(2):
                c.link(nc.vector.tensor_tensor_scan(nb2[:, i, :], reset[:, :], zb[:, i, :], 0.0, ALU.mult, ALU.add))
            c.at("bg.scan")
            dve.wait_ge(a["bg"], STEP["bg.exp"])
            dve.wait_ge(a["bp"], 2)
            c.link(nc.vector.scalar_tensor_tensor(qg[:, :, :], qg[:, :, :], 0.125, eb[:, :, :], ALU.mult, ALU.mult))
            c.link(nc.vector.tensor_tensor(kg[:, :, :], kg[:, :, :], enb[:, :, :], ALU.mult))
            c.at("bg.kt")
            c.link(nc.vector.tensor_copy(gdec[:, :, :], chunk2(eb)[:, :, :, CH - 1]))
            c.link(nc.vector.tensor_tensor(chunk2(kend2), chunk2(kg), gdec[:, :, :].unsqueeze(3).to_broadcast([P, 2, NC, CH]),
                                           ALU.mult))
            c.at("bg.kend")
            dve.wait_ge(g["bp"], STEP["bp.len"])
            for tt in range(TT):
                dve.wait_ge(t["bg"], STEP["bg.at0"] + tt)
                c.link(nc.vector.tensor_tensor(at[:, tt], ps[:, 2 + tt, :].rearrange("p (h t) -> p h t", h=4),
                                               m_rb.unsqueeze(1).to_broadcast([P, 4, P]), ALU.mult))
            c.at("bg.at")
            dve.wait_ge(t["bg"], STEP["bg.ds"])
            dve.wait_ge(g["bp"], STEP["bp.zero"])
            for ch in range(NC - 1):
                for hh in range(2):
                    q, e = slice(64 * hh, 64 * hh + 64), slice(P * hh, P * hh + P)
                    st, nx = sg_state[q, ch, :, e], sg_state[q, ch + 1, :, e]
                    c.link(nc.vector.tensor_tensor(nx, st, gdec[q, :, ch].unsqueeze(2).to_broadcast([64, 2, P]), ALU.mult))
                    c.link(nc.vector.tensor_tensor(nx, nx, ps[q, ds_bank[ch], :].rearrange("p (i n) -> p i n", i=2)[:, :, e], ALU.add))
            c.at("bg.state")
            cp = Counter(dve, v["bp"])
            for i in (4, 5):
                dve.wait_ge(a["bp"], i + 1)
                gs = ggs[:, :, 256 * (i - 4):256 * (i - 4) + 256]
                cp.link(nc.vector.tensor_tensor(gs, gs, bin_bank(i).rearrange("p (a n) -> p a n", a=2), ALU.mult))
            dve.wait_ge(t["bg"], STEP["bg.o"])
            og = y2[:, :, 0:512]
            c.link(nc.vector.tensor_copy(og, ps[:, 0:2, :]))
            c.link(nc.vector.tensor_tensor(gsq[:, :, :], og, og, ALU.mult))
            c.link(nc.vector.tensor_reduce(small[:, 8:16], gsq[:, :, :].rearrange("p a (h n) -> p (a h) n", h=4), AX_X, ALU.add))
            c.link(nc.vector.tensor_scalar(small[:, 8:16], small[:, 8:16], 1 / P, EPS, ALU.mult, ALU.add))
            c.at("bg.ss")
            dve.wait_ge(g["bg"], STEP["bg.rs"])
            for tt in range(TT):
                ov = og[:, tt, :].rearrange("p (h n) -> p h n", h=4)
                c.link(nc.vector.tensor_tensor(ov, ov, small[:, 8 + 4 * tt:12 + 4 * tt].unsqueeze(2).to_broadcast([P, 4, P]), ALU.mult))
                c.link(nc.vector.tensor_tensor(ov, ov, ggn.unsqueeze(1).to_broadcast([P, 4, P]), ALU.mult))
            c.link(nc.vector.tensor_tensor(og, og, ggs[:, :, :], ALU.mult))
            c.at("bg.y")
            c = Counter(dve, v["bs"])
            mx, es, dn = swm[:, 0:16], swm[:, 16:32], swm[:, 32:48]
            parts = ((0, sc[:, :, 0:P], P), (8, sc[:, :, P:3 * P], 2 * P))

            def under_maximum(o, s_, n):
                c.link(nc.vector.tensor_reduce(mx[:, o:o + 8], s_, AX_X, ALU.max))
                c.link(nc.vector.tensor_tensor(mx[:, o:o + 8], mx[:, o:o + 8], sink_b, ALU.max))
                c.link(nc.vector.tensor_tensor(es[:, o:o + 8], sink_b, mx[:, o:o + 8], ALU.subtract))
                c.link(nc.vector.tensor_tensor(s_, s_, mx[:, o:o + 8].unsqueeze(2).to_broadcast([P, 8, n]), ALU.subtract))

            dve.wait_ge(bias_in, 16)
            for j in range(6):
                dve.wait_ge(t["bs"], STEP["bs.s0"] + j)
                if j < 2:
                    c.link(nc.vector.scalar_tensor_tensor(sc[:, 4 * j:4 * j + 4, 0:P], ps[:, bs_bank[j], :].rearrange("p (h k) -> p h k", h=4),
                                                          0.125, bias8[:, 4 * j:4 * j + 4, P:2 * P], ALU.mult, ALU.add))
                    if j == 1:
                        under_maximum(*parts[0])
                        c.at("bs.sub0")
                else:
                    hs = slice(2 * (j - 2), 2 * (j - 2) + 2)
                    c.link(nc.vector.scalar_tensor_tensor(sc[:, hs, P:3 * P], ps[:, bs_bank[j], :].rearrange("p (h k) -> p h k", h=2),
                                                          0.125, bias8[:, hs, :], ALU.mult, ALU.add))
            under_maximum(*parts[1])
            c.at("bs.sub1")
            dve.wait_ge(a["bs"], STEP["bs.exp1"])
            for o, s_, n in parts:
                c.link(nc.vector.tensor_reduce(dn[:, o:o + 8], s_, AX_X, ALU.add))
            c.link(nc.vector.tensor_tensor(dn, dn, es, ALU.add))
            c.link(nc.vector.reciprocal(dn, dn))
            c.at("bs.den")
            dve.wait_ge(a["bs"], STEP["bs.hi3"])
            c.link(trailing(nc.vector, ring_lo[:, 12 % RING, :], ring[:, 12 % RING, :], out_hi[3]))
            for tt in range(TT):
                dve.wait_ge(t["bs"], STEP["bs.o"])
                c.link(nc.vector.tensor_tensor(y2[:, tt, 512:1024].rearrange("p (h n) -> p h n", h=8),
                                               ps[:, tt, :].rearrange("p (h n) -> p h n", h=8),
                                               dn[:, 8 * tt:8 * tt + 8].unsqueeze(2).to_broadcast([P, 8, 64]), ALU.mult))
            c.at("bs.y")
            c = Counter(dve, v["bo"])
            for k in range(0, KT, 2):
                dve.wait_ge(a["bo"], k // 2 + 1)
                c.link(trailing(nc.vector, hT_lo[:, k:k + 2, :], ps[:, k // 2, :].rearrange("p (k t) -> p k t", k=2),
                                gT_hi[:, k:k + 2, :]))
            c.at("bo.lo")
            dve.wait_ge(g["bp"], STEP["bp.len"])
            c.link(nc.vector.reciprocal(pinvc[:, :, :], pinvc[:, :, :]))
            c.at("bo.len")
            v_residual_norm(dve, c, "bo", gate2[:, 0, :], 4, lambda j: dve.wait_ge(t_bout, j + 1), "l0", *mod_of[1])
            v_hT_lo(dve, "l0", gT_hi, 1)
            v_w1_lo(dve, 0, 0, 0)
            v_mlp_loop(dve, 0)
            def mod_pool(c):
                dve.wait_ge(t_cols, 1)
                c.link(nc.vector.tensor_tensor(mod2[:, 2, 16:32], ps[:, 4, 0:16], prm_c[:, 64:80], ALU.add))
                c.link(nc.vector.scalar_tensor_tensor(mod2[:, 2, 24:32], mod2[:, 2, 24:32], 1.0, prm_c[:, 56:64],
                                                      ALU.add, ALU.mult))

            c = Counter(dve, v["l0"], STEP["l0.v"])
            v_residual_norm(dve, c, "l0", gate2[:, 1, :], 0, lambda j: dve.wait_ge(t_fd, 15 + j // 2), "pn", *mod_of[2],
                            mod=mod_pool, out=hp_tok)
            c = Counter(dve, v["pp"])
            dve.wait_ge(a["pn"], STEP["pn.a"])
            dve.wait_ge(g["pp"], STEP["pp.zero"])
            window_sum(c, nc.vector, pa, hp, 4, 8, 1)
            window_sum(c, nc.vector, pb_, pa, 4, 8, 2)
            window_sum(c, nc.vector, pa, pb_, 4, 8, 4)
            window_sum(c, nc.vector, pb_, pa, 6, 8, 8)
            mean_less_input(c, nc.vector, 2, pa)
            mean_less_input(c, nc.vector, 3, pb_)
            dve.wait_ge(g["pp"], STEP["pp.g"])
            less_input(c, nc.vector, 1, pb_[:, 0:2, PAD:])
            c.at("pp.h")
            dve.wait_ge(pool_in, 32)
            c.link(nc.vector.tensor_tensor(gate2[:, 2, :], gate2[:, 2, :], psc_b, ALU.mult))
            v_residual_norm(dve, c, "pp", gate2[:, 2, :], 4, lambda j: dve.wait_ge(t["pp"], j + 1), "l1", *mod_of[3])
            v_hT_lo(dve, "l1", gT_hi, 2)
            v_w1_lo(dve, 1, 0, 0)
            v_mlp_loop(dve, 1)
            c = Counter(dve, v["l1"], STEP["l1.v"])
            cz = Counter(dve, v["z"])
            dve.wait_ge(nrm2_in, 16)
            for tt in range(TT):
                v_residual(dve, c, "l1", gate2[:, 3, :], 0, tt, lambda j: dve.wait_ge(t_fd, 31 + j // 2))
                v_mean(dve, cz, "z", tt)
                dve.wait_ge(g["z"], STEP[f"z.rstd{tt}"])
                cz.link(nc.vector.scalar_tensor_tensor(x_sb[:, tt, :], x_sb[:, tt, :], small[:, tt:tt + 1], gate2[:, 0, :],
                                                       ALU.mult, ALU.mult))
                cz.at(f"z.out{tt}")

        @block.tensor
        def _(pe):
            pe.wait_ge(hot_in, 32)
            nc.tensor.matmul(ps[0:SWA_H, 4, 0:384], rel_sb[0:33, :], hots[0:33, :], start=True, stop=True).then_inc(t_bias, 1)
            pe.wait_ge(g["c"], STEP["c.ident"])
            pe.wait_ge(v_ada, 8)
            t_columns(macc[:, 0, :], ps[:, 6, :]).then_inc(t_ada, 1)
            t_norm(pe, "n")
            pe.wait_ge(v_ada, 16)
            t_columns(macc[:, 1, :], ps[:, 7, :]).then_inc(t_ada, 1)

            c = Counter(pe, t["w"])
            pe.wait_ge(prm_in, 16 * 11)
            pe.wait_ge(a["n"], STEP["n.a"])
            pe.wait_ge(v["n"], STEP["n.v"])
            c.mark(nc.tensor.transpose(ps[:, 0, 256:336], prm[0:80, :], ident[0:80, 0:80]))
            c.at("w.prm")
            def columns(n):
                i = win_order.index(n)
                loaded(pe, ("win", n))
                if i >= 2:
                    pe.wait_ge(a["w"], STEP[f"w.col{win_order[i - 2]}"])
                w = slot(("win", n)).rearrange("p (t n) -> p t n", t=8)
                for j in range(2):
                    o = ps[:, 6 + i % 2, 256 * j:256 * j + 256]
                    for k in range(KT):
                        if n < 9:
                            ins = nc.tensor.matmul(o, w[:, k, P * j:P * j + P], hT[:, k, :], start=k == 0, stop=k == KT - 1)
                        else:
                            ins = nc.tensor.matmul(o, hT[:, k, P * j:P * j + P], w[:, k, :], start=k == 0, stop=k == KT - 1)
                ins.then_inc(t_win, 1)

            def scores(h):
                q = slice(64 * (h % 2), 64 * (h % 2) + 64)
                nc.tensor.matmul(ps[:, sc_bank[h], 0:256], qk[q, 2 + h // 2, 0:P], qk[q, h // 2, :], start=True, stop=True)
                return nc.tensor.matmul(ps[:, sc_bank[h], 256:384], qk[q, 2 + h // 2, P:2 * P], qk[q, h // 2, P:2 * P],
                                        start=True, stop=True)

            for n in (7, 8):
                columns(n)
            pe.wait_ge(gate_in, 16 * 7)
            pe.wait_ge(v["w"], STEP["w.prmc"])
            for k in range(KT):
                ins = nc.tensor.matmul(ps[0:36, 0, 0:256], w_if[:, k, :], hT[:, k, :], start=k == 0, stop=k == KT - 1)
            c.mark(ins)
            c.at("w.if")

            for n in (9, 10):
                columns(n)
            m = Counter(pe, t["m"])
            pe.wait_ge(v["m"], STEP["m.rows"])
            for tt in range(TT):
                nc.tensor.transpose(ps[:, 0, 64 * tt:64 * tt + 64], mrow[:, 4, P * tt:P * tt + P], ident[0:64, 0:64])
            for h in range(4):
                ins = nc.tensor.matmul(ps[:, 2 + h // 2, (h % 2) * 256:(h % 2) * 256 + 256], sel4[:, h, :], mrow[0:4, 5, :],
                                       start=True, stop=True)
            m.mark(ins)
            m.at("m.bc")
            scores(0)
            m.mark(scores(1))
            m.at("m.sc0")
            columns(11)
            pe.wait_ge(v["m"], STEP["m.z"])
            scores(2)
            m.mark(scores(3))
            m.at("m.sc1")
            columns(12)
            columns(0)
            pe.wait_ge(v["m"], STEP["m.pt"])
            for tt in range(TT):
                for h in range(4):
                    parts = [(0, 0)] if tt == 0 else [(0, 128), (1, 256)]
                    for i, (s_, o) in enumerate(parts):
                        nc.tensor.matmul(ps[:, tt, P * h:P * h + P], mz[:, h, o:o + P], vm[:, s_, P * h:P * h + P],
                                         start=i == 0, stop=i == len(parts) - 1)
                    for i, (s_, o) in enumerate(parts):
                        ins = nc.tensor.matmul(ps[:, 2, 4 * tt + h:4 * tt + h + 1], mz[:, h, o:o + P], ones[:, 0:1],
                                               start=i == 0, stop=i == len(parts) - 1)
            m.mark(ins)
            m.at("m.num")
            for n in range(1, 6):
                columns(n)
            pe.wait_ge(v["m"], STEP["m.ss"])
            for vec in range(2, 5):
                pe.wait_ge(v_ada, 8 * (vec + 1))
                if vec == 2:
                    for j in range(2):
                        ins = nc.tensor.matmul(ps[:, 1 + j, :], ones[:, :], macc[:, 2, 512 * j:512 * j + 512],
                                               start=True, stop=True)
                else:
                    ins = t_columns(macc[:, vec % 3, :], ps[:, 3, 8 * (vec - 3):8 * (vec - 3) + 8])
                ins.then_inc(t_ada, 1)
            columns(6)

            c = Counter(pe, t["r"])
            pe.wait_ge(a["r"], STEP["r.u"])
            for tt in range(TT):
                nc.tensor.matmul(ps[:, 4 + tt, :], u[:, 13, P * tt:P * tt + P], gup[:, :], start=True, stop=True)
            pe.wait_ge(v["r"], STEP["r.sq"])
            for i in range(4):
                ins = nc.tensor.matmul(ps[:, 6 + i // 2, (i % 2) * 256:(i % 2) * 256 + 256], headblk[:, :], sq[:, i, :],
                                       start=True, stop=True)
            c.mark(ins)
            c.at("r.n2")
            pe.wait_ge(v["w"], STEP["w.mod"])
            for j in range(2):
                for i in range(4):
                    o = (i % 2) * 256
                    ins = nc.tensor.matmul(ps[:, 2 * j + i // 2, o:o + 256], wup[:, j, P * i:P * i + P], u[:, 12, :],
                                           start=True, stop=True)
            c.mark(ins)
            c.at("r.wa")

            def to_tokens(src, bank, name):
                for tt in range(TT):
                    for i in range(4):
                        ins = nc.tensor.transpose(ps[:, bank + tt, P * i:P * i + P], src[:, i, P * tt:P * tt + P], ident[:, :])
                c.mark(ins)
                c.at(name)

            pe.wait_ge(a["r"], STEP["r.gtok"])
            to_tokens(u[:, 8:12, :], 0, "r.vt")
            pe.wait_ge(g["r"], STEP["r.rkp"])
            for tt in range(TT):
                for i in range(4):
                    ins = nc.tensor.matmul(ps[:, 3, 8 * tt + 2 * i:8 * tt + 2 * i + 2], rkp[:, i, P * tt:P * tt + P],
                                           headsel[:, :], start=True, stop=True)
            c.mark(ins)
            c.at("r.bonus")
            pe.wait_ge(v["r"], STEP["r.bend"])
            to_tokens(bend, 4, "r.bt")
            pe.wait_ge(g["r"], STEP["r.kend"])
            to_tokens(kend, 6, "r.kt")

            c = Counter(pe, t["i"])
            pe.wait_ge(a["r"], STEP["r.pad"])
            pe.wait_ge(v["r"], STEP["r.bon"])
            for step, (kind, lhs, rhs, need_a, need_v, free) in enumerate(INV_T):
                if step == 1:
                    pe.wait_ge(a["r"], STEP["r.tok"])
                for gi in range(4):
                    tt, hf = gi // 2, gi % 2
                    if need_a is not None:
                        pe.wait_ge(a["i"], 4 * need_a + gi + 1)
                    if need_v is not None:
                        pe.wait_ge(v["i"], 4 * need_v + gi + 1)
                    if free is not None:
                        pe.wait_ge({"a": a, "v": v}[free[0]]["i"], 4 * free[1] + gi + 1)
                    tok = slice(P * tt, P * tt + P)
                    for hh in range(4):
                        h = 4 * hf + hh
                        o = bank4(step, gi)[:, hh]
                        if kind == "F":
                            ins = nc.tensor.matmul(o, ar[:, h // 2, 0, tok], bhz[:, h, tok], start=True, stop=True)
                        elif kind == "G":
                            ins = nc.tensor.matmul(o, lhs[:, h, tok], ar[:, h // 2, rhs, tok], start=True, stop=True)
                        elif kind == "T":
                            ins = nc.tensor.transpose(o, lhs[:, gi, hh], ident[:, :])
                        elif kind == "V":
                            ins = nc.tensor.matmul(ps[:, bank_of(step, gi), 64 * hh:64 * hh + 64], lhs[:, gi, hh],
                                                   vtok[:, tt, 64 * h:64 * h + 64], start=True, stop=True)
                        else:
                            ins = nc.tensor.matmul(o, lhs[:, gi, hh], rhs[:, gi, hh], start=True, stop=True)
                    c.mark(ins)

            def mixer_out(tt):
                for i in range(4):
                    cols = slice(P * i, P * i + P)
                    for hf in range(2):
                        ch = 2 * tt + hf
                        nc.tensor.matmul(ps[CH * hf:CH * hf + CH, 4 + tt, cols], ar[:, i, 1, CH * ch:CH * ch + CH],
                                         state[:, ch, i, :], start=True, stop=False, skip_group_check=True)
                    for h in (2 * i, 2 * i + 1):
                        hc = slice(64 * h, 64 * h + 64)
                        nc.tensor.matmul(ps[:, 4 + tt, hc], grb[:, 2 * tt + h // 4, h % 4, :], ubuf[:, tt, hc],
                                         start=False, stop=False, skip_group_check=True)
                        ins = nc.tensor.matmul(ps[:, 4 + tt, hc], grk[:, 2 * tt + h // 4, h % 4, :], vtok[:, tt, hc],
                                               start=False, stop=True, skip_group_check=True)
                ins.then_inc(t_y, 1)

            pe.wait_ge(v["i"], STEP["i.done"])
            pe.wait_ge(g["r"], STEP["r.zero"])
            for ch in range(NC):
                r0, tt = CH * (ch % 2), ch // 2
                rows, toks = slice(r0, r0 + CH), slice(CH * ch, CH * ch + CH)
                if ch == NC - 1:
                    mixer_out(0)
                if ch:
                    pe.wait_ge(v["s"], 5 * ch)
                    for i in range(4):
                        ins = nc.tensor.matmul(ps[rows, 0, P * i:P * i + P], ar[:, i, 0, toks], state[:, ch, i, :],
                                               start=True, stop=True)
                    ins.then_inc(t_as, 1)
                pe.wait_ge(v["s"], 5 * ch + 1)
                for h in range(8):
                    ins = nc.tensor.matmul(ps[rows, 1, 64 * h:64 * h + 64], iQ[:, 2 * tt + h // 4, h % 4, rows],
                                           rbuf[:, tt, 64 * h:64 * h + 64], start=True, stop=True)
                ins.then_inc(t_u, 1)
                if ch < NC - 1:
                    pe.wait_ge(a["s"], ch + 1)
                    for i in range(4):
                        cols = slice(P * i, P * i + P)
                        nc.tensor.matmul(ps[:, 2, cols], bend_t[rows, tt, cols], ubuf[rows, tt, cols], start=True, stop=False)
                        ins = nc.tensor.matmul(ps[:, 2, cols], kend_t[rows, tt, cols], vtok[rows, tt, cols],
                                               start=False, stop=True)
                    ins.then_inc(t_ds, 1)
            pe.wait_ge(a["s"], NC)
            mixer_out(1)

            c = Counter(pe, t["o"])

            def turned(tt):
                pe.wait_ge(v["y"], STEP[f"y.done{tt}"])
                for k in range(KT):
                    o = (k % 2) * 256 + tt * P
                    ins = nc.tensor.transpose(ps[:, k // 2, o:o + P], ytok[:, tt, k::8], ident[:, :])
                    if k % 2:
                        c.mark(ins)

            turned(0)
            for j in range(2):
                ins = nc.tensor.matmul(ps[:, 6 + j, :], ones[:, :], macc[:, 2, 512 * j:512 * j + 512], start=True, stop=True)
            ins.then_inc(t_ada, 1)
            pe.wait_ge(wout_in, 64)
            pe.wait_ge(a["o"], STEP["o.hT0"])
            for j in range(4):
                if j == 1:
                    turned(1)
                    c.at("o.t")
                if j == 2:
                    pe.wait_ge(v["o"], STEP["o.gate"])
                    pe.wait_ge(a["o"], STEP["o.hT1"])
                for k in range(KT):
                    w = ring[:, k // 2, :].rearrange("p (t n) -> p t n", t=2)[:, k % 2, 512 * (j % 2):512 * (j % 2) + 512]
                    ins = nc.tensor.matmul(ps[:, 4 + j, :], hT[:, k, P * (j // 2):P * (j // 2) + P], w,
                                           start=k == 0, stop=k == KT - 1)
                ins.then_inc(t_out, 1)
            t_norm(pe, "q")
            c = Counter(pe, t["e"])
            pe.wait_ge(rt_in, 64)
            pe.wait_ge(a["q"], STEP["q.a"])
            pe.wait_ge(v["q"], STEP["q.v"])
            for tt in range(TT):
                for k in range(KT):
                    ins = nc.tensor.matmul(ps[:, 7, 64 * tt:64 * tt + 36], hT[:, k, P * tt:P * tt + P], w_rt[:, k, :],
                                           start=k == 0, stop=k == KT - 1)
            c.mark(ins)
            c.at("e.rt")
            t_zero(pe)
            pe.wait_ge(v_lo, 2)

            def gate_up(m, e, tt, first=False):
                s0 = 3 * (e % 2)
                x2 = 2 * (E_BODY * m + e)
                if tt == 0:
                    pe.wait_ge(g_gate, E_BODY * m + e + 1)
                    pe.wait_ge(v_gate_up, E_BODY * m + e + 1)
                if not first:
                    pe.wait_ge(v_eact, x2 + tt - 1)
                o = ps[:, 4 + tt, :].rearrange("p (i n) -> p i n", i=2)
                tok = slice(P * tt, P * tt + P)
                for k in range(KT):
                    cols = slice(FE * k, FE * k + FE)
                    ins = mm3(o, hT_hi[:, k, tok], hT_lo[:, k, tok], gate_up_hi[e % 2][:, :, cols],
                              ring_lo[:, s0:s0 + 2, cols], start=k == 0, stop=k == KT - 1)
                ins.then_inc(t_gu, 1)

            def turn(m, e, tt, first=False):
                x4 = 4 * (E_BODY * m + e)
                pe.wait_ge(v_eact, 2 * (E_BODY * m + e) + tt + 1)
                if not first:
                    pe.wait_ge(v_eact_t, x4 + 2 * tt)
                for f in range(2):
                    ins = nc.tensor.transpose(ps[:, 6, FE * tt + P * f:FE * tt + P * f + P], eact[:, tt, f::2], ident[:, :])
                ins.then_inc(t_tr, 1)

            def down(m, e, tt):
                s_ = 3 * (e % 2) + 2
                if tt == 0:
                    pe.wait_ge(v_dn, E_BODY * m + e + 1)
                pe.wait_ge(v_eact_t, 4 * (E_BODY * m + e) + 2 * tt + 2)
                for f in range(2):
                    for h in range(2):
                        cols = slice(D * f + 512 * h, D * f + 512 * h + 512)
                        ins = mm3(ps[:, 2 * tt + h, :], eact_hi[:, tt, f, :], eact_lo[:, tt, f, :], moe_hi[s_][:, cols],
                                  ring_lo[:, s_, cols])
                ins.then_inc(t_dn, 1)

            def modulation_row(m, i):
                if i == 0:
                    pe.wait_ge(v_ada2, 24 * m + 24 + CREDIT)
                pe.wait_ge(v_mod, 6 * m + i + CREDIT)
                nc.tensor.matmul(ps[:, 7, :], ones[:, :], macc[:, i // 2, 512 * (i % 2):512 * (i % 2) + 512],
                                 start=True, stop=True).then_inc(t_mod, 1)

            def expert(m, j):
                row = {7: (0, 1, 2, 3), 8: (4, 5)}.get(j, ())
                gate_up(m, j, 0)
                if len(row) > 0:
                    modulation_row(m, row[0])
                turn(m, j - 1, 1)
                down(m, j - 1, 0)
                if len(row) > 1:
                    modulation_row(m, row[1])
                gate_up(m, j, 1)
                turn(m, j, 0)
                if len(row) > 2:
                    modulation_row(m, row[2])
                down(m, j - 1, 1)
                if len(row) > 3:
                    modulation_row(m, row[3])

            gate_up(0, 0, 0, first=True)
            gate_up(0, 0, 1, first=True)
            turn(0, 0, 0, first=True)
            with pe.Fori(0, LAST_PASS) as m:
                for j in range(1, E_BODY + 1):
                    expert(m, j)
            for j in range(1, E_BODY):
                expert(LAST_PASS, j)
            turn(LAST_PASS, E_BODY - 1, 1)
            modulation_row(LAST_PASS, 4)
            down(LAST_PASS, E_BODY - 1, 0)
            modulation_row(LAST_PASS, 5)
            down(LAST_PASS, E_BODY - 1, 1)
            pe.wait_ge(v["f"], STEP["f.mod"])
            t_norm(pe, "bn", after="f")
            pe.wait_ge(v["bn"], STEP["bn.v"])
            pe.wait_ge(a["bn"], STEP["bn.a"])
            pe.wait_ge(v_mod, 24 + CREDIT)
            def projection(i):
                pe.wait_ge(ring2[i % RING], 16 * (i // RING + 1))
                if i >= 2:
                    pe.wait_ge(a["bp"], i - 1)
                if i in (6, 7):
                    pe.wait_ge(v["bp"], i - 5)
                bank = bin_bank(i)
                w = ring[:, i % RING, :].rearrange("p (t n) -> p t n", t=8)
                for j in range(2):
                    for k in range(KT):
                        o = bank[:, 256 * j:256 * j + 256]
                        if i in (0, 1, 6, 7) or (i, j) == (8, 0):
                            ins = nc.tensor.matmul(o, w[:, k, P * j:P * j + P], hT[:, k, :], start=k == 0, stop=k == KT - 1)
                        elif i < 8:
                            ins = nc.tensor.matmul(o, hT[:, k, P * j:P * j + P], w[:, k, :], start=k == 0, stop=k == KT - 1)
                if i == 8:
                    for tt in range(TT):
                        for k in range(KT):
                            ins = nc.tensor.matmul(bank[:, 256 + P * tt:256 + P * tt + P], hT[:, k, P * tt:P * tt + P],
                                                   w[:, k, P:2 * P], start=k == 0, stop=k == KT - 1)
                ins.then_inc(t_bin, 1)

            c = Counter(pe, t["bg"])
            for k in range(KT):
                ins = nc.tensor.matmul(ps[0:16, 0, 0:256], w_glr[:, k, :], hT[:, k, :], start=k == 0, stop=k == KT - 1)
            c.mark(ins)
            c.at("bg.lr")
            projection(0)
            pe.wait_ge(a["bg"], STEP["bg.glr"])
            for i in range(2):
                ins = nc.tensor.matmul(ps[:, 1, 256 * i:256 * i + 256], w_gg[:, P * i:P * i + P], glr_t, start=True, stop=True)
            c.mark(ins)
            c.at("bg.z")
            projection(1)
            projection(2)
            projection(3)
            pe.wait_ge(a["bg"], STEP["bg.pad"])
            for tt in range(TT):
                tok = slice(P * tt, P * tt + P)
                for h in range(GLA_H):
                    ins = nc.tensor.matmul(ps[:, 2 + tt, P * h:P * h + P], ktz[:, h, tok], qg[:, h // 2, tok], start=True, stop=True)
                c.mark(ins)
                if tt == 0:
                    c.at("bg.at0")
            pe.wait_ge(v["bg"], STEP["bg.kend"])
            for tt in range(TT):
                for i in range(2):
                    ins = nc.tensor.transpose(ps[:, 0, 256 * tt + P * i:256 * tt + P * i + P], kend2[:, i, P * tt:P * tt + P], ident[:, :])
            c.mark(ins)
            c.at("bg.tr")
            projection(4)
            pe.wait_ge(a["bg"], STEP["bg.ket"])
            pe.wait_ge(v["bg"], STEP["bg.at"])
            for ch in range(NC - 1):
                rows, tt = slice(CH * (ch % 2), CH * (ch % 2) + CH), ch // 2
                for i in range(2):
                    ins = nc.tensor.matmul(ps[:, ds_bank[ch], 256 * i:256 * i + 256], ket[rows, tt, P * i:P * i + P],
                                           vg[rows, tt, 256 * i:256 * i + 256], start=True, stop=True)
            c.mark(ins)
            c.at("bg.ds")
            projection(5)
            projection(6)
            pe.wait_ge(v["bg"], STEP["bg.state"])
            for tt in range(TT):
                for i in range(2):
                    for hf in range(2):
                        ch = 2 * tt + hf
                        nc.tensor.matmul(ps[CH * hf:CH * hf + CH, tt, 256 * i:256 * i + 256], qg[:, i, CH * ch:CH * ch + CH],
                                         sg_state[:, ch, i, :], start=True, stop=False, skip_group_check=True)
                    for h in (2 * i, 2 * i + 1):
                        ins = nc.tensor.matmul(ps[:, tt, P * h:P * h + P], at[:, tt, h, :], vg[:, tt, P * h:P * h + P],
                                               start=False, stop=True, skip_group_check=True)
            c.mark(ins)
            c.at("bg.o")
            projection(7)
            projection(8)
            c = Counter(pe, t["bs"])
            pe.wait_ge(a["bp"], STEP["bp.a"])
            for j in range(6):
                hs = range(4 * j, 4 * j + 4) if j < 2 else range(2 * (j - 2), 2 * (j - 2) + 2)
                n = P if j < 2 else 2 * P
                for i, h in enumerate(hs):
                    q = slice(0, P) if j < 2 else slice(P, 2 * P)
                    ins = nc.tensor.matmul(ps[:, bs_bank[j], n * i:n * i + n], sq_t[:, h // 2, q], kz[:, h // 4, h % 2, 0:n],
                                           start=True, stop=True)
                c.mark(ins)
                if j == 0:
                    c.at("bs.s0")
            for j in range(6):
                if j in (0, 2):
                    pe.wait_ge(a["bs"], STEP[f"bs.exp{j // 2}"])
                for i in range(4):
                    n = 4 * j + i
                    h, o = (n, 0) if n < 8 else ((n - 8) // 2, P + P * (n % 2))
                    ins = nc.tensor.transpose(ps[:, bs_bank[j], P * i:P * i + P], sc[:, h, o:o + P], ident[:, :])
                c.mark(ins)
                if j == 0:
                    c.at("bs.pt0")
            pe.wait_ge(a["bs"], STEP["bs.pt"])
            for h in range(SWA_H):
                kv = slice(64 * (h // 4), 64 * (h // 4) + 64)
                nc.tensor.matmul(ps[:, 0, 64 * h:64 * h + 64], p_t[:, h, :], svt[:, 0, kv], start=True, stop=True)
                for r in range(2):
                    ins = nc.tensor.matmul(ps[:, 1, 64 * h:64 * h + 64], p_t[:, 8 + 2 * h + r, :], svt[:, r, kv],
                                           start=r == 0, stop=r == 1)
            c.mark(ins)
            c.at("bs.o")
            c = Counter(pe, t["bo"])
            pe.wait_ge(v["bs"], STEP["bs.y"])
            for k in range(KT):
                for tt in range(TT):
                    o = (k % 2) * 256 + tt * P
                    ins = nc.tensor.transpose(ps[:, k // 2, o:o + P], y2[:, tt, k::8], ident[:, :])
                if k % 2:
                    c.mark(ins)
            pe.wait_ge(g["bg"], STEP["bg.lo"])
            for j in range(4):
                for k in range(KT):
                    if j == 0 and k % 2 == 0:
                        pe.wait_ge(v["bo"], k // 2 + 1)
                    cols = slice(D * (k % 2) + 512 * (j % 2), D * (k % 2) + 512 * (j % 2) + 512)
                    tok = slice(P * (j // 2), P * (j // 2) + P)
                    ins = mm3(ps[:, 4 + j, :], gT_hi[:, k, tok], hT_lo[:, k, tok], out_hi[k // 2][:, cols],
                              ring_lo[:, (9 + k // 2) % RING, cols], start=k == 0, stop=k == KT - 1)
                ins.then_inc(t_bout, 1)
            t_norm(pe, "l0")
            t_mlp_loop(pe, 0)
            pe.wait_ge(cols_in, 16)
            nc.tensor.transpose(ps[:, 4, 0:16], prm[0:16, :], ident[0:16, 0:16]).then_inc(t_cols, 1)
            t_norm(pe, "pn", tiles=True, after="l0")
            c = Counter(pe, t["pp"])
            pe.wait_ge(g["pp"], STEP["pp.g"])
            pe.wait_ge(v["pp"], STEP["pp.h"])
            pe.wait_ge(pool_in, 32)
            for j in range(4):
                for i in range(2):
                    gi = 2 * (j % 2) + i
                    for r in range(2):
                        ins = nc.tensor.matmul(ps[:, 4 + j, 256 * i:256 * i + 256], hT[:, 2 * gi + r, P * (j // 2):P * (j // 2) + P],
                                               poolw[:, gi, r, :], start=r == 0, stop=r == 1)
                c.mark(ins)
            c.at("pp.mm")
            t_norm(pe, "l1")
            t_mlp_loop(pe, 1)


_INS = [
    "x", "c", "ada_w", "ada_b", "mix_norm_w", "w_in", "rwkv_mu", "rwkv_w0", "rwkv_w_up", "rwkv_a0",
    "rwkv_a_up", "rwkv_g_up", "rwkv_k_k", "rwkv_k_a", "rwkv_r_k", "rwkv_gn_w", "rwkv_gn_b", "mlstm_conv_w",
    "mlstm_conv_b", "mlstm_i_b", "mlstm_f_b", "mlstm_hn_w", "w_out", "ffn_norm_w", "moe_w_group",
    "moe_b_group", "moe_w_router", "moe_b_router", "moe_w_gate", "moe_w_up", "moe_w_down", "final_norm_w",
    "c_2", "norm_w_2", "ada_w_2", "ada_b_2", "attn_w_in_2", "gla_w_gate_2", "gla_b_gate_2", "gla_norm_w_2",
    "attn_sinks_2", "attn_w_out_2", "rel_bias_2", "pool_w_2", "pool_scale_2", "mlp_w1_2", "mlp_w2_2",
    "final_norm_w_2",
]


def distance_buckets():
    import numpy as np

    half = N_BUCKETS // 2
    dist = 2 * WINDOW - 1 - np.arange(3 * P)
    far = half + (np.log(np.maximum(dist, 1) / half) / np.log(MAX_DIST / half) * half).astype(np.int32)
    bucket = np.where(dist < half, dist, np.minimum(far, N_BUCKETS - 1))
    row = np.where((dist >= 0) & (dist < WINDOW), bucket, N_BUCKETS)
    return (np.arange(N_BUCKETS + 1)[:, None] == row[None, :]).astype(np.float32)


def kernel(**inputs):
    import numpy as _np
    import concourse.bacc as _bacc
    from concourse import mybir as _mybir
    from concourse.bass_utils import run_bass_kernel_spmd as _run

    nc = _bacc.Bacc("TRN2", target_bir_lowering=False, num_devices=1)
    arrays, A = {}, {}
    for name in _INS + ["hots"]:
        a = distance_buckets() if name == "hots" else _np.ascontiguousarray(inputs[name])
        arrays[f"in_{name}_dram"] = a
        A[name] = nc.dram_tensor(f"in_{name}_dram", a.shape, _mybir.dt.from_np(a.dtype), kind="ExternalInput").ap()
    out = nc.dram_tensor("out_0_dram", (1, SEQ, D), F32, kind="ExternalOutput").ap()
    program(nc, A, out)
    r = _run(nc, [arrays], core_ids=[0])
    return r.results[0]["out_0_dram"]
```
